# Optimizing a Trainium2 kernel written in Bass

```python
import math
import jax
import jax.numpy as jnp
from jax import lax
import numpy as np
import jax, jax.numpy as jnp

D_MODEL = 1024
BATCH = 1
SEQ = 512
DEPTH = 2

N_MIXERS = 2
N_HYENA = (DEPTH + 1) // 2
N_RWKV = DEPTH // 2
RMS_EPS = 1e-6

HY_ORDER = 2
HY_N_PROJ = HY_ORDER + 1
HY_SHORT_CONV = 3
HY_EMB = 33
HY_BANDS = (HY_EMB - 1) // 2
HY_FILTER_WIDTH = 64
HY_DECAY_TARGET = 1e-2
HY_FAST_DECAY_PCT = 0.3
HY_SLOW_DECAY_PCT = 1.5

RW_HEAD = 64
RW_HEADS = D_MODEL // RW_HEAD
RW_DECAY_LORA = 64
RW_ICLR_LORA = 64
RW_VRES_LORA = 32
RW_GATE_LORA = 128
RW_GN_EPS = RW_HEAD * 1e-5
RW_N_LERP = 6

D_FF = ((8 * D_MODEL // 3 + 255) // 256) * 256
FFN_CONV = 3


def _rmsnorm(x, g):
    x32 = x.astype(jnp.float32)
    y = x32 * lax.rsqrt(jnp.mean(x32 * x32, axis=-1, keepdims=True) + RMS_EPS)
    return (y * g.astype(jnp.float32)).astype(x.dtype)

def _dwconv_centred(x, w, b):
    K, C = w.shape
    y = lax.conv_general_dilated(
        x, w[:, None, :].astype(x.dtype), window_strides=(1,),
        padding=((K // 2, K // 2),), dimension_numbers=('NWC', 'WIO', 'NWC'),
        feature_group_count=C)
    return y + b.astype(x.dtype)

def _hyena_filter(L, w1, b1, w2, b2, w3, b3, w4, freq):
    f32 = jnp.float32
    n = jnp.arange(L, dtype=f32)
    t = (n / max(L - 1, 1))[:, None]
    fr = jnp.linspace(1e-4, HY_BANDS - 1, HY_BANDS, dtype=f32)
    ang = (2.0 * math.pi / L) * n[:, None] * fr[None, :]
    z = jnp.concatenate([t, jnp.cos(ang), -jnp.sin(ang)], axis=-1)
    fq = freq.astype(f32)
    hdn = jnp.sin(fq * (z @ w1.astype(f32) + b1.astype(f32)))
    hdn = jnp.sin(fq * (hdn @ w2.astype(f32) + b2.astype(f32)))
    hdn = jnp.sin(fq * (hdn @ w3.astype(f32) + b3.astype(f32)))
    k = hdn @ w4.astype(f32)
    D = w4.shape[-1] // 2
    deltas = jnp.abs(jnp.linspace(math.log(HY_DECAY_TARGET) / HY_SLOW_DECAY_PCT,
                                  math.log(HY_DECAY_TARGET) / HY_FAST_DECAY_PCT, D, dtype=f32))
    k = k * jnp.exp(-t * jnp.tile(deltas, 2)[None, :])
    return k[:, :D], k[:, D:]

def _bidir_fftconv(u, k_fwd, k_bwd):
    L = u.shape[1]
    n = 2 * L
    D = k_fwd.shape[1]
    k_c = jnp.concatenate([k_fwd.at[0].add(k_bwd[0]),
                           jnp.zeros((1, D), jnp.float32),
                           k_bwd[:0:-1]], axis=0)
    kf = jnp.fft.rfft(k_c, n=n, axis=0)
    uf = jnp.fft.rfft(u, n=n, axis=1)
    return jnp.fft.irfft(uf * kf[None], n=n, axis=1)[:, :L]

def _hyena_mixer(h, w_in, b_in, conv_w, conv_b, f_w1, f_b1, f_w2, f_b2, f_w3, f_b3,
                 f_w4, f_freq, skip, w_out, b_out):
    B, L, D = h.shape
    z = _dwconv_centred(h @ w_in + b_in, conv_w, conv_b)
    x0, x1, v = jnp.split(z, HY_N_PROJ, axis=-1)
    k_fwd, k_bwd = _hyena_filter(L, f_w1, f_b1, f_w2, f_b2, f_w3, f_b3, f_w4, f_freq)
    u = (v * x1).astype(jnp.float32)
    y = _bidir_fftconv(u, k_fwd, k_bwd) + u * skip.astype(jnp.float32)
    y = y.astype(h.dtype) * x0
    return y @ w_out + b_out

def _token_shift_delta(h):
    prev = jnp.pad(h[:, :-1], ((0, 0), (1, 0), (0, 0)))
    nxt = jnp.pad(h[:, 1:], ((0, 0), (0, 1), (0, 0)))
    return 0.5 * (prev + nxt) - h

def _decay(xw, w0, w1, w2):
    wl = w0.astype(jnp.float32) + (jnp.tanh(xw @ w1) @ w2).astype(jnp.float32)
    wl = -jax.nn.softplus(-wl) - 0.5
    return jnp.exp(-jnp.exp(wl))

def _wkv7_scan(r, w, k, v, kk, a):
    B, L, H, N = r.shape

    def step(state, inp):
        r_t, w_t, k_t, v_t, kk_t, a_t = inp
        sa = jnp.einsum('bhvk,bhk->bhv', state, kk_t)
        state = (state * w_t[:, :, None, :]
                 - sa[..., None] * (kk_t * a_t)[:, :, None, :]
                 + v_t[..., None] * k_t[:, :, None, :])
        return state, jnp.einsum('bhvk,bhk->bhv', state, r_t)

    xs = tuple(jnp.swapaxes(t, 0, 1) for t in (r, w, k, v, kk, a))
    s0 = jnp.zeros((B, H, N, N), jnp.float32)
    _, ys = lax.scan(step, s0, xs)
    return jnp.swapaxes(ys, 0, 1)

def _rwkv7_mixer(h, v_first, mu, w_r, w_k, w_v, w_o, w0, w1, w2, a0, a1, a2,
                 g1, g2, k_k, k_a, r_k, ln_w, ln_b, vres):
    B, L, D = h.shape
    H, N = RW_HEADS, RW_HEAD
    f32 = jnp.float32
    xx = _token_shift_delta(h)
    xr, xw, xk, xv, xa, xg = [h + xx * mu[j] for j in range(RW_N_LERP)]
    r = xr @ w_r
    k = xk @ w_k
    v = xv @ w_v
    a = jax.nn.sigmoid(a0 + (xa @ a1) @ a2)
    g = jax.nn.sigmoid(xg @ g1) @ g2
    if vres is None:
        v_first = v
    else:
        v0, v1, v2 = vres
        v = v + (v_first - v) * jax.nn.sigmoid(v0 + (xv @ v1) @ v2)

    def heads(t):
        return t.astype(f32).reshape(B, L, H, N)

    kk = heads(k * k_k)
    kk = kk / jnp.maximum(jnp.linalg.norm(kk, axis=-1, keepdims=True), 1e-12)
    k = k * (1.0 + (a - 1.0) * k_a)
    rh, kh, vh, ah = heads(r), heads(k), heads(v), heads(a)
    w_f = heads(_decay(xw, w0[0], w1[0], w2[0]))
    w_b = heads(_decay(xw, w0[1], w1[1], w2[1]))

    def flip(t):
        return jnp.flip(t, axis=1)

    y = _wkv7_scan(rh, w_f, kh, vh, kk, ah)
    y = y + flip(_wkv7_scan(flip(rh), flip(w_b), flip(kh), flip(vh), flip(kk), flip(ah)))
    mean = jnp.mean(y, axis=-1, keepdims=True)
    var = jnp.mean(jnp.square(y - mean), axis=-1, keepdims=True)
    y = ((y - mean) * lax.rsqrt(var + RW_GN_EPS)).reshape(B, L, D)
    y = y * ln_w.astype(f32) + ln_b.astype(f32)
    bonus = jnp.sum(rh * kh * r_k.astype(f32), axis=-1, keepdims=True) * vh
    y = y + bonus.reshape(B, L, D)
    return (y.astype(h.dtype) * g) @ w_o, v_first

def _conv_ffn(h, w_up, conv_w, conv_b, w_down):
    u = _dwconv_centred(h @ w_up, conv_w, conv_b)
    gate, val = jnp.split(u, 2, axis=-1)
    return (jax.nn.silu(gate) * val) @ w_down

def first_inputs(seed: int = 0) -> dict:
    key = jax.random.key(seed)
    ks = iter(jax.random.split(key, 64))
    f32 = jnp.float32

    def nrm(shape, scale):
        return scale * jax.random.normal(next(ks), shape, f32)

    D, F, W = D_MODEL, D_FF, HY_FILTER_WIDTH
    NH, NR = N_HYENA, N_RWKV
    C3 = HY_N_PROJ * D
    ramp = (jnp.arange(D, dtype=f32) / (D - 1)) ** 0.85
    return {
        'x': nrm((BATCH, SEQ, D), 1.0),
        'norm_mix_g': 1.0 + nrm((DEPTH, D), 0.02),
        'norm_ffn_g': 1.0 + nrm((DEPTH, D), 0.02),
        'final_norm_g': 1.0 + nrm((D,), 0.02),
        'hy_w_in': nrm((NH, D, C3), D ** -0.5),
        'hy_b_in': nrm((NH, C3), 0.02),
        'hy_conv_w': nrm((NH, HY_SHORT_CONV, C3), HY_SHORT_CONV ** -0.5),
        'hy_conv_b': nrm((NH, C3), 0.02),
        'hy_f_w1': nrm((NH, HY_EMB, W), HY_EMB ** -0.5),
        'hy_f_b1': nrm((NH, W), 0.1),
        'hy_f_w2': nrm((NH, W, W), W ** -0.5),
        'hy_f_b2': nrm((NH, W), 0.1),
        'hy_f_w3': nrm((NH, W, W), W ** -0.5),
        'hy_f_b3': nrm((NH, W), 0.1),
        'hy_f_w4': nrm((NH, W, 2 * D), 0.01),
        'hy_f_freq': 1.0 + nrm((NH, W), 0.1),
        'hy_skip': nrm((NH, D), 1.0),
        'hy_w_out': nrm((NH, D, D), D ** -0.5),
        'hy_b_out': nrm((NH, D), 0.02),
        'rw_mu': jax.random.uniform(next(ks), (NR, RW_N_LERP, D), f32),
        'rw_w_r': nrm((NR, D, D), D ** -0.5),
        'rw_w_k': nrm((NR, D, D), D ** -0.5),
        'rw_w_v': nrm((NR, D, D), D ** -0.5),
        'rw_w_o': nrm((NR, D, D), D ** -0.5),
        'rw_w0': -6.5 + 5.0 * ramp + nrm((NR, 2, D), 0.1),
        'rw_w1': nrm((NR, 2, D, RW_DECAY_LORA), D ** -0.5),
        'rw_w2': nrm((NR, 2, RW_DECAY_LORA, D), 0.5 * RW_DECAY_LORA ** -0.5),
        'rw_a0': nrm((NR, D), 0.1),
        'rw_a1': nrm((NR, D, RW_ICLR_LORA), D ** -0.5),
        'rw_a2': nrm((NR, RW_ICLR_LORA, D), 0.5 * RW_ICLR_LORA ** -0.5),
        'rw_v0': 1.0 + nrm((NR - 1, D), 0.1),
        'rw_v1': nrm((NR - 1, D, RW_VRES_LORA), D ** -0.5),
        'rw_v2': nrm((NR - 1, RW_VRES_LORA, D), 0.5 * RW_VRES_LORA ** -0.5),
        'rw_g1': nrm((NR, D, RW_GATE_LORA), D ** -0.5),
        'rw_g2': nrm((NR, RW_GATE_LORA, D), RW_GATE_LORA ** -0.5),
        'rw_k_k': 0.85 + nrm((NR, D), 0.02),
        'rw_k_a': 1.0 + nrm((NR, D), 0.02),
        'rw_r_k': -0.04 + nrm((NR, RW_HEADS, RW_HEAD), 0.1),
        'rw_ln_w': 1.0 + nrm((NR, D), 0.02),
        'rw_ln_b': nrm((NR, D), 0.02),
        'ff_w_up': nrm((DEPTH, D, 2 * F), D ** -0.5),
        'ff_conv_w': nrm((DEPTH, FFN_CONV, 2 * F), FFN_CONV ** -0.5),
        'ff_conv_b': nrm((DEPTH, 2 * F), 0.02),
        'ff_w_down': nrm((DEPTH, F, D), F ** -0.5),
    }

def first_block(x, norm_mix_g, norm_ffn_g, final_norm_g,
              hy_w_in, hy_b_in, hy_conv_w, hy_conv_b,
              hy_f_w1, hy_f_b1, hy_f_w2, hy_f_b2, hy_f_w3, hy_f_b3, hy_f_w4, hy_f_freq,
              hy_skip, hy_w_out, hy_b_out,
              rw_mu, rw_w_r, rw_w_k, rw_w_v, rw_w_o, rw_w0, rw_w1, rw_w2,
              rw_a0, rw_a1, rw_a2, rw_v0, rw_v1, rw_v2, rw_g1, rw_g2,
              rw_k_k, rw_k_a, rw_r_k, rw_ln_w, rw_ln_b,
              ff_w_up, ff_conv_w, ff_conv_b, ff_w_down):
    v_first = None
    for i in range(DEPTH):
        h = _rmsnorm(x, norm_mix_g[i])
        j = i // N_MIXERS
        if i % N_MIXERS == 0:
            y = _hyena_mixer(h, hy_w_in[j], hy_b_in[j], hy_conv_w[j], hy_conv_b[j],
                             hy_f_w1[j], hy_f_b1[j], hy_f_w2[j], hy_f_b2[j],
                             hy_f_w3[j], hy_f_b3[j], hy_f_w4[j], hy_f_freq[j],
                             hy_skip[j], hy_w_out[j], hy_b_out[j])
        else:
            vres = (rw_v0[j - 1], rw_v1[j - 1], rw_v2[j - 1]) if j > 0 else None
            y, v_first = _rwkv7_mixer(h, v_first, rw_mu[j], rw_w_r[j], rw_w_k[j], rw_w_v[j], rw_w_o[j],
                                      rw_w0[j], rw_w1[j], rw_w2[j], rw_a0[j], rw_a1[j], rw_a2[j],
                                      rw_g1[j], rw_g2[j], rw_k_k[j], rw_k_a[j], rw_r_k[j],
                                      rw_ln_w[j], rw_ln_b[j], vres)
        x = x + y
        h = _rmsnorm(x, norm_ffn_g[i])
        x = x + _conv_ffn(h, ff_w_up[i], ff_conv_w[i], ff_conv_b[i], ff_w_down[i])
    return _rmsnorm(x, final_norm_g)


_first_inputs = first_inputs


def first_inputs(seed=0):
    import zlib

    import numpy as np

    out = dict(_first_inputs(seed))
    spreads = {}
    factors = {'norm_ffn_g': 3.204,
     'final_norm_g': 9.024,
     'hy_b_out': 2.838,
     'rw_w1': 5.03,
     'rw_w2': 4.976,
     'rw_a0': 4.448,
     'rw_k_k': 64.0,
     'rw_k_a': 20.231,
     'rw_ln_w': 39.858,
     'rw_ln_b': 36.951,
     'ff_conv_b': 3.385}
    for name, (base, spread) in spreads.items():
        noise = np.random.default_rng([zlib.crc32(name.encode()), seed]).standard_normal(out[name].shape)
        drawn = base * np.exp(spread * noise) if base else spread * noise
        out[name] = jnp.asarray(drawn.astype(out[name].dtype))
    for name, factor in factors.items():
        out[name] = (out[name] * factor).astype(out[name].dtype)
    return out


_narrow_inputs = first_inputs


def first_inputs(seed=0):

    out = dict(_narrow_inputs(seed))
    wider = {'final_norm_g': 3.39, 'rw_k_k': 6.14, 'rw_ln_w': 3.3, 'rw_ln_b': 3.27}
    for name, times in wider.items():
        mean = out[name].mean()
        out[name] = (mean + times * (out[name] - mean)).astype(out[name].dtype)
    return out


DEPTH_2 = 1

MLA_HEADS = 4
QK_NOPE_DIM = 64
QK_ROPE_DIM = 32
V_HEAD_DIM = 64
Q_RANK = D_MODEL // 4
KV_RANK = D_MODEL // 8
ROPE_BASE = 10000.0
Q_BLOCK = 128
SG_GROUPS = 4
SG_WIDTH = D_MODEL // 4
SG_CHUNK = 128
CONV_WIDTH = D_MODEL // 4
CONV_K = 3
POOL_WINDOWS = (2, 4, 8, 16)
POOL_WIDTH = D_MODEL // 4
POOL_GROUP = POOL_WIDTH // 4
N_BRANCH = 4
D_FF_2 = 4 * D_MODEL
EPS = 1e-6
N_IN = Q_RANK + KV_RANK + QK_ROPE_DIM + 2 * SG_WIDTH + 3 * CONV_WIDTH + POOL_WIDTH + N_BRANCH * D_MODEL


def rmsnorm(x, g):
    xf = x.astype(jnp.float32)
    y = xf * lax.rsqrt(jnp.mean(xf * xf, axis=-1, keepdims=True) + EPS)
    return (y * g.astype(jnp.float32)).astype(x.dtype)

def layernorm(x, g, b):
    xf = x.astype(jnp.float32)
    mu = jnp.mean(xf, axis=-1, keepdims=True)
    xc = xf - mu
    y = xc * lax.rsqrt(jnp.mean(xc * xc, axis=-1, keepdims=True) + EPS)
    return (y * g.astype(jnp.float32) + b.astype(jnp.float32)).astype(x.dtype)

def split_cols(proj):
    sizes = (Q_RANK, KV_RANK, QK_ROPE_DIM, SG_WIDTH, SG_WIDTH, CONV_WIDTH, CONV_WIDTH, CONV_WIDTH,
             POOL_WIDTH, N_BRANCH * D_MODEL)
    offs = []
    acc = 0
    for s in sizes[:-1]:
        acc += s
        offs.append(acc)
    return jnp.split(proj, offs, axis=-1)

def rope(x, cos, sin):
    x1, x2 = jnp.split(x, 2, axis=-1)
    return jnp.concatenate([x1 * cos - x2 * sin, x2 * cos + x1 * sin], axis=-1)

def mla(c_q, c_kv, k_rope, positions, q_norm, w_uq, kv_norm, w_ukv):
    B_, S_, _ = c_q.shape
    q = (rmsnorm(c_q, q_norm) @ w_uq).reshape(B_, S_, MLA_HEADS, QK_NOPE_DIM + QK_ROPE_DIM)
    q_nope, q_rope = q[..., :QK_NOPE_DIM], q[..., QK_NOPE_DIM:]
    kv = (rmsnorm(c_kv, kv_norm) @ w_ukv).reshape(B_, S_, MLA_HEADS, QK_NOPE_DIM + V_HEAD_DIM)
    k_nope, v = kv[..., :QK_NOPE_DIM], kv[..., QK_NOPE_DIM:]
    inv_freq = ROPE_BASE ** (-jnp.arange(0, QK_ROPE_DIM, 2, dtype=jnp.float32) / QK_ROPE_DIM)
    ang = positions.astype(jnp.float32)[..., None] * inv_freq
    cos = jnp.cos(ang).astype(q.dtype)
    sin = jnp.sin(ang).astype(q.dtype)
    q_rope = rope(q_rope, cos[:, :, None, :], sin[:, :, None, :])
    k_rope = rope(k_rope, cos, sin)
    scale = (QK_NOPE_DIM + QK_ROPE_DIM) ** -0.5
    nb = S_ // Q_BLOCK

    def to_blocks(a):
        return jnp.moveaxis(a.reshape((B_, nb, Q_BLOCK) + a.shape[2:]), 1, 0)

    k_idx = jnp.arange(S_)

    def block(args):
        qn, qr, start = args
        s = jnp.einsum('bqhd,bkhd->bhqk', qn, k_nope) + jnp.einsum('bqhr,bkr->bhqk', qr, k_rope)
        s = s.astype(jnp.float32) * scale
        q_idx = start + jnp.arange(Q_BLOCK)
        s = jnp.where(k_idx[None, :] <= q_idx[:, None], s, -jnp.inf)
        p = jax.nn.softmax(s, axis=-1).astype(v.dtype)
        return jnp.einsum('bhqk,bkhd->bqhd', p, v)

    starts = jnp.arange(nb, dtype=jnp.int32) * Q_BLOCK
    o = lax.map(block, (to_blocks(q_nope), to_blocks(q_rope), starts))
    return jnp.moveaxis(o, 0, 1).reshape(B_, S_, MLA_HEADS * V_HEAD_DIM)

def spatial_gating(u, v, ln_g, ln_b, w_s, b_s):
    B_, S_, _ = u.shape
    u = jax.nn.gelu(u)
    v = layernorm(jax.nn.gelu(v), ln_g, ln_b)
    n = S_ // SG_CHUNK
    vc = v.reshape(B_, n, SG_CHUNK, SG_GROUPS, SG_WIDTH // SG_GROUPS)
    mask = jnp.tril(jnp.ones((SG_CHUNK, SG_CHUNK), dtype=bool))
    w = jnp.where(mask, w_s, 0)
    s = jnp.einsum('gts,bnsgc->bntgc', w, vc) + b_s.T[:, :, None]
    return u * s.reshape(B_, S_, SG_WIDTH)

def short_conv(xin, bg, cg, conv_w):
    z = cg * xin
    S_ = z.shape[1]
    zp = jnp.pad(z, ((0, 0), (CONV_K - 1, 0), (0, 0)))
    y = sum(conv_w[k] * zp[:, k:k + S_] for k in range(CONV_K))
    return bg * y

def multiscale_pool(p, w_pool, scale):
    B_, S_, _ = p.shape
    pg = p.reshape(B_, S_, len(POOL_WINDOWS), POOL_GROUP).astype(jnp.float32)
    cs = jnp.cumsum(pg, axis=1)
    t = jnp.arange(S_)
    outs = []
    for g, win in enumerate(POOL_WINDOWS):
        c = cs[:, :, g]
        lagged = jnp.pad(c, ((0, 0), (win, 0), (0, 0)))[:, :S_]
        cnt = jnp.minimum(t + 1, win).astype(jnp.float32)[None, :, None]
        outs.append((c - lagged) / cnt - pg[:, :, g])
    pooled = jnp.stack(outs, axis=2).astype(p.dtype)
    mixed = jnp.einsum('bsgc,gcd->bsgd', pooled, w_pool)
    return mixed.reshape(B_, S_, POOL_WIDTH) * scale

def second_inputs(seed: int = 0) -> dict:
    key = jax.random.key(seed)
    ks = jax.random.split(key, 26)
    L = DEPTH_2

    def nrm(k, shape, fan_in):
        return jax.random.normal(k, shape, jnp.float32) * fan_in ** -0.5

    def gain(k, shape):
        return 1.0 + 0.05 * jax.random.normal(k, shape, jnp.float32)

    def small(k, shape, s):
        return s * jax.random.normal(k, shape, jnp.float32)

    x = jax.random.normal(ks[0], (BATCH, SEQ, D_MODEL), jnp.float32)
    positions = (jax.random.randint(ks[1], (BATCH, 1), 0, 4096, dtype=jnp.int32)
                 + jnp.arange(SEQ, dtype=jnp.int32)[None, :])
    return {
        'x': x,
        'positions': positions,
        'norm_mix_pre': gain(ks[2], (L, D_MODEL)),
        'w_in': nrm(ks[3], (L, D_MODEL, N_IN), D_MODEL),
        'gate_b': small(ks[4], (L, N_BRANCH * D_MODEL), 0.01),
        'q_norm': gain(ks[5], (L, Q_RANK)),
        'w_uq': nrm(ks[6], (L, Q_RANK, MLA_HEADS * (QK_NOPE_DIM + QK_ROPE_DIM)), Q_RANK),
        'kv_norm': gain(ks[7], (L, KV_RANK)),
        'w_ukv': nrm(ks[8], (L, KV_RANK, MLA_HEADS * (QK_NOPE_DIM + V_HEAD_DIM)), KV_RANK),
        'w_br_mla': nrm(ks[9], (L, MLA_HEADS * V_HEAD_DIM, D_MODEL), MLA_HEADS * V_HEAD_DIM),
        'sg_ln_g': gain(ks[10], (L, SG_WIDTH)),
        'sg_ln_b': small(ks[11], (L, SG_WIDTH), 0.02),
        'sg_w': nrm(ks[12], (L, SG_GROUPS, SG_CHUNK, SG_CHUNK), SG_CHUNK),
        'sg_b': gain(ks[13], (L, SG_GROUPS, SG_CHUNK)),
        'w_br_sg': nrm(ks[14], (L, SG_WIDTH, D_MODEL), SG_WIDTH),
        'conv_w': nrm(ks[15], (L, CONV_K, CONV_WIDTH), CONV_K),
        'w_br_conv': nrm(ks[16], (L, CONV_WIDTH, D_MODEL), CONV_WIDTH),
        'pool_w': nrm(ks[17], (L, len(POOL_WINDOWS), POOL_GROUP, POOL_GROUP), POOL_GROUP),
        'pool_scale': gain(ks[18], (L, POOL_WIDTH)),
        'w_br_pool': nrm(ks[19], (L, POOL_WIDTH, D_MODEL), POOL_WIDTH),
        'w_out': nrm(ks[20], (L, D_MODEL, D_MODEL), D_MODEL),
        'norm_mix_post': gain(ks[21], (L, D_MODEL)),
        'norm_ffn_pre': gain(ks[22], (L, D_MODEL)),
        'w_ff1': nrm(ks[23], (L, D_MODEL, D_FF_2), D_MODEL),
        'w_ff2': nrm(ks[24], (L, D_FF_2, D_MODEL), D_FF_2),
        'norm_ffn_post': gain(ks[25], (L, D_MODEL)),
    }

def second_block(x, positions, norm_mix_pre, w_in, gate_b, q_norm, w_uq, kv_norm, w_ukv, w_br_mla,
              sg_ln_g, sg_ln_b, sg_w, sg_b, w_br_sg, conv_w, w_br_conv, pool_w, pool_scale, w_br_pool,
              w_out, norm_mix_post, norm_ffn_pre, w_ff1, w_ff2, norm_ffn_post):
    B_, S_, D_ = x.shape
    for l in range(DEPTH_2):
        h = rmsnorm(x, norm_mix_pre[l])
        (c_q, c_kv, k_r, sg_u, sg_v, cv_x, cv_b, cv_c, pool_in, gate_pre) = split_cols(h @ w_in[l])
        gates = jax.nn.sigmoid(gate_pre + gate_b[l]).reshape(B_, S_, N_BRANCH, D_)
        y_a = mla(c_q, c_kv, k_r, positions, q_norm[l], w_uq[l], kv_norm[l], w_ukv[l]) @ w_br_mla[l]
        y_b = spatial_gating(sg_u, sg_v, sg_ln_g[l], sg_ln_b[l], sg_w[l], sg_b[l]) @ w_br_sg[l]
        y_c = short_conv(cv_x, cv_b, cv_c, conv_w[l]) @ w_br_conv[l]
        y_d = multiscale_pool(pool_in, pool_w[l], pool_scale[l]) @ w_br_pool[l]
        merged = (gates[:, :, 0] * y_a + gates[:, :, 1] * y_b
                  + gates[:, :, 2] * y_c + gates[:, :, 3] * y_d)
        x = x + rmsnorm(merged @ w_out[l], norm_mix_post[l])
        h = rmsnorm(x, norm_ffn_pre[l])
        f = jnp.square(jax.nn.relu(h @ w_ff1[l])) @ w_ff2[l]
        x = x + rmsnorm(f, norm_ffn_post[l])
    return x


_first_inputs_2 = second_inputs


def second_inputs(seed=0):
    import zlib

    import numpy as np

    out = dict(_first_inputs_2(seed))
    spreads = {}
    factors = {'gate_b': 8.0,
     'q_norm': 8.0,
     'kv_norm': 8.0,
     'sg_ln_g': 4.952,
     'sg_ln_b': 8.0,
     'sg_b': 3.712,
     'pool_scale': 2.803}
    for name, (base, spread) in spreads.items():
        noise = np.random.default_rng([zlib.crc32(name.encode()), seed]).standard_normal(out[name].shape)
        drawn = base * np.exp(spread * noise) if base else spread * noise
        out[name] = __import__('jax').numpy.asarray(drawn.astype(out[name].dtype))
    for name, factor in factors.items():
        out[name] = (out[name] * factor).astype(out[name].dtype)
    return out


_narrow_inputs_2 = second_inputs


def second_inputs(seed=0):

    out = dict(_narrow_inputs_2(seed))
    wider = {'sg_ln_g': 6.3, 'sg_ln_b': 10.56, 'sg_b': 6.23, 'pool_scale': 6.32}
    for name, times in wider.items():
        mean = out[name].mean()
        out[name] = (mean + times * (out[name] - mean)).astype(out[name].dtype)
    return out


DEPTH_3 = 1

CHUNK = 64
ATTN_HEADS = 8
HEAD_DIM = 64
ATTN_WIDTH = ATTN_HEADS * HEAD_DIM
CONV_WIDTH_3 = D_MODEL - ATTN_WIDTH
CONV_GROUPS = 8
CONV_KERNEL = 31
IDX_HEADS = 8
IDX_DIM = 64
TOPK_MAX = 256
ROT_DIM = HEAD_DIM // 4
ROPE_THETA = 500000.0
D_FF_3 = 4 * D_MODEL
N_MOD = 6
IN_SIZES = (ATTN_WIDTH, ATTN_WIDTH, ATTN_WIDTH, IDX_HEADS * IDX_DIM, IDX_DIM, IDX_HEADS, CONV_WIDTH_3, CONV_WIDTH_3)
IN_COLS = 3 * ATTN_WIDTH + IDX_HEADS * IDX_DIM + IDX_DIM + IDX_HEADS + 2 * CONV_WIDTH_3


def _split_points():
    pts, acc = [], 0
    for s in IN_SIZES[:-1]:
        acc += s
        pts.append(acc)
    return pts

def rms_norm(x, g):
    xf = x.astype(jnp.float32)
    y = xf * lax.rsqrt(jnp.mean(xf * xf, axis=-1, keepdims=True) + EPS)
    return (y * g.astype(jnp.float32)).astype(x.dtype)

def layer_norm(x, g, b):
    xf = x.astype(jnp.float32)
    mu = jnp.mean(xf, axis=-1, keepdims=True)
    var = jnp.mean(jnp.square(xf - mu), axis=-1, keepdims=True)
    y = (xf - mu) * lax.rsqrt(var + EPS)
    return (y * g.astype(jnp.float32) + b.astype(jnp.float32)).astype(x.dtype)

def rope_tables(seq_len, dtype):
    pos = jnp.arange(seq_len, dtype=jnp.float32)
    inv_freq = ROPE_THETA ** (-jnp.arange(0, ROT_DIM, 2, dtype=jnp.float32) / ROT_DIM)
    ang = pos[:, None] * inv_freq[None, :]
    return jnp.cos(ang).astype(dtype), jnp.sin(ang).astype(dtype)

def partial_rope(x, cos, sin):
    half = ROT_DIM // 2
    x1 = x[..., :half]
    x2 = x[..., half:ROT_DIM]
    c = cos[None, :, None, :]
    s = sin[None, :, None, :]
    return jnp.concatenate([x1 * c - x2 * s, x2 * c + x1 * s, x[..., ROT_DIM:]], axis=-1)

def dsa_sparse_attention(q, k, v, iq, ik, iw):
    B, S, H, dh = q.shape
    n_blk = S // Q_BLOCK
    top_k = min(TOPK_MAX, S // 4)
    key_chunk = jnp.arange(S) // CHUNK
    ik_f = ik.astype(jnp.float32)

    def block(i):
        start = i * Q_BLOCK
        q_b = lax.dynamic_slice_in_dim(q, start, Q_BLOCK, axis=1)
        iq_b = lax.dynamic_slice_in_dim(iq, start, Q_BLOCK, axis=1).astype(jnp.float32)
        iw_b = lax.dynamic_slice_in_dim(iw, start, Q_BLOCK, axis=1).astype(jnp.float32)
        q_chunk = (start + jnp.arange(Q_BLOCK)) // CHUNK
        admissible = key_chunk[None, :] <= q_chunk[:, None]
        rel = jax.nn.relu(jnp.einsum('bthd,bsd->bths', iq_b, ik_f) * (IDX_DIM ** -0.5))
        score = jnp.einsum('bths,bth->bts', rel, iw_b)
        score = jnp.where(admissible[None], score, -jnp.inf)
        _, idx = lax.top_k(score, top_k)
        valid = key_chunk[idx] <= q_chunk[None, :, None]
        k_sel = jax.vmap(lambda kb, ib: kb[ib])(k, idx)
        v_sel = jax.vmap(lambda vb, ib: vb[ib])(v, idx)
        logits = jnp.einsum('bthd,btkhd->bthk', q_b, k_sel).astype(jnp.float32) * (dh ** -0.5)
        logits = jnp.where(valid[:, :, None, :], logits, -jnp.inf)
        p = jax.nn.softmax(logits, axis=-1).astype(v.dtype)
        return jnp.einsum('bthk,btkhd->bthd', p, v_sel)

    out = lax.map(block, jnp.arange(n_blk))
    return jnp.transpose(out, (1, 0, 2, 3, 4)).reshape(B, S, H * dh)

def conformer_conv(a, g, w_dw, b_dw, ln_g, ln_b):
    u = a * jax.nn.sigmoid(g)
    u = jnp.pad(u, ((0, 0), (CONV_KERNEL - 1, 0), (0, 0)))
    y = lax.conv_general_dilated(u, w_dw[:, None, :], window_strides=(1,), padding='VALID',
                                 dimension_numbers=('NWC', 'WIO', 'NWC'),
                                 feature_group_count=CONV_WIDTH_3) + b_dw
    y = layer_norm(y, ln_g, ln_b)
    return jax.nn.silu(y)

def third_inputs(seed: int = 0) -> dict:
    key = jax.random.key(seed)
    ks = jax.random.split(key, 20)

    def nrm(k, shape, scale):
        return jax.random.normal(k, shape, jnp.float32) * scale

    L = DEPTH_3
    return {
        "x": nrm(ks[0], (BATCH, SEQ, D_MODEL), 1.0),
        "c": nrm(ks[1], (BATCH, D_MODEL), 1.0),
        "w_ada": nrm(ks[2], (L, D_MODEL, N_MOD * D_MODEL), 0.5 * D_MODEL ** -0.5),
        "b_ada": nrm(ks[3], (L, N_MOD * D_MODEL), 0.02),
        "g_norm1": 1.0 + nrm(ks[4], (L, D_MODEL), 0.02),
        "w_in": nrm(ks[5], (L, D_MODEL, IN_COLS), D_MODEL ** -0.5),
        "g_q": 1.0 + nrm(ks[6], (L, HEAD_DIM), 0.02),
        "g_k": 1.0 + nrm(ks[7], (L, HEAD_DIM), 0.02),
        "w_dw": nrm(ks[8], (L, CONV_KERNEL, CONV_WIDTH_3), CONV_KERNEL ** -0.5),
        "b_dw": nrm(ks[9], (L, CONV_WIDTH_3), 0.02),
        "g_conv_ln": 1.0 + nrm(ks[10], (L, CONV_WIDTH_3), 0.02),
        "b_conv_ln": nrm(ks[11], (L, CONV_WIDTH_3), 0.02),
        "g_out_attn": 1.0 + nrm(ks[12], (L, ATTN_WIDTH), 0.02),
        "g_out_conv": 1.0 + nrm(ks[13], (L, CONV_WIDTH_3), 0.02),
        "w_out": nrm(ks[14], (L, D_MODEL, D_MODEL), D_MODEL ** -0.5),
        "g_norm2": 1.0 + nrm(ks[15], (L, D_MODEL), 0.02),
        "w_ff1": nrm(ks[16], (L, D_MODEL, D_FF_3), D_MODEL ** -0.5),
        "w_ff2": nrm(ks[17], (L, D_FF_3, D_MODEL), D_FF_3 ** -0.5),
    }

def third_block(x, c, w_ada, b_ada, g_norm1, w_in, g_q, g_k, w_dw, b_dw, g_conv_ln, b_conv_ln,
              g_out_attn, g_out_conv, w_out, g_norm2, w_ff1, w_ff2):
    B, S, _ = x.shape
    cos, sin = rope_tables(S, x.dtype)
    c_act = jax.nn.silu(c)
    split_pts = _split_points()
    for l in range(DEPTH_3):
        mod = (c_act @ w_ada[l] + b_ada[l])[:, None, :]
        sh1, sc1, gt1, sh2, sc2, gt2 = jnp.split(mod, N_MOD, axis=-1)

        h = rms_norm(x, g_norm1[l]) * (1.0 + sc1) + sh1
        u = h @ w_in[l]
        q, k, v, iq, ik, iw, ca, cg = jnp.split(u, split_pts, axis=-1)
        q = partial_rope(rms_norm(q.reshape(B, S, ATTN_HEADS, HEAD_DIM), g_q[l]), cos, sin)
        k = partial_rope(rms_norm(k.reshape(B, S, ATTN_HEADS, HEAD_DIM), g_k[l]), cos, sin)
        v = v.reshape(B, S, ATTN_HEADS, HEAD_DIM)
        iq = partial_rope(iq.reshape(B, S, IDX_HEADS, IDX_DIM), cos, sin)
        ik = partial_rope(ik.reshape(B, S, 1, IDX_DIM), cos, sin)[:, :, 0, :]
        iw = iw * (IDX_HEADS ** -0.5)
        attn = dsa_sparse_attention(q, k, v, iq, ik, iw)
        conv = conformer_conv(ca, cg, w_dw[l], b_dw[l], g_conv_ln[l], b_conv_ln[l])
        mixed = jnp.concatenate([rms_norm(attn, g_out_attn[l]), rms_norm(conv, g_out_conv[l])], axis=-1)
        x = x + gt1 * (mixed @ w_out[l])

        h2 = rms_norm(x, g_norm2[l]) * (1.0 + sc2) + sh2
        f = jnp.square(jax.nn.relu(h2 @ w_ff1[l])) @ w_ff2[l]
        x = x + gt2 * f
    return x


_first_inputs_3 = third_inputs


def third_inputs(seed=0):
    import zlib

    import numpy as np

    out = dict(_first_inputs_3(seed))
    spreads = {}
    factors = {'g_norm1': 4.627,
     'g_q': 8.0,
     'g_k': 8.0,
     'b_dw': 7.529,
     'g_conv_ln': 8.0,
     'b_conv_ln': 8.0,
     'g_out_attn': 8.0,
     'g_out_conv': 8.0,
     'g_norm2': 6.851}
    for name, (base, spread) in spreads.items():
        noise = np.random.default_rng([zlib.crc32(name.encode()), seed]).standard_normal(out[name].shape)
        drawn = base * np.exp(spread * noise) if base else spread * noise
        out[name] = __import__('jax').numpy.asarray(drawn.astype(out[name].dtype))
    for name, factor in factors.items():
        out[name] = (out[name] * factor).astype(out[name].dtype)
    return out


_narrow_inputs_3 = third_inputs


def third_inputs(seed=0):

    out = dict(_narrow_inputs_3(seed))
    wider = {'g_conv_ln': 4.02, 'b_conv_ln': 4.08, 'g_out_attn': 4.34, 'g_out_conv': 4.28}
    for name, times in wider.items():
        mean = out[name].mean()
        out[name] = (mean + times * (out[name] - mean)).astype(out[name].dtype)
    return out


def setup_inputs(seed=0):
    out = dict(first_inputs(seed))
    for name, value in second_inputs(seed + 1).items():
        if name != "x":
            out[name + "_2"] = value
    for name, value in third_inputs(seed + 2).items():
        if name != "x":
            out[name + "_3"] = value
    return out


def reference(
    x, norm_mix_g, norm_ffn_g, final_norm_g, hy_w_in, hy_b_in, hy_conv_w, hy_conv_b, hy_f_w1,
    hy_f_b1, hy_f_w2, hy_f_b2, hy_f_w3, hy_f_b3, hy_f_w4, hy_f_freq, hy_skip, hy_w_out,
    hy_b_out, rw_mu, rw_w_r, rw_w_k, rw_w_v, rw_w_o, rw_w0, rw_w1, rw_w2, rw_a0, rw_a1, rw_a2,
    rw_v0, rw_v1, rw_v2, rw_g1, rw_g2, rw_k_k, rw_k_a, rw_r_k, rw_ln_w, rw_ln_b, ff_w_up,
    ff_conv_w, ff_conv_b, ff_w_down, positions_2, norm_mix_pre_2, w_in_2, gate_b_2, q_norm_2,
    w_uq_2, kv_norm_2, w_ukv_2, w_br_mla_2, sg_ln_g_2, sg_ln_b_2, sg_w_2, sg_b_2, w_br_sg_2,
    conv_w_2, w_br_conv_2, pool_w_2, pool_scale_2, w_br_pool_2, w_out_2, norm_mix_post_2,
    norm_ffn_pre_2, w_ff1_2, w_ff2_2, norm_ffn_post_2, c_3, w_ada_3, b_ada_3, g_norm1_3, w_in_3,
    g_q_3, g_k_3, w_dw_3, b_dw_3, g_conv_ln_3, b_conv_ln_3, g_out_attn_3, g_out_conv_3, w_out_3,
    g_norm2_3, w_ff1_3, w_ff2_3,
):
    x = first_block(
        x, norm_mix_g, norm_ffn_g, final_norm_g, hy_w_in, hy_b_in, hy_conv_w, hy_conv_b,
        hy_f_w1, hy_f_b1, hy_f_w2, hy_f_b2, hy_f_w3, hy_f_b3, hy_f_w4, hy_f_freq, hy_skip,
        hy_w_out, hy_b_out, rw_mu, rw_w_r, rw_w_k, rw_w_v, rw_w_o, rw_w0, rw_w1, rw_w2, rw_a0,
        rw_a1, rw_a2, rw_v0, rw_v1, rw_v2, rw_g1, rw_g2, rw_k_k, rw_k_a, rw_r_k, rw_ln_w,
        rw_ln_b, ff_w_up, ff_conv_w, ff_conv_b, ff_w_down,
    )
    x = second_block(
        x, positions_2, norm_mix_pre_2, w_in_2, gate_b_2, q_norm_2, w_uq_2, kv_norm_2, w_ukv_2,
        w_br_mla_2, sg_ln_g_2, sg_ln_b_2, sg_w_2, sg_b_2, w_br_sg_2, conv_w_2, w_br_conv_2,
        pool_w_2, pool_scale_2, w_br_pool_2, w_out_2, norm_mix_post_2, norm_ffn_pre_2, w_ff1_2,
        w_ff2_2, norm_ffn_post_2,
    )
    return third_block(
        x, c_3, w_ada_3, b_ada_3, g_norm1_3, w_in_3, g_q_3, g_k_3, w_dw_3, b_dw_3, g_conv_ln_3,
        b_conv_ln_3, g_out_attn_3, g_out_conv_3, w_out_3, g_norm2_3, w_ff1_3, w_ff2_3,
    )


_drawn_inputs = setup_inputs


def setup_inputs(seed=0):
    import zlib

    import numpy as np

    out = dict(_drawn_inputs(seed))
    spreads = {}
    factors = {'gate_b_2': 3.44,
     'b_dw_3': 5.614,
     'g_conv_ln_3': 3.853,
     'b_conv_ln_3': 3.636,
     'g_out_attn_3': 3.644,
     'g_out_conv_3': 3.742,
     'g_norm2_3': 2.696}
    for name, (base, spread) in spreads.items():
        noise = np.random.default_rng([zlib.crc32(name.encode()), seed]).standard_normal(out[name].shape)
        drawn = base * np.exp(spread * noise) if base else spread * noise
        out[name] = jnp.asarray(drawn.astype(out[name].dtype))
    for name, factor in factors.items():
        out[name] = (out[name] * factor).astype(out[name].dtype)
    return out
```

```python
from contextlib import ExitStack, nullcontext

import numpy as np

import concourse.bass as bass
from concourse import mybir

F32 = mybir.dt.float32
I32 = mybir.dt.int32
ACT = mybir.ActivationFunctionType
ALU = mybir.AluOpType
AX = mybir.AxisListType

P = 128
S = 512
D = 1024
DT = D // P
F1 = 2816
F1T = F1 // P
F2T = 4 * D // P
RING = 8
SLAB = 1024
BANKS = 4
NT = 66
EPS = 1e-6
NEG = -1e30

HD = 64
CH = 64
NCH = S // CH
KAPPA = float(np.exp(-0.5))
LEVELS = 6

HY_EMB, HY_W = 33, 64

MLA_H, NOPE, ROPE, VH = 4, 64, 32, 64
QKD = NOPE + ROPE
SGC = 128
POOL_WIN = (2, 4, 8, 16)

AH = 8
CONVK = 31
TOPK = 128

PARAMS = [
    ("norm_mix", 16), ("norm_ffn", 16), ("final_norm", 8),
    ("hy_b_in", 24), ("hy_conv_w", 72), ("hy_conv_b", 24), ("hy_skip", 8), ("hy_b_out", 8),
    ("hy_f_b", 3), ("hy_f_freq", 1),
    ("rw_mu", 48), ("rw_w0", 16), ("rw_a0", 8), ("rw_k_k", 8), ("rw_k_a", 8), ("rw_r_k", 8),
    ("rw_ln_w", 8), ("rw_ln_b", 8),
    ("ff_conv_w", 2 * 3 * 2 * F1T), ("ff_conv_b", 2 * 2 * F1T),
    ("norm_mix_pre2", 8), ("gate_b2", 32), ("q_norm2", 2), ("kv_norm2", 1), ("sg_ln_g2", 2), ("sg_ln_b2", 2),
    ("conv_w2", 6), ("pool_scale2", 2), ("norm_mix_post2", 8), ("norm_ffn_pre2", 8), ("norm_ffn_post2", 8),
    ("c3", 8), ("b_ada3", 48), ("g_norm13", 8), ("g_q3", 1), ("g_k3", 1), ("w_dw3", 4 * CONVK), ("b_dw3", 4),
    ("g_conv_ln3", 4), ("b_conv_ln3", 4), ("g_out_attn3", 4), ("g_out_conv3", 4), ("g_norm23", 8),
]
POFF, NPAR = {}, 0
for _name, _w in PARAMS:
    POFF[_name] = NPAR
    NPAR += _w

CONSTS = [("ident", 128), ("ones", 128), ("bones", 128), ("eye64", 64), ("strict", 128), ("incl", 128),
          ("level", LEVELS * 64), ("causal", 128), ("chunked", 64), ("perm_mla", 96), ("perm_dsa", 128),
          ("eps", 1), ("gn_eps", 1), ("invf", 1), ("rsign", 1), ("ntime", 4)]
COFF, NCST = {}, 0
for _name, _w in CONSTS:
    COFF[_name] = NCST
    NCST += _w

STREAM = [
    ("hy_in", 24, 1, 24), ("hy_dft", 0, 0, 4), ("hy_idft", 8, 0, 4), ("hy_out", 8, 1, 8),
    ("up0", 2 * F1T, 1, 2 * F1T), ("down0", 8, 3, 24),
    ("rw_lora1", 3, 1, 3), ("rw_r", 8, 1, 8), ("rw_k", 8, 1, 8), ("rw_v", 8, 1, 8), ("rw_a2", 8, 0, 1),
    ("rw_w2", 16, 0, 1), ("rw_g2", 8, 0, 1), ("rw_o", 8, 1, 8),
    ("up1", 2 * F1T, 1, 2 * F1T), ("down1", 8, 3, 24),
    ("in2", 16, 1, 16), ("gate2", 32, 1, 32), ("br2_0", 8, 0, 2), ("br2_1", 8, 0, 2), ("br2_2", 8, 0, 2),
    ("br2_3", 8, 0, 2), ("out2", 8, 1, 8), ("ff1_2", F2T, 1, F2T), ("ff2_2", 8, 4, 32),
    ("ada3", 0, 0, 48), ("in3", 21, 1, 21), ("iw3", 4, 0, 1), ("v3", 4, 0, 4), ("out3", 8, 1, 8),
    ("ff1_3", F2T, 1, F2T), ("ff2_3", 8, 4, 32),
]


class Stage:

    def __init__(self, name, tiles, per_tile, slabs, slab0, tile0, shared0):
        self.name, self.tiles, self.per_tile, self.slabs = name, tiles, per_tile, slabs
        self.slab0, self.tile0, self.shared0 = slab0, tile0, shared0


STAGE = {}
NSLAB = _tile = _shared = 0
for _name, _n, _s, _all in STREAM:
    STAGE[_name] = Stage(_name, _n, _s, _all, NSLAB, _tile, _shared)
    NSLAB += _all
    _tile += _n
    _shared += 0 if _s or not _n else _n - 1


class Steps:

    def __init__(self, eng, sem):
        self.eng, self.sem, self.n = eng, sem, 0

    def go(self, ins):
        ins.then_inc(self.sem, 1)
        self.n += 1

    def settle(self):
        if self.n:
            self.eng.wait_ge(self.sem, self.n)

    def __call__(self, ins):
        self.go(ins)
        self.settle()

    def tell(self, *sems):
        self.settle()
        for s in sems:
            self.eng.sem_inc(s, 1)

    def restart(self):
        self.settle()
        if self.n:
            self.eng.sem_clear(self.sem)
        self.n = 0


class Tile:

    def __init__(self, st, j, it, body):
        self.st, self.j, self.it, self.body = st, j, it, body
        self.idx = j if it is None else it * body + j
        self.bank = (st.tile0 + j) % BANKS

    def ready(self):
        v = self.st.slab0 + (self.j + 1) * self.st.per_tile
        return v if self.it is None else self.it * (self.body * self.st.per_tile) + v

    def bank_uses(self):
        v = (self.st.tile0 + self.j) // BANKS
        return v if self.it is None else self.it * (self.body // BANKS) + v


def loop_tiles(eng, st, steps=None, body=8):
    full = st.tiles // body if st.per_tile and st.tiles >= 2 * body else 0
    if full:
        if steps:
            steps.restart()
        with eng.Fori(0, full) as it:
            for j in range(body):
                yield Tile(st, j, it, body)
            if steps:
                steps.restart()
    for j in range(full * body, st.tiles):
        yield Tile(st, j, None, body)


def build(nc, d, out, phases=99):
    ctx = ExitStack()
    with ctx:
        sems = {}

        def sem(name):
            if name not in sems:
                sems[name] = ctx.enter_context(nc.semaphore(name))
            return sems[name]

        def sb(name, shape, dt=F32):
            return ctx.enter_context(nc.sbuf_tensor(name, shape, dt))

        ring = sb("ring", [P, RING, SLAB])
        X = sb("X", [P, DT, S])
        H = sb("H", [P, DT, S])
        arena = sb("arena", [P, NT, S])
        root = sb("root", [P, S])
        par = sb("par", [P, NPAR])
        cst = sb("cst", [P, NCST])
        gp = ctx.enter_context(nc.psum_tensor("gp", [P, BANKS, S], F32))
        aux = ctx.enter_context(nc.psum_tensor("aux", [P, BANKS, S], F32))

        def pcol(name, i=0):
            return par[:, bass.ds(POFF[name] + i, 1)]

        def const(name, lo=0, hi=None):
            w = dict(CONSTS)[name]
            return cst[:, COFF[name] + lo:COFF[name] + (w if hi is None else hi)]

        ident, ones, bones = const("ident"), const("ones"), const("bones")

        landed = [sem(f"landed{i}") for i in range(RING)]
        slab_done = sem("slab_done")
        shared_done = sem("shared_done")
        drained = [sem(f"drained{i}") for i in range(BANKS)]
        x_ready = sem("x_ready")
        h_ready = sem("h_ready")
        inputs_in = sem("inputs_in")
        sum_ready, stat_ready = sem("sum_ready"), sem("stat_ready")
        sq_ready = sem("sq_ready")
        out_stored = sem("out_stored")
        pe_s = sem("pe_steps")

        class Count:

            def __init__(self):
                self.x = self.h = self.sums = self.sq = 0

        def slab_wait(pe, slab, it=None, per_it=0):
            v = 16 * (slab // RING + 1)
            pe.wait_ge(landed[slab % RING], v if it is None else it * (16 * per_it // RING) + v)

        def bank_wait(pe, t):
            if t.it is not None or t.st.tile0 + t.j >= BANKS:
                pe.wait_ge(drained[t.bank], t.bank_uses())

        def stream_pe(pe, name, rhs, ksizes=None, width=P, before=None, body=8):
            st = STAGE[name]
            kt = ksizes or [DT] * st.per_tile
            for t in loop_tiles(pe, st, None, body):
                if before:
                    before(t)
                bank_wait(pe, t)
                k = 0
                for s, n in enumerate(kt):
                    slab = st.slab0 + t.j * st.per_tile + s
                    slab_wait(pe, slab, t.it, t.body * st.per_tile)
                    for i in range(n):
                        last = nc.tensor.matmul(gp[0:width, t.bank, :], ring[:, slab % RING, i * P:i * P + width],
                                                rhs(k, t), start=(k == 0), stop=(k == sum(kt) - 1))
                        k += 1
                    last.then_inc(slab_done, 1)

        def consume_wait(eng, t):
            st = t.st
            if st.per_tile:
                eng.wait_ge(slab_done, t.ready())
            elif t.j < st.tiles - 1:
                eng.wait_ge(shared_done, st.shared0 + t.j + 1)
            else:
                eng.wait_ge(slab_done, st.slab0 + st.slabs)

        def shared_tile_done(t, last):
            if t.j < t.st.tiles - 1:
                last.then_inc(shared_done, 1)

        def at(base, t, per):
            return base + per * t.j if t.it is None else t.it * (per * t.body) + (base + per * t.j)

        def norm_act(act, a, n, src, sq, src_wait, scale, eps="eps", root_wait=None):
            for k in range(n):
                src_wait(k)
                nc.scalar.activation(sq(k), src(k), ACT.Square).then_inc(sq_ready, 1)
            n_act.sums += 1
            act.wait_ge(sum_ready, n_act.sums)
            if root_wait:
                root_wait()
            nc.scalar.activation(root[:], aux[:, 0, :], ACT.Sqrt, scale=scale, bias=const(eps)).then_inc(stat_ready, 1)

        def norm_pe(pe, n, sq):
            if n_pe.sums:
                pe.wait_ge(stat_ready, n_pe.sums)
            for k in range(n):
                n_pe.sq += 1
                pe.wait_ge(sq_ready, n_pe.sq)
                last = nc.tensor.matmul(aux[:, 0, :], ones, sq(k), start=(k == 0), stop=(k == n - 1))
            last.then_inc(sum_ready, 1)
            n_pe.sums += 1

        def norm_dve(dve, v, n, src, gain, dst, done):
            n_dve.sums += 1
            dve.wait_ge(stat_ready, n_dve.sums)
            v(nc.vector.reciprocal(root[:], root[:]))
            for k in range(n):
                nc.vector.scalar_tensor_tensor(out=dst(k), in0=src(k), scalar=gain(k), in1=root[:],
                                               op0=ALU.mult, op1=ALU.mult).then_inc(done, 1)

        n_pe, n_act, n_dve = Count(), Count(), Count()
        Xk, Hk = (lambda k: X[:, k, :]), (lambda k: H[:, k, :])

        def arena_tiles(base):
            return lambda k: arena[:, base + k, :]

        def x_wait(eng, count):
            base = count.x - DT

            def wait(k):
                if base >= 0:
                    eng.wait_ge(x_ready, base + k + 1)
                else:
                    eng.wait_ge(inputs_in, INPUTS)
            return wait

        INPUTS = 16 * 3

        def pre_norm_act(act, a):
            norm_act(act, a, DT, Xk, Hk, x_wait(act, n_act), 1.0 / D)
            n_act.x += DT

        def pre_norm_dve(dve, v, gain, g0=0):
            norm_dve(dve, v, DT, Xk, lambda k: pcol(gain, g0 + k), Hk, h_ready)
            n_dve.h += DT

        def h_before(pe):
            n_pe.h += DT
            need = n_pe.h

            def before(t):
                if t.j == 0:
                    pe.wait_ge(h_ready, need)
            return before

        def residual_dve(dve, v, name, bias=None, body=8):
            st = STAGE[name]
            for t in loop_tiles(dve, st, v, body):
                consume_wait(dve, t)
                if bias is None:
                    ins = nc.vector.tensor_tensor(X[:, t.idx, :], gp[:, t.bank, :], X[:, t.idx, :], ALU.add)
                else:
                    ins = nc.vector.scalar_tensor_tensor(out=X[:, t.idx, :], in0=gp[:, t.bank, :],
                                                         scalar=bias(t.idx), in1=X[:, t.idx, :],
                                                         op0=ALU.add, op1=ALU.add)
                v.go(ins)
                v.tell(drained[t.bank], x_ready)
            n_dve.x += DT

        def copy_act(act, a, name, dst, func=ACT.Copy, bias=None, rows=P, done=None, body=8):
            st = STAGE[name]
            for t in loop_tiles(act, st, a, body):
                consume_wait(act, t)
                kw = {} if bias is None else {"bias": bias(t.idx)}
                a.go(nc.scalar.activation(dst(t.idx), gp[0:rows, t.bank, :], func, **kw))
                a.tell(*([drained[t.bank]] + ([done] if done else [])))

        hX1, hU, hX0, hKS, hKD, hDEC, hYR, hYI, hTMP = 0, 8, 16, 24, 32, 40, 48, 56, 64
        hUT = hDEC
        f_in = sem("hy_filter_in")
        f_w4 = arena[0:HY_W, hYR:hYR + 4, :].rearrange("p a b -> p (a b)")
        f_delta = arena[:, hYR + 4:hYR + 6, :].rearrange("p a b -> p (a b)")
        f_z = arena[0:HY_EMB, hYR + 6, :]
        f_w = arena[0:HY_W, hYR + 7, 0:3 * HY_W]
        f_h = [arena[0:HY_W, hYI + i, :] for i in range(3)]
        f_t = [arena[0:HY_W, hYI + 3 + i, :] for i in range(2)]
        f_pre, f_arg, f_sin = sem("f_pre"), sem("f_arg"), sem("f_sin")
        f_k, f_kread = sem("f_k"), sem("f_kread")
        f_dec, f_comb = sem("f_dec"), sem("f_comb")
        hz_ready, hz_used, hc_ready = sem("hz_ready"), sem("hz_used"), sem("hc_ready")
        u_ready, ut_psum, ut_ready = sem("u_ready"), sem("ut_psum"), sem("ut_ready")
        dft_set, kspec, yspec = sem("dft_set"), sem("kspec"), sem("yspec")
        hy_ready = sem("hy_ready")
        TWO_PI_HI = 6.28125
        TWO_PI_LO = float(2 * np.pi - 6.28125)
        MAGIC = 12582912.0

        def reduce_angle(v, eng, x, tmp, shift=0.0):
            v(eng.tensor_scalar(tmp, x, float(1 / (2 * np.pi)), MAGIC + shift, ALU.mult, ALU.add) if not shift else
              eng.tensor_scalar(tmp, x, float(1 / (2 * np.pi)), shift, ALU.mult, ALU.add))
            if shift:
                v(eng.tensor_scalar(tmp, tmp, MAGIC, None, ALU.add))
            v(eng.tensor_scalar(tmp, tmp, -MAGIC, None, ALU.add))
            v(eng.scalar_tensor_tensor(out=x, in0=tmp, scalar=-TWO_PI_HI, in1=x, op0=ALU.mult, op1=ALU.add))
            v(eng.scalar_tensor_tensor(out=x, in0=tmp, scalar=-TWO_PI_LO, in1=x, op0=ALU.mult, op1=ALU.add))

        def hyena_pe(pe):
            pe.wait_ge(f_in, 16 * 5)
            pe.wait_ge(inputs_in, INPUTS)
            for i in range(3):
                if i:
                    pe.wait_ge(f_sin, i)
                rows = HY_EMB if i == 0 else HY_W
                nc.tensor.matmul(aux[0:HY_W, 1, :], f_w[0:rows, i * HY_W:(i + 1) * HY_W],
                                 f_z if i == 0 else f_h[i - 1], start=True, stop=True).then_inc(f_pre, 1)
            norm_pe(pe, DT, Hk)
            pe.wait_ge(f_sin, 3)
            for tk in range(4):
                for c in range(2):
                    n = tk * 2 + c
                    for b in range(2):
                        if 2 * n + b >= 2:
                            pe.wait_ge(f_kread, 2 * n + b - 1)
                        nc.tensor.matmul(aux[:, 2 + b, :], f_h[2][:, tk * P:(tk + 1) * P],
                                         f_w4[:, b * D + c * S:b * D + (c + 1) * S],
                                         start=True, stop=True).then_inc(f_k, 1)
            stream_pe(pe, "hy_in", lambda k, t: H[:, k, :], before=h_before(pe))
            pe.wait_ge(f_kread, 16)
            for i in range(DT):
                pe.wait_ge(u_ready, i + 1)
                if i >= 2:
                    pe.wait_ge(ut_ready, i - 1)
                for tk in range(4):
                    last = nc.tensor.transpose(aux[:, 2 + i % 2, tk * P:(tk + 1) * P],
                                               arena[:, hU + i, tk * P:(tk + 1) * P], ident)
                last.then_inc(ut_psum, 1)
            pe.wait_ge(ut_ready, DT)
            pe.wait_ge(f_comb, 8)
            for b in range(BANKS):
                pe.wait_ge(drained[b], 24 // BANKS)
            st = STAGE["hy_dft"]
            for j in range(4):
                slot = (st.slab0 + j) % RING
                slab_wait(pe, st.slab0 + j)
                for c in range(2):
                    ps = gp if c == 0 else aux
                    if j:
                        pe.wait_ge(yspec, 2 * (j - 1) + c + 1)
                    for q, (lo, base) in enumerate(((0, hUT), (P, hUT), (0, hKS), (P, hKD))):
                        for tk in range(4):
                            last = nc.tensor.matmul(ps[:, q, :],
                                                    ring[:, slot, tk * 256 + lo:tk * 256 + lo + P],
                                                    arena[:, base + 2 * tk + c, :], start=(tk == 0), stop=(tk == 3))
                    if j == 0:
                        for tk in range(4):
                            last = nc.tensor.matmul(ps[0:1, 3, :], ring[:, slot, tk * 256 + P:tk * 256 + P + 1],
                                                    arena[:, hKS + 2 * tk + c, :], start=(tk == 0), stop=(tk == 3))
                    last.then_inc(dft_set if c == 0 else slab_done, 1)
            pe.wait_ge(yspec, 8)
            st = STAGE["hy_idft"]
            for t in loop_tiles(pe, st):
                bank_wait(pe, t)
                for s in range(4):
                    slot = (st.slab0 + s) % RING
                    if t.j == 0:
                        slab_wait(pe, st.slab0 + s)
                    for f in range(2):
                        fi = (s % 2) * 2 + f
                        y = arena[:, (hYR if s < 2 else hYI) + 2 * fi + t.j // 4, (t.j % 4) * P:(t.j % 4 + 1) * P]
                        last = nc.tensor.matmul(gp[:, t.bank, :], y, ring[:, slot, f * S:(f + 1) * S],
                                                start=(s == 0 and f == 0), stop=(s == 3 and f == 1))
                    if t.j == st.tiles - 1:
                        last.then_inc(slab_done, 1)
                shared_tile_done(t, last)
            pe.wait_ge(hy_ready, DT)
            stream_pe(pe, "hy_out", lambda k, t: arena[:, hU + k, :])

        def hyena_act(act, a):
            for i in range(3):
                act.wait_ge(f_arg, i + 1)
                nc.scalar.activation(f_h[i], f_t[0], ACT.Sin).then_inc(f_sin, 1)
            for tk in range(4):
                for c in range(2):
                    nc.scalar.activation(arena[:, hDEC + 2 * tk + c, :], f_delta[:, c * S:(c + 1) * S], ACT.Exp,
                                         scale=const("ntime", tk, tk + 1)).then_inc(f_dec, 1)
            pre_norm_act(act, a)
            for t in loop_tiles(act, STAGE["hy_in"], a):
                consume_wait(act, t)
                act.wait_ge(hz_used, at(1, t, 1))
                a.go(nc.scalar.activation(arena[:, hTMP + t.j % 2, :], gp[:, t.bank, :], ACT.Identity,
                                          bias=pcol("hy_b_in", t.idx)))
                a.tell(drained[t.bank])
                nc.scalar.activation(arena[:, hX1 + t.idx, :], arena[:, hTMP + t.j % 2, :], ACT.Identity,
                                     scale=pcol("hy_conv_w", 24 + t.idx),
                                     bias=pcol("hy_conv_b", t.idx)).then_inc(hz_ready, 1)
            for i in range(DT):
                act.wait_ge(ut_psum, i + 1)
                dst = arena[:, hUT:hUT + 8, :].rearrange("p (t c) s -> p t (c s)", c=2)[:, :, i * P:(i + 1) * P]
                if i == 0:
                    act.wait_ge(f_comb, 8)
                nc.scalar.activation(dst, aux[:, 2 + i % 2, :].rearrange("p (t c) -> p t c", t=4),
                                     ACT.Copy).then_inc(ut_ready, 1)
            st = STAGE["hy_dft"]
            for j in range(4):
                for c in range(2):
                    ps = gp if c == 0 else aux
                    if c == 0:
                        act.wait_ge(dft_set, j + 1)
                    else:
                        act.wait_ge(slab_done, st.slab0 + j + 1)
                    if j:
                        act.wait_ge(yspec, 2 * (j - 1) + c + 1)
                    a(nc.scalar.activation(arena[:, hX1 + 2 * c, :], ps[:, 2, :], ACT.Copy))
                    nc.scalar.activation(arena[:, hX1 + 2 * c + 1, :], ps[:, 3, :], ACT.Copy).then_inc(kspec, 1)

        def hyena_dve(dve, v):
            dve.sem_inc(hz_used, 2)
            dve.wait_ge(inputs_in, INPUTS)
            dve.wait_ge(f_in, 16 * 5)
            for i in range(3):
                dve.wait_ge(f_pre, i + 1)
                v(nc.vector.tensor_scalar(f_t[0], aux[0:HY_W, 1, :], pcol("hy_f_b", i)[0:HY_W],
                                          pcol("hy_f_freq")[0:HY_W], ALU.add, ALU.mult))
                reduce_angle(v, nc.vector, f_t[0], f_t[1])
                v.tell(f_arg)
            pre_norm_dve(dve, v, "norm_mix", 0)
            for n in range(8):
                dve.wait_ge(f_dec, n + 1)
                dec = arena[:, hDEC + n, :]
                kb = arena[:, hYI + 5 + n % 2, :]
                dve.wait_ge(f_k, 2 * n + 1)
                v(nc.vector.tensor_tensor(arena[:, hKD + n, :], aux[:, 2, :], dec, ALU.mult))
                v.tell(f_kread)
                dve.wait_ge(f_k, 2 * n + 2)
                v(nc.vector.tensor_tensor(kb, aux[:, 3, :], dec, ALU.mult))
                v.tell(f_kread)
                v(nc.vector.tensor_tensor(arena[:, hKS + n, :], arena[:, hKD + n, :], kb, ALU.add))
                v(nc.vector.tensor_tensor(arena[:, hKD + n, :], arena[:, hKD + n, :], kb, ALU.subtract))
                v.tell(f_comb)
            for t in loop_tiles(dve, STAGE["hy_in"], v):
                z, y = arena[:, hTMP + t.j % 2, :], arena[:, hX1 + t.idx, :]
                dve.wait_ge(hz_ready, at(1, t, 1))
                v(nc.vector.scalar_tensor_tensor(out=y[:, 1:S], in0=z[:, 0:S - 1], scalar=pcol("hy_conv_w", t.idx),
                                                 in1=y[:, 1:S], op0=ALU.mult, op1=ALU.add))
                v.go(nc.vector.scalar_tensor_tensor(out=y[:, 0:S - 1], in0=z[:, 1:S],
                                                    scalar=pcol("hy_conv_w", 48 + t.idx), in1=y[:, 0:S - 1],
                                                    op0=ALU.mult, op1=ALU.add))
                v.tell(hz_used)
            for i in range(DT):
                v.go(nc.vector.tensor_tensor(arena[:, hU + i, :], arena[:, hU + i, :], arena[:, hX1 + i, :], ALU.mult))
                v.tell(u_ready)
            for j in range(4):
                for c in range(2):
                    ps = gp if c == 0 else aux
                    dve.wait_ge(kspec, 2 * j + c + 1)
                    kr, ki = arena[:, hX1 + 2 * c, :], arena[:, hX1 + 2 * c + 1, :]
                    t1, t2, t3, t4 = (arena[:, hX1 + 4 + i, :] for i in range(4))
                    yr, yi = arena[:, hYR + 2 * j + c, :], arena[:, hYI + 2 * j + c, :]
                    v.go(nc.vector.tensor_tensor(t1, ps[:, 0, :], kr, ALU.mult))
                    v.go(nc.vector.tensor_tensor(t2, ps[:, 1, :], ki, ALU.mult))
                    v.go(nc.vector.tensor_tensor(t3, ps[:, 0, :], ki, ALU.mult))
                    v(nc.vector.tensor_tensor(t4, ps[:, 1, :], kr, ALU.mult))
                    v.go(nc.vector.tensor_tensor(yr, t1, t2, ALU.subtract))
                    v(nc.vector.tensor_tensor(yi, t3, t4, ALU.add))
                    if j == 0:
                        v.go(nc.vector.tensor_copy(yr[0:1, :], t1[0:1, :]))
                        v(nc.vector.tensor_copy(yi[0:1, :], t2[0:1, :]))
                    v.tell(yspec)
            for t in loop_tiles(dve, STAGE["hy_idft"]):
                consume_wait(dve, t)
                u = arena[:, hU + t.j, :]
                v(nc.vector.scalar_tensor_tensor(out=u, in0=u, scalar=pcol("hy_skip", t.j), in1=gp[:, t.bank, :],
                                                 op0=ALU.mult, op1=ALU.add))
                v.go(nc.vector.tensor_tensor(u, u, arena[:, hX0 + t.j, :], ALU.mult))
                v.tell(drained[t.bank], hy_ready)
            residual_dve(dve, v, "hy_out", lambda i: pcol("hy_b_out", i))

        ffG, ffT = 0, F1T
        aff_ready, gate_conv, gate_act, pair_done = sem("aff_ready"), sem("gate_conv"), sem("gate_act"), sem("pair_done")

        def ffn1_pe(pe, layer):
            norm_pe(pe, DT, Hk)
            stream_pe(pe, f"up{layer}", lambda k, t: H[:, k, :], before=h_before(pe))
            pe.wait_ge(pair_done, (layer + 1) * F1T + 2)
            stream_pe(pe, f"down{layer}", lambda k, t: arena[:, ffG + k, :], ksizes=[8, 8, 6])

        def ff_cols(layer, t, tap):
            return pcol("ff_conv_w", layer * 6 * F1T + tap * 2 * F1T + t.idx)

        def ffn1_act(act, a, layer):
            pre_norm_act(act, a)
            base = layer * F1T
            for t in loop_tiles(act, STAGE[f"up{layer}"], a):
                tmp = arena[:, ffT + t.j % 4, :]
                consume_wait(act, t)
                p = t.j // 2 if t.it is None else t.it * 4 + t.j // 2
                act.wait_ge(pair_done, p + (base + 1))
                nc.scalar.activation(tmp, gp[:, t.bank, :], ACT.Identity, scale=ff_cols(layer, t, 1),
                                     bias=pcol("ff_conv_b", layer * 2 * F1T + t.idx)).then_inc(aff_ready, 1)
                if t.j % 2:
                    g = arena[:, ffT + (t.j - 1) % 4, :]
                    act.wait_ge(gate_conv, p + (base + 1))
                    nc.scalar.activation(g, g, ACT.Silu).then_inc(gate_act, 1)

        def ffn1_dve(dve, v, layer):
            if layer == 0:
                dve.sem_inc(pair_done, 2)
            pre_norm_dve(dve, v, "norm_ffn", layer * DT)
            base = layer * F1T
            for t in loop_tiles(dve, STAGE[f"up{layer}"], v):
                y = arena[:, ffT + t.j % 4, :]
                z = gp[:, t.bank, :]
                p = t.j // 2 if t.it is None else t.it * 4 + t.j // 2
                dve.wait_ge(aff_ready, at(2 * base + 1, t, 1))
                v(nc.vector.scalar_tensor_tensor(out=y[:, 1:S], in0=z[:, 0:S - 1], scalar=ff_cols(layer, t, 0),
                                                 in1=y[:, 1:S], op0=ALU.mult, op1=ALU.add))
                v.go(nc.vector.scalar_tensor_tensor(out=y[:, 0:S - 1], in0=z[:, 1:S], scalar=ff_cols(layer, t, 2),
                                                    in1=y[:, 0:S - 1], op0=ALU.mult, op1=ALU.add))
                if t.j % 2 == 0:
                    v.tell(drained[t.bank], gate_conv)
                else:
                    v.tell(drained[t.bank])
                    dve.wait_ge(gate_act, p + (base + 1))
                    v.go(nc.vector.tensor_tensor(arena[:, ffG + p, :], y, arena[:, ffT + (t.j - 1) % 4, :], ALU.mult))
                    v.tell(pair_done)
            residual_dve(dve, v, f"down{layer}")

        wR, wK, wV, wA, wS, wXX, wMA, wMB = 0, 8, 16, 24, 32, 48, 56, 24
        wTA, wTG = 64, 65
        rw_xx = sem("rw_mix")
        MIX = (1, 4, 5, 0, 2, 3)
        MIX_STAGE = ("rw_lora1", "rw_lora1", "rw_lora1", "rw_r", "rw_k", "rw_v")
        lora_ready = sem("lora_ready")
        rkv_ready = sem("rkv_ready")

        def bd(t):
            return t.rearrange("p (c x) -> p c x", x=2 * CH)

        Hf = H[:, :, :].rearrange("p a b -> p (a b)")
        BETA, KT, MAK, XTB = (bd(Hf[:, i * 1024:(i + 1) * 1024]) for i in range(4))
        MBD, T1B = BETA, KT
        pair2 = lambda i: bd(arena[:, i:i + 2, :].rearrange("p a b -> p (a b)"))
        BTOK, KTOK, AR = pair2(48), pair2(50), pair2(52)
        KK, T1, T2, T3 = (arena[:, 54 + i, :] for i in range(4))
        MST, ARB, ARK, XT, VT = (arena[:, 58 + i, :] for i in range(5))
        XS, T1S = T1, T2
        SS, SPC, WS, US = (arena[:, 63, i * 64:(i + 1) * 64] for i in range(4))
        PC = arena[:, 63, 256:264]
        RESET = arena[:, wTA, :]
        ch = lambda t: t.rearrange("p (c x) -> p c x", x=CH)
        two = lambda ps, b: ps[:, b:b + 2, :].rearrange("p b (c x) -> p (b c) x", x=2 * CH)
        over = lambda m: m.unsqueeze(1).broadcast_to((P, NCH, CH))
        (rw_kkr, rw_ksq, rw_ksum, rw_kroot, rw_vtok, rw_cum, rw_exp, rw_prep, rw_M, rw_tok, rw_tokst, rw_Mst,
         rw_Mbd, rw_XTst, rw_XT, rw_X1, rw_X, rw_T1, rw_T1st, rw_T1bd, rw_dX, rw_dXT, rw_W, rw_Wst, rw_U, rw_Ust,
         rw_Sp, rw_S, rw_Y, rw_bon, rw_bsum, rw_y, rw_mean, rw_yc, rw_sq2, rw_var, rw_root2, rw_pair, rw_zero) = (
            sem("rw_" + x) for x in
            ("kkr ksq ksum kroot vtok cum exp prep M tok tokst Mst Mbd XTst XT X1 X T1 T1st T1bd dX dXT W Wst U "
             "Ust Sp S Y bon bsum y mean yc sq2 var root2 pair zero").split())
        LO, HI = slice(0, 64), slice(64, 128)
        yg_ready = sem("yg_ready")
        order = lambda d: range(NCH) if d == 0 else range(NCH - 1, -1, -1)

        def rwkv_pe(pe):
            norm_pe(pe, DT, Hk)
            n_pe.h += DT

            def mix_before(m):
                def before(t):
                    if t.j == 0 or m == 0:
                        pe.wait_ge(rw_xx, (m + (t.j if m == 0 else 0) + 1) * DT)
                return before

            buf = lambda m: wMA if m % 2 == 0 else wMB
            stream_pe(pe, "rw_lora1", lambda k, t: arena[:, buf(t.j) + k, :], before=mix_before(0))
            for m in (3, 4, 5):
                stream_pe(pe, MIX_STAGE[m], lambda k, t, m=m: arena[:, buf(m) + k, :], before=mix_before(m))
            pe.wait_ge(lora_ready, 3)
            for name in ("rw_a2", "rw_w2"):
                st = STAGE[name]
                slab_wait(pe, st.slab0)
                slot = st.slab0 % RING
                for t in loop_tiles(pe, st):
                    bank_wait(pe, t)
                    half = LO if t.j < DT else HI
                    src = arena[LO, wTA, :] if name == "rw_a2" else root[half, :]
                    i = t.j % DT
                    last = nc.tensor.matmul(gp[:, t.bank, :], ring[half, slot, i * P:(i + 1) * P], src,
                                            start=True, stop=True)
                    if t.j == st.tiles - 1:
                        last.then_inc(slab_done, 1)
                    shared_tile_done(t, last)
            t0 = STAGE["rw_g2"].tile0
            for b in range(BANKS):
                pe.wait_ge(drained[b], (t0 - b + BANKS - 1) // BANKS)
            pe.wait_ge(rw_zero, 1)
            with pe.Fori(0, DT) as it:
                pe.wait_ge(rw_ksq, it + 1)
                nc.tensor.matmul(aux[:, 3, :], bones, T2, start=True, stop=True).then_inc(rw_ksum, 1)
                for c in range(NCH):
                    for h in (LO, HI):
                        last = nc.tensor.matmul(gp[h, 0, c * CH:(c + 1) * CH], T3[h, c * CH:(c + 1) * CH],
                                                cst[h, COFF["eye64"]:COFF["eye64"] + 64], start=True, stop=True)
                last.then_inc(rw_vtok, 1)
                for d in range(2):
                    pe.wait_ge(rw_prep, it * 2 + (d + 1))
                    for q, src in enumerate((BETA, KT)):
                        for c in range(NCH):
                            last = nc.tensor.matmul(two(gp, 2 * q)[:, c, :], src[:, c, :], AR[:, c, :],
                                                    start=True, stop=True)
                    last.then_inc(rw_M, 1)
                    for q, src in enumerate((BETA, KT)):
                        for c in range(NCH):
                            last = nc.tensor.matmul(two(aux, 2 * q)[:, c, :], src[:, c, :], ident,
                                                    start=True, stop=True)
                    last.then_inc(rw_tok, 1)
                    pe.wait_ge(rw_XT, it * 12 + (6 * d + 1))
                    for c in range(NCH):
                        last = nc.tensor.matmul(gp[:, 0, c * CH:(c + 1) * CH], XTB[:, c, :],
                                                const("eye64"), start=True, stop=True)
                    last.then_inc(rw_X1, 1)
                    for lv in range(1, LEVELS):
                        n5 = 5 * d + lv
                        pe.wait_ge(rw_Mbd, it * 10 + n5)
                        pe.wait_ge(rw_X, it * 10 + n5)
                        for c in range(NCH):
                            last = nc.tensor.matmul(gp[:, 0, c * CH:(c + 1) * CH], MBD[:, c, :],
                                                    XS[:, c * CH:(c + 1) * CH], start=True, stop=True)
                        last.then_inc(rw_T1, 1)
                        if lv < LEVELS - 1:
                            pe.wait_ge(rw_T1st, it * 10 + n5)
                            pe.wait_ge(rw_XT, it * 12 + (6 * d + lv))
                            for c in range(NCH):
                                last = nc.tensor.matmul(gp[:, 1, c * CH:(c + 1) * CH], XTB[:, c, :],
                                                        T1S[:, c * CH:(c + 1) * CH], start=True, stop=True)
                            last.then_inc(rw_dX, 1)
                        pe.wait_ge(rw_T1bd, it * 10 + n5)
                        for c in range(NCH):
                            last = nc.tensor.matmul(gp[:, 2, c * CH:(c + 1) * CH], T1B[:, c, :],
                                                    XT[:, c * CH:(c + 1) * CH], start=True, stop=True)
                        last.then_inc(rw_dXT, 1)
                    pe.wait_ge(rw_XT, it * 12 + (6 * d + 6))
                    pe.wait_ge(rw_tokst, it * 2 + (d + 1))
                    for j, c in enumerate(order(d)):
                        cs = slice(c * CH, (c + 1) * CH)
                        n8 = 8 * d + j + 1
                        pe.wait_ge(rw_S, it * 18 + (9 * d + j + 1))
                        nc.tensor.matmul(gp[:, 3, 0:64], MAK[:, c, :], VT[:, cs], start=True, stop=False,
                                         skip_group_check=True)
                        for h in (LO, HI):
                            last = nc.tensor.matmul(gp[h, 3, 0:64], AR[h, c, 0:64], SS[h, :], start=False, stop=True,
                                                    skip_group_check=True)
                        last.then_inc(rw_W, 1)
                        for h in (LO, HI):
                            nc.tensor.matmul(aux[h, 2, cs], SS[h, :], AR[h, c, 64:128], start=True, stop=False)
                        for h in (LO, HI):
                            nc.tensor.matmul(aux[h, 2, cs], VT[h, cs], ARK[h, cs], start=False, stop=False)
                        pe.wait_ge(rw_Wst, it * 16 + n8)
                        nc.tensor.matmul(aux[:, 0, 0:64], XTB[:, c, :], WS, start=True, stop=True).then_inc(rw_U, 1)
                        nc.tensor.matmul(aux[:, 1, 0:64], KTOK[:, c, :], VT[:, cs], start=True, stop=False)
                        pe.wait_ge(rw_Ust, it * 16 + n8)
                        nc.tensor.matmul(aux[:, 1, 0:64], BTOK[:, c, :], US, start=False,
                                         stop=True).then_inc(rw_Sp, 1)
                        for h in (LO, HI):
                            last = nc.tensor.matmul(aux[h, 2, cs], US[h, :], ARB[h, cs], start=False, stop=True)
                    last.then_inc(rw_Y, 1)
                pe.wait_ge(rw_bon, it + 1)
                nc.tensor.matmul(gp[:, 2, :], bones, T3, start=True, stop=True).then_inc(rw_bsum, 1)
                pe.wait_ge(rw_y, it + 1)
                nc.tensor.matmul(gp[:, 0, :], bones, T1, start=True, stop=True).then_inc(rw_mean, 1)
                pe.wait_ge(rw_sq2, it + 1)
                nc.tensor.matmul(gp[:, 1, :], bones, T2, start=True, stop=True).then_inc(rw_var, 1)
            pe.wait_ge(rw_pair, DT)
            st = STAGE["rw_g2"]
            slab_wait(pe, st.slab0)
            for t in loop_tiles(pe, st):
                bank_wait(pe, t)
                last = nc.tensor.matmul(gp[:, t.bank, :], ring[:, st.slab0 % RING, t.j * P:(t.j + 1) * P],
                                        arena[:, wTG, :], start=True, stop=True)
                if t.j == st.tiles - 1:
                    last.then_inc(slab_done, 1)
                shared_tile_done(t, last)
            pe.wait_ge(yg_ready, DT)
            stream_pe(pe, "rw_o", lambda k, t: arena[:, wS + k, :])

        def rwkv_act(act, a):
            pre_norm_act(act, a)
            for t, (dst, func) in zip(loop_tiles(act, STAGE["rw_lora1"]),
                                      ((root[:], ACT.Tanh), (arena[:, wTA, :], ACT.Copy),
                                       (arena[:, wTG, :], ACT.Sigmoid))):
                consume_wait(act, t)
                a.go(nc.scalar.activation(dst, gp[:, t.bank, :], func))
                a.tell(drained[t.bank], lora_ready)
            for name, base in (("rw_r", wR), ("rw_k", wK), ("rw_v", wV)):
                copy_act(act, a, name, arena_tiles(base), done=rkv_ready)
            copy_act(act, a, "rw_a2", arena_tiles(wA), ACT.Sigmoid, lambda i: pcol("rw_a0", i), done=rkv_ready)
            copy_act(act, a, "rw_w2", arena_tiles(wS), ACT.Sigmoid, lambda i: pcol("rw_w0", i), done=rkv_ready)
            act.wait_ge(rw_zero, 1)
            a.restart()
            with act.Fori(0, DT) as it:
                act.wait_ge(rw_pair, it)
                a.go(nc.scalar.activation(T3, arena[:, wV + it, :], ACT.Copy))
                act.wait_ge(rw_kkr, it + 1)
                nc.scalar.activation(T2, KK, ACT.Square).then_inc(rw_ksq, 1)
                act.wait_ge(rw_ksum, it + 1)
                nc.scalar.activation(root[:], aux[:, 3, :], ACT.Sqrt).then_inc(rw_kroot, 1)
                for d in range(2):
                    act.wait_ge(rw_cum, it * 2 + (d + 1))
                    a.go(nc.scalar.activation(PC, PC, ACT.Exp, scale=-KAPPA))
                    a.go(nc.scalar.activation(T2, T2, ACT.Exp, scale=-KAPPA))
                    a(nc.scalar.activation(T3, T1, ACT.Exp, scale=KAPPA))
                    nc.scalar.activation(T1, T1, ACT.Exp, scale=-KAPPA).then_inc(rw_exp, 1)
                    act.wait_ge(rw_tok, it * 2 + (d + 1))
                    a.go(nc.scalar.activation(BTOK, two(aux, 0), ACT.Copy))
                    nc.scalar.activation(KTOK, two(aux, 2), ACT.Copy).then_inc(rw_tokst, 1)
                    for lv in range(LEVELS):
                        if lv:
                            act.wait_ge(rw_T1st, it * 10 + (5 * d + lv))
                            a.go(nc.scalar.activation(T1B[LO, :, 0:64], ch(T1S)[LO], ACT.Copy))
                            nc.scalar.activation(T1B[HI, :, 64:128], ch(T1S)[HI], ACT.Copy).then_inc(rw_T1bd, 1)
                        act.wait_ge(rw_XTst, it * 12 + (6 * d + lv + 1))
                        a.go(nc.scalar.activation(XTB[LO, :, 0:64], ch(XT)[LO], ACT.Copy))
                        nc.scalar.activation(XTB[HI, :, 64:128], ch(XT)[HI], ACT.Copy).then_inc(rw_XT, 1)
                act.wait_ge(rw_yc, it + 1)
                nc.scalar.activation(T2, T1, ACT.Square).then_inc(rw_sq2, 1)
                act.wait_ge(rw_var, it + 1)
                nc.scalar.activation(root[:], gp[:, 1, :], ACT.Sqrt, scale=1.0 / HD,
                                     bias=const("gn_eps")).then_inc(rw_root2, 1)
                a.restart()

        def rwkv_pool(pool, g):
            pool.wait_ge(rw_xx, 6 * DT)
            g(nc.gpsimd.memset(Hf, 0.0))
            pool.wait_ge(slab_done, STAGE["rw_a2"].slab0 + 1)
            g(nc.gpsimd.memset(RESET, 1.0))
            g(nc.gpsimd.memset(ch(RESET)[:, :, 0:1], 0.0))
            g.tell(rw_zero)
            g.restart()
            with pool.Fori(0, DT) as it:
                for d in range(2):
                    pool.wait_ge(rw_Mst, it * 2 + (d + 1))
                    pool.wait_ge(rw_tok, it * 2 + (d + 1))
                    for lv in range(1, LEVELS):
                        if lv > 1:
                            pool.wait_ge(rw_T1, it * 10 + (5 * d + lv - 1))
                        m = const("level", lv * 64, lv * 64 + 64)
                        g.go(nc.gpsimd.tensor_tensor(MBD[LO, :, 0:64], ch(MST)[LO], over(m)[LO], ALU.mult))
                        g.go(nc.gpsimd.tensor_tensor(MBD[HI, :, 64:128], ch(MST)[HI], over(m)[HI], ALU.mult))
                        g.tell(rw_Mbd)
                g.restart()

        def rwkv_dve(dve, v):
            pre_norm_dve(dve, v, "norm_mix", DT)
            v.settle()
            dve.wait_ge(h_ready, n_dve.h)
            for i in range(DT):
                xx, h = arena[:, wXX + i, :], H[:, i, :]
                v.go(nc.vector.tensor_tensor(xx[:, 1:S - 1], h[:, 0:S - 2], h[:, 2:S], ALU.add))
                v.go(nc.vector.tensor_copy(xx[:, 0:1], h[:, 1:2]))
                v(nc.vector.tensor_copy(xx[:, S - 1:S], h[:, S - 2:S - 1]))
                v(nc.vector.scalar_tensor_tensor(out=xx, in0=xx, scalar=0.5, in1=h, op0=ALU.mult, op1=ALU.subtract))
            for m, j in enumerate(MIX):
                if m >= 2:
                    st = STAGE[MIX_STAGE[m - 2]]
                    dve.wait_ge(slab_done, st.slab0 + (m - 1 if m - 2 < 3 else st.slabs))
                for i in range(DT):
                    dst = arena[:, (wMA if m % 2 == 0 else wMB) + i, :]
                    nc.vector.scalar_tensor_tensor(out=dst, in0=arena[:, wXX + i, :], scalar=pcol("rw_mu", j * DT + i),
                                                   in1=H[:, i, :], op0=ALU.mult, op1=ALU.add).then_inc(rw_xx, 1)
            dve.wait_ge(rkv_ready, 6 * DT)
            dve.wait_ge(rw_zero, 1)
            dve.wait_ge(slab_done, STAGE["rw_w2"].slab0 + 1)
            v.restart()
            with dve.Fori(0, DT) as it:
                r, k, val, aa = (arena[:, b + it, :] for b in (wR, wK, wV, wA))
                yt = arena[:, wS + it, :]
                v(nc.vector.tensor_scalar(KK, k, pcol("rw_k_k", it), None, ALU.mult))
                v.tell(rw_kkr)
                v(nc.vector.tensor_scalar(T1, aa, 1.0, pcol("rw_k_a", it), ALU.subtract, ALU.mult))
                v.go(nc.vector.scalar_tensor_tensor(out=k, in0=T1, scalar=1.0, in1=k, op0=ALU.add, op1=ALU.mult))
                dve.wait_ge(rw_vtok, it + 1)
                v.go(nc.vector.tensor_copy(VT, gp[:, 0, :]))
                dve.wait_ge(rw_kroot, it + 1)
                v(nc.vector.tensor_scalar(root[:], root[:], 1e-12, None, ALU.max))
                v(nc.vector.reciprocal(root[:], root[:]))
                v(nc.vector.tensor_tensor(KK, KK, root[:], ALU.mult))
                v(nc.vector.tensor_tensor(aa, KK, aa, ALU.mult))
                for d in range(2):
                    s = arena[:, wS + DT * d + it, :]
                    c0 = T1 if d == 0 else T3
                    v(nc.vector.tensor_tensor_scan(c0, RESET, s, 0.0, ALU.mult, ALU.add))
                    ends = ch(c0)[:, :, CH - 1:CH]
                    v.go(nc.vector.tensor_copy(PC.unsqueeze(2), ends))
                    if d == 0:
                        v(nc.vector.tensor_tensor(T2, T1, s, ALU.subtract))
                    else:
                        v(nc.vector.tensor_tensor(ch(T2), ends.broadcast_to((P, NCH, CH)), ch(T3), ALU.subtract))
                        v(nc.vector.tensor_tensor(T1, T2, s, ALU.add))
                    v.tell(rw_cum)
                    dve.wait_ge(rw_exp, it * 2 + (d + 1))
                    v.go(nc.vector.scalar_tensor_tensor(out=AR[:, :, 0:64], in0=ch(KK), scalar=-1.0, in1=ch(T2),
                                                        op0=ALU.mult, op1=ALU.mult))
                    v.go(nc.vector.tensor_tensor(AR[:, :, 64:128], ch(r), ch(T1), ALU.mult))
                    for dst, src in ((BETA, aa), (KT, k)):
                        for h, cols in ((LO, slice(0, 64)), (HI, slice(64, 128))):
                            v.go(nc.vector.tensor_tensor(dst[h, :, cols], ch(src)[h], ch(T3)[h], ALU.mult))
                    v.go(nc.vector.memset(SS, 0.0))
                    v.tell(rw_prep, rw_S)
                    dve.wait_ge(rw_M, it * 2 + (d + 1))
                    strict, incl = over(const("strict", 64 * d, 64 * d + 64)), over(const("incl", 64 * d, 64 * d + 64))
                    pb, pk = two(gp, 0), two(gp, 2)
                    v.go(nc.vector.tensor_tensor(ch(MST), pb[:, :, 0:64], strict, ALU.mult))
                    v.tell(rw_Mst)
                    v.go(nc.vector.tensor_tensor(ch(XT), ch(MST), over(const("level", 0, 64)), ALU.mult))
                    v.go(nc.vector.tensor_tensor(ch(ARB), pb[:, :, 64:128], incl, ALU.mult))
                    v.go(nc.vector.tensor_tensor(ch(ARK), pk[:, :, 64:128], incl, ALU.mult))
                    v.go(nc.vector.tensor_tensor(MAK[LO, :, 0:64], pk[LO, :, 0:64], strict[LO], ALU.mult))
                    v(nc.vector.tensor_tensor(MAK[HI, :, 64:128], pk[HI, :, 0:64], strict[HI], ALU.mult))
                    v.go(nc.vector.tensor_tensor(ch(XT), ch(XT), over(const("eye64")), ALU.add))
                    v.tell(rw_XTst)
                    dve.wait_ge(rw_X1, it * 2 + (d + 1))
                    nc.vector.tensor_copy(XS, gp[:, 0, :]).then_inc(rw_X, 1)
                    for lv in range(1, LEVELS):
                        n5 = 5 * d + lv
                        dve.wait_ge(rw_T1, it * 10 + n5)
                        nc.vector.tensor_copy(T1S, gp[:, 0, :]).then_inc(rw_T1st, 1)
                        if lv < LEVELS - 1:
                            dve.wait_ge(rw_dX, it * 8 + (4 * d + lv))
                            dve.wait_ge(rw_X, it * 10 + n5)
                            nc.vector.tensor_tensor(XS, gp[:, 1, :], XS, ALU.add).then_inc(rw_X, 1)
                        dve.wait_ge(rw_dXT, it * 10 + n5)
                        dve.wait_ge(rw_XT, it * 12 + (6 * d + lv))
                        nc.vector.tensor_tensor(XT, gp[:, 2, :], XT, ALU.add).then_inc(rw_XTst, 1)
                    for j, c in enumerate(order(d)):
                        n8 = 8 * d + j + 1
                        pc = PC[:, c:c + 1]
                        dve.wait_ge(rw_S, it * 18 + (9 * d + j + 1))
                        v.go(nc.vector.tensor_scalar(SPC, SS, pc, None, ALU.mult))
                        dve.wait_ge(rw_W, it * 16 + n8)
                        nc.vector.tensor_copy(WS, gp[:, 3, 0:64]).then_inc(rw_Wst, 1)
                        dve.wait_ge(rw_U, it * 16 + n8)
                        nc.vector.tensor_copy(US, aux[:, 0, 0:64]).then_inc(rw_Ust, 1)
                        dve.wait_ge(rw_Sp, it * 16 + n8)
                        v.settle()
                        nc.vector.scalar_tensor_tensor(out=SS, in0=aux[:, 1, 0:64], scalar=pc, in1=SPC,
                                                       op0=ALU.mult, op1=ALU.add).then_inc(rw_S, 1)
                    dve.wait_ge(rw_Y, it * 2 + (d + 1))
                    if d == 0:
                        v(nc.vector.tensor_scalar(yt, aux[:, 2, :], 1.0, None, ALU.mult))
                    else:
                        v(nc.vector.tensor_tensor(T1, aux[:, 2, :], yt, ALU.add))
                    dve.wait_ge(rw_S, it * 18 + (9 * d + 9))
                v.tell(rw_y)
                v(nc.vector.scalar_tensor_tensor(out=T3, in0=r, scalar=pcol("rw_r_k", it), in1=k,
                                                 op0=ALU.mult, op1=ALU.mult))
                v.tell(rw_bon)
                dve.wait_ge(rw_mean, it + 1)
                v(nc.vector.scalar_tensor_tensor(out=T1, in0=gp[:, 0, :], scalar=-1.0 / HD, in1=T1,
                                                 op0=ALU.mult, op1=ALU.add))
                v.tell(rw_yc)
                dve.wait_ge(rw_bsum, it + 1)
                v(nc.vector.tensor_tensor(T3, gp[:, 2, :], val, ALU.mult))
                dve.wait_ge(rw_root2, it + 1)
                v(nc.vector.reciprocal(root[:], root[:]))
                v(nc.vector.scalar_tensor_tensor(out=T1, in0=T1, scalar=pcol("rw_ln_w", it), in1=root[:],
                                                 op0=ALU.mult, op1=ALU.mult))
                v(nc.vector.scalar_tensor_tensor(out=yt, in0=T1, scalar=pcol("rw_ln_b", it), in1=T3,
                                                 op0=ALU.add, op1=ALU.add))
                v.tell(rw_pair)
                v.restart()
            for t in loop_tiles(dve, STAGE["rw_g2"]):
                consume_wait(dve, t)
                y = arena[:, wS + t.j, :]
                v.go(nc.vector.tensor_tensor(y, gp[:, t.bank, :], y, ALU.mult))
                v.tell(drained[t.bank], yg_ready)
            residual_dve(dve, v, "rw_o")

        def final1_pe(pe):
            norm_pe(pe, DT, Hk)

        def final1_act(act, a):
            pre_norm_act(act, a)

        def final1_dve(dve, v):
            norm_dve(dve, v, DT, Xk, lambda k: pcol("final_norm", k), Xk, x_ready)
            n_dve.x += DT

        lat_ready, ln_c, ln_ready = sem("lat_ready"), sem("ln_c"), sem("ln_ready")

        def sum_pe(pe, n, src):
            pe.wait_ge(stat_ready, n_pe.sums)
            for k in range(n):
                last = nc.tensor.matmul(aux[:, 0, :], ones, src(k), start=(k == 0), stop=(k == n - 1))
            last.then_inc(sum_ready, 1)
            n_pe.sums += 1

        def mean_act(act, width):
            n_act.sums += 1
            act.wait_ge(sum_ready, n_act.sums)
            nc.scalar.activation(root[:], aux[:, 0, :], ACT.Copy, scale=1.0 / width).then_inc(stat_ready, 1)

        def centre_dve(dve, v, n, src):
            n_dve.sums += 1
            dve.wait_ge(stat_ready, n_dve.sums)
            for k in range(n):
                v.go(nc.vector.tensor_tensor(src(k), src(k), root[:], ALU.subtract))
            v.tell(ln_c)

        def scale_shift_dve(dve, v, n, src, gain, bias, dst, done):
            n_dve.sums += 1
            dve.wait_ge(stat_ready, n_dve.sums)
            v(nc.vector.reciprocal(root[:], root[:]))
            for k in range(n):
                v(nc.vector.scalar_tensor_tensor(out=dst(k), in0=src(k), scalar=gain(k), in1=root[:],
                                                 op0=ALU.mult, op1=ALU.mult))
                nc.vector.tensor_scalar(dst(k), dst(k), bias(k), None, ALU.add).then_inc(done, 1)

        at_score, at_max, at_exp, at_norm, at_tr, at_pt, at_pv = (
            sem("at_" + x) for x in "score max exp norm tr pt pv".split())

        class Unit:
            def __init__(self, q, k, mask, nk, v, out):
                self.q, self.k, self.mask, self.nk, self.v, self.out = q, k, mask, nk, v, out

        class Attention:

            def __init__(self, units, p, pt, scale, u0):
                self.units, self.p, self.pt, self.scale, self.u0 = units, p, pt, scale, u0

        def attention_pe(pe, A):
            def score(i):
                u, n = A.units[i], A.u0 + i
                if n >= 2:
                    pe.wait_ge(at_exp, n - 1)
                nc.tensor.matmul(gp[:, n % 2, 0:u.nk], u.q, u.k, start=True, stop=False, skip_group_check=True)
                lo, m = u.mask
                nc.tensor.matmul(gp[:, n % 2, lo:u.nk], ident, m, start=False, stop=True,
                                 skip_group_check=True).then_inc(at_score, 1)

            score(0)
            for i, u in enumerate(A.units):
                n = A.u0 + i
                if i + 1 < len(A.units):
                    score(i + 1)
                pe.wait_ge(at_norm, n + 1)
                if n >= 2:
                    pe.wait_ge(at_pt, n - 1)
                for b in range(u.nk // P):
                    last = nc.tensor.transpose(gp[:, 2 + n % 2, b * P:(b + 1) * P], A.p(n)[:, b * P:(b + 1) * P], ident)
                last.then_inc(at_tr, 1)
                pe.wait_ge(at_pt, n + 1)
                for b in range(u.nk // P):
                    last = nc.tensor.matmul(u.out, u.v(b), A.pt(n)[:, b * P:(b + 1) * P],
                                            start=(b == 0), stop=(b == u.nk // P - 1))
                last.then_inc(at_pv, 1)

        def stat(n, i):
            return root[:, 4 * (n % 2) + i:4 * (n % 2) + i + 1]

        def attention_act(act, A):
            def copy(i):
                u, n = A.units[i], A.u0 + i
                act.wait_ge(at_tr, n + 1)
                if n >= 2:
                    act.wait_ge(at_pv, n - 1)
                nc.scalar.activation(A.pt(n)[:, 0:u.nk], gp[:, 2 + n % 2, 0:u.nk], ACT.Copy).then_inc(at_pt, 1)

            for i, u in enumerate(A.units):
                n = A.u0 + i
                act.wait_ge(at_max, n + 1)
                if n >= 2:
                    act.wait_ge(at_tr, n - 1)
                nc.scalar.activation(A.p(n)[:, 0:u.nk], gp[:, n % 2, 0:u.nk], ACT.Exp, bias=stat(n, 1), scale=A.scale,
                                     accum_out=stat(n, 2)).then_inc(at_exp, 1)
                if i:
                    copy(i - 1)
            copy(len(A.units) - 1)

        def attention_dve(dve, v, A):
            def maximum(i):
                u, n = A.units[i], A.u0 + i
                dve.wait_ge(at_score, n + 1)
                v(nc.vector.tensor_reduce(stat(n, 0), gp[:, n % 2, 0:u.nk], AX.X, ALU.max))
                nc.vector.tensor_scalar(stat(n, 1), stat(n, 0), -A.scale, None, ALU.mult).then_inc(at_max, 1)

            maximum(0)
            for i, u in enumerate(A.units):
                n = A.u0 + i
                if i + 1 < len(A.units):
                    maximum(i + 1)
                dve.wait_ge(at_exp, n + 1)
                v(nc.vector.reciprocal(stat(n, 3), stat(n, 2)))
                p = A.p(n)[:, 0:u.nk]
                nc.vector.tensor_scalar(p, p, stat(n, 3), None, ALU.mult).then_inc(at_norm, 1)

        relu_ready, f_ready = sem("relu_ready"), sem("f_ready")
        fF = 16

        def ffn2_pe(pe, b):
            stream_pe(pe, f"ff1_{b}", lambda k, t: H[:, k, :], before=h_before(pe))
            pe.wait_ge(f_ready, F2T * (b - 1))
            stream_pe(pe, f"ff2_{b}", lambda k, t: arena[:, fF + k, :], ksizes=[DT] * 4, body=4)

        def ffn2_act(act, a, b):
            copy_act(act, a, f"ff1_{b}", lambda i: arena[:, fF + i, :], ACT.Relu, done=relu_ready)

        def ffn2_dve(dve, v, b):
            for t in loop_tiles(dve, STAGE[f"ff1_{b}"]):
                f = arena[:, fF + t.idx, :]
                dve.wait_ge(relu_ready, at(F2T * (b - 2) + 1, t, 1))
                nc.vector.tensor_tensor(f, f, f, ALU.mult).then_inc(f_ready, 1)

        bCQ, bCKV, bKR, bU, bV, bCX, bCB, bCC, bP, bG, bOUT = 0, 2, 3, 4, 6, 8, 10, 12, 14, 16, 48
        sm = arena[:, 56:61, :].rearrange("p a b -> p (a b)")
        UQ = sm[:, 0:768].rearrange("p (k n) -> p k n", k=2)
        WK, WV = sm[:, 768:1024], sm[:, 1024:1280]
        SGW = sm[:, 1280:1792]
        POOLW = sm[:, 1792:1920].rearrange("p (t n) -> p t n", t=2)
        UPPER = sm[:, 1920:2048]
        SGB = sm[0:1, 2048:2560]
        POS = arena[:, 61, :]
        RCNT = arena[:, 62:64, :]
        VM = arena[:, 64:66, :].rearrange("p a b -> p (a b)").rearrange("p (t n) -> p t n", t=4)
        COS, SIN, ANG, TMP = (arena[:, 8 + i, :] for i in range(4))
        RP = slice(NOPE, QKD)
        sm_in, sm_free = sem("sm_in"), sem("sm_free")
        in2_ready, gate_ready = sem("in2_ready"), sem("gate_ready")
        sgw_ready, sgt_psum, sgt_ready, sg_psum, sg_out = (sem(x) for x in "sgw_ready sgt_psum sgt_ready sg_psum sg_out".split())
        pooled, pool_psum, pool_out, conv_out = (sem(x) for x in "pooled pool_psum pool_out conv_out".split())
        mq_psum, mq_ready, mrot, mroped, mk_psum, mk_ready, mv_psum, mv_ready, trig, mla_out = (
            sem(x) for x in "mq_psum mq_ready mrot mroped mk_psum mk_ready mv_psum mv_ready trig mla_out".split())
        merged = sem("merged")
        mla_units = [Unit(H[0:QKD, h, qb * P:(qb + 1) * P], H[0:QKD, 4 + h, 0:(qb + 1) * P],
                          (qb * P, const("causal")), (qb + 1) * P,
                          lambda b, h=h: VM[:, b, h * VH:(h + 1) * VH],
                          aux[(h % 2) * 64:(h % 2) * 64 + 64, 1 + h // 2, qb * P:(qb + 1) * P])
                     for h in range(MLA_H) for qb in range(4)]
        MLA = Attention(mla_units, lambda n: arena[:, 10 + n % 2, :], lambda n: arena[:, 12 + n % 2, :],
                        float(QKD) ** -0.5, 0)
        bsq = arena_tiles(bOUT)

        def two_pool(pool, g):
            pool.wait_ge(h_ready, 5 * DT)
            for dst, name in ((sm[:, 0:2048], "sm2"), (SGB, "sg_b"), (RCNT, "rcnt")):
                pool.dma_start(dst, d[name]).then_inc(sm_in, 16)
            pool.dma_start(POS.bitcast(I32), d["pos"].partition_broadcast(P)).then_inc(sm_in, 16)

        def two_pe(pe):
            norm_pe(pe, DT, Hk)
            stream_pe(pe, "in2", lambda k, t: H[:, k, :], before=h_before(pe))
            norm_pe(pe, 2, bsq)
            norm_pe(pe, 1, arena_tiles(bOUT + 2))
            pe.wait_ge(in2_ready, 8)
            sum_pe(pe, 2, arena_tiles(bV))
            norm_pe(pe, 2, arena_tiles(bOUT + 3))
            stream_pe(pe, "gate2", lambda k, t: H[:, k, :])
            for b in range(BANKS):
                pe.wait_ge(drained[b], (STAGE["br2_0"].tile0 - b + BANKS - 1) // BANKS)
            pe.wait_ge(sm_in, 16 * 4)
            pe.wait_ge(ln_ready, 2)
            for i in range(2):
                for n in range(4):
                    last = nc.tensor.transpose(gp[:, i, n * P:(n + 1) * P], arena[:, bV + i, n * P:(n + 1) * P], ident)
                last.then_inc(sgt_psum, 1)
            pe.wait_ge(sgw_ready, 1)
            pe.wait_ge(sgt_ready, 2)
            for g in range(4):
                rows = slice((g % 2) * 64, (g % 2) * 64 + 64)
                for n in range(4):
                    o = gp[rows, 2 + g // 2, n * P:(n + 1) * P]
                    nc.tensor.matmul(o, arena[:, bOUT + g // 2, n * P + (g % 2) * 64:n * P + (g % 2) * 64 + 64],
                                     SGW[:, g * P:(g + 1) * P], start=True, stop=False)
                    last = nc.tensor.matmul(o, ones[0:1, 0:64], SGB[:, g * P:(g + 1) * P], start=False, stop=True)
                if g % 2:
                    last.then_inc(sg_psum, 1)
            pe.wait_ge(pooled, 2)
            for i in range(2):
                for h in (LO, HI):
                    last = nc.tensor.matmul(aux[h, 2 + i, :], POOLW[h, i, :], arena[h, bP + i, :], start=True, stop=True)
                last.then_inc(pool_psum, 1)
            pe.wait_ge(lat_ready, 3)
            pe.wait_ge(sgt_ready, 2)
            pe.wait_ge(sg_out, 2)
            for h in range(MLA_H):
                for k in range(2):
                    last = nc.tensor.matmul(gp[0:QKD, h, :], UQ[:, k, h * QKD:(h + 1) * QKD], arena[:, bCQ + k, :],
                                            start=(k == 0), stop=(k == 1))
                last.then_inc(mq_psum, 1)
            pe.wait_ge(stat_ready, n_pe.sums)
            nc.tensor.matmul(aux[0:QKD, 0, :], const("perm_mla")[0:QKD], arena[0:QKD, bKR, :], start=True,
                             stop=True).then_inc(mrot, 1)
            for h in range(MLA_H):
                pe.wait_ge(mq_ready, h + 1)
                pe.wait_ge(mroped, h + 1)
                nc.tensor.matmul(aux[0:QKD, 0, :], const("perm_mla")[0:QKD], H[0:QKD, h, :], start=True,
                                 stop=True).then_inc(mrot, 1)
                nc.tensor.matmul(gp[0:NOPE, h, :], WK[:, h * NOPE:(h + 1) * NOPE], arena[:, bCKV, :], start=True,
                                 stop=True).then_inc(mk_psum, 1)
            pe.wait_ge(pool_out, 2)
            for tk in range(4):
                last = nc.tensor.matmul(aux[:, 2 + tk // 2, (tk % 2) * 256:(tk % 2) * 256 + 256],
                                        arena[:, bCKV, tk * P:(tk + 1) * P], WV, start=True, stop=True)
            last.then_inc(mv_psum, 1)
            pe.wait_ge(mk_ready, MLA_H)
            pe.wait_ge(mv_ready, 1)
            pe.wait_ge(mroped, MLA_H + 1)
            attention_pe(pe, MLA)
            for b in range(4):
                pe.wait_ge((mla_out, sg_out, conv_out, pool_out)[b], 2)
                st = STAGE[f"br2_{b}"]
                for t in loop_tiles(pe, st):
                    bank_wait(pe, t)
                    for k in range(2):
                        slab = st.slab0 + k
                        if t.j == 0:
                            slab_wait(pe, slab)
                        last = nc.tensor.matmul(gp[:, t.bank, :], ring[:, slab % RING, t.j * P:(t.j + 1) * P],
                                                arena[:, bOUT + 2 * b + k, :], start=(k == 0), stop=(k == 1))
                        if t.j == st.tiles - 1:
                            last.then_inc(slab_done, 1)
                    shared_tile_done(t, last)
            pe.wait_ge(merged, DT)
            stream_pe(pe, "out2", lambda k, t: H[:, k, :])
            norm_pe(pe, DT, arena_tiles(8))
            norm_pe(pe, DT, Hk)
            ffn2_pe(pe, 2)
            norm_pe(pe, DT, arena_tiles(8))

        def post_norm_act(act, a, name, ready, base, body=8):
            copy_act(act, a, name, arena_tiles(0), done=ready, body=body)
            norm_act(act, a, DT, arena_tiles(0), arena_tiles(8), lambda k: act.wait_ge(ready, base + k + 1), 1.0 / D)

        def post_norm_dve(dve, v, gain):
            n_dve.sums += 1
            dve.wait_ge(stat_ready, n_dve.sums)
            v(nc.vector.reciprocal(root[:], root[:]))
            for k in range(DT):
                o = arena[:, k, :]
                v(nc.vector.scalar_tensor_tensor(out=o, in0=o, scalar=pcol(gain, k), in1=root[:],
                                                 op0=ALU.mult, op1=ALU.mult))
                nc.vector.tensor_tensor(X[:, k, :], X[:, k, :], o, ALU.add).then_inc(x_ready, 1)
            n_dve.x += DT

        o_ready = sem("o_ready")

        def two_act(act, a):
            pre_norm_act(act, a)
            for t in loop_tiles(act, STAGE["in2"], a, body=16):
                consume_wait(act, t)
                a.go(nc.scalar.activation(arena[:, t.j, :], gp[:, t.bank, :],
                                          ACT.Gelu_apprx_tanh if bU <= t.j < bCX else ACT.Copy))
                a.tell(drained[t.bank], in2_ready)
            norm_act(act, a, 2, arena_tiles(bCQ), bsq, lambda k: None, 1.0 / 256)
            norm_act(act, a, 1, arena_tiles(bCKV), arena_tiles(bOUT + 2), lambda k: None, 1.0 / 128,
                     root_wait=lambda: act.wait_ge(lat_ready, 2))
            act.wait_ge(lat_ready, 3)
            mean_act(act, 256)
            norm_act(act, a, 2, arena_tiles(bV), arena_tiles(bOUT + 3), lambda k: act.wait_ge(ln_c, 1), 1.0 / 256)
            copy_act(act, a, "gate2", lambda i: arena[:, bG + i, :], ACT.Sigmoid, lambda i: pcol("gate_b2", i),
                     done=gate_ready)
            act.wait_ge(trig, 1)
            for x in (SIN, COS):
                nc.scalar.activation(x[RP], x[RP], ACT.Sin).then_inc(trig_done, 1)
            for i in range(2):
                act.wait_ge(sgt_psum, i + 1)
                nc.scalar.activation(arena[:, bOUT + i, :], gp[:, i, :], ACT.Copy).then_inc(sgt_ready, 1)
            for i in range(2):
                act.wait_ge(pool_psum, i + 1)
                nc.scalar.activation(arena[:, bOUT + 6 + i, :], aux[:, 2 + i, :], ACT.Copy,
                                     scale=pcol("pool_scale2", i)).then_inc(pool_out, 1)
            for h in range(MLA_H):
                act.wait_ge(mq_psum, h + 1)
                nc.scalar.activation(H[0:QKD, h, :], gp[0:QKD, h, :], ACT.Copy).then_inc(mq_ready, 1)
            act.wait_ge(mroped, 1)
            for h in range(MLA_H):
                a.go(nc.scalar.activation(H[RP, 4 + h, :], arena[RP, bKR, :], ACT.Copy))
                act.wait_ge(mk_psum, h + 1)
                nc.scalar.activation(H[0:NOPE, 4 + h, :], gp[0:NOPE, h, :], ACT.Copy).then_inc(mk_ready, 1)
            act.wait_ge(mv_psum, 1)
            nc.scalar.activation(VM, aux[:, 2:4, :].rearrange("p a (c n) -> p (a c) n", c=2),
                                 ACT.Copy).then_inc(mv_ready, 1)
            attention_act(act, MLA)
            act.wait_ge(at_pv, len(mla_units))
            act.wait_ge(sg_psum, 2)
            for i in range(2):
                nc.scalar.activation(arena[:, bOUT + i, :], aux[:, 1 + i, :], ACT.Copy).then_inc(mla_out, 1)
            post_norm_act(act, a, "out2", o_ready, 0)
            pre_norm_act(act, a)
            ffn2_act(act, a, 2)
            post_norm_act(act, a, "ff2_2", o_ready, DT, body=4)

        def trig_dve(v):
            ang, s, c, t = ANG[RP], SIN[RP], COS[RP], TMP[RP]
            v(nc.vector.tensor_copy(ang, POS[RP].bitcast(I32)))
            v(nc.vector.tensor_scalar(ang, ang, const("invf")[RP], None, ALU.mult))
            v(nc.vector.tensor_copy(s, ang))
            reduce_angle(v, nc.vector, s, t)
            v(nc.vector.tensor_copy(c, ang))
            reduce_angle(v, nc.vector, c, t, 0.25)
            v(nc.vector.tensor_scalar(c, c, float(np.pi / 2), None, ALU.add))
            for x in (s, c):
                v(nc.vector.tensor_scalar(x, x, float(np.float32(3.1415925)), float(np.float32(-3.1415925)), ALU.min, ALU.max))

        def two_dve(dve, v):
            pre_norm_dve(dve, v, "norm_mix_pre2")
            for n, base, gain in ((2, bCQ, "q_norm2"), (1, bCKV, "kv_norm2")):
                norm_dve(dve, v, n, arena_tiles(base), lambda k, gain=gain: pcol(gain, k), arena_tiles(base), lat_ready)
            centre_dve(dve, v, 2, arena_tiles(bV))
            scale_shift_dve(dve, v, 2, arena_tiles(bV), lambda k: pcol("sg_ln_g2", k), lambda k: pcol("sg_ln_b2", k),
                            arena_tiles(bV), ln_ready)
            dve.wait_ge(sm_in, 16 * 4)
            for g in range(4):
                v.go(nc.vector.tensor_tensor(SGW[:, g * P:(g + 1) * P], SGW[:, g * P:(g + 1) * P], UPPER,
                                             ALU.mult))
            v.tell(sgw_ready)
            dve.wait_ge(in2_ready, 16)
            for i in range(2):
                z, y = arena[:, bCC + i, :], arena[:, bOUT + 4 + i, :]
                v(nc.vector.tensor_tensor(z, z, arena[:, bCX + i, :], ALU.mult))
                v(nc.vector.tensor_scalar(y, z, pcol("conv_w2", 4 + i), None, ALU.mult))
                for k in (1, 0):
                    lag = 2 - k
                    v(nc.vector.scalar_tensor_tensor(out=y[:, lag:S], in0=z[:, 0:S - lag],
                                                     scalar=pcol("conv_w2", 2 * k + i), in1=y[:, lag:S],
                                                     op0=ALU.mult, op1=ALU.add))
                v.go(nc.vector.tensor_tensor(y, y, arena[:, bCB + i, :], ALU.mult))
                v.tell(conv_out)
            for i in range(2):
                x = arena[:, bP + i, :]
                src, lag = x, 1
                for lv in range(2 * i + 2):
                    dst = arena[:, bOUT + 2 + lv % 2, :]
                    v.go(nc.vector.tensor_copy(dst[:, 0:lag], src[:, 0:lag]))
                    v(nc.vector.tensor_tensor(dst[:, lag:S], src[:, lag:S], src[:, 0:S - lag], ALU.add))
                    if lv >= 2 * i:
                        h = (LO, HI)[lv - 2 * i]
                        v(nc.vector.tensor_tensor(RCNT[h, i, :], dst[h], RCNT[h, i, :], ALU.mult))
                    src, lag = dst, lag * 2
                v.go(nc.vector.tensor_tensor(x, RCNT[:, i, :], x, ALU.subtract))
                v.tell(pooled)
            trig_dve(v)
            v.tell(trig)
            dve.wait_ge(trig_done, 2)
            v(nc.vector.tensor_scalar(SIN[RP], SIN[RP], const("rsign")[RP], None, ALU.mult))
            for i in range(2):
                dve.wait_ge(sg_psum, i + 1)
                v.go(nc.vector.tensor_tensor(arena[:, bOUT + 2 + i, :], gp[:, 2 + i, :], arena[:, bU + i, :], ALU.mult))
                v.tell(sg_out)
            for h in range(MLA_H + 1):
                x = arena[RP, bKR, :] if h == 0 else H[RP, h - 1, :]
                dve.wait_ge(mrot, h + 1)
                v.go(nc.vector.tensor_tensor(TMP[RP], aux[RP, 0, :], SIN[RP], ALU.mult))
                v(nc.vector.tensor_tensor(x, x, COS[RP], ALU.mult))
                v.go(nc.vector.tensor_tensor(x, x, TMP[RP], ALU.add))
                v.tell(mroped)
            attention_dve(dve, v, MLA)
            for b in range(4):
                for t in loop_tiles(dve, STAGE[f"br2_{b}"]):
                    g, m = arena[:, bG + b * DT + t.j, :], H[:, t.j, :]
                    consume_wait(dve, t)
                    if b == 0:
                        v.go(nc.vector.tensor_tensor(m, gp[:, t.bank, :], g, ALU.mult))
                        v.tell(drained[t.bank])
                    else:
                        v(nc.vector.tensor_tensor(g, gp[:, t.bank, :], g, ALU.mult))
                        dve.sem_inc(drained[t.bank], 1)
                        v(nc.vector.tensor_tensor(m, m, g, ALU.add))
                        if b == 3:
                            dve.sem_inc(merged, 1)
            post_norm_dve(dve, v, "norm_mix_post2")
            pre_norm_dve(dve, v, "norm_ffn_pre2")
            ffn2_dve(dve, v, 2)
            post_norm_dve(dve, v, "norm_ffn_post2")

        trig_done = sem("trig_done")

        dCA, dCG, dIQ, dIK, dQ, dK, dV, dAT, dCV = 0, 4, 8, 12, 13, 17, 21, 25, 29
        ROTC, ROTS = arena[:, 33, :], arena[:, 34, :]
        SELM = lambda qb: arena[:, 34 + qb, 0:(qb + 1) * P]
        SCORE, WORK = arena[:, 38, :], arena[:, 40, :]
        REL = lambda n: arena[:, 39 + 2 * (n % 2), :]
        IW = arena[:, 45, 0:4 * AH]
        TOP8 = arena[:, 45, 64:72]
        CNT = arena[:, 45, 72:73]
        PAD = arena[:, 51:53, :].rearrange("p a b -> p (a b)")[:, 0:CONVK - 1 + S]
        hsq = arena_tiles(53)
        MOD = lambda j, k: pcol("b_ada3", j * DT + k)
        mod_act, mod_ready = sem("mod_act"), sem("mod_ready")
        rot_in = sem("rot_in")
        in3_ready, iw_ready, v3_ready = sem("in3_ready"), sem("iw_ready"), sem("v3_ready")
        hd_sum, hd_root, hd_normed = sem("hd_sum"), sem("hd_root"), sem("hd_normed")
        ro_psum, ro_ready = sem("ro_psum"), sem("ro_ready")
        ix_psum, ix_relu, ix_used, sel_ready = sem("ix_psum"), sem("ix_relu"), sem("ix_used"), sem("sel_ready")
        dsa_out, an_ready, cv_ready, cl_ready, cs_ready, cn_ready = (
            sem(x) for x in "dsa_out an_ready cv_ready cl_ready cs_ready cn_ready".split())
        half = lambda h: slice((h % 2) * 64, (h % 2) * 64 + 64)
        dsa_units = [Unit(arena[half(h), dQ + h // 2, qb * P:(qb + 1) * P], arena[half(h), dK + h // 2, 0:(qb + 1) * P],
                          (64, const("chunked")) if qb == 0 else (0, SELM(qb)), (qb + 1) * P,
                          lambda b, h=h: arena[:, dV + b, h * HD:(h + 1) * HD],
                          aux[half(h), h // 2, qb * P:(qb + 1) * P])
                     for qb in range(4) for h in range(AH)]
        DSA = Attention(dsa_units, lambda n: arena[:, 42 + n % 2, :], lambda n: arena[:, 46 + n % 2, :],
                        HD ** -0.5, len(mla_units))
        ROTATED = list(range(dIQ, dIK + 1)) + list(range(dQ, dV))

        def three_pool(pool, g):
            pool.wait_ge(x_ready, 7 * DT)
            pool.dma_start(ROTC, d["rotc"]).then_inc(rot_in, 16)
            pool.dma_start(ROTS, d["rots"]).then_inc(rot_in, 16)

        def three_pe(pe):
            st = STAGE["ada3"]
            pe.wait_ge(mod_act, 1)
            with pe.Fori(0, st.slabs // RING) as it:
                for j in range(RING):
                    slab = st.slab0 + j
                    slab_wait(pe, slab, it, RING)
                    for k in range(DT):
                        last = nc.tensor.matmul(aux[:, 1, bass.ds(it * RING + j, 1)],
                                                ring[:, slab % RING, k * P:(k + 1) * P], pcol("c3", k),
                                                start=(k == 0), stop=(k == DT - 1))
                    last.then_inc(slab_done, 1)
            norm_pe(pe, DT, Hk)
            stream_pe(pe, "in3", lambda k, t: H[:, k, :], before=h_before(pe))
            st = STAGE["iw3"]
            slab_wait(pe, st.slab0)
            for t in loop_tiles(pe, st):
                bank_wait(pe, t)
                for k in range(DT):
                    last = nc.tensor.matmul(gp[:, t.bank, 0:AH], H[:, k, t.j * P:(t.j + 1) * P],
                                            ring[:, st.slab0 % RING, k * AH:(k + 1) * AH],
                                            start=(k == 0), stop=(k == DT - 1))
                if t.j == st.tiles - 1:
                    last.then_inc(slab_done, 1)
                shared_tile_done(t, last)
            st = STAGE["v3"]
            for t in loop_tiles(pe, st):
                bank_wait(pe, t)
                for k in range(DT):
                    slab = st.slab0 + k // 2
                    if t.j == 0 and k % 2 == 0:
                        slab_wait(pe, slab)
                    last = nc.tensor.matmul(gp[:, t.bank, :], H[:, k, t.j * P:(t.j + 1) * P],
                                            ring[:, slab % RING, (k % 2) * S:(k % 2 + 1) * S],
                                            start=(k == 0), stop=(k == DT - 1))
                    if t.j == st.tiles - 1 and k % 2:
                        last.then_inc(slab_done, 1)
                shared_tile_done(t, last)
            for b in range(BANKS):
                pe.wait_ge(drained[b], (STAGE["out3"].tile0 - b + BANKS - 1) // BANKS)
            pe.wait_ge(stat_ready, n_pe.sums)
            pe.wait_ge(mod_ready, 1)
            for i in range(8):
                n_pe.sq += 1
                pe.wait_ge(sq_ready, n_pe.sq)
                nc.tensor.matmul((gp if i < 4 else aux)[:, i % 4, :], bones, hsq(i), start=True,
                                 stop=True).then_inc(hd_sum, 1)
            pe.wait_ge(hd_root, 8)
            for n, i in enumerate(ROTATED):
                if n >= 5:
                    pe.wait_ge(hd_normed, n - 4)
                if n >= 4:
                    pe.wait_ge(ro_ready, n - 3)
                nc.tensor.matmul(gp[:, n % 4, :], const("perm_dsa"), arena[:, i, :], start=True,
                                 stop=True).then_inc(ro_psum, 1)
            pe.wait_ge(ro_ready, len(ROTATED))
            n = 0
            for qb in range(1, 4):
                for h in range(AH):
                    if n >= 2:
                        pe.wait_ge(ix_relu, n - 1)
                    nc.tensor.matmul(gp[:, n % 2, 0:(qb + 1) * P], arena[half(h), dIQ + h // 2, qb * P:(qb + 1) * P],
                                     arena[half(h), dIK, 0:(qb + 1) * P], start=True, stop=True).then_inc(ix_psum, 1)
                    n += 1
            pe.wait_ge(sel_ready, 3)
            pe.wait_ge(ix_relu, 3 * AH)
            attention_pe(pe, DSA)
            norm_pe_at(pe)
            stream_pe(pe, "out3", lambda k, t: arena[:, dAT + k, :])
            norm_pe(pe, DT, Hk)
            ffn2_pe(pe, 3)

        def norm_pe_at(pe):
            pe.wait_ge(dsa_out, 4)
            pe.wait_ge(cv_ready, 4)
            sum_pe(pe, 4, arena_tiles(dCV))
            norm_pe(pe, 4, arena_tiles(46))
            norm_pe(pe, 4, arena_tiles(46))
            norm_pe(pe, 4, arena_tiles(46))
            pe.wait_ge(an_ready, 4)
            pe.wait_ge(cn_ready, 4)

        def three_act(act, a):
            act.wait_ge(x_ready, 7 * DT)
            c = par[:, POFF["c3"]:POFF["c3"] + DT]
            nc.scalar.activation(c, c, ACT.Silu).then_inc(mod_act, 1)
            pre_norm_act(act, a)
            for t in loop_tiles(act, STAGE["in3"], a, body=32):
                consume_wait(act, t)
                a.go(nc.scalar.activation(arena[:, t.j, :], gp[:, t.bank, :],
                                          ACT.Sigmoid if dCG <= t.j < dIQ else ACT.Copy))
                a.tell(drained[t.bank], in3_ready)
            for t in loop_tiles(act, STAGE["iw3"]):
                consume_wait(act, t)
                a.go(nc.scalar.activation(IW[:, t.j * AH:(t.j + 1) * AH], gp[:, t.bank, 0:AH], ACT.Copy,
                                          scale=float(AH ** -0.5 * HD ** -0.5)))
                a.tell(drained[t.bank], iw_ready)
            copy_act(act, a, "v3", arena_tiles(dV), done=v3_ready)
            for i in range(8):
                nc.scalar.activation(hsq(i), arena[:, dQ + i, :], ACT.Square).then_inc(sq_ready, 1)
            for i in range(8):
                act.wait_ge(hd_sum, i + 1)
                nc.scalar.activation(hsq(i), (gp if i < 4 else aux)[:, i % 4, :], ACT.Sqrt, scale=1.0 / HD,
                                     bias=const("eps")).then_inc(hd_root, 1)
            n = 0
            for qb in range(1, 4):
                for h in range(AH):
                    act.wait_ge(ix_psum, n + 1)
                    if n >= 2:
                        act.wait_ge(ix_used, n - 1)
                    w = (qb + 1) * P
                    nc.scalar.activation(REL(n)[:, 0:w], gp[:, n % 2, 0:w], ACT.Relu).then_inc(ix_relu, 1)
                    n += 1
            attention_act(act, DSA)
            act.wait_ge(at_pv, DSA.u0 + len(dsa_units))
            for i in range(4):
                nc.scalar.activation(arena[:, dAT + i, :], aux[:, i, :], ACT.Copy).then_inc(dsa_out, 1)
            mean_act(act, 512)
            act.wait_ge(ln_c, 2)
            norm_act(act, a, 4, arena_tiles(dCV), arena_tiles(46), lambda k: None, 1.0 / 512)
            for k in range(4):
                act.wait_ge(cl_ready, k + 1)
                a(nc.scalar.activation(arena[:, dCV + k, :], arena[:, dCV + k, :], ACT.Silu))
            norm_act(act, a, 4, arena_tiles(dCV), arena_tiles(46), lambda k: None, 1.0 / 512)
            act.wait_ge(cn_ready, 4)
            norm_act(act, a, 4, arena_tiles(dAT), arena_tiles(46), lambda k: act.wait_ge(dsa_out, k + 1), 1.0 / 512)
            pre_norm_act(act, a)
            ffn2_act(act, a, 3)

        def modulated_norm_dve(dve, v, gain, shift):
            n_dve.sums += 1
            dve.wait_ge(stat_ready, n_dve.sums)
            v(nc.vector.reciprocal(root[:], root[:]))
            for k in range(DT):
                v(nc.vector.scalar_tensor_tensor(out=H[:, k, :], in0=X[:, k, :], scalar=pcol(gain, k), in1=root[:],
                                                 op0=ALU.mult, op1=ALU.mult))
                nc.vector.tensor_scalar(H[:, k, :], H[:, k, :], MOD(shift, k), None, ALU.add).then_inc(h_ready, 1)
            n_dve.h += DT

        def gated_residual_dve(dve, v, name, gate, body=8):
            for t in loop_tiles(dve, STAGE[name], v, body):
                consume_wait(dve, t)
                x = X[:, t.idx, :]
                v.go(nc.vector.scalar_tensor_tensor(out=x, in0=gp[:, t.bank, :], scalar=MOD(gate, t.idx), in1=x,
                                                    op0=ALU.mult, op1=ALU.add))
                v.tell(drained[t.bank], x_ready)
            n_dve.x += DT

        def three_dve(dve, v):
            dve.wait_ge(slab_done, STAGE["ada3"].slab0 + 48)
            mod = par[:, POFF["b_ada3"]:POFF["b_ada3"] + 48]
            v(nc.vector.tensor_tensor(mod, aux[:, 1, 0:48], mod, ALU.add))
            for gain, j in (("g_norm13", 1), ("g_norm23", 4)):
                g = par[:, POFF[gain]:POFF[gain] + DT]
                v(nc.vector.scalar_tensor_tensor(out=g, in0=mod[:, j * DT:(j + 1) * DT], scalar=1.0, in1=g,
                                                 op0=ALU.add, op1=ALU.mult))
            v.tell(mod_ready)
            modulated_norm_dve(dve, v, "g_norm13", 0)
            v(nc.vector.memset(PAD[:, 0:CONVK - 1], 0.0))
            for i in range(4):
                y = arena[:, dCV + i, :]
                tap = lambda k: pcol("w_dw3", i * CONVK + k)
                dve.wait_ge(in3_ready, dCG + i + 1)
                v(nc.vector.tensor_tensor(PAD[:, CONVK - 1:], arena[:, dCA + i, :], arena[:, dCG + i, :], ALU.mult))
                v(nc.vector.tensor_scalar(y, PAD[:, CONVK - 1:], tap(CONVK - 1), pcol("b_dw3", i), ALU.mult, ALU.add))
                for k in range(CONVK - 1):
                    v(nc.vector.scalar_tensor_tensor(out=y, in0=PAD[:, k:k + S], scalar=tap(k), in1=y,
                                                     op0=ALU.mult, op1=ALU.add))
                v.tell(cv_ready)
            for i in range(8):
                dve.wait_ge(hd_root, i + 1)
                v(nc.vector.reciprocal(hsq(i), hsq(i)))
                x = arena[:, dQ + i, :]
                nc.vector.scalar_tensor_tensor(out=x, in0=x, scalar=pcol("g_q3" if i < 4 else "g_k3"), in1=hsq(i),
                                               op0=ALU.mult, op1=ALU.mult).then_inc(hd_normed, 1)
            dve.wait_ge(rot_in, 32)
            dve.wait_ge(hd_normed, 8)
            tmp = arena[:, 48, :]
            for n, i in enumerate(ROTATED):
                x = arena[:, i, :]
                dve.wait_ge(ro_psum, n + 1)
                v.go(nc.vector.tensor_tensor(tmp, gp[:, n % 4, :], ROTS, ALU.mult))
                v(nc.vector.tensor_tensor(x, x, ROTC, ALU.mult))
                v.go(nc.vector.tensor_tensor(x, x, tmp, ALU.add))
                v.tell(ro_ready)
            dve.wait_ge(iw_ready, 4)
            n = 0
            for qb in range(1, 4):
                w = (qb + 1) * P
                sc, wk = SCORE[:, 0:w], WORK[:, 0:w]
                for h in range(AH):
                    iw = IW[:, qb * AH + h:qb * AH + h + 1]
                    dve.wait_ge(ix_relu, n + 1)
                    if h == 0:
                        v(nc.vector.tensor_scalar(sc, REL(n)[:, 0:w], iw, None, ALU.mult))
                    else:
                        v(nc.vector.scalar_tensor_tensor(out=sc, in0=REL(n)[:, 0:w], scalar=iw, in1=sc,
                                                         op0=ALU.mult, op1=ALU.add))
                    dve.sem_inc(ix_used, 1)
                    n += 1
                last = SCORE[:, w - 64:w]
                v(nc.vector.tensor_tensor(last, last, const("chunked"), ALU.add))
                v(nc.vector.max(out=TOP8, in_=sc))
                for k in range(TOPK // 8 - 1):
                    v(nc.vector.match_replace(out=wk, in_to_replace=TOP8, in_values=sc if k == 0 else wk,
                                              imm_value=-3e38))
                    v(nc.vector.max(out=TOP8, in_=wk))
                thr = TOP8[:, 7:8]
                sel = SELM(qb)
                v(nc.vector.tensor_scalar(sel, sc, thr, None, ALU.is_gt))
                v(nc.vector.tensor_reduce(CNT, sel, AX.X, ALU.add))
                v(nc.vector.tensor_scalar(CNT, CNT, -1.0, float(TOPK), ALU.mult, ALU.add))
                v(nc.vector.tensor_scalar(sc, sc, thr, None, ALU.is_equal))
                v(nc.vector.tensor_tensor_scan(wk, sc, sc, 0.0, ALU.add, ALU.max))
                v(nc.vector.tensor_scalar(wk, wk, CNT, None, ALU.is_le))
                v(nc.vector.tensor_tensor(wk, wk, sc, ALU.mult))
                v(nc.vector.tensor_tensor(sel, sel, wk, ALU.add))
                v(nc.vector.tensor_scalar(sel, sel, -NEG, NEG, ALU.mult, ALU.add))
                v.tell(sel_ready)
            attention_dve(dve, v, DSA)
            centre_dve(dve, v, 4, arena_tiles(dCV))
            scale_shift_dve(dve, v, 4, arena_tiles(dCV), lambda k: pcol("g_conv_ln3", k), lambda k: pcol("b_conv_ln3", k),
                            arena_tiles(dCV), cl_ready)
            norm_dve(dve, v, 4, arena_tiles(dCV), lambda k: pcol("g_out_conv3", k), arena_tiles(dCV), cn_ready)
            norm_dve(dve, v, 4, arena_tiles(dAT), lambda k: pcol("g_out_attn3", k), arena_tiles(dAT), an_ready)
            gated_residual_dve(dve, v, "out3", 2)
            modulated_norm_dve(dve, v, "g_norm23", 3)
            ffn2_dve(dve, v, 3)
            gated_residual_dve(dve, v, "ff2_3", 5, body=4)

        def store(sp):
            for k in range(DT):
                sp.wait_ge(x_ready, n_store.x - DT + k + 1)
                sp.dma_start(out[k], X[:, k, :]).then_inc(out_stored, 16)
            sp.wait_ge(out_stored, 16 * DT)

        n_store = Count()
        PH = [
            (hyena_pe, hyena_act, hyena_dve, None, ()),
            (ffn1_pe, ffn1_act, ffn1_dve, None, (0,)),
            (rwkv_pe, rwkv_act, rwkv_dve, rwkv_pool, ()),
            (ffn1_pe, ffn1_act, ffn1_dve, None, (1,)),
            (final1_pe, final1_act, final1_dve, None, ()),
            (two_pe, two_act, two_dve, two_pool, ()),
            (three_pe, three_act, three_dve, three_pool, ()),
        ][:phases]
        LAST = {1: 'hy_out', 2: 'down0', 3: 'rw_o', 4: 'down1', 5: 'down1', 6: 'ff2_2', 7: 'ff2_3'}
        NXUP = [1, 1, 1, 1, 1, 2, 2][:phases]
        block = ctx.enter_context(nc.Block())

        @block.sync
        def _(sp):
            sp.dma_start(par[:], d["par"]).then_inc(inputs_in, 16)
            sp.dma_start(cst[:], d["cst"]).then_inc(inputs_in, 16)
            sp.dma_start(X[:], d["x"]).then_inc(inputs_in, 16)
            w = d["weights"]
            NSLAB = STAGE[LAST[len(PH)]].slab0 + STAGE[LAST[len(PH)]].slabs
            for s in range(RING):
                sp.dma_start(ring[:, s, :], w[s]).then_inc(landed[s], 16)
            with sp.Fori(0, NSLAB // RING - 1) as it:
                for s in range(RING):
                    sp.wait_ge(slab_done, it * RING + s + 1)
                    sp.dma_start(ring[:, s, :], w[RING:NSLAB // RING * RING].rearrange("(n s) p c -> n s p c", s=RING)[it, s]
                                 ).then_inc(landed[s], 16)
            for g in range(NSLAB // RING * RING, NSLAB):
                sp.wait_ge(slab_done, g - RING + 1)
                sp.dma_start(ring[:, g % RING, :], w[g]).then_inc(landed[g % RING], 16)

        @block.gpsimd
        def _(pool):
            pool.dma_start(f_z, d["hy_z"]).then_inc(f_in, 16)
            pool.dma_start(f_w[0:HY_EMB, 0:HY_W], d["hy_f_w1"]).then_inc(f_in, 16)
            pool.dma_start(f_w[:, HY_W:3 * HY_W], d["hy_f_w23"]).then_inc(f_in, 16)
            pool.dma_start(f_w4, d["hy_f_w4"]).then_inc(f_in, 16)
            pool.dma_start(f_delta, d["hy_delta"]).then_inc(f_in, 16)
            g = Steps(pool, sem("pool_steps"))
            for _, _, _, f, args in PH:
                if f:
                    f(pool, g, *args)

        @block.tensor
        def _(pe):
            for f, _, _, _, args in PH:
                f(pe, *args)

        @block.scalar
        def _(act):
            a = Steps(act, sem("act_steps"))
            act.wait_ge(inputs_in, INPUTS)
            act.wait_ge(f_in, 16 * 5)
            for _, f, _, _, args in PH:
                f(act, a, *args)

        @block.vector
        def _(dve):
            v = Steps(dve, sem("dve_steps"))
            for _, _, f, _, args in PH:
                f(dve, v, *args)

        @block.sync
        def _(sp):
            n_store.x = DT * sum(NXUP)
            store(sp)


def vec(a):
    return np.asarray(a).reshape(-1, P).T


def col64(a):
    a = np.asarray(a).reshape(-1, 64)
    return np.concatenate([a, np.zeros_like(a)], axis=1).T


def tall(w):
    k, n = w.shape
    pad = (-n) % P
    if pad:
        w = np.concatenate([w, np.zeros((k, pad), w.dtype)], axis=1)
    return w.reshape(DT, P, -1, P).transpose(2, 1, 0, 3).reshape(-1, P, SLAB)


def deep(w):
    k = w.shape[0] // P
    groups = -(-k // DT)
    w = np.concatenate([w, np.zeros(((groups * DT - k) * P, w.shape[1]), w.dtype)])
    return w.reshape(groups, DT, P, -1, P).transpose(3, 0, 2, 1, 4).reshape(-1, P, SLAB)


def pairs(a):
    return np.stack([a[..., :F1].reshape(a.shape[:-1] + (F1T, P)), a[..., F1:].reshape(a.shape[:-1] + (F1T, P))],
                    axis=-2).reshape(a.shape)


def dft_tables():
    n = 2 * S
    tok = np.arange(S)
    f = np.arange(S)
    ang = 2 * np.pi * ((f[:, None] * tok[None, :]) % n) / n
    re, im = np.cos(ang), -np.sin(ang)
    im[0] = np.cos(np.pi * tok)
    fw = np.stack([re.reshape(4, P, 4, P), im.reshape(4, P, 4, P)], axis=2)
    fw = fw.transpose(0, 4, 3, 2, 1).reshape(4, P, SLAB)
    cr = 2 * re / n
    cr[0] = 1 / n
    ci = 2 * im / n
    ci[0] = im[0] / n
    inv = np.stack([cr.reshape(2, 2, P, S), ci.reshape(2, 2, P, S)])
    inv = inv.transpose(0, 1, 3, 2, 4).reshape(4, P, SLAB)
    return fw.astype(np.float32), inv.astype(np.float32)


def constants():
    c = np.zeros((P, NCST), np.float32)

    def put(name, a):
        a = np.asarray(a, np.float32)
        c[:a.shape[0], COFF[name]:COFF[name] + a.shape[1]] = a

    p = np.arange(P)
    put("ident", np.eye(P))
    put("ones", np.ones((P, P)))
    put("bones", (p[:, None] // HD == p[None, :] // HD))
    s, t = p[:, None] % CH, np.arange(CH)[None, :]
    put("eye64", s == t)
    put("strict", np.concatenate([s < t, s > t], axis=1))
    put("incl", np.concatenate([s <= t, s >= t], axis=1))
    put("level", np.concatenate([(s >> (i + 1) == t >> (i + 1)) & (s >> i != t >> i) for i in range(LEVELS)], axis=1))
    put("causal", np.where(p[None, :] <= p[:, None], 0.0, NEG))
    put("chunked", np.tile(np.where(p[:, None] < 64, NEG, 0.0), (1, 64)))
    half = ROPE // 2
    m = np.zeros((P, QKD))
    for i in range(half):
        m[NOPE + half + i, NOPE + i] = 1
        m[NOPE + i, NOPE + half + i] = 1
    put("perm_mla", m)
    m = np.zeros((P, P))
    for h in range(2):
        for i in range(8):
            m[h * 64 + 8 + i, h * 64 + i] = 1
            m[h * 64 + i, h * 64 + 8 + i] = 1
    put("perm_dsa", m)
    put("eps", np.full((P, 1), EPS))
    put("gn_eps", np.full((P, 1), HD * 1e-5))
    inv = 10000.0 ** (-np.arange(0, ROPE, 2, dtype=np.float32) / ROPE)
    col = np.zeros((P, 1))
    col[NOPE:NOPE + ROPE, 0] = np.concatenate([inv, inv])
    put("invf", col)
    sg = np.zeros((P, 1))
    sg[NOPE:NOPE + half], sg[NOPE + half:NOPE + ROPE] = -1, 1
    put("rsign", sg)
    put("ntime", -(np.arange(S).reshape(4, P).T / (S - 1)))
    return c


def filter_constants():
    bands = (HY_EMB - 1) // 2
    n = np.arange(S, dtype=np.float32)
    fr = np.linspace(1e-4, bands - 1, bands, dtype=np.float32)
    ang = np.float32(2 * np.pi / S) * n[:, None] * fr[None, :]
    z = np.concatenate([(n / np.float32(S - 1))[:, None], np.cos(ang), -np.sin(ang)], axis=-1)
    deltas = np.abs(np.linspace(np.log(1e-2) / 1.5, np.log(1e-2) / 0.3, D, dtype=np.float32))
    return np.ascontiguousarray(z.T.astype(np.float32)), np.ascontiguousarray(np.tile(deltas, (P, 1)))


def weight_stream(a):
    fw, inv = dft_tables()
    z = np.zeros
    f32 = np.float32
    w_in = a["hy_w_in"][0]
    parts = {
        "hy_in": tall(np.concatenate([w_in[:, D:2 * D], w_in[:, 2 * D:], w_in[:, :D]], axis=1)),
        "hy_dft": fw, "hy_idft": inv, "hy_out": tall(a["hy_w_out"][0]),
    }
    for i in range(2):
        parts[f"up{i}"] = tall(pairs(a["ff_w_up"][i]))
        parts[f"down{i}"] = deep(a["ff_w_down"][i])
    w1 = a["rw_w1"][0]
    lora1 = [np.concatenate([w1[0], w1[1]], axis=1), np.concatenate([a["rw_a1"][0], z((D, 64), f32)], axis=1),
             a["rw_g1"][0]]
    parts.update({
        "rw_lora1": tall(np.concatenate(lora1, axis=1)),
        "rw_r": tall(a["rw_w_r"][0]), "rw_k": tall(a["rw_w_k"][0]), "rw_v": tall(a["rw_w_v"][0]),
        "rw_a2": np.concatenate([a["rw_a2"][0], z((64, D), f32)])[None],
        "rw_w2": a["rw_w2"][0].reshape(1, P, D), "rw_g2": a["rw_g2"], "rw_o": tall(a["rw_w_o"][0]),
    })
    w = a["w_in_2"][0]
    rot = z((D, P), f32)
    rot[:, NOPE:QKD] = w[:, 384:416]
    br = [a[n][0].reshape(2, P, D) for n in ("w_br_mla_2", "w_br_sg_2", "w_br_conv_2", "w_br_pool_2")]
    parts.update({
        "in2": tall(np.concatenate([w[:, :384], rot, w[:, 416:1952]], axis=1)), "gate2": tall(w[:, 1952:]),
        "br2_0": br[0], "br2_1": br[1], "br2_2": br[2], "br2_3": br[3], "out2": tall(a["w_out_2"][0]),
        "ff1_2": tall(a["w_ff1_2"][0]), "ff2_2": deep(a["w_ff2_2"][0]),
    })
    w = a["w_in_3"][0]
    q, k, v, iq, ik, iw, ca, cg = np.split(w, np.cumsum([512, 512, 512, 512, 64, 8, 512]), axis=1)
    iws = z((1, P, SLAB), f32)
    iws[0, :, :DT * AH] = iw.reshape(DT, P, AH).transpose(1, 0, 2).reshape(P, DT * AH)
    parts.update({
        "ada3": tall(a["w_ada_3"][0]), "in3": tall(np.concatenate([ca, cg, iq, ik, ik, q, k], axis=1)), "iw3": iws,
        "v3": v.reshape(4, 2, P, S).transpose(0, 2, 1, 3).reshape(4, P, SLAB), "out3": tall(a["w_out_3"][0]),
        "ff1_3": tall(a["w_ff1_3"][0]), "ff2_3": deep(a["w_ff2_3"][0]),
    })
    out = [parts[n] if n in parts else z((s, P, SLAB), f32) for n, _, _, s in STREAM]
    for (n, _, _, s), part in zip(STREAM, out):
        assert part.shape == (s, P, SLAB), (n, part.shape)
    return np.concatenate(out)


def parameters(a):
    order = lambda v: np.concatenate([v[..., D:2 * D], v[..., 2 * D:], v[..., :D]], axis=-1)
    p = {
        "norm_mix": vec(a["norm_mix_g"]), "norm_ffn": vec(a["norm_ffn_g"]), "final_norm": vec(a["final_norm_g"]),
        "hy_b_in": vec(order(a["hy_b_in"][0])), "hy_conv_w": vec(order(a["hy_conv_w"][0])),
        "hy_conv_b": vec(order(a["hy_conv_b"][0])), "hy_skip": vec(a["hy_skip"]), "hy_b_out": vec(a["hy_b_out"]),
        "hy_f_b": np.concatenate([col64(a["hy_f_b1"]), col64(a["hy_f_b2"]), col64(a["hy_f_b3"])], axis=1),
        "hy_f_freq": col64(a["hy_f_freq"]),
        "ff_conv_w": vec(pairs(a["ff_conv_w"])), "ff_conv_b": vec(pairs(a["ff_conv_b"])),
    }
    p.update({"rw_" + n: vec(a["rw_" + n]) for n in ("mu", "w0", "a0", "k_k", "k_a", "r_k", "ln_w", "ln_b")})
    p.update({
        "norm_mix_pre2": vec(a["norm_mix_pre_2"]), "gate_b2": vec(a["gate_b_2"]), "q_norm2": vec(a["q_norm_2"]),
        "kv_norm2": vec(a["kv_norm_2"]), "sg_ln_g2": vec(a["sg_ln_g_2"]), "sg_ln_b2": vec(a["sg_ln_b_2"]),
        "conv_w2": vec(a["conv_w_2"]), "pool_scale2": vec(a["pool_scale_2"]),
        "norm_mix_post2": vec(a["norm_mix_post_2"]), "norm_ffn_pre2": vec(a["norm_ffn_pre_2"]),
        "norm_ffn_post2": vec(a["norm_ffn_post_2"]),
    })
    two = lambda g: vec(np.concatenate([g[0], g[0]]))
    p.update({
        "c3": vec(a["c_3"]), "b_ada3": vec(a["b_ada_3"]), "g_norm13": vec(a["g_norm1_3"]), "g_q3": two(a["g_q_3"]),
        "g_k3": two(a["g_k_3"]), "w_dw3": a["w_dw_3"][0].reshape(CONVK, 4, P).transpose(2, 1, 0).reshape(P, -1),
        "b_dw3": vec(a["b_dw_3"]), "g_conv_ln3": vec(a["g_conv_ln_3"]), "b_conv_ln3": vec(a["b_conv_ln_3"]),
        "g_out_attn3": vec(a["g_out_attn_3"]), "g_out_conv3": vec(a["g_out_conv_3"]), "g_norm23": vec(a["g_norm2_3"]),
    })
    cols = [p[n] if n in p else np.zeros((P, w), np.float32) for n, w in PARAMS]
    for (n, w), c in zip(PARAMS, cols):
        assert c.shape == (P, w), (n, c.shape)
    return np.ascontiguousarray(np.concatenate(cols, axis=1))


def small_two(a):
    kv = a["w_ukv_2"][0].reshape(P, MLA_H, NOPE + VH)
    pw = a["pool_w_2"][0]
    return np.ascontiguousarray(np.concatenate([
        a["w_uq_2"][0].reshape(2, P, MLA_H * QKD).transpose(1, 0, 2).reshape(P, -1),
        kv[:, :, :NOPE].reshape(P, -1), kv[:, :, NOPE:].reshape(P, -1),
        a["sg_w_2"][0].transpose(2, 0, 1).reshape(P, -1),
        pw.reshape(2, 2, 64, 64).transpose(1, 2, 0, 3).reshape(P, -1),
        np.triu(np.ones((P, P), np.float32))], axis=1))


def window_counts():
    t = np.arange(S)
    c = np.stack([1.0 / np.minimum(t + 1, w) for w in POOL_WIN])
    return np.ascontiguousarray(np.repeat(c, 64, axis=0).reshape(2, P, S).transpose(1, 0, 2).astype(np.float32))


def rotation():
    inv = (500000.0 ** (-np.arange(0, 16, 2, dtype=np.float32) / 16)).astype(np.float32)
    ang = np.arange(S, dtype=np.float32)[None, :] * inv[:, None]
    c, s = np.ones((2, 64, S), np.float32), np.zeros((2, 64, S), np.float32)
    c[:, 0:8] = c[:, 8:16] = np.cos(ang)
    s[:, 0:8], s[:, 8:16] = -np.sin(ang), np.sin(ang)
    return c.reshape(P, S), s.reshape(P, S)


PHASES = 99


def host_arrays(a):
    z, delta = filter_constants()
    x = np.ascontiguousarray(a["x"][0].T.reshape(DT, P, S).transpose(1, 0, 2))
    return {
        "x": x, "par": parameters(a), "cst": constants(), "weights": weight_stream(a),
        "hy_z": z, "hy_delta": delta, "hy_f_w1": np.ascontiguousarray(a["hy_f_w1"][0]),
        "hy_f_w23": np.ascontiguousarray(np.concatenate([a["hy_f_w2"][0], a["hy_f_w3"][0]], axis=1)),
        "hy_f_w4": np.ascontiguousarray(a["hy_f_w4"][0]),
        "sm2": small_two(a), "sg_b": np.ascontiguousarray(a["sg_b_2"][0].reshape(1, 4 * SGC)),
        "rcnt": window_counts(), "pos": np.ascontiguousarray(a["positions_2"].reshape(S).astype(np.int32)),
        "rotc": rotation()[0], "rots": rotation()[1],
    }


def kernel(**inputs):
    import concourse.bacc as bacc
    from concourse.bass_utils import run_bass_kernel_spmd

    arrays = host_arrays({k: np.asarray(v) for k, v in inputs.items()})
    nc = bacc.Bacc("TRN2", target_bir_lowering=False, num_devices=1)
    d = {n: nc.dram_tensor(f"in_{n}", list(a.shape), mybir.dt.from_np(a.dtype), kind="ExternalInput").ap()
         for n, a in arrays.items()}
    out = nc.dram_tensor("out_x", [DT, P, S], F32, kind="ExternalOutput").ap()
    build(nc, d, out, PHASES)
    r = run_bass_kernel_spmd(nc, [{f"in_{n}": a for n, a in arrays.items()}], core_ids=[0])
    y = r.results[0]["out_x"]
    return np.ascontiguousarray(y.reshape(D, S).T).reshape(1, S, D)
```

```python
from contextlib import ExitStack, nullcontext

import numpy as np

import concourse.bass as bass
from concourse import mybir

F32 = mybir.dt.float32
F32R = mybir.dt.float32r
I32 = mybir.dt.int32
ACT = mybir.ActivationFunctionType
ALU = mybir.AluOpType
AX = mybir.AxisListType

P = 128
S = 512
D = 1024
DT = D // P
F1 = 2816
F1T = F1 // P
F2T = 4 * D // P
RING = 4
PARTS = 2
SLAB = 1024
BANKS = 4
NT = 66
EPS = 1e-6
NEG = -1e30

HD = 64
CH = 64
NCH = S // CH
KAPPA = float(np.exp(-0.5))
LEVELS = 6

HY_EMB, HY_W = 33, 64

MLA_H, NOPE, ROPE, VH = 4, 64, 32, 64
QKD = NOPE + ROPE
SGC = 128
POOL_WIN = (2, 4, 8, 16)

AH = 8
CONVK = 31
TOPK = 128

PARAMS = [
    ("norm_mix", 16), ("norm_ffn", 16), ("final_norm", 8),
    ("hy_b_in", 24), ("hy_conv_w", 72), ("hy_conv_b", 24), ("hy_skip", 8), ("hy_b_out", 8),
    ("hy_f_b", 3), ("hy_f_freq", 1),
    ("rw_mu", 48), ("rw_w0", 16), ("rw_a0", 8), ("rw_k_k", 8), ("rw_k_a", 8), ("rw_r_k", 8),
    ("rw_ln_w", 8), ("rw_ln_b", 8),
    ("ff_conv_w", 2 * 3 * 2 * F1T), ("ff_conv_b", 2 * 2 * F1T),
    ("norm_mix_pre2", 8), ("gate_b2", 32), ("q_norm2", 2), ("kv_norm2", 1), ("sg_ln_g2", 2), ("sg_ln_b2", 2),
    ("conv_w2", 6), ("pool_scale2", 2), ("norm_mix_post2", 8), ("norm_ffn_pre2", 8), ("norm_ffn_post2", 8),
    ("c3", 8), ("b_ada3", 48), ("g_norm13", 8), ("g_q3", 1), ("g_k3", 1), ("w_dw3", 4 * CONVK), ("b_dw3", 4),
    ("g_conv_ln3", 4), ("b_conv_ln3", 4), ("g_out_attn3", 4), ("g_out_conv3", 4), ("g_norm23", 8),
]
POFF, NPAR = {}, 0
for _name, _w in PARAMS:
    POFF[_name] = NPAR
    NPAR += _w

CONSTS = [("ident", 128), ("ones", 128), ("bones", 128), ("eye64", 64), ("strict", 128), ("incl", 128),
          ("level", (LEVELS + 1) * 64), ("causal", 128), ("chunked", 64), ("perm_mla", 96), ("perm_dsa", 128),
          ("eps", 1), ("gn_eps", 1), ("invf", 1), ("rsign", 1), ("ntime", 4)]
COFF, NCST = {}, 0
for _name, _w in CONSTS:
    COFF[_name] = NCST
    NCST += _w

STREAM = [
    ("hy_in", 24, 1, 24), ("hy_dft", 0, 0, 4), ("hy_idft", 8, 0, 4), ("hy_out", 8, 1, 8),
    ("up0", 2 * F1T, 1, 2 * F1T), ("down0", 8, 3, 24),
    ("rw_lora1", 3, 1, 3), ("rw_r", 8, 1, 8), ("rw_k", 8, 1, 8), ("rw_v", 8, 1, 8), ("rw_a2", 8, 0, 1),
    ("rw_w2", 16, 0, 1), ("rw_g2", 8, 0, 1), ("rw_o", 8, 1, 8),
    ("up1", 2 * F1T, 1, 2 * F1T), ("down1", 8, 3, 24),
    ("in2", 16, 1, 16), ("gate2", 32, 1, 32), ("br2_0", 8, 0, 2), ("br2_1", 8, 0, 2), ("br2_2", 8, 0, 2),
    ("br2_3", 8, 0, 2), ("out2", 8, 1, 8),
    ("ff1a_2", F2T // 2, 1, F2T // 2), ("ff2a_2", 8, 2, 16), ("ff1b_2", F2T // 2, 1, F2T // 2), ("ff2b_2", 8, 2, 16),
    ("ada3", 0, 0, 48), ("in3", 21, 1, 21), ("iw3", 4, 0, 1), ("v3", 4, 0, 4), ("out3", 8, 1, 8),
    ("ff1a_3", F2T // 2, 1, F2T // 2), ("ff2a_3", 8, 2, 16), ("ff1b_3", F2T // 2, 1, F2T // 2), ("ff2b_3", 8, 2, 16),
]
SPLIT = [("up0", "down0"), ("up1", "down1"), ("in2",), ("ff1a_2", "ff2a_2", "ff1b_2", "ff2b_2"), ("in3",),
         ("ff1a_3", "ff2a_3", "ff1b_3", "ff2b_3")]


class Stage:

    def __init__(self, name, tiles, per_tile, slabs, slab0, tile0, shared0):
        self.name, self.tiles, self.per_tile, self.slabs = name, tiles, per_tile, slabs
        self.slab0, self.tile0, self.shared0 = slab0, tile0, shared0
        self.split0 = self.run_end = None


STAGE = {}
NSLAB = _tile = _shared = 0
for _name, _n, _s, _all in STREAM:
    STAGE[_name] = Stage(_name, _n, _s, _all, NSLAB, _tile, _shared)
    NSLAB += _all
    _tile += _n
    _shared += 0 if _s or not _n else _n - 1
_split = 0
for _run in SPLIT:
    for _name in _run:
        STAGE[_name].split0, STAGE[_name].run_end = _split, STAGE[_run[-1]].slab0 + STAGE[_run[-1]].slabs
        _split += STAGE[_name].slabs


class Steps:

    def __init__(self, eng, sem):
        self.eng, self.sem, self.n = eng, sem, 0

    def go(self, ins):
        ins.then_inc(self.sem, 1)
        self.n += 1

    def carry(self):
        self.eng.sem_inc(self.sem, 1)
        self.n += 1

    def settle(self):
        if self.n:
            self.eng.wait_ge(self.sem, self.n)

    def __call__(self, ins):
        self.go(ins)
        self.settle()

    def tell(self, *sems):
        self.settle()
        for s in sems:
            self.eng.sem_inc(s, 1)

    def restart(self):
        self.settle()
        if self.n:
            self.eng.sem_clear(self.sem)
        self.n = 0


class Tile:

    def __init__(self, st, j, it, body):
        self.st, self.j, self.it, self.body = st, j, it, body
        self.idx = j if it is None else it * body + j
        self.bank = (st.tile0 + j) % BANKS

    def ready(self):
        v = self.st.slab0 + (self.j + 1) * self.st.per_tile
        return v if self.it is None else self.it * (self.body * self.st.per_tile) + v

    def bank_uses(self):
        v = (self.st.tile0 + self.j) // BANKS
        return v if self.it is None else self.it * (self.body // BANKS) + v


def loop_tiles(eng, st, steps=None, body=8):
    full = st.tiles // body if st.per_tile and st.tiles >= 2 * body else 0
    if full:
        if steps:
            steps.restart()
        with eng.Fori(0, full) as it:
            for j in range(body):
                yield Tile(st, j, it, body)
            if steps:
                steps.restart()
    for j in range(full * body, st.tiles):
        yield Tile(st, j, None, body)


def build(nc, d, out, phases=99):
    ctx = ExitStack()
    with ctx:
        sems = {}

        def sem(name):
            if name not in sems:
                sems[name] = ctx.enter_context(nc.semaphore(name))
            return sems[name]

        def sb(name, shape, dt=F32):
            return ctx.enter_context(nc.sbuf_tensor(name, shape, dt))

        with nc.sbuf_tensor("w_high", [P, PARTS, SLAB], F32R) as w_high, \
                nc.sbuf_tensor("w_low", [P, PARTS, SLAB], F32R) as w_low:
            pass
        scratch = sb("scratch", [P, 2 * PARTS, SLAB])

        def in_arena(*tensors):
            with ExitStack() as place:
                return [place.enter_context(nc.sbuf_tensor(n, [P, tiles, S], F32R)) for n, tiles in tensors]

        ffG_high, ffG_low, _, ffH = in_arena(("ffn1_high", F1T), ("ffn1_low", F1T), ("gap1", 4), ("ffn1_h", 2 * DT))
        _, f_high, f_low, fH = in_arena(("gap2", 16), ("ffn2_high", F2T // 2), ("ffn2_low", F2T // 2),
                                        ("ffn2_h", 2 * DT))
        _, bH = in_arena(("gap3", 16), ("in2_h", 2 * DT))
        _, H3 = in_arena(("gap4", 35), ("in3_h", 2 * DT))
        arena = sb("arena", [P, NT, S])
        ring = sb("ring", [P, RING, SLAB])
        X = sb("X", [P, DT, S])
        H = sb("H", [P, DT, S])
        root = sb("root", [P, S])
        par = sb("par", [P, NPAR])
        cst = sb("cst", [P, NCST])
        gp = ctx.enter_context(nc.psum_tensor("gp", [P, BANKS, S], F32))
        aux = ctx.enter_context(nc.psum_tensor("aux", [P, BANKS, S], F32))

        def pcol(name, i=0):
            return par[:, bass.ds(POFF[name] + i, 1)]

        def const(name, lo=0, hi=None):
            w = dict(CONSTS)[name]
            return cst[:, COFF[name] + lo:COFF[name] + (w if hi is None else hi)]

        ident, ones, bones = const("ident"), const("ones"), const("bones")

        landed = [sem(f"landed{i}") for i in range(RING)]
        slab_done = sem("slab_done")
        shared_done = sem("shared_done")
        drained = [sem(f"drained{i}") for i in range(BANKS)]
        x_ready = sem("x_ready")
        h_ready = sem("h_ready")
        inputs_in = sem("inputs_in")
        sum_ready, stat_ready = sem("sum_ready"), sem("stat_ready")
        sq_ready = sem("sq_ready")
        out_stored = sem("out_stored")
        pe_s = sem("pe_steps")

        class Count:

            def __init__(self):
                self.x = self.h = self.sums = self.sq = 0

        def slab_wait(pe, slab, it=None, per_it=0):
            v = 16 * (slab // RING + 1)
            pe.wait_ge(landed[slab % RING], v if it is None else it * (16 * per_it // RING) + v)

        def bank_wait(pe, t):
            if t.it is not None or t.st.tile0 + t.j >= BANKS:
                pe.wait_ge(drained[t.bank], t.bank_uses())

        def stream_pe(pe, name, rhs, ksizes=None, width=P, before=None, body=8):
            st = STAGE[name]
            kt = ksizes or [DT] * st.per_tile
            for t in loop_tiles(pe, st, None, body):
                if before:
                    before(t)
                bank_wait(pe, t)
                k = 0
                for s, n in enumerate(kt):
                    slab = st.slab0 + t.j * st.per_tile + s
                    slab_wait(pe, slab, t.it, t.body * st.per_tile)
                    for i in range(n):
                        last = nc.tensor.matmul(gp[0:width, t.bank, :], ring[:, slab % RING, i * P:i * P + width],
                                                rhs(k, t), start=(k == 0), stop=(k == sum(kt) - 1))
                        k += 1
                    last.then_inc(slab_done, 1)

        high_ready, low_ready = sem("high_ready"), sem("low_ready")

        def split_act(act, slab, st, it=None, per_it=0):
            v = 16 * (slab // RING + 1)
            act.wait_ge(landed[slab % RING], v if it is None else it * (16 * per_it // RING) + v)
            nc.scalar.activation(w_high[:, slab % PARTS, :], ring[:, slab % RING, :], ACT.Copy).then_inc(high_ready, 1)

        def split_first_act(act, name):
            st = STAGE[name]
            for s in range(PARTS):
                split_act(act, st.slab0 + s, st)

        def split_ahead_act(act, t):
            st, per = t.st, t.st.per_tile
            for s in range(per):
                slab = st.slab0 + t.j * per + s
                if t.it is None and slab + PARTS >= st.run_end:
                    continue
                act.wait_ge(slab_done, slab + 1 if t.it is None else t.it * (t.body * per) + (slab + 1))
                split_act(act, slab + PARTS, st, t.it, t.body * per)

        def split_stage_act(act, a, name, body=8):
            for t in loop_tiles(act, STAGE[name], a, body):
                split_ahead_act(act, t)

        def split_pool(pool, g, run, lo=0, hi=None):
            st = STAGE[run[0]]
            n = (st.run_end - st.slab0 if hi is None else hi) - lo
            slab0, split0, body = st.slab0 + lo, st.split0 + lo, 8

            def low(slab, count):
                pool.wait_ge(high_ready, count)
                nc.gpsimd.tensor_tensor(w_low[:, slab % PARTS, :], ring[:, slab % RING, :], w_high[:, slab % PARTS, :],
                                        ALU.subtract).then_inc(low_ready, 1)

            if n >= body:
                with pool.Fori(0, n // body) as it:
                    for j in range(body):
                        low(slab0 + j, it * body + (split0 + j + 1))
            for j in range(n // body * body, n):
                low(slab0 + j, split0 + j + 1)

        def split_pe(pe, name, high, low, ksizes=None, before=None, body=8):
            st = STAGE[name]
            kt = ksizes or [DT] * st.per_tile
            for t in loop_tiles(pe, st, None, body):
                bank_wait(pe, t)
                k = 0
                for s, n in enumerate(kt):
                    j = t.j * st.per_tile + s
                    slab = st.slab0 + j
                    pe.wait_ge(low_ready, st.split0 + j + 1 if t.it is None else
                               t.it * (t.body * st.per_tile) + (st.split0 + j + 1))
                    for i in range(n):
                        if before and t.j == 0:
                            before(k)
                        w = slice(i * P, (i + 1) * P)
                        for q, (wt, x) in enumerate(((w_high, high), (w_high, low), (w_low, high))):
                            last = nc.tensor.matmul(gp[:, t.bank, :], wt[:, slab % PARTS, w], x(k),
                                                    start=(k == 0 and q == 0), stop=(k == sum(kt) - 1 and q == 2))
                        k += 1
                    last.then_inc(slab_done, 1)

        def tiles_of(tensor, base=0):
            return lambda k: tensor[:, base + k, :]

        def split_h_dve(dve, v, parts, make):
            made = []
            for k in range(DT + 2):
                if k < DT:
                    v.go(make(k))
                    made.append(v.n)
                if 1 <= k <= DT:
                    dve.wait_ge(v.sem, made[k - 1])
                    v.go(nc.vector.tensor_copy(parts[:, k - 1, :], H[:, k - 1, :]))
                    made[k - 1] = v.n
                if k >= 2:
                    dve.wait_ge(v.sem, made[k - 2])
                    nc.vector.tensor_tensor(parts[:, DT + k - 2, :], H[:, k - 2, :], parts[:, k - 2, :],
                                            ALU.subtract).then_inc(h_ready, 1)
            v.settle()
            n_dve.h += DT

        def split_norm_dve(dve, v, gain, parts, g0=0):
            n_dve.sums += 1
            dve.wait_ge(stat_ready, n_dve.sums)
            v(nc.vector.reciprocal(root[:], root[:]))
            split_h_dve(dve, v, parts, lambda k: nc.vector.scalar_tensor_tensor(
                out=H[:, k, :], in0=X[:, k, :], scalar=pcol(gain, g0 + k), in1=root[:], op0=ALU.mult, op1=ALU.mult))

        def h_parts_before(pe):
            n_pe.h += DT
            base = n_pe.h - DT
            return lambda k: pe.wait_ge(h_ready, base + k + 1)

        def split_tile_dve(dve, v, src, high, low, done):
            v(nc.vector.tensor_copy(high, src))
            v.go(nc.vector.tensor_tensor(low, src, high, ALU.subtract))
            v.tell(done)

        def consume_wait(eng, t):
            st = t.st
            if st.per_tile:
                eng.wait_ge(slab_done, t.ready())
            elif t.j < st.tiles - 1:
                eng.wait_ge(shared_done, st.shared0 + t.j + 1)
            else:
                eng.wait_ge(slab_done, st.slab0 + st.slabs)

        def shared_tile_done(t, last):
            if t.j < t.st.tiles - 1:
                last.then_inc(shared_done, 1)

        def at(base, t, per):
            return base + per * t.j if t.it is None else t.it * (per * t.body) + (base + per * t.j)

        def norm_act(act, a, n, src, sq, src_wait, scale, eps="eps", root_wait=None):
            for k in range(n):
                src_wait(k)
                nc.scalar.activation(sq(k), src(k), ACT.Square).then_inc(sq_ready, 1)
            n_act.sums += 1
            act.wait_ge(sum_ready, n_act.sums)
            if root_wait:
                root_wait()
            nc.scalar.activation(root[:], aux[:, 0, :], ACT.Sqrt, scale=scale, bias=const(eps)).then_inc(stat_ready, 1)

        def norm_pe(pe, n, sq):
            if n_pe.sums:
                pe.wait_ge(stat_ready, n_pe.sums)
            for k in range(n):
                n_pe.sq += 1
                pe.wait_ge(sq_ready, n_pe.sq)
                last = nc.tensor.matmul(aux[:, 0, :], ones, sq(k), start=(k == 0), stop=(k == n - 1))
            last.then_inc(sum_ready, 1)
            n_pe.sums += 1

        def norm_dve(dve, v, n, src, gain, dst, done):
            n_dve.sums += 1
            dve.wait_ge(stat_ready, n_dve.sums)
            v(nc.vector.reciprocal(root[:], root[:]))
            for k in range(n):
                nc.vector.scalar_tensor_tensor(out=dst(k), in0=src(k), scalar=gain(k), in1=root[:],
                                               op0=ALU.mult, op1=ALU.mult).then_inc(done, 1)

        n_pe, n_act, n_dve = Count(), Count(), Count()
        Xk, Hk = (lambda k: X[:, k, :]), (lambda k: H[:, k, :])

        def arena_tiles(base):
            return lambda k: arena[:, base + k, :]

        def x_wait(eng, count):
            base = count.x - DT

            def wait(k):
                if base >= 0:
                    eng.wait_ge(x_ready, base + k + 1)
                else:
                    eng.wait_ge(inputs_in, INPUTS)
            return wait

        INPUTS = 16 * 3

        def pre_norm_act(act, a):
            norm_act(act, a, DT, Xk, Hk, x_wait(act, n_act), 1.0 / D)
            n_act.x += DT

        def pre_norm_dve(dve, v, gain, g0=0):
            norm_dve(dve, v, DT, Xk, lambda k: pcol(gain, g0 + k), Hk, h_ready)
            n_dve.h += DT

        def h_before(pe):
            n_pe.h += DT
            need = n_pe.h

            def before(t):
                if t.j == 0:
                    pe.wait_ge(h_ready, need)
            return before

        def residual_dve(dve, v, name, bias=None, body=8):
            st = STAGE[name]
            for t in loop_tiles(dve, st, v, body):
                consume_wait(dve, t)
                if bias is None:
                    ins = nc.vector.tensor_tensor(X[:, t.idx, :], gp[:, t.bank, :], X[:, t.idx, :], ALU.add)
                else:
                    ins = nc.vector.scalar_tensor_tensor(out=X[:, t.idx, :], in0=gp[:, t.bank, :],
                                                         scalar=bias(t.idx), in1=X[:, t.idx, :],
                                                         op0=ALU.add, op1=ALU.add)
                v.go(ins)
                v.tell(drained[t.bank], x_ready)
            n_dve.x += DT

        def copy_act(act, a, name, dst, func=ACT.Copy, bias=None, rows=P, done=None, body=8):
            st = STAGE[name]
            for t in loop_tiles(act, st, a, body):
                if st.split0 is not None:
                    split_ahead_act(act, t)
                consume_wait(act, t)
                kw = {} if bias is None else {"bias": bias(t.idx)}
                a.go(nc.scalar.activation(dst(t.idx), gp[0:rows, t.bank, :], func, **kw))
                a.tell(*([drained[t.bank]] + ([done] if done else [])))

        hX1, hU, hX0, hKS, hKD, hDEC, hYR, hYI, hTMP = 0, 8, 16, 24, 32, 40, 48, 56, 64
        hUT = hDEC
        f_in = sem("hy_filter_in")
        f_w4 = arena[0:HY_W, hYR:hYR + 4, :].rearrange("p a b -> p (a b)")
        f_delta = arena[:, hYR + 4:hYR + 6, :].rearrange("p a b -> p (a b)")
        f_z = arena[0:HY_EMB, hYR + 6, :]
        f_w = arena[0:HY_W, hYR + 7, 0:3 * HY_W]
        f_h = [arena[0:HY_W, hYI + i, :] for i in range(3)]
        f_t = [arena[0:HY_W, hYI + 3 + i, :] for i in range(2)]
        f_pre, f_arg, f_sin = sem("f_pre"), sem("f_arg"), sem("f_sin")
        f_k, f_kread = sem("f_k"), sem("f_kread")
        f_dec, f_comb = sem("f_dec"), sem("f_comb")
        hz_ready, hz_used, hc_ready = sem("hz_ready"), sem("hz_used"), sem("hc_ready")
        u_ready, ut_psum, ut_ready = sem("u_ready"), sem("ut_psum"), sem("ut_ready")
        dft_set, kspec, yspec = sem("dft_set"), sem("kspec"), sem("yspec")
        hy_ready = sem("hy_ready")
        TWO_PI_HI = 6.28125
        TWO_PI_LO = float(2 * np.pi - 6.28125)
        MAGIC = 12582912.0

        def reduce_angle(v, eng, x, tmp, shift=0.0):
            v(eng.tensor_scalar(tmp, x, float(1 / (2 * np.pi)), MAGIC + shift, ALU.mult, ALU.add) if not shift else
              eng.tensor_scalar(tmp, x, float(1 / (2 * np.pi)), shift, ALU.mult, ALU.add))
            if shift:
                v(eng.tensor_scalar(tmp, tmp, MAGIC, None, ALU.add))
            v(eng.tensor_scalar(tmp, tmp, -MAGIC, None, ALU.add))
            v(eng.scalar_tensor_tensor(out=x, in0=tmp, scalar=-TWO_PI_HI, in1=x, op0=ALU.mult, op1=ALU.add))
            v(eng.scalar_tensor_tensor(out=x, in0=tmp, scalar=-TWO_PI_LO, in1=x, op0=ALU.mult, op1=ALU.add))

        def hyena_pe(pe):
            pe.wait_ge(f_in, 16 * 5)
            pe.wait_ge(inputs_in, INPUTS)
            for i in range(3):
                if i:
                    pe.wait_ge(f_sin, i)
                rows = HY_EMB if i == 0 else HY_W
                nc.tensor.matmul(aux[0:HY_W, 1, :], f_w[0:rows, i * HY_W:(i + 1) * HY_W],
                                 f_z if i == 0 else f_h[i - 1], start=True, stop=True).then_inc(f_pre, 1)
            norm_pe(pe, DT, Hk)
            pe.wait_ge(f_sin, 3)
            for tk in range(4):
                for c in range(2):
                    n = tk * 2 + c
                    for b in range(2):
                        if 2 * n + b >= 2:
                            pe.wait_ge(f_kread, 2 * n + b - 1)
                        nc.tensor.matmul(aux[:, 2 + b, :], f_h[2][:, tk * P:(tk + 1) * P],
                                         f_w4[:, b * D + c * S:b * D + (c + 1) * S],
                                         start=True, stop=True).then_inc(f_k, 1)
            stream_pe(pe, "hy_in", lambda k, t: H[:, k, :], before=h_before(pe))
            pe.wait_ge(f_kread, 16)
            for i in range(DT):
                pe.wait_ge(u_ready, i + 1)
                if i >= 2:
                    pe.wait_ge(ut_ready, i - 1)
                for tk in range(4):
                    last = nc.tensor.transpose(aux[:, 2 + i % 2, tk * P:(tk + 1) * P],
                                               arena[:, hU + i, tk * P:(tk + 1) * P], ident)
                last.then_inc(ut_psum, 1)
            pe.wait_ge(ut_ready, DT)
            pe.wait_ge(f_comb, 8)
            for b in range(BANKS):
                pe.wait_ge(drained[b], 24 // BANKS)
            st = STAGE["hy_dft"]
            for j in range(4):
                slot = (st.slab0 + j) % RING
                slab_wait(pe, st.slab0 + j)
                for c in range(2):
                    ps = gp if c == 0 else aux
                    if j:
                        pe.wait_ge(yspec, 2 * (j - 1) + c + 1)
                    for q, (lo, base) in enumerate(((0, hUT), (P, hUT), (0, hKS), (P, hKD))):
                        for tk in range(4):
                            last = nc.tensor.matmul(ps[:, q, :],
                                                    ring[:, slot, tk * 256 + lo:tk * 256 + lo + P],
                                                    arena[:, base + 2 * tk + c, :], start=(tk == 0), stop=(tk == 3))
                    if j == 0:
                        for tk in range(4):
                            last = nc.tensor.matmul(ps[0:1, 3, :], ring[:, slot, tk * 256 + P:tk * 256 + P + 1],
                                                    arena[:, hKS + 2 * tk + c, :], start=(tk == 0), stop=(tk == 3))
                    last.then_inc(dft_set if c == 0 else slab_done, 1)
            pe.wait_ge(yspec, 8)
            st = STAGE["hy_idft"]
            for t in loop_tiles(pe, st):
                bank_wait(pe, t)
                for s in range(4):
                    slot = (st.slab0 + s) % RING
                    if t.j == 0:
                        slab_wait(pe, st.slab0 + s)
                    for f in range(2):
                        fi = (s % 2) * 2 + f
                        y = arena[:, (hYR if s < 2 else hYI) + 2 * fi + t.j // 4, (t.j % 4) * P:(t.j % 4 + 1) * P]
                        last = nc.tensor.matmul(gp[:, t.bank, :], y, ring[:, slot, f * S:(f + 1) * S],
                                                start=(s == 0 and f == 0), stop=(s == 3 and f == 1))
                    if t.j == st.tiles - 1:
                        last.then_inc(slab_done, 1)
                shared_tile_done(t, last)
            pe.wait_ge(hy_ready, DT)
            stream_pe(pe, "hy_out", lambda k, t: arena[:, hU + k, :])

        def hyena_act(act, a):
            for i in range(3):
                act.wait_ge(f_arg, i + 1)
                nc.scalar.activation(f_h[i], f_t[0], ACT.Sin).then_inc(f_sin, 1)
            for tk in range(4):
                for c in range(2):
                    nc.scalar.activation(arena[:, hDEC + 2 * tk + c, :], f_delta[:, c * S:(c + 1) * S], ACT.Exp,
                                         scale=const("ntime", tk, tk + 1)).then_inc(f_dec, 1)
            pre_norm_act(act, a)
            for t in loop_tiles(act, STAGE["hy_in"], a):
                consume_wait(act, t)
                act.wait_ge(hz_used, at(1, t, 1))
                a.go(nc.scalar.activation(arena[:, hTMP + t.j % 2, :], gp[:, t.bank, :], ACT.Identity,
                                          bias=pcol("hy_b_in", t.idx)))
                a.tell(drained[t.bank])
                nc.scalar.activation(arena[:, hX1 + t.idx, :], arena[:, hTMP + t.j % 2, :], ACT.Identity,
                                     scale=pcol("hy_conv_w", 24 + t.idx),
                                     bias=pcol("hy_conv_b", t.idx)).then_inc(hz_ready, 1)
            for i in range(DT):
                act.wait_ge(ut_psum, i + 1)
                dst = arena[:, hUT:hUT + 8, :].rearrange("p (t c) s -> p t (c s)", c=2)[:, :, i * P:(i + 1) * P]
                if i == 0:
                    act.wait_ge(f_comb, 8)
                nc.scalar.activation(dst, aux[:, 2 + i % 2, :].rearrange("p (t c) -> p t c", t=4),
                                     ACT.Copy).then_inc(ut_ready, 1)
            st = STAGE["hy_dft"]
            for j in range(4):
                for c in range(2):
                    ps = gp if c == 0 else aux
                    if c == 0:
                        act.wait_ge(dft_set, j + 1)
                    else:
                        act.wait_ge(slab_done, st.slab0 + j + 1)
                    if j:
                        act.wait_ge(yspec, 2 * (j - 1) + c + 1)
                    a(nc.scalar.activation(arena[:, hX1 + 2 * c, :], ps[:, 2, :], ACT.Copy))
                    nc.scalar.activation(arena[:, hX1 + 2 * c + 1, :], ps[:, 3, :], ACT.Copy).then_inc(kspec, 1)

        def hyena_dve(dve, v):
            dve.sem_inc(hz_used, 2)
            dve.wait_ge(inputs_in, INPUTS)
            dve.wait_ge(f_in, 16 * 5)
            for i in range(3):
                dve.wait_ge(f_pre, i + 1)
                v(nc.vector.tensor_scalar(f_t[0], aux[0:HY_W, 1, :], pcol("hy_f_b", i)[0:HY_W],
                                          pcol("hy_f_freq")[0:HY_W], ALU.add, ALU.mult))
                reduce_angle(v, nc.vector, f_t[0], f_t[1])
                v.tell(f_arg)
            pre_norm_dve(dve, v, "norm_mix", 0)
            for n in range(8):
                dve.wait_ge(f_dec, n + 1)
                dec = arena[:, hDEC + n, :]
                kb = arena[:, hYI + 5 + n % 2, :]
                dve.wait_ge(f_k, 2 * n + 1)
                v(nc.vector.tensor_tensor(arena[:, hKD + n, :], aux[:, 2, :], dec, ALU.mult))
                v.tell(f_kread)
                dve.wait_ge(f_k, 2 * n + 2)
                v(nc.vector.tensor_tensor(kb, aux[:, 3, :], dec, ALU.mult))
                v.tell(f_kread)
                v(nc.vector.tensor_tensor(arena[:, hKS + n, :], arena[:, hKD + n, :], kb, ALU.add))
                v(nc.vector.tensor_tensor(arena[:, hKD + n, :], arena[:, hKD + n, :], kb, ALU.subtract))
                v.tell(f_comb)
            for t in loop_tiles(dve, STAGE["hy_in"], v):
                z, y = arena[:, hTMP + t.j % 2, :], arena[:, hX1 + t.idx, :]
                dve.wait_ge(hz_ready, at(1, t, 1))
                v(nc.vector.scalar_tensor_tensor(out=y[:, 1:S], in0=z[:, 0:S - 1], scalar=pcol("hy_conv_w", t.idx),
                                                 in1=y[:, 1:S], op0=ALU.mult, op1=ALU.add))
                v.go(nc.vector.scalar_tensor_tensor(out=y[:, 0:S - 1], in0=z[:, 1:S],
                                                    scalar=pcol("hy_conv_w", 48 + t.idx), in1=y[:, 0:S - 1],
                                                    op0=ALU.mult, op1=ALU.add))
                v.tell(hz_used)
            for i in range(DT):
                v.go(nc.vector.tensor_tensor(arena[:, hU + i, :], arena[:, hU + i, :], arena[:, hX1 + i, :], ALU.mult))
                v.tell(u_ready)
            for j in range(4):
                for c in range(2):
                    ps = gp if c == 0 else aux
                    dve.wait_ge(kspec, 2 * j + c + 1)
                    kr, ki = arena[:, hX1 + 2 * c, :], arena[:, hX1 + 2 * c + 1, :]
                    t1, t2, t3, t4 = (arena[:, hX1 + 4 + i, :] for i in range(4))
                    yr, yi = arena[:, hYR + 2 * j + c, :], arena[:, hYI + 2 * j + c, :]
                    v.go(nc.vector.tensor_tensor(t1, ps[:, 0, :], kr, ALU.mult))
                    v.go(nc.vector.tensor_tensor(t2, ps[:, 1, :], ki, ALU.mult))
                    v.go(nc.vector.tensor_tensor(t3, ps[:, 0, :], ki, ALU.mult))
                    v(nc.vector.tensor_tensor(t4, ps[:, 1, :], kr, ALU.mult))
                    v.go(nc.vector.tensor_tensor(yr, t1, t2, ALU.subtract))
                    v(nc.vector.tensor_tensor(yi, t3, t4, ALU.add))
                    if j == 0:
                        v.go(nc.vector.tensor_copy(yr[0:1, :], t1[0:1, :]))
                        v(nc.vector.tensor_copy(yi[0:1, :], t2[0:1, :]))
                    v.tell(yspec)
            for t in loop_tiles(dve, STAGE["hy_idft"]):
                consume_wait(dve, t)
                u = arena[:, hU + t.j, :]
                v(nc.vector.scalar_tensor_tensor(out=u, in0=u, scalar=pcol("hy_skip", t.j), in1=gp[:, t.bank, :],
                                                 op0=ALU.mult, op1=ALU.add))
                v.go(nc.vector.tensor_tensor(u, u, arena[:, hX0 + t.j, :], ALU.mult))
                v.tell(drained[t.bank], hy_ready)
            residual_dve(dve, v, "hy_out", lambda i: pcol("hy_b_out", i))

        ffT = 2 * F1T
        aff_ready, gate_conv, gate_act, pair_done = sem("aff_ready"), sem("gate_conv"), sem("gate_act"), sem("pair_done")

        def ffn1_pe(pe, layer):
            norm_pe(pe, DT, Hk)
            split_pe(pe, f"up{layer}", tiles_of(ffH), tiles_of(ffH, DT), before=h_parts_before(pe))
            pe.wait_ge(pair_done, (layer + 1) * F1T + 2)
            split_pe(pe, f"down{layer}", tiles_of(ffG_high), tiles_of(ffG_low), ksizes=[8, 8, 6])

        def ffn1_pool(pool, g, layer):
            split_pool(pool, g, (f"up{layer}", f"down{layer}"))

        def ff_cols(layer, t, tap):
            return pcol("ff_conv_w", layer * 6 * F1T + tap * 2 * F1T + t.idx)

        def ffn1_act(act, a, layer):
            pre_norm_act(act, a)
            split_first_act(act, f"up{layer}")
            base = layer * F1T
            for t in loop_tiles(act, STAGE[f"up{layer}"], a):
                tmp = arena[:, ffT + t.j % 4, :]
                split_ahead_act(act, t)
                consume_wait(act, t)
                p = t.j // 2 if t.it is None else t.it * 4 + t.j // 2
                act.wait_ge(pair_done, p + (base + 1))
                nc.scalar.activation(tmp, gp[:, t.bank, :], ACT.Identity, scale=ff_cols(layer, t, 1),
                                     bias=pcol("ff_conv_b", layer * 2 * F1T + t.idx)).then_inc(aff_ready, 1)
                if t.j % 2:
                    g = arena[:, ffT + (t.j - 1) % 4, :]
                    act.wait_ge(gate_conv, p + (base + 1))
                    nc.scalar.activation(g, g, ACT.Silu).then_inc(gate_act, 1)
            split_stage_act(act, a, f"down{layer}")

        def ffn1_dve(dve, v, layer):
            if layer == 0:
                dve.sem_inc(pair_done, 2)
            split_norm_dve(dve, v, "norm_ffn", ffH, layer * DT)
            base = layer * F1T
            for t in loop_tiles(dve, STAGE[f"up{layer}"], v):
                y = arena[:, ffT + t.j % 4, :]
                z = gp[:, t.bank, :]
                p = t.j // 2 if t.it is None else t.it * 4 + t.j // 2
                dve.wait_ge(aff_ready, at(2 * base + 1, t, 1))
                v(nc.vector.scalar_tensor_tensor(out=y[:, 1:S], in0=z[:, 0:S - 1], scalar=ff_cols(layer, t, 0),
                                                 in1=y[:, 1:S], op0=ALU.mult, op1=ALU.add))
                v.go(nc.vector.scalar_tensor_tensor(out=y[:, 0:S - 1], in0=z[:, 1:S], scalar=ff_cols(layer, t, 2),
                                                    in1=y[:, 0:S - 1], op0=ALU.mult, op1=ALU.add))
                if t.j % 2 == 0:
                    v.tell(drained[t.bank], gate_conv)
                else:
                    v.tell(drained[t.bank])
                    dve.wait_ge(gate_act, p + (base + 1))
                    v(nc.vector.tensor_tensor(y, y, arena[:, ffT + (t.j - 1) % 4, :], ALU.mult))
                    split_tile_dve(dve, v, y, ffG_high[:, p, :], ffG_low[:, p, :], pair_done)
            residual_dve(dve, v, f"down{layer}")

        wR, wK, wV, wA, wS, wXX, wMA, wMB = 0, 8, 16, 24, 32, 48, 56, 24
        wTA, wTG = 64, 65
        HOLD = STAGE["rw_g2"].slab0
        rw_xx = sem("rw_mix")
        MIX = (1, 4, 5, 0, 2, 3)
        MIX_STAGE = ("rw_lora1", "rw_lora1", "rw_lora1", "rw_r", "rw_k", "rw_v")
        lora_ready = sem("lora_ready")
        rkv_ready = sem("rkv_ready")

        def bd(t):
            return t.rearrange("p (c x) -> p c x", x=2 * CH)

        Hf = H[:, :, :].rearrange("p a b -> p (a b)")
        LO, HI = slice(0, 64), slice(64, 128)
        BETA, KT = ([bd(Hf[:, (2 * i + d_) * 1024:(2 * i + d_ + 1) * 1024]) for d_ in range(2)] for i in range(2))
        XTB, BTOK = ([bd(ring[:, 2 * i + d_, :]) for d_ in range(2)] for i in range(2))
        AR = [bd(scratch[:, d_, :]) for d_ in range(2)]
        MAK = bd(scratch[:, 2, :])
        MBD, KTOK, T1B = BETA, KT, KT
        ARB, ARK, W0, KVP, XT, T1 = ([arena[:, 48 + 2 * i + d_, :] for d_ in range(2)] for i in range(6))
        XS = T1
        T3 = [arena[:, 60, :], root[:]]
        VCOPY = arena[:, 60, :]
        KK, VT, VTN = (arena[:, 61 + i, :] for i in range(3))
        RESET = arena[:, wTA, :]
        small = lambda lo, n: [scratch[:, 3, lo + d_ * n:lo + (d_ + 1) * n] for d_ in range(2)]
        SB, SPC, WS, US = small(0, 128), small(256, 64), small(384, 64), small(512, 64)
        PC, PCN = small(640, NCH), small(640 + 2 * NCH, NCH)
        ZEROED = BETA + KT + XTB + [MAK]
        ch = lambda t: t.rearrange("p (c x) -> p c x", x=CH)
        two = lambda ps, b: ps[:, b:b + 2, :].rearrange("p b (c x) -> p (b c) x", x=2 * CH)
        over = lambda m: m.unsqueeze(1).broadcast_to((P, NCH, CH))
        (rw_kkr, rw_ksq, rw_ksum, rw_kroot, rw_vtok, rw_vnext, rw_vt, rw_cum, rw_exp, rw_prep, rw_beta, rw_M,
         rw_tok, rw_tokst, rw_mask, rw_w0, rw_kv, rw_w0st, rw_kvst, rw_XTst, rw_XT, rw_X1, rw_X1st, rw_X, rw_T1,
         rw_T1st, rw_T1bd, rw_dX, rw_dXT, rw_W, rw_Wst, rw_U, rw_Ust, rw_Sp, rw_S, rw_Y, rw_yst, rw_bon, rw_bsum,
         rw_mean, rw_yc, rw_sq2, rw_var, rw_root2, rw_gn, rw_zero) = (
            sem("rw_" + x) for x in
            ("kkr ksq ksum kroot vtok vnext vt cum exp prep beta M tok tokst mask w0 kv w0st kvst XTst XT X1 "
             "X1st X T1 T1st T1bd dX dXT W Wst U Ust Sp S Y yst bon bsum mean yc sq2 var root2 gn zero").split())
        DIRS = range(2)
        BONUS, YSQ, YROOT = (lambda p: H[:, p % 4, :]), (lambda p: H[:, 4 + p % 2, :]), (lambda p: H[:, 6 + p % 2, :])

        def n2(it, d):
            return it * 2 + (d + 1)

        def n_level(it, lv, d):
            return it * (2 * (LEVELS - 1)) + (2 * (lv - 1) + d + 1)

        def n_xt(it, lv, d):
            return it * (2 * LEVELS) + (2 * lv + d + 1)

        def n_x(it, lv, d):
            return it * (2 * (LEVELS - 2)) + (2 * (lv - 1) + d + 1)

        def n_chunk(it, j, d):
            return it * (2 * NCH) + (2 * j + d + 1)

        def n_link(it, j, d):
            return it * (2 * (NCH - 1)) + (2 * j + d + 1)

        def each_pair(eng, body, steps=None):
            if steps:
                steps.restart()
            with eng.Fori(0, DT - 1) as it:
                body(it, True)
                if steps:
                    steps.restart()
            body(DT - 1, False)

        yg_ready = sem("yg_ready")
        order = lambda d: range(NCH) if d == 0 else range(NCH - 1, -1, -1)

        def rwkv_pe(pe):
            norm_pe(pe, DT, Hk)
            n_pe.h += DT

            def mix_before(m):
                def before(t):
                    if t.j == 0 or m == 0:
                        pe.wait_ge(rw_xx, (m + (t.j if m == 0 else 0) + 1) * DT)
                return before

            buf = lambda m: wMA if m % 2 == 0 else wMB
            stream_pe(pe, "rw_lora1", lambda k, t: arena[:, buf(t.j) + k, :], before=mix_before(0))
            for m in (3, 4, 5):
                stream_pe(pe, MIX_STAGE[m], lambda k, t, m=m: arena[:, buf(m) + k, :], before=mix_before(m))
            pe.wait_ge(lora_ready, 3)
            for name in ("rw_a2", "rw_w2"):
                st = STAGE[name]
                slab_wait(pe, st.slab0)
                slot = st.slab0 % RING
                for t in loop_tiles(pe, st):
                    bank_wait(pe, t)
                    half = LO if t.j < DT else HI
                    src = arena[LO, wTA, :] if name == "rw_a2" else root[half, :]
                    i = t.j % DT
                    last = nc.tensor.matmul(gp[:, t.bank, :], ring[half, slot, i * P:(i + 1) * P], src,
                                            start=True, stop=True)
                    if t.j == st.tiles - 1:
                        last.then_inc(slab_done, 1)
                    shared_tile_done(t, last)
            t0 = STAGE["rw_g2"].tile0
            for b in range(BANKS):
                pe.wait_ge(drained[b], (t0 - b + BANKS - 1) // BANKS)
            pe.wait_ge(rw_zero, 1)

            def keys_values(nxt):
                pe.wait_ge(rw_ksq, nxt + 1)
                nc.tensor.matmul(gp[:, 0, :], bones, root[:], start=True, stop=True).then_inc(rw_ksum, 1)
                for c in range(NCH):
                    for h in (LO, HI):
                        last = nc.tensor.matmul(gp[h, 1, c * CH:(c + 1) * CH], VCOPY[h, c * CH:(c + 1) * CH],
                                                cst[h, COFF["eye64"]:COFF["eye64"] + 64], start=True, stop=True)
                last.then_inc(rw_vtok, 1)

            def inner_values(d, c, start):
                cs = slice(c * CH, (c + 1) * CH)
                for h in (LO, HI):
                    nc.tensor.matmul(aux[h, 2 + d, cs], VT[h, cs], ARK[d][h, cs], start=start, stop=False,
                                     skip_group_check=True)

            def pair(it, more):
                for d in DIRS:
                    pe.wait_ge(rw_beta, n2(it, d))
                    if d:
                        pe.wait_ge(rw_tokst, n2(it, 0))
                    for q, src in enumerate((BETA[d], KT[d])):
                        for c in range(NCH):
                            last = nc.tensor.matmul(two(gp, 2 * q)[:, c, :], src[:, c, :], ident,
                                                    start=True, stop=True)
                    last.then_inc(rw_tok, 1)
                    pe.wait_ge(rw_prep, n2(it, d))
                    if d:
                        pe.wait_ge(rw_mask, n2(it, 0))
                    else:
                        pe.wait_ge(rw_yst, it)
                    for q, src in enumerate((BETA[d], KT[d])):
                        for c in range(NCH):
                            last = nc.tensor.matmul(two(aux, 2 * q)[:, c, :], src[:, c, :], AR[d][:, c, :],
                                                    start=True, stop=True)
                    last.then_inc(rw_M, 1)
                pe.wait_ge(rw_tokst, n2(it, 1))
                pe.wait_ge(rw_vt, it + 1)
                for d in DIRS:
                    pe.wait_ge(rw_mask, n2(it, d))
                    bank = (gp, aux)[d]
                    for c in range(NCH):
                        cs = slice(c * CH, (c + 1) * CH)
                        last = nc.tensor.matmul(bank[:, 2 * d, cs], MAK[:, c, :], VT[:, cs], start=True, stop=True)
                    last.then_inc(rw_w0, 1)
                    for c in range(NCH):
                        cs = slice(c * CH, (c + 1) * CH)
                        last = nc.tensor.matmul(bank[:, 2 * d + 1, cs], KTOK[d][:, c, :], VT[:, cs],
                                                start=True, stop=True)
                    last.then_inc(rw_kv, 1)
                    pe.wait_ge(rw_XT, n_xt(it, 0, d))
                    for c in range(NCH):
                        last = nc.tensor.matmul(gp[:, 2 + d, c * CH:(c + 1) * CH], XTB[d][:, c, :],
                                                const("eye64"), start=True, stop=True)
                    last.then_inc(rw_X1, 1)
                for lv in range(1, LEVELS):
                    for d in DIRS:
                        if lv == 1:
                            pe.wait_ge(rw_X1st, n2(it, d))
                        else:
                            pe.wait_ge(rw_X, n_x(it, lv - 1, d))
                        for c in range(NCH):
                            last = nc.tensor.matmul(aux[:, d, c * CH:(c + 1) * CH], MBD[d][:, c, :],
                                                    XS[d][:, c * CH:(c + 1) * CH], start=True, stop=True)
                        last.then_inc(rw_T1, 1)
                    if lv < LEVELS - 1:
                        for d in DIRS:
                            if lv == 1:
                                pe.wait_ge(rw_w0st, n2(it, 1))
                                pe.wait_ge(rw_kvst, n2(it, 1))
                            pe.wait_ge(rw_T1st, n_level(it, lv, d))
                            pe.wait_ge(rw_XT, n_xt(it, lv - 1, d))
                            for c in range(NCH):
                                last = nc.tensor.matmul(aux[:, 2 + d, c * CH:(c + 1) * CH], XTB[d][:, c, :],
                                                        arena[:, wS + DT * d + it, c * CH:(c + 1) * CH],
                                                        start=True, stop=True)
                            last.then_inc(rw_dX, 1)
                    for d in DIRS:
                        pe.wait_ge(rw_XT, n_xt(it, lv - 1, d))
                        pe.wait_ge(rw_T1bd, n_level(it, lv, d))
                        for c in range(NCH):
                            last = nc.tensor.matmul(gp[:, 2 + d, c * CH:(c + 1) * CH], T1B[d][:, c, :],
                                                    XT[d][:, c * CH:(c + 1) * CH], start=True, stop=True)
                        last.then_inc(rw_dXT, 1)
                    if lv == 2 and more:
                        keys_values(it + 1)
                if more:
                    pe.wait_ge(rw_kroot, it + 2)
                    pe.wait_ge(rw_vnext, it + 2)
                for j in range(NCH):
                    for d in DIRS:
                        c = order(d)[j]
                        cs = slice(c * CH, (c + 1) * CH)
                        if j:
                            pe.wait_ge(rw_S, n_link(it, j - 1, d))
                            pe.sem_inc(pe_s, 1)
                            for h in (LO, HI):
                                last = nc.tensor.matmul(gp[h, d, 0:64], AR[d][h, c, 0:64], SB[d][h, h],
                                                        start=True, stop=True)
                            last.then_inc(rw_W, 1)
                            nc.tensor.matmul(aux[:, 2 + d, cs], SB[d], AR[d][:, c, 64:128], start=True, stop=False,
                                             skip_group_check=True)
                            inner_values(d, c, False)
                    for d in DIRS:
                        c = order(d)[j]
                        if j:
                            pe.wait_ge(rw_Wst, n_link(it, j - 1, d))
                        else:
                            pe.wait_ge(rw_XT, n_xt(it, LEVELS - 1, d))
                        nc.tensor.matmul(gp[:, 2 + d, 0:64], XTB[d][:, c, :],
                                         WS[d] if j else W0[d][:, c * CH:(c + 1) * CH],
                                         start=True, stop=True).then_inc(rw_U, 1)
                        if not j:
                            inner_values(d, c, True)
                    for d in DIRS:
                        c = order(d)[j]
                        cs = slice(c * CH, (c + 1) * CH)
                        pe.wait_ge(rw_Ust, n_chunk(it, j, d))
                        last = nc.tensor.matmul(aux[:, d, 0:64], BTOK[d][:, c, :], US[d], start=True, stop=True)
                        if j < NCH - 1:
                            last.then_inc(rw_Sp, 1)
                        for h in (LO, HI):
                            last = nc.tensor.matmul(aux[h, 2 + d, cs], US[d][h, :], ARB[d][h, cs], start=False,
                                                    stop=True, skip_group_check=True)
                        if j == NCH - 1 and d:
                            last.then_inc(rw_Y, 1)

            keys_values(0)
            pe.wait_ge(rw_kroot, 1)
            pe.wait_ge(rw_vnext, 1)
            each_pair(pe, pair)
            pe.wait_ge(rw_yst, DT)
            for p in range(DT + 1):
                if p < DT:
                    if p >= BANKS:
                        pe.wait_ge(rw_root2, p - BANKS + 1)
                    nc.tensor.matmul(aux[:, p % BANKS, :], bones, arena[:, wS + p, :], start=True,
                                     stop=True).then_inc(rw_mean, 1)
                    pe.wait_ge(rw_bon, p + 1)
                    if p >= BANKS:
                        pe.wait_ge(rw_gn, p - BANKS + 1)
                    nc.tensor.matmul(gp[:, p % BANKS, :], bones, BONUS(p), start=True, stop=True).then_inc(rw_bsum, 1)
                if p:
                    pe.wait_ge(rw_sq2, p)
                    nc.tensor.matmul(aux[:, (p - 1) % BANKS, :], bones, YSQ(p - 1), start=True,
                                     stop=True).then_inc(rw_var, 1)
            pe.wait_ge(rw_gn, DT)
            st = STAGE["rw_g2"]
            slab_wait(pe, st.slab0)
            for t in loop_tiles(pe, st):
                bank_wait(pe, t)
                last = nc.tensor.matmul(gp[:, t.bank, :], ring[:, st.slab0 % RING, t.j * P:(t.j + 1) * P],
                                        arena[:, wTG, :], start=True, stop=True)
                if t.j == st.tiles - 1:
                    last.then_inc(slab_done, 1)
                shared_tile_done(t, last)
            pe.wait_ge(yg_ready, DT)
            stream_pe(pe, "rw_o", lambda k, t: arena[:, wS + k, :])

        def rwkv_act(act, a):
            pre_norm_act(act, a)
            for t, (dst, func) in zip(loop_tiles(act, STAGE["rw_lora1"]),
                                      ((root[:], ACT.Tanh), (arena[:, wTA, :], ACT.Copy),
                                       (arena[:, wTG, :], ACT.Sigmoid))):
                consume_wait(act, t)
                a.go(nc.scalar.activation(dst, gp[:, t.bank, :], func))
                a.tell(drained[t.bank], lora_ready)
            for name, base in (("rw_r", wR), ("rw_k", wK), ("rw_v", wV)):
                copy_act(act, a, name, arena_tiles(base), done=rkv_ready)
            copy_act(act, a, "rw_a2", arena_tiles(wA), ACT.Sigmoid, lambda i: pcol("rw_a0", i), done=rkv_ready)
            copy_act(act, a, "rw_w2", arena_tiles(wS), ACT.Sigmoid, lambda i: pcol("rw_w0", i), done=rkv_ready)
            act.wait_ge(rw_zero, 1)

            def keys_values(nxt):
                act.wait_ge(rw_kkr, nxt + 1)
                a.go(nc.scalar.activation(root[:], KK, ACT.Square))
                nc.scalar.activation(VCOPY, arena[:, wV + nxt, :], ACT.Copy).then_inc(rw_ksq, 1)

            def keys_root(nxt):
                act.wait_ge(rw_ksum, nxt + 1)
                nc.scalar.activation(root[:], gp[:, 0, :], ACT.Sqrt).then_inc(rw_kroot, 1)

            def decays(nxt, d, part):
                before = arena[:, wS + DT * d + nxt, :]
                if part == 0:
                    act.wait_ge(rw_cum, n2(nxt, d))
                    a.go(nc.scalar.activation(T3[d], T1[d], ACT.Exp, scale=KAPPA))
                    a.go(nc.scalar.activation(before, before, ACT.Exp, scale=-KAPPA))
                else:
                    a.go(nc.scalar.activation(PCN[d], PCN[d], ACT.Exp, scale=-KAPPA))
                    a.settle()
                    nc.scalar.activation(T1[d], T1[d], ACT.Exp, scale=-KAPPA).then_inc(rw_exp, 1)

            def pair(it, more):
                act.wait_ge(rw_prep, n2(it, 0))
                act.wait_ge(rw_vnext, it + 1)
                nc.scalar.activation(VT, VTN, ACT.Copy).then_inc(rw_vt, 1)
                for d in DIRS:
                    act.wait_ge(rw_tok, n2(it, d))
                    a.go(nc.scalar.activation(BTOK[d], two(gp, 0), ACT.Copy))
                    act.wait_ge(rw_M, n2(it, d))
                    nc.scalar.activation(KTOK[d], two(gp, 2), ACT.Copy).then_inc(rw_tokst, 1)
                    act.wait_ge(rw_XTst, n_xt(it, 0, d))
                    a.go(nc.scalar.activation(XTB[d][LO, :, 0:64], ch(XT[d])[LO], ACT.Copy))
                    nc.scalar.activation(XTB[d][HI, :, 64:128], ch(XT[d])[HI], ACT.Copy).then_inc(rw_XT, 1)
                for d in DIRS:
                    act.wait_ge(rw_w0, n2(it, d))
                    nc.scalar.activation(W0[d], (gp, aux)[d][:, 2 * d, :], ACT.Copy).then_inc(rw_w0st, 1)
                    act.wait_ge(rw_X1, n2(it, d))
                    nc.scalar.activation(XS[d], gp[:, 2 + d, :], ACT.Copy).then_inc(rw_X1st, 1)
                for lv in range(1, LEVELS):
                    for d in DIRS:
                        if lv == 1:
                            act.wait_ge(rw_kv, n2(it, d))
                        act.wait_ge(rw_T1st, n_level(it, lv, d))
                        a.carry()
                        t = ch(arena[:, wS + DT * d + it, :])
                        a.go(nc.scalar.activation(T1B[d][LO, :, 0:64], t[LO], ACT.Copy))
                        nc.scalar.activation(T1B[d][HI, :, 64:128], t[HI], ACT.Copy).then_inc(rw_T1bd, 1)
                    if more and lv == LEVELS - 1:
                        decays(it + 1, 0, 0)
                        decays(it + 1, 0, 1)
                    for d in DIRS:
                        act.wait_ge(rw_XTst, n_xt(it, lv, d))
                        a.go(nc.scalar.activation(XTB[d][LO, :, 0:64], ch(XT[d])[LO], ACT.Copy))
                        nc.scalar.activation(XTB[d][HI, :, 64:128], ch(XT[d])[HI], ACT.Copy).then_inc(rw_XT, 1)
                    if more and lv == 1:
                        keys_values(it + 1)
                    if more and lv == 2:
                        keys_root(it + 1)
                for j in range(NCH):
                    for d in DIRS:
                        act.wait_ge(rw_U, n_chunk(it, j, d))
                        nc.scalar.activation(US[d], gp[:, 2 + d, 0:64], ACT.Copy).then_inc(rw_Ust, 1)
                    if more and j in (5, 6):
                        decays(it + 1, 1, j - 5)

            keys_values(0)
            keys_root(0)
            for d in DIRS:
                decays(0, d, 0)
                decays(0, d, 1)
            each_pair(act, pair, a)
            for p in range(DT + 1):
                if p < DT:
                    act.wait_ge(rw_yc, p + 1)
                    nc.scalar.activation(YSQ(p), arena[:, wS + p, :], ACT.Square).then_inc(rw_sq2, 1)
                if p:
                    act.wait_ge(rw_var, p)
                    if p > 2:
                        act.wait_ge(rw_gn, p - 2)
                    nc.scalar.activation(YROOT(p - 1), aux[:, (p - 1) % BANKS, :], ACT.Sqrt, scale=1.0 / HD,
                                         bias=const("gn_eps")).then_inc(rw_root2, 1)

        def rwkv_pool(pool, g):
            pool.wait_ge(rw_xx, 6 * DT)
            g.go(nc.gpsimd.memset(Hf[:, 0:4 * 1024], 0.0))
            pool.wait_ge(slab_done, HOLD)
            for buf in XTB + [MAK]:
                g.go(nc.gpsimd.memset(buf, 0.0))
            for d in DIRS:
                g.go(nc.gpsimd.memset(SB[d], 0.0))
            g(nc.gpsimd.memset(RESET, 1.0))
            g(nc.gpsimd.memset(ch(RESET)[:, :, 0:1], 0.0))
            g.tell(rw_zero)

            def betas(nxt, before):
                for d in DIRS:
                    if before is not None:
                        pool.wait_ge(rw_dXT, n_level(before, LEVELS - 1, d))
                    pool.wait_ge(rw_exp, n2(nxt, d))
                    g.carry()
                    for dst, base in ((BETA, wA), (KT, wK)):
                        for h, cols in ((LO, slice(0, 64)), (HI, slice(64, 128))):
                            last = nc.gpsimd.tensor_tensor(dst[d][h, :, cols], ch(arena[:, base + nxt, :])[h],
                                                           ch(T3[d])[h], ALU.mult)
                            if dst is BETA or h is LO:
                                g.go(last)
                    last.then_inc(rw_beta, 1)

            def pair(it, more):
                if more:
                    betas(it + 1, it)

            betas(0, None)
            each_pair(pool, pair, g)

        def rwkv_dve(dve, v):
            pre_norm_dve(dve, v, "norm_mix", DT)
            v.settle()
            dve.wait_ge(h_ready, n_dve.h)
            for i in range(DT):
                xx, h = arena[:, wXX + i, :], H[:, i, :]
                v.go(nc.vector.tensor_tensor(xx[:, 1:S - 1], h[:, 0:S - 2], h[:, 2:S], ALU.add))
                v.go(nc.vector.tensor_copy(xx[:, 0:1], h[:, 1:2]))
                v(nc.vector.tensor_copy(xx[:, S - 1:S], h[:, S - 2:S - 1]))
                v(nc.vector.scalar_tensor_tensor(out=xx, in0=xx, scalar=0.5, in1=h, op0=ALU.mult, op1=ALU.subtract))
            for m, j in enumerate(MIX):
                if m >= 2:
                    st = STAGE[MIX_STAGE[m - 2]]
                    dve.wait_ge(slab_done, st.slab0 + (m - 1 if m - 2 < 3 else st.slabs))
                for i in range(DT):
                    dst = arena[:, (wMA if m % 2 == 0 else wMB) + i, :]
                    nc.vector.scalar_tensor_tensor(out=dst, in0=arena[:, wXX + i, :], scalar=pcol("rw_mu", j * DT + i),
                                                   in1=H[:, i, :], op0=ALU.mult, op1=ALU.add).then_inc(rw_xx, 1)
            dve.wait_ge(rkv_ready, 6 * DT)
            dve.wait_ge(rw_zero, 1)
            dve.wait_ge(slab_done, STAGE["rw_w2"].slab0 + 1)

            def keys(nxt):
                k, aa = arena[:, wK + nxt, :], arena[:, wA + nxt, :]
                v.go(nc.vector.tensor_scalar(KK, k, pcol("rw_k_k", nxt), None, ALU.mult))
                v(nc.vector.tensor_scalar(root[:], aa, 1.0, pcol("rw_k_a", nxt), ALU.subtract, ALU.mult))
                v(nc.vector.scalar_tensor_tensor(out=k, in0=root[:], scalar=1.0, in1=k, op0=ALU.add, op1=ALU.mult))
                v.tell(rw_kkr)

            def keys_normed(nxt):
                aa = arena[:, wA + nxt, :]
                dve.wait_ge(rw_kroot, nxt + 1)
                v(nc.vector.tensor_scalar(root[:], root[:], 1e-12, None, ALU.max))
                v(nc.vector.reciprocal(root[:], root[:]))
                v(nc.vector.tensor_tensor(KK, KK, root[:], ALU.mult))
                v(nc.vector.tensor_tensor(aa, KK, aa, ALU.mult))

            def values(nxt, more):
                dve.wait_ge(rw_vtok, nxt + 1)
                if more:
                    dve.wait_ge(rw_vt, nxt)
                nc.vector.tensor_copy(VTN, gp[:, 1, :]).then_inc(rw_vnext, 1)

            def decays(nxt, d, parts_):
                s = arena[:, wS + DT * d + nxt, :]
                c0 = (T1[0], root[:])[d]
                ends = ch(c0)[:, :, CH - 1:CH]
                if 0 in parts_:
                    v(nc.vector.tensor_tensor_scan(c0, RESET, s, 0.0, ALU.mult, ALU.add))
                    v.go(nc.vector.tensor_copy(PCN[d].unsqueeze(2), ends))
                if 1 in parts_:
                    v(nc.vector.tensor_tensor(s, c0, s, ALU.subtract))
                if d and 2 in parts_:
                    v(nc.vector.tensor_tensor(ch(T1[d]), ends.broadcast_to((P, NCH, CH)), ch(s), ALU.subtract))
                if d and 3 in parts_:
                    v(nc.vector.tensor_tensor(ch(s), ends.broadcast_to((P, NCH, CH)), ch(c0), ALU.subtract))
                if 3 in parts_:
                    v.tell(rw_cum)

            def alphas(nxt, d):
                dve.wait_ge(rw_exp, n2(nxt, d))
                v.go(nc.vector.tensor_copy(PC[d], PCN[d]))
                v.go(nc.vector.scalar_tensor_tensor(out=AR[d][:, :, 0:64], in0=ch(KK), scalar=-1.0,
                                                    in1=ch(arena[:, wS + DT * d + nxt, :]), op0=ALU.mult, op1=ALU.mult))
                nc.vector.tensor_tensor(AR[d][:, :, 64:128], ch(arena[:, wR + nxt, :]), ch(T1[d]),
                                        ALU.mult).then_inc(rw_prep, 1)

            def pair(it, more):
                yt = arena[:, wS + it, :]
                for d in DIRS:
                    strict, incl = over(const("strict", 64 * d, 64 * d + 64)), over(const("incl", 64 * d, 64 * d + 64))
                    first = over(const("level", (0, LEVELS * 64)[d], (0, LEVELS * 64)[d] + 64))
                    pb, pk = two(aux, 0), two(aux, 2)
                    dve.wait_ge(rw_M, n2(it, d))
                    v(nc.vector.tensor_tensor(ch(XT[d]), pb[:, :, 0:64], first, ALU.mult))
                    nc.vector.tensor_tensor(ch(XT[d]), ch(XT[d]), over(const("eye64")), ALU.add).then_inc(rw_XTst, 1)
                    v.go(nc.vector.tensor_tensor(ch(ARB[d]), pb[:, :, 64:128], incl, ALU.mult))
                    v.go(nc.vector.tensor_tensor(ch(ARK[d]), pk[:, :, 64:128], incl, ALU.mult))
                    dve.wait_ge(rw_tok, n2(it, d))
                    for h, cols in ((LO, slice(0, 64)), (HI, slice(64, 128))):
                        v.go(nc.vector.tensor_tensor(MBD[d][h, :, cols], pb[h, :, 0:64], strict[h], ALU.mult))
                    if d:
                        dve.wait_ge(rw_w0, n2(it, 0))
                    v.go(nc.vector.tensor_tensor(MAK[LO, :, 0:64], pk[LO, :, 0:64], strict[LO], ALU.mult))
                    nc.vector.tensor_tensor(MAK[HI, :, 64:128], pk[HI, :, 0:64], strict[HI],
                                            ALU.mult).then_inc(rw_mask, 1)
                for d in DIRS:
                    dve.wait_ge(rw_kv, n2(it, d))
                    nc.vector.tensor_tensor(ch(KVP[d]), ch((gp, aux)[d][:, 2 * d + 1, :]),
                                            PC[d].unsqueeze(2).broadcast_to((P, NCH, CH)), ALU.mult).then_inc(rw_kvst, 1)
                for lv in range(1, LEVELS):
                    m = over(const("level", lv * 64, lv * 64 + 64))
                    for d in DIRS:
                        dve.wait_ge(rw_T1, n_level(it, lv, d))
                        nc.vector.tensor_tensor(ch(arena[:, wS + DT * d + it, :]), ch(aux[:, d, :]), m,
                                                ALU.mult).then_inc(rw_T1st, 1)
                    if lv < LEVELS - 1:
                        for d in DIRS:
                            dve.wait_ge(rw_dX, n_x(it, lv, d))
                            if lv == 1:
                                dve.wait_ge(rw_X1st, n2(it, d))
                            else:
                                dve.wait_ge(rw_X, n_x(it, lv - 1, d))
                            nc.vector.tensor_tensor(XS[d], aux[:, 2 + d, :], XS[d], ALU.add).then_inc(rw_X, 1)
                    if more and lv == LEVELS - 1:
                        decays(it + 1, 0, (0, 1, 3))
                    for d in DIRS:
                        dve.wait_ge(rw_dXT, n_level(it, lv, d))
                        dve.wait_ge(rw_XT, n_xt(it, lv - 1, d))
                        nc.vector.tensor_tensor(XT[d], gp[:, 2 + d, :], XT[d], ALU.add).then_inc(rw_XTst, 1)
                    if more and lv == 1:
                        keys(it + 1)
                    if more and lv == 3:
                        keys_normed(it + 1)
                        values(it + 1, True)
                dve.wait_ge(rw_kvst, n2(it, 1))
                dve.wait_ge(rw_w0st, n2(it, 1))
                v.settle()
                halves = ((LO, slice(0, 64)), (HI, slice(64, 128)))
                for j in range(NCH):
                    for d in DIRS:
                        c = order(d)[j]
                        if j:
                            dve.wait_ge(rw_W, n_link(it, j - 1, d))
                            nc.vector.tensor_tensor(WS[d], gp[:, d, 0:64], W0[d][:, c * CH:(c + 1) * CH],
                                                    ALU.add).then_inc(rw_Wst, 1)
                    for d in DIRS:
                        c = order(d)[j]
                        pc, kv = PC[d][:, c:c + 1], KVP[d][:, c * CH:(c + 1) * CH]
                        if 0 < j < NCH - 1:
                            dve.wait_ge(rw_S, n_link(it, j - 1, d))
                            for h, cols in halves:
                                v.go(nc.vector.scalar_tensor_tensor(out=SPC[d][h, :], in0=SB[d][h, cols], scalar=pc[h],
                                                                    in1=kv[h], op0=ALU.mult, op1=ALU.add))
                    if more and 0 < j < 5:
                        decays(it + 1, 1, (j - 1,))
                    if j < NCH - 1:
                        v.settle()
                        for d in DIRS:
                            c = order(d)[j]
                            pc = PC[d][:, c:c + 1]
                            dve.wait_ge(rw_Sp, n_link(it, j, d))
                            for h, cols in halves:
                                last = nc.vector.scalar_tensor_tensor(
                                    out=SB[d][h, cols], in0=aux[h, d, 0:64], scalar=pc[h],
                                    in1=SPC[d][h, :] if j else KVP[d][h, c * CH:(c + 1) * CH], op0=ALU.mult, op1=ALU.add)
                            last.then_inc(rw_S, 1)
                dve.wait_ge(rw_Y, it + 1)
                if more:
                    alphas(it + 1, 0)
                v(nc.vector.tensor_scalar(yt, aux[:, 2, :], 1.0, None, ALU.mult))
                nc.vector.tensor_tensor(yt, aux[:, 3, :], yt, ALU.add).then_inc(rw_yst, 1)
                if more:
                    alphas(it + 1, 1)

            keys(0)
            keys_normed(0)
            values(0, False)
            for d in DIRS:
                decays(0, d, range(4))
            for d in DIRS:
                alphas(0, d)
            each_pair(dve, pair, v)
            dve.wait_ge(rw_yst, DT)
            for p in range(DT + 1):
                if p < DT:
                    y = arena[:, wS + p, :]
                    nc.vector.scalar_tensor_tensor(out=BONUS(p), in0=arena[:, wR + p, :], scalar=pcol("rw_r_k", p),
                                                   in1=arena[:, wK + p, :], op0=ALU.mult, op1=ALU.mult).then_inc(rw_bon, 1)
                    dve.wait_ge(rw_mean, p + 1)
                    nc.vector.scalar_tensor_tensor(out=y, in0=aux[:, p % BANKS, :], scalar=-1.0 / HD, in1=y,
                                                   op0=ALU.mult, op1=ALU.add).then_inc(rw_yc, 1)
                if p:
                    q = p - 1
                    y = arena[:, wS + q, :]
                    dve.wait_ge(rw_bsum, p)
                    v.go(nc.vector.tensor_tensor(BONUS(q), gp[:, q % BANKS, :], arena[:, wV + q, :], ALU.mult))
                    dve.wait_ge(rw_root2, p)
                    v(nc.vector.reciprocal(YROOT(q), YROOT(q)))
                    v(nc.vector.scalar_tensor_tensor(out=y, in0=y, scalar=pcol("rw_ln_w", q), in1=YROOT(q),
                                                     op0=ALU.mult, op1=ALU.mult))
                    nc.vector.scalar_tensor_tensor(out=y, in0=y, scalar=pcol("rw_ln_b", q), in1=BONUS(q),
                                                   op0=ALU.add, op1=ALU.add).then_inc(rw_gn, 1)
            dve.wait_ge(rw_gn, DT)
            for t in loop_tiles(dve, STAGE["rw_g2"]):
                consume_wait(dve, t)
                y = arena[:, wS + t.j, :]
                v.go(nc.vector.tensor_tensor(y, gp[:, t.bank, :], y, ALU.mult))
                v.tell(drained[t.bank], yg_ready)
            residual_dve(dve, v, "rw_o")

        def final1_pe(pe):
            norm_pe(pe, DT, Hk)

        def final1_act(act, a):
            pre_norm_act(act, a)

        def final1_dve(dve, v):
            norm_dve(dve, v, DT, Xk, lambda k: pcol("final_norm", k), Xk, x_ready)
            n_dve.x += DT

        lat_ready, ln_c, ln_ready = sem("lat_ready"), sem("ln_c"), sem("ln_ready")

        def sum_pe(pe, n, src):
            pe.wait_ge(stat_ready, n_pe.sums)
            for k in range(n):
                last = nc.tensor.matmul(aux[:, 0, :], ones, src(k), start=(k == 0), stop=(k == n - 1))
            last.then_inc(sum_ready, 1)
            n_pe.sums += 1

        def mean_act(act, width):
            n_act.sums += 1
            act.wait_ge(sum_ready, n_act.sums)
            nc.scalar.activation(root[:], aux[:, 0, :], ACT.Copy, scale=1.0 / width).then_inc(stat_ready, 1)

        def centre_dve(dve, v, n, src):
            n_dve.sums += 1
            dve.wait_ge(stat_ready, n_dve.sums)
            for k in range(n):
                v.go(nc.vector.tensor_tensor(src(k), src(k), root[:], ALU.subtract))
            v.tell(ln_c)

        def scale_shift_dve(dve, v, n, src, gain, bias, dst, done):
            n_dve.sums += 1
            dve.wait_ge(stat_ready, n_dve.sums)
            v(nc.vector.reciprocal(root[:], root[:]))
            for k in range(n):
                v(nc.vector.scalar_tensor_tensor(out=dst(k), in0=src(k), scalar=gain(k), in1=root[:],
                                                 op0=ALU.mult, op1=ALU.mult))
                nc.vector.tensor_scalar(dst(k), dst(k), bias(k), None, ALU.add).then_inc(done, 1)

        at_score, at_max, at_exp, at_norm, at_tr, at_pt, at_pv = (
            sem("at_" + x) for x in "score max exp norm tr pt pv".split())

        class Unit:
            def __init__(self, q, k, mask, nk, v, out):
                self.q, self.k, self.mask, self.nk, self.v, self.out = q, k, mask, nk, v, out

        class Attention:

            def __init__(self, units, p, pt, scale, u0):
                self.units, self.p, self.pt, self.scale, self.u0 = units, p, pt, scale, u0

        def attention_pe(pe, A):
            def score(i):
                u, n = A.units[i], A.u0 + i
                if n >= 2:
                    pe.wait_ge(at_exp, n - 1)
                nc.tensor.matmul(gp[:, n % 2, 0:u.nk], u.q, u.k, start=True, stop=False, skip_group_check=True)
                lo, m = u.mask
                nc.tensor.matmul(gp[:, n % 2, lo:u.nk], ident, m, start=False, stop=True,
                                 skip_group_check=True).then_inc(at_score, 1)

            score(0)
            for i, u in enumerate(A.units):
                n = A.u0 + i
                if i + 1 < len(A.units):
                    score(i + 1)
                pe.wait_ge(at_norm, n + 1)
                if n >= 2:
                    pe.wait_ge(at_pt, n - 1)
                for b in range(u.nk // P):
                    last = nc.tensor.transpose(gp[:, 2 + n % 2, b * P:(b + 1) * P], A.p(n)[:, b * P:(b + 1) * P], ident)
                last.then_inc(at_tr, 1)
                pe.wait_ge(at_pt, n + 1)
                for b in range(u.nk // P):
                    last = nc.tensor.matmul(u.out, u.v(b), A.pt(n)[:, b * P:(b + 1) * P],
                                            start=(b == 0), stop=(b == u.nk // P - 1))
                last.then_inc(at_pv, 1)

        def stat(n, i):
            return root[:, 4 * (n % 2) + i:4 * (n % 2) + i + 1]

        def attention_act(act, A):
            def copy(i):
                u, n = A.units[i], A.u0 + i
                act.wait_ge(at_tr, n + 1)
                if n >= 2:
                    act.wait_ge(at_pv, n - 1)
                nc.scalar.activation(A.pt(n)[:, 0:u.nk], gp[:, 2 + n % 2, 0:u.nk], ACT.Copy).then_inc(at_pt, 1)

            for i, u in enumerate(A.units):
                n = A.u0 + i
                act.wait_ge(at_max, n + 1)
                if n >= 2:
                    act.wait_ge(at_tr, n - 1)
                nc.scalar.activation(A.p(n)[:, 0:u.nk], gp[:, n % 2, 0:u.nk], ACT.Exp, bias=stat(n, 1), scale=A.scale,
                                     accum_out=stat(n, 2)).then_inc(at_exp, 1)
                if i:
                    copy(i - 1)
            copy(len(A.units) - 1)

        def attention_dve(dve, v, A):
            def maximum(i):
                u, n = A.units[i], A.u0 + i
                dve.wait_ge(at_score, n + 1)
                v(nc.vector.tensor_reduce(stat(n, 0), gp[:, n % 2, 0:u.nk], AX.X, ALU.max))
                nc.vector.tensor_scalar(stat(n, 1), stat(n, 0), -A.scale, None, ALU.mult).then_inc(at_max, 1)

            maximum(0)
            for i, u in enumerate(A.units):
                n = A.u0 + i
                if i + 1 < len(A.units):
                    maximum(i + 1)
                dve.wait_ge(at_exp, n + 1)
                v(nc.vector.reciprocal(stat(n, 3), stat(n, 2)))
                p = A.p(n)[:, 0:u.nk]
                nc.vector.tensor_scalar(p, p, stat(n, 3), None, ALU.mult).then_inc(at_norm, 1)

        relu_ready, f_ready, o_sum = sem("relu_ready"), sem("f_ready"), sem("o_sum")
        fT = 64
        F2H = F2T // 2

        def ffn2_pe(pe, b):
            before = h_parts_before(pe)
            for i, half_ in enumerate("ab"):
                split_pe(pe, f"ff1{half_}_{b}", tiles_of(fH), tiles_of(fH, DT), before=None if i else before)
                pe.wait_ge(f_ready, F2T * (b - 2) + F2H * (i + 1) + 2)
                split_pe(pe, f"ff2{half_}_{b}", tiles_of(f_high), tiles_of(f_low), ksizes=[DT] * 2)

        def ffn2_pool(pool, g, b):
            split_pool(pool, g, SPLIT[3 if b == 2 else 5])

        def ffn2_relu_act(act, a, b, i):
            base = F2T * (b - 2) + F2H * i
            for t in loop_tiles(act, STAGE[f"ff1{'ab'[i]}_{b}"], a):
                split_ahead_act(act, t)
                consume_wait(act, t)
                act.wait_ge(f_ready, at(base + 1, t, 1))
                a.go(nc.scalar.activation(arena[:, fT + t.j % 2, :], gp[:, t.bank, :], ACT.Relu))
                a.tell(drained[t.bank], relu_ready)

        def ffn2_square_dve(dve, v, b, i):
            base = F2T * (b - 2) + F2H * i
            if base == 0:
                dve.sem_inc(f_ready, 2)
            for t in loop_tiles(dve, STAGE[f"ff1{'ab'[i]}_{b}"], v):
                f = arena[:, fT + t.j % 2, :]
                dve.wait_ge(relu_ready, at(base + 1, t, 1))
                v(nc.vector.tensor_tensor(f, f, f, ALU.mult))
                split_tile_dve(dve, v, f, f_high[:, t.idx, :], f_low[:, t.idx, :], f_ready)

        bCQ, bCKV, bKR, bU, bV, bCX, bCB, bCC, bP, bG, bOUT = 0, 2, 3, 4, 6, 8, 10, 12, 14, 16, 48
        sm = arena[:, 56:61, :].rearrange("p a b -> p (a b)")
        UQ = sm[:, 0:768].rearrange("p (k n) -> p k n", k=2)
        WK, WV = sm[:, 768:1024], sm[:, 1024:1280]
        SGW = sm[:, 1280:1792]
        POOLW = sm[:, 1792:1920].rearrange("p (t n) -> p t n", t=2)
        UPPER = sm[:, 1920:2048]
        SGB = sm[0:1, 2048:2560]
        POS = arena[:, 61, :]
        RCNT = arena[:, 62:64, :]
        VM = arena[:, 64:66, :].rearrange("p a b -> p (a b)").rearrange("p (t n) -> p t n", t=4)
        COS, SIN, ANG, TMP = (arena[:, 8 + i, :] for i in range(4))
        RP = slice(NOPE, QKD)
        sm_in, sm_free = sem("sm_in"), sem("sm_free")
        in2_ready, gate_ready = sem("in2_ready"), sem("gate_ready")
        sgw_ready, sgt_psum, sgt_ready, sg_psum, sg_out = (sem(x) for x in "sgw_ready sgt_psum sgt_ready sg_psum sg_out".split())
        pooled, pool_psum, pool_out, conv_out = (sem(x) for x in "pooled pool_psum pool_out conv_out".split())
        mq_psum, mq_ready, mrot, mroped, mk_psum, mk_ready, mv_psum, mv_ready, trig, mla_out = (
            sem(x) for x in "mq_psum mq_ready mrot mroped mk_psum mk_ready mv_psum mv_ready trig mla_out".split())
        merged = sem("merged")
        mla_units = [Unit(H[0:QKD, h, qb * P:(qb + 1) * P], H[0:QKD, 4 + h, 0:(qb + 1) * P],
                          (qb * P, const("causal")), (qb + 1) * P,
                          lambda b, h=h: VM[:, b, h * VH:(h + 1) * VH],
                          aux[(h % 2) * 64:(h % 2) * 64 + 64, 1 + h // 2, qb * P:(qb + 1) * P])
                     for h in range(MLA_H) for qb in range(4)]
        MLA = Attention(mla_units, lambda n: arena[:, 10 + n % 2, :], lambda n: arena[:, 12 + n % 2, :],
                        float(QKD) ** -0.5, 0)
        bsq = arena_tiles(bOUT)

        def two_pool(pool, g):
            split_pool(pool, g, SPLIT[2], 0, PARTS)
            pool.wait_ge(h_ready, 5 * DT)
            for dst, name in ((sm[:, 0:2048], "sm2"), (SGB, "sg_b"), (RCNT, "rcnt")):
                pool.dma_start(dst, d[name]).then_inc(sm_in, 16)
            pool.dma_start(POS.bitcast(I32), d["pos"].partition_broadcast(P)).then_inc(sm_in, 16)
            split_pool(pool, g, SPLIT[2], PARTS)
            ffn2_pool(pool, g, 2)

        def two_pe(pe):
            norm_pe(pe, DT, Hk)
            split_pe(pe, "in2", tiles_of(bH), tiles_of(bH, DT), before=h_parts_before(pe))
            norm_pe(pe, 2, bsq)
            norm_pe(pe, 1, arena_tiles(bOUT + 2))
            pe.wait_ge(in2_ready, 8)
            sum_pe(pe, 2, arena_tiles(bV))
            norm_pe(pe, 2, arena_tiles(bOUT + 3))
            stream_pe(pe, "gate2", lambda k, t: H[:, k, :])
            for b in range(BANKS):
                pe.wait_ge(drained[b], (STAGE["br2_0"].tile0 - b + BANKS - 1) // BANKS)
            pe.wait_ge(sm_in, 16 * 4)
            pe.wait_ge(ln_ready, 2)
            for i in range(2):
                for n in range(4):
                    last = nc.tensor.transpose(gp[:, i, n * P:(n + 1) * P], arena[:, bV + i, n * P:(n + 1) * P], ident)
                last.then_inc(sgt_psum, 1)
            pe.wait_ge(sgw_ready, 1)
            pe.wait_ge(sgt_ready, 2)
            for g in range(4):
                rows = slice((g % 2) * 64, (g % 2) * 64 + 64)
                for n in range(4):
                    o = gp[rows, 2 + g // 2, n * P:(n + 1) * P]
                    nc.tensor.matmul(o, arena[:, bOUT + g // 2, n * P + (g % 2) * 64:n * P + (g % 2) * 64 + 64],
                                     SGW[:, g * P:(g + 1) * P], start=True, stop=False)
                    last = nc.tensor.matmul(o, ones[0:1, 0:64], SGB[:, g * P:(g + 1) * P], start=False, stop=True)
                if g % 2:
                    last.then_inc(sg_psum, 1)
            pe.wait_ge(pooled, 2)
            for i in range(2):
                for h in (LO, HI):
                    last = nc.tensor.matmul(aux[h, 2 + i, :], POOLW[h, i, :], arena[h, bP + i, :], start=True, stop=True)
                last.then_inc(pool_psum, 1)
            pe.wait_ge(lat_ready, 3)
            pe.wait_ge(sgt_ready, 2)
            pe.wait_ge(sg_out, 2)
            for h in range(MLA_H):
                for k in range(2):
                    last = nc.tensor.matmul(gp[0:QKD, h, :], UQ[:, k, h * QKD:(h + 1) * QKD], arena[:, bCQ + k, :],
                                            start=(k == 0), stop=(k == 1))
                last.then_inc(mq_psum, 1)
            pe.wait_ge(stat_ready, n_pe.sums)
            nc.tensor.matmul(aux[0:QKD, 0, :], const("perm_mla")[0:QKD], arena[0:QKD, bKR, :], start=True,
                             stop=True).then_inc(mrot, 1)
            for h in range(MLA_H):
                pe.wait_ge(mq_ready, h + 1)
                pe.wait_ge(mroped, h + 1)
                nc.tensor.matmul(aux[0:QKD, 0, :], const("perm_mla")[0:QKD], H[0:QKD, h, :], start=True,
                                 stop=True).then_inc(mrot, 1)
                nc.tensor.matmul(gp[0:NOPE, h, :], WK[:, h * NOPE:(h + 1) * NOPE], arena[:, bCKV, :], start=True,
                                 stop=True).then_inc(mk_psum, 1)
            pe.wait_ge(pool_out, 2)
            for tk in range(4):
                last = nc.tensor.matmul(aux[:, 2 + tk // 2, (tk % 2) * 256:(tk % 2) * 256 + 256],
                                        arena[:, bCKV, tk * P:(tk + 1) * P], WV, start=True, stop=True)
            last.then_inc(mv_psum, 1)
            pe.wait_ge(mk_ready, MLA_H)
            pe.wait_ge(mv_ready, 1)
            pe.wait_ge(mroped, MLA_H + 1)
            attention_pe(pe, MLA)
            for b in range(4):
                pe.wait_ge((mla_out, sg_out, conv_out, pool_out)[b], 2)
                st = STAGE[f"br2_{b}"]
                for t in loop_tiles(pe, st):
                    bank_wait(pe, t)
                    for k in range(2):
                        slab = st.slab0 + k
                        if t.j == 0:
                            slab_wait(pe, slab)
                        last = nc.tensor.matmul(gp[:, t.bank, :], ring[:, slab % RING, t.j * P:(t.j + 1) * P],
                                                arena[:, bOUT + 2 * b + k, :], start=(k == 0), stop=(k == 1))
                        if t.j == st.tiles - 1:
                            last.then_inc(slab_done, 1)
                    shared_tile_done(t, last)
            pe.wait_ge(merged, DT)
            stream_pe(pe, "out2", lambda k, t: H[:, k, :])
            norm_pe(pe, DT, arena_tiles(8))
            norm_pe(pe, DT, Hk)
            ffn2_pe(pe, 2)
            norm_pe(pe, DT, arena_tiles(8))

        def post_norm_act(act, a, name, ready, base):
            copy_act(act, a, name, arena_tiles(0), done=ready)
            norm_act(act, a, DT, arena_tiles(0), arena_tiles(8), lambda k: act.wait_ge(ready, base + k + 1), 1.0 / D)

        def post_norm_dve(dve, v, gain):
            n_dve.sums += 1
            dve.wait_ge(stat_ready, n_dve.sums)
            v(nc.vector.reciprocal(root[:], root[:]))
            for k in range(DT):
                o = arena[:, k, :]
                v(nc.vector.scalar_tensor_tensor(out=o, in0=o, scalar=pcol(gain, k), in1=root[:],
                                                 op0=ALU.mult, op1=ALU.mult))
                nc.vector.tensor_tensor(X[:, k, :], X[:, k, :], o, ALU.add).then_inc(x_ready, 1)
            n_dve.x += DT

        o_ready = sem("o_ready")

        def two_act(act, a):
            pre_norm_act(act, a)
            split_first_act(act, "in2")
            for t in loop_tiles(act, STAGE["in2"], a, body=16):
                split_ahead_act(act, t)
                consume_wait(act, t)
                a.go(nc.scalar.activation(arena[:, t.j, :], gp[:, t.bank, :],
                                          ACT.Gelu_apprx_tanh if bU <= t.j < bCX else ACT.Copy))
                a.tell(drained[t.bank], in2_ready)
            norm_act(act, a, 2, arena_tiles(bCQ), bsq, lambda k: None, 1.0 / 256)
            norm_act(act, a, 1, arena_tiles(bCKV), arena_tiles(bOUT + 2), lambda k: None, 1.0 / 128,
                     root_wait=lambda: act.wait_ge(lat_ready, 2))
            act.wait_ge(lat_ready, 3)
            mean_act(act, 256)
            norm_act(act, a, 2, arena_tiles(bV), arena_tiles(bOUT + 3), lambda k: act.wait_ge(ln_c, 1), 1.0 / 256)
            copy_act(act, a, "gate2", lambda i: arena[:, bG + i, :], ACT.Sigmoid, lambda i: pcol("gate_b2", i),
                     done=gate_ready)
            act.wait_ge(trig, 1)
            for x in (SIN, COS):
                nc.scalar.activation(x[RP], x[RP], ACT.Sin).then_inc(trig_done, 1)
            for i in range(2):
                act.wait_ge(sgt_psum, i + 1)
                nc.scalar.activation(arena[:, bOUT + i, :], gp[:, i, :], ACT.Copy).then_inc(sgt_ready, 1)
            for i in range(2):
                act.wait_ge(pool_psum, i + 1)
                nc.scalar.activation(arena[:, bOUT + 6 + i, :], aux[:, 2 + i, :], ACT.Copy,
                                     scale=pcol("pool_scale2", i)).then_inc(pool_out, 1)
            for h in range(MLA_H):
                act.wait_ge(mq_psum, h + 1)
                nc.scalar.activation(H[0:QKD, h, :], gp[0:QKD, h, :], ACT.Copy).then_inc(mq_ready, 1)
            act.wait_ge(mroped, 1)
            for h in range(MLA_H):
                a.go(nc.scalar.activation(H[RP, 4 + h, :], arena[RP, bKR, :], ACT.Copy))
                act.wait_ge(mk_psum, h + 1)
                nc.scalar.activation(H[0:NOPE, 4 + h, :], gp[0:NOPE, h, :], ACT.Copy).then_inc(mk_ready, 1)
            act.wait_ge(mv_psum, 1)
            nc.scalar.activation(VM, aux[:, 2:4, :].rearrange("p a (c n) -> p (a c) n", c=2),
                                 ACT.Copy).then_inc(mv_ready, 1)
            attention_act(act, MLA)
            act.wait_ge(at_pv, len(mla_units))
            act.wait_ge(sg_psum, 2)
            for i in range(2):
                nc.scalar.activation(arena[:, bOUT + i, :], aux[:, 1 + i, :], ACT.Copy).then_inc(mla_out, 1)
            post_norm_act(act, a, "out2", o_ready, 0)
            pre_norm_act(act, a)
            split_first_act(act, "ff1a_2")
            ffn2_relu_act(act, a, 2, 0)
            copy_act(act, a, "ff2a_2", arena_tiles(0), done=o_ready)
            ffn2_relu_act(act, a, 2, 1)
            split_stage_act(act, a, "ff2b_2")
            norm_act(act, a, DT, arena_tiles(0), arena_tiles(8), lambda k: act.wait_ge(o_sum, k + 1), 1.0 / D)

        def trig_dve(v):
            ang, s, c, t = ANG[RP], SIN[RP], COS[RP], TMP[RP]
            v(nc.vector.tensor_copy(ang, POS[RP].bitcast(I32)))
            v(nc.vector.tensor_scalar(ang, ang, const("invf")[RP], None, ALU.mult))
            v(nc.vector.tensor_copy(s, ang))
            reduce_angle(v, nc.vector, s, t)
            v(nc.vector.tensor_copy(c, ang))
            reduce_angle(v, nc.vector, c, t, 0.25)
            v(nc.vector.tensor_scalar(c, c, float(np.pi / 2), None, ALU.add))
            for x in (s, c):
                v(nc.vector.tensor_scalar(x, x, float(np.float32(3.1415925)), float(np.float32(-3.1415925)), ALU.min, ALU.max))

        def two_dve(dve, v):
            split_norm_dve(dve, v, "norm_mix_pre2", bH)
            for n, base, gain in ((2, bCQ, "q_norm2"), (1, bCKV, "kv_norm2")):
                norm_dve(dve, v, n, arena_tiles(base), lambda k, gain=gain: pcol(gain, k), arena_tiles(base), lat_ready)
            centre_dve(dve, v, 2, arena_tiles(bV))
            scale_shift_dve(dve, v, 2, arena_tiles(bV), lambda k: pcol("sg_ln_g2", k), lambda k: pcol("sg_ln_b2", k),
                            arena_tiles(bV), ln_ready)
            dve.wait_ge(sm_in, 16 * 4)
            for g in range(4):
                v.go(nc.vector.tensor_tensor(SGW[:, g * P:(g + 1) * P], SGW[:, g * P:(g + 1) * P], UPPER,
                                             ALU.mult))
            v.tell(sgw_ready)
            dve.wait_ge(in2_ready, 16)
            for i in range(2):
                z, y = arena[:, bCC + i, :], arena[:, bOUT + 4 + i, :]
                v(nc.vector.tensor_tensor(z, z, arena[:, bCX + i, :], ALU.mult))
                v(nc.vector.tensor_scalar(y, z, pcol("conv_w2", 4 + i), None, ALU.mult))
                for k in (1, 0):
                    lag = 2 - k
                    v(nc.vector.scalar_tensor_tensor(out=y[:, lag:S], in0=z[:, 0:S - lag],
                                                     scalar=pcol("conv_w2", 2 * k + i), in1=y[:, lag:S],
                                                     op0=ALU.mult, op1=ALU.add))
                v.go(nc.vector.tensor_tensor(y, y, arena[:, bCB + i, :], ALU.mult))
                v.tell(conv_out)
            for i in range(2):
                x = arena[:, bP + i, :]
                src, lag = x, 1
                for lv in range(2 * i + 2):
                    dst = arena[:, bOUT + 2 + lv % 2, :]
                    v.go(nc.vector.tensor_copy(dst[:, 0:lag], src[:, 0:lag]))
                    v(nc.vector.tensor_tensor(dst[:, lag:S], src[:, lag:S], src[:, 0:S - lag], ALU.add))
                    if lv >= 2 * i:
                        h = (LO, HI)[lv - 2 * i]
                        v(nc.vector.tensor_tensor(RCNT[h, i, :], dst[h], RCNT[h, i, :], ALU.mult))
                    src, lag = dst, lag * 2
                v.go(nc.vector.tensor_tensor(x, RCNT[:, i, :], x, ALU.subtract))
                v.tell(pooled)
            trig_dve(v)
            v.tell(trig)
            dve.wait_ge(trig_done, 2)
            v(nc.vector.tensor_scalar(SIN[RP], SIN[RP], const("rsign")[RP], None, ALU.mult))
            for i in range(2):
                dve.wait_ge(sg_psum, i + 1)
                v.go(nc.vector.tensor_tensor(arena[:, bOUT + 2 + i, :], gp[:, 2 + i, :], arena[:, bU + i, :], ALU.mult))
                v.tell(sg_out)
            for h in range(MLA_H + 1):
                x = arena[RP, bKR, :] if h == 0 else H[RP, h - 1, :]
                dve.wait_ge(mrot, h + 1)
                v.go(nc.vector.tensor_tensor(TMP[RP], aux[RP, 0, :], SIN[RP], ALU.mult))
                v(nc.vector.tensor_tensor(x, x, COS[RP], ALU.mult))
                v.go(nc.vector.tensor_tensor(x, x, TMP[RP], ALU.add))
                v.tell(mroped)
            attention_dve(dve, v, MLA)
            for b in range(4):
                for t in loop_tiles(dve, STAGE[f"br2_{b}"]):
                    g, m = arena[:, bG + b * DT + t.j, :], H[:, t.j, :]
                    consume_wait(dve, t)
                    if b == 0:
                        v.go(nc.vector.tensor_tensor(m, gp[:, t.bank, :], g, ALU.mult))
                        v.tell(drained[t.bank])
                    else:
                        v(nc.vector.tensor_tensor(g, gp[:, t.bank, :], g, ALU.mult))
                        dve.sem_inc(drained[t.bank], 1)
                        v(nc.vector.tensor_tensor(m, m, g, ALU.add))
                        if b == 3:
                            dve.sem_inc(merged, 1)
            post_norm_dve(dve, v, "norm_mix_post2")
            split_norm_dve(dve, v, "norm_ffn_pre2", fH)
            ffn2_square_dve(dve, v, 2, 0)
            ffn2_square_dve(dve, v, 2, 1)
            for t in loop_tiles(dve, STAGE["ff2b_2"], v):
                o = arena[:, t.idx, :]
                dve.wait_ge(o_ready, DT + t.j + 1)
                consume_wait(dve, t)
                v.go(nc.vector.tensor_tensor(o, gp[:, t.bank, :], o, ALU.add))
                v.tell(drained[t.bank], o_sum)
            post_norm_dve(dve, v, "norm_ffn_post2")

        trig_done = sem("trig_done")

        dCA, dCG, dIQ, dIK, dQ, dK, dV, dAT, dCV = 0, 4, 8, 12, 13, 17, 21, 25, 29
        ROTC, ROTS = arena[:, 33, :], arena[:, 34, :]
        SELM = lambda qb: arena[:, 34 + qb, 0:(qb + 1) * P]
        SCORE, WORK = arena[:, 38, :], arena[:, 40, :]
        REL = lambda n: arena[:, 39 + 2 * (n % 2), :]
        IW = arena[:, 45, 0:4 * AH]
        TOP8 = arena[:, 45, 64:72]
        CNT = arena[:, 45, 72:73]
        PAD = arena[:, 51:53, :].rearrange("p a b -> p (a b)")[:, 0:CONVK - 1 + S]
        hsq = arena_tiles(53)
        MOD = lambda j, k: pcol("b_ada3", j * DT + k)
        mod_act, mod_ready = sem("mod_act"), sem("mod_ready")
        rot_in = sem("rot_in")
        in3_ready, iw_ready, v3_ready = sem("in3_ready"), sem("iw_ready"), sem("v3_ready")
        hd_sum, hd_root, hd_normed = sem("hd_sum"), sem("hd_root"), sem("hd_normed")
        ro_psum, ro_ready = sem("ro_psum"), sem("ro_ready")
        ix_psum, ix_relu, ix_used, sel_ready = sem("ix_psum"), sem("ix_relu"), sem("ix_used"), sem("sel_ready")
        dsa_out, an_ready, cv_ready, cl_ready, cs_ready, cn_ready = (
            sem(x) for x in "dsa_out an_ready cv_ready cl_ready cs_ready cn_ready".split())
        half = lambda h: slice((h % 2) * 64, (h % 2) * 64 + 64)
        dsa_units = [Unit(arena[half(h), dQ + h // 2, qb * P:(qb + 1) * P], arena[half(h), dK + h // 2, 0:(qb + 1) * P],
                          (64, const("chunked")) if qb == 0 else (0, SELM(qb)), (qb + 1) * P,
                          lambda b, h=h: arena[:, dV + b, h * HD:(h + 1) * HD],
                          aux[half(h), h // 2, qb * P:(qb + 1) * P])
                     for qb in range(4) for h in range(AH)]
        DSA = Attention(dsa_units, lambda n: arena[:, 42 + n % 2, :], lambda n: arena[:, 46 + n % 2, :],
                        HD ** -0.5, len(mla_units))
        ROTATED = list(range(dIQ, dIK + 1)) + list(range(dQ, dV))

        def three_pool(pool, g):
            pool.wait_ge(x_ready, 7 * DT)
            pool.dma_start(ROTC, d["rotc"]).then_inc(rot_in, 16)
            pool.dma_start(ROTS, d["rots"]).then_inc(rot_in, 16)
            split_pool(pool, g, SPLIT[4])
            ffn2_pool(pool, g, 3)

        def three_pe(pe):
            st = STAGE["ada3"]
            pe.wait_ge(mod_act, 1)
            with pe.Fori(0, st.slabs // RING) as it:
                for j in range(RING):
                    slab = st.slab0 + j
                    slab_wait(pe, slab, it, RING)
                    for k in range(DT):
                        last = nc.tensor.matmul(aux[:, 1, bass.ds(it * RING + j, 1)],
                                                ring[:, slab % RING, k * P:(k + 1) * P], pcol("c3", k),
                                                start=(k == 0), stop=(k == DT - 1))
                    last.then_inc(slab_done, 1)
            norm_pe(pe, DT, Hk)
            split_pe(pe, "in3", tiles_of(H3), tiles_of(H3, DT), before=h_parts_before(pe))
            st = STAGE["iw3"]
            slab_wait(pe, st.slab0)
            for t in loop_tiles(pe, st):
                bank_wait(pe, t)
                for k in range(DT):
                    last = nc.tensor.matmul(gp[:, t.bank, 0:AH], H[:, k, t.j * P:(t.j + 1) * P],
                                            ring[:, st.slab0 % RING, k * AH:(k + 1) * AH],
                                            start=(k == 0), stop=(k == DT - 1))
                if t.j == st.tiles - 1:
                    last.then_inc(slab_done, 1)
                shared_tile_done(t, last)
            st = STAGE["v3"]
            for t in loop_tiles(pe, st):
                bank_wait(pe, t)
                for k in range(DT):
                    slab = st.slab0 + k // 2
                    if t.j == 0 and k % 2 == 0:
                        slab_wait(pe, slab)
                    last = nc.tensor.matmul(gp[:, t.bank, :], H[:, k, t.j * P:(t.j + 1) * P],
                                            ring[:, slab % RING, (k % 2) * S:(k % 2 + 1) * S],
                                            start=(k == 0), stop=(k == DT - 1))
                    if t.j == st.tiles - 1 and k % 2:
                        last.then_inc(slab_done, 1)
                shared_tile_done(t, last)
            for b in range(BANKS):
                pe.wait_ge(drained[b], (STAGE["out3"].tile0 - b + BANKS - 1) // BANKS)
            pe.wait_ge(stat_ready, n_pe.sums)
            pe.wait_ge(mod_ready, 1)
            for i in range(8):
                n_pe.sq += 1
                pe.wait_ge(sq_ready, n_pe.sq)
                nc.tensor.matmul((gp if i < 4 else aux)[:, i % 4, :], bones, hsq(i), start=True,
                                 stop=True).then_inc(hd_sum, 1)
            pe.wait_ge(hd_root, 8)
            for n, i in enumerate(ROTATED):
                if n >= 5:
                    pe.wait_ge(hd_normed, n - 4)
                if n >= 4:
                    pe.wait_ge(ro_ready, n - 3)
                nc.tensor.matmul(gp[:, n % 4, :], const("perm_dsa"), arena[:, i, :], start=True,
                                 stop=True).then_inc(ro_psum, 1)
            pe.wait_ge(ro_ready, len(ROTATED))
            n = 0
            for qb in range(1, 4):
                for h in range(AH):
                    if n >= 2:
                        pe.wait_ge(ix_relu, n - 1)
                    nc.tensor.matmul(gp[:, n % 2, 0:(qb + 1) * P], arena[half(h), dIQ + h // 2, qb * P:(qb + 1) * P],
                                     arena[half(h), dIK, 0:(qb + 1) * P], start=True, stop=True).then_inc(ix_psum, 1)
                    n += 1
            pe.wait_ge(sel_ready, 3)
            pe.wait_ge(ix_relu, 3 * AH)
            attention_pe(pe, DSA)
            norm_pe_at(pe)
            stream_pe(pe, "out3", lambda k, t: arena[:, dAT + k, :])
            norm_pe(pe, DT, Hk)
            ffn2_pe(pe, 3)

        def norm_pe_at(pe):
            pe.wait_ge(dsa_out, 4)
            pe.wait_ge(cv_ready, 4)
            sum_pe(pe, 4, arena_tiles(dCV))
            norm_pe(pe, 4, arena_tiles(46))
            norm_pe(pe, 4, arena_tiles(46))
            norm_pe(pe, 4, arena_tiles(46))
            pe.wait_ge(an_ready, 4)
            pe.wait_ge(cn_ready, 4)

        def three_act(act, a):
            act.wait_ge(x_ready, 7 * DT)
            c = par[:, POFF["c3"]:POFF["c3"] + DT]
            nc.scalar.activation(c, c, ACT.Silu).then_inc(mod_act, 1)
            pre_norm_act(act, a)
            split_first_act(act, "in3")
            for t in loop_tiles(act, STAGE["in3"], a, body=32):
                split_ahead_act(act, t)
                consume_wait(act, t)
                a.go(nc.scalar.activation(arena[:, t.j, :], gp[:, t.bank, :],
                                          ACT.Sigmoid if dCG <= t.j < dIQ else ACT.Copy))
                a.tell(drained[t.bank], in3_ready)
            for t in loop_tiles(act, STAGE["iw3"]):
                consume_wait(act, t)
                a.go(nc.scalar.activation(IW[:, t.j * AH:(t.j + 1) * AH], gp[:, t.bank, 0:AH], ACT.Copy,
                                          scale=float(AH ** -0.5 * HD ** -0.5)))
                a.tell(drained[t.bank], iw_ready)
            copy_act(act, a, "v3", arena_tiles(dV), done=v3_ready)
            for i in range(8):
                nc.scalar.activation(hsq(i), arena[:, dQ + i, :], ACT.Square).then_inc(sq_ready, 1)
            for i in range(8):
                act.wait_ge(hd_sum, i + 1)
                nc.scalar.activation(hsq(i), (gp if i < 4 else aux)[:, i % 4, :], ACT.Sqrt, scale=1.0 / HD,
                                     bias=const("eps")).then_inc(hd_root, 1)
            n = 0
            for qb in range(1, 4):
                for h in range(AH):
                    act.wait_ge(ix_psum, n + 1)
                    if n >= 2:
                        act.wait_ge(ix_used, n - 1)
                    w = (qb + 1) * P
                    nc.scalar.activation(REL(n)[:, 0:w], gp[:, n % 2, 0:w], ACT.Relu).then_inc(ix_relu, 1)
                    n += 1
            attention_act(act, DSA)
            act.wait_ge(at_pv, DSA.u0 + len(dsa_units))
            for i in range(4):
                nc.scalar.activation(arena[:, dAT + i, :], aux[:, i, :], ACT.Copy).then_inc(dsa_out, 1)
            mean_act(act, 512)
            act.wait_ge(ln_c, 2)
            norm_act(act, a, 4, arena_tiles(dCV), arena_tiles(46), lambda k: None, 1.0 / 512)
            for k in range(4):
                act.wait_ge(cl_ready, k + 1)
                a(nc.scalar.activation(arena[:, dCV + k, :], arena[:, dCV + k, :], ACT.Silu))
            norm_act(act, a, 4, arena_tiles(dCV), arena_tiles(46), lambda k: None, 1.0 / 512)
            act.wait_ge(cn_ready, 4)
            norm_act(act, a, 4, arena_tiles(dAT), arena_tiles(46), lambda k: act.wait_ge(dsa_out, k + 1), 1.0 / 512)
            pre_norm_act(act, a)
            split_first_act(act, "ff1a_3")
            for i in range(2):
                ffn2_relu_act(act, a, 3, i)
                split_stage_act(act, a, f"ff2{'ab'[i]}_3")

        def modulated_norm_dve(dve, v, gain, shift, parts):
            n_dve.sums += 1
            dve.wait_ge(stat_ready, n_dve.sums)
            v(nc.vector.reciprocal(root[:], root[:]))

            def make(k):
                v(nc.vector.scalar_tensor_tensor(out=H[:, k, :], in0=X[:, k, :], scalar=pcol(gain, k), in1=root[:],
                                                 op0=ALU.mult, op1=ALU.mult))
                return nc.vector.tensor_scalar(H[:, k, :], H[:, k, :], MOD(shift, k), None, ALU.add)

            split_h_dve(dve, v, parts, make)

        def gated_residual_dve(dve, v, name, gate, body=8):
            for t in loop_tiles(dve, STAGE[name], v, body):
                consume_wait(dve, t)
                x = X[:, t.idx, :]
                v.go(nc.vector.scalar_tensor_tensor(out=x, in0=gp[:, t.bank, :], scalar=MOD(gate, t.idx), in1=x,
                                                    op0=ALU.mult, op1=ALU.add))
                v.tell(drained[t.bank], x_ready)
            n_dve.x += DT

        def three_dve(dve, v):
            dve.wait_ge(slab_done, STAGE["ada3"].slab0 + 48)
            mod = par[:, POFF["b_ada3"]:POFF["b_ada3"] + 48]
            v(nc.vector.tensor_tensor(mod, aux[:, 1, 0:48], mod, ALU.add))
            for gain, j in (("g_norm13", 1), ("g_norm23", 4)):
                g = par[:, POFF[gain]:POFF[gain] + DT]
                v(nc.vector.scalar_tensor_tensor(out=g, in0=mod[:, j * DT:(j + 1) * DT], scalar=1.0, in1=g,
                                                 op0=ALU.add, op1=ALU.mult))
            v.tell(mod_ready)
            modulated_norm_dve(dve, v, "g_norm13", 0, H3)
            v(nc.vector.memset(PAD[:, 0:CONVK - 1], 0.0))
            for i in range(4):
                y = arena[:, dCV + i, :]
                tap = lambda k: pcol("w_dw3", i * CONVK + k)
                dve.wait_ge(in3_ready, dCG + i + 1)
                v(nc.vector.tensor_tensor(PAD[:, CONVK - 1:], arena[:, dCA + i, :], arena[:, dCG + i, :], ALU.mult))
                v(nc.vector.tensor_scalar(y, PAD[:, CONVK - 1:], tap(CONVK - 1), pcol("b_dw3", i), ALU.mult, ALU.add))
                for k in range(CONVK - 1):
                    v(nc.vector.scalar_tensor_tensor(out=y, in0=PAD[:, k:k + S], scalar=tap(k), in1=y,
                                                     op0=ALU.mult, op1=ALU.add))
                v.tell(cv_ready)
            for i in range(8):
                dve.wait_ge(hd_root, i + 1)
                v(nc.vector.reciprocal(hsq(i), hsq(i)))
                x = arena[:, dQ + i, :]
                nc.vector.scalar_tensor_tensor(out=x, in0=x, scalar=pcol("g_q3" if i < 4 else "g_k3"), in1=hsq(i),
                                               op0=ALU.mult, op1=ALU.mult).then_inc(hd_normed, 1)
            dve.wait_ge(rot_in, 32)
            dve.wait_ge(hd_normed, 8)
            tmp = arena[:, 48, :]
            for n, i in enumerate(ROTATED):
                x = arena[:, i, :]
                dve.wait_ge(ro_psum, n + 1)
                v.go(nc.vector.tensor_tensor(tmp, gp[:, n % 4, :], ROTS, ALU.mult))
                v(nc.vector.tensor_tensor(x, x, ROTC, ALU.mult))
                v.go(nc.vector.tensor_tensor(x, x, tmp, ALU.add))
                v.tell(ro_ready)
            dve.wait_ge(iw_ready, 4)
            n = 0
            for qb in range(1, 4):
                w = (qb + 1) * P
                sc, wk = SCORE[:, 0:w], WORK[:, 0:w]
                for h in range(AH):
                    iw = IW[:, qb * AH + h:qb * AH + h + 1]
                    dve.wait_ge(ix_relu, n + 1)
                    if h == 0:
                        v(nc.vector.tensor_scalar(sc, REL(n)[:, 0:w], iw, None, ALU.mult))
                    else:
                        v(nc.vector.scalar_tensor_tensor(out=sc, in0=REL(n)[:, 0:w], scalar=iw, in1=sc,
                                                         op0=ALU.mult, op1=ALU.add))
                    dve.sem_inc(ix_used, 1)
                    n += 1
                last = SCORE[:, w - 64:w]
                v(nc.vector.tensor_tensor(last, last, const("chunked"), ALU.add))
                v(nc.vector.max(out=TOP8, in_=sc))
                for k in range(TOPK // 8 - 1):
                    v(nc.vector.match_replace(out=wk, in_to_replace=TOP8, in_values=sc if k == 0 else wk,
                                              imm_value=-3e38))
                    v(nc.vector.max(out=TOP8, in_=wk))
                thr = TOP8[:, 7:8]
                sel = SELM(qb)
                v(nc.vector.tensor_scalar(sel, sc, thr, None, ALU.is_gt))
                v(nc.vector.tensor_reduce(CNT, sel, AX.X, ALU.add))
                v(nc.vector.tensor_scalar(CNT, CNT, -1.0, float(TOPK), ALU.mult, ALU.add))
                v(nc.vector.tensor_scalar(sc, sc, thr, None, ALU.is_equal))
                v(nc.vector.tensor_tensor_scan(wk, sc, sc, 0.0, ALU.add, ALU.max))
                v(nc.vector.tensor_scalar(wk, wk, CNT, None, ALU.is_le))
                v(nc.vector.tensor_tensor(wk, wk, sc, ALU.mult))
                v(nc.vector.tensor_tensor(sel, sel, wk, ALU.add))
                v(nc.vector.tensor_scalar(sel, sel, -NEG, NEG, ALU.mult, ALU.add))
                v.tell(sel_ready)
            attention_dve(dve, v, DSA)
            centre_dve(dve, v, 4, arena_tiles(dCV))
            scale_shift_dve(dve, v, 4, arena_tiles(dCV), lambda k: pcol("g_conv_ln3", k), lambda k: pcol("b_conv_ln3", k),
                            arena_tiles(dCV), cl_ready)
            norm_dve(dve, v, 4, arena_tiles(dCV), lambda k: pcol("g_out_conv3", k), arena_tiles(dCV), cn_ready)
            norm_dve(dve, v, 4, arena_tiles(dAT), lambda k: pcol("g_out_attn3", k), arena_tiles(dAT), an_ready)
            gated_residual_dve(dve, v, "out3", 2)
            modulated_norm_dve(dve, v, "g_norm23", 3, fH)
            for i in range(2):
                ffn2_square_dve(dve, v, 3, i)
                gated_residual_dve(dve, v, f"ff2{'ab'[i]}_3", 5)

        def store(sp):
            for k in range(DT):
                sp.wait_ge(x_ready, n_store.x - DT + k + 1)
                sp.dma_start(out[k], X[:, k, :]).then_inc(out_stored, 16)
            sp.wait_ge(out_stored, 16 * DT)

        def load_slabs(sp, lo, hi):
            w = d["weights"]
            full = (hi - lo) // RING
            groups = w[lo:lo + full * RING].rearrange("(n s) p c -> n s p c", s=RING)
            with sp.Fori(0, full) as it:
                for j in range(RING):
                    sp.wait_ge(slab_done, it * RING + (lo + j - RING + 1))
                    sp.dma_start(ring[:, (lo + j) % RING, :], groups[it, j]).then_inc(landed[(lo + j) % RING], 16)
            for g in range(lo + full * RING, hi):
                sp.wait_ge(slab_done, g - RING + 1)
                sp.dma_start(ring[:, g % RING, :], w[g]).then_inc(landed[g % RING], 16)

        n_store = Count()
        PH = [
            (hyena_pe, hyena_act, hyena_dve, None, ()),
            (ffn1_pe, ffn1_act, ffn1_dve, ffn1_pool, (0,)),
            (rwkv_pe, rwkv_act, rwkv_dve, rwkv_pool, ()),
            (ffn1_pe, ffn1_act, ffn1_dve, ffn1_pool, (1,)),
            (final1_pe, final1_act, final1_dve, None, ()),
            (two_pe, two_act, two_dve, two_pool, ()),
            (three_pe, three_act, three_dve, three_pool, ()),
        ][:phases]
        LAST = {1: 'hy_out', 2: 'down0', 3: 'rw_o', 4: 'down1', 5: 'down1', 6: 'ff2b_2', 7: 'ff2b_3'}
        NXUP = [1, 1, 1, 1, 1, 2, 3][:phases]
        block = ctx.enter_context(nc.Block())

        @block.sync
        def _(sp):
            sp.dma_start(par[:], d["par"]).then_inc(inputs_in, 16)
            sp.dma_start(cst[:], d["cst"]).then_inc(inputs_in, 16)
            sp.dma_start(X[:], d["x"]).then_inc(inputs_in, 16)
            w = d["weights"]
            NSLAB = STAGE[LAST[len(PH)]].slab0 + STAGE[LAST[len(PH)]].slabs
            for s in range(RING):
                sp.dma_start(ring[:, s, :], w[s]).then_inc(landed[s], 16)
            load_slabs(sp, RING, min(HOLD, NSLAB))
            if NSLAB > HOLD:
                sp.wait_ge(rw_yst, DT)
                load_slabs(sp, HOLD, NSLAB)

        @block.gpsimd
        def _(pool):
            pool.dma_start(f_z, d["hy_z"]).then_inc(f_in, 16)
            pool.dma_start(f_w[0:HY_EMB, 0:HY_W], d["hy_f_w1"]).then_inc(f_in, 16)
            pool.dma_start(f_w[:, HY_W:3 * HY_W], d["hy_f_w23"]).then_inc(f_in, 16)
            pool.dma_start(f_w4, d["hy_f_w4"]).then_inc(f_in, 16)
            pool.dma_start(f_delta, d["hy_delta"]).then_inc(f_in, 16)
            g = Steps(pool, sem("pool_steps"))
            for _, _, _, f, args in PH:
                if f:
                    f(pool, g, *args)

        @block.tensor
        def _(pe):
            for f, _, _, _, args in PH:
                f(pe, *args)

        @block.scalar
        def _(act):
            a = Steps(act, sem("act_steps"))
            act.wait_ge(inputs_in, INPUTS)
            act.wait_ge(f_in, 16 * 5)
            for _, f, _, _, args in PH:
                f(act, a, *args)

        @block.vector
        def _(dve):
            v = Steps(dve, sem("dve_steps"))
            for _, _, f, _, args in PH:
                f(dve, v, *args)

        @block.sync
        def _(sp):
            n_store.x = DT * sum(NXUP)
            store(sp)


def vec(a):
    return np.asarray(a).reshape(-1, P).T


def col64(a):
    a = np.asarray(a).reshape(-1, 64)
    return np.concatenate([a, np.zeros_like(a)], axis=1).T


def tall(w):
    k, n = w.shape
    pad = (-n) % P
    if pad:
        w = np.concatenate([w, np.zeros((k, pad), w.dtype)], axis=1)
    return w.reshape(DT, P, -1, P).transpose(2, 1, 0, 3).reshape(-1, P, SLAB)


def deep(w):
    k = w.shape[0] // P
    groups = -(-k // DT)
    w = np.concatenate([w, np.zeros(((groups * DT - k) * P, w.shape[1]), w.dtype)])
    return w.reshape(groups, DT, P, -1, P).transpose(3, 0, 2, 1, 4).reshape(-1, P, SLAB)


def pairs(a):
    return np.stack([a[..., :F1].reshape(a.shape[:-1] + (F1T, P)), a[..., F1:].reshape(a.shape[:-1] + (F1T, P))],
                    axis=-2).reshape(a.shape)


def dft_tables():
    n = 2 * S
    tok = np.arange(S)
    f = np.arange(S)
    ang = 2 * np.pi * ((f[:, None] * tok[None, :]) % n) / n
    re, im = np.cos(ang), -np.sin(ang)
    im[0] = np.cos(np.pi * tok)
    fw = np.stack([re.reshape(4, P, 4, P), im.reshape(4, P, 4, P)], axis=2)
    fw = fw.transpose(0, 4, 3, 2, 1).reshape(4, P, SLAB)
    cr = 2 * re / n
    cr[0] = 1 / n
    ci = 2 * im / n
    ci[0] = im[0] / n
    inv = np.stack([cr.reshape(2, 2, P, S), ci.reshape(2, 2, P, S)])
    inv = inv.transpose(0, 1, 3, 2, 4).reshape(4, P, SLAB)
    return fw.astype(np.float32), inv.astype(np.float32)


def constants():
    c = np.zeros((P, NCST), np.float32)

    def put(name, a):
        a = np.asarray(a, np.float32)
        c[:a.shape[0], COFF[name]:COFF[name] + a.shape[1]] = a

    p = np.arange(P)
    put("ident", np.eye(P))
    put("ones", np.ones((P, P)))
    put("bones", (p[:, None] // HD == p[None, :] // HD))
    s, t = p[:, None] % CH, np.arange(CH)[None, :]
    put("eye64", s == t)
    put("strict", np.concatenate([s < t, s > t], axis=1))
    put("incl", np.concatenate([s <= t, s >= t], axis=1))
    merge = [(s >> (i + 1) == t >> (i + 1)) & (s >> i != t >> i) for i in range(LEVELS)]
    put("level", np.concatenate([merge[0] & (s < t)] + merge[1:] + [merge[0] & (s > t)], axis=1))
    put("causal", np.where(p[None, :] <= p[:, None], 0.0, NEG))
    put("chunked", np.tile(np.where(p[:, None] < 64, NEG, 0.0), (1, 64)))
    half = ROPE // 2
    m = np.zeros((P, QKD))
    for i in range(half):
        m[NOPE + half + i, NOPE + i] = 1
        m[NOPE + i, NOPE + half + i] = 1
    put("perm_mla", m)
    m = np.zeros((P, P))
    for h in range(2):
        for i in range(8):
            m[h * 64 + 8 + i, h * 64 + i] = 1
            m[h * 64 + i, h * 64 + 8 + i] = 1
    put("perm_dsa", m)
    put("eps", np.full((P, 1), EPS))
    put("gn_eps", np.full((P, 1), HD * 1e-5))
    inv = 10000.0 ** (-np.arange(0, ROPE, 2, dtype=np.float32) / ROPE)
    col = np.zeros((P, 1))
    col[NOPE:NOPE + ROPE, 0] = np.concatenate([inv, inv])
    put("invf", col)
    sg = np.zeros((P, 1))
    sg[NOPE:NOPE + half], sg[NOPE + half:NOPE + ROPE] = -1, 1
    put("rsign", sg)
    put("ntime", -(np.arange(S).reshape(4, P).T / (S - 1)))
    return c


def filter_constants():
    bands = (HY_EMB - 1) // 2
    n = np.arange(S, dtype=np.float32)
    fr = np.linspace(1e-4, bands - 1, bands, dtype=np.float32)
    ang = np.float32(2 * np.pi / S) * n[:, None] * fr[None, :]
    z = np.concatenate([(n / np.float32(S - 1))[:, None], np.cos(ang), -np.sin(ang)], axis=-1)
    deltas = np.abs(np.linspace(np.log(1e-2) / 1.5, np.log(1e-2) / 0.3, D, dtype=np.float32))
    return np.ascontiguousarray(z.T.astype(np.float32)), np.ascontiguousarray(np.tile(deltas, (P, 1)))


def ffn_halves(b, up, down):
    down = down.reshape(DT, 4, P, SLAB)
    return {f"ff1a_{b}": up[:F2T // 2], f"ff1b_{b}": up[F2T // 2:],
            f"ff2a_{b}": down[:, :2].reshape(16, P, SLAB), f"ff2b_{b}": down[:, 2:].reshape(16, P, SLAB)}


def weight_stream(a):
    fw, inv = dft_tables()
    z = np.zeros
    f32 = np.float32
    w_in = a["hy_w_in"][0]
    parts = {
        "hy_in": tall(np.concatenate([w_in[:, D:2 * D], w_in[:, 2 * D:], w_in[:, :D]], axis=1)),
        "hy_dft": fw, "hy_idft": inv, "hy_out": tall(a["hy_w_out"][0]),
    }
    for i in range(2):
        parts[f"up{i}"] = tall(pairs(a["ff_w_up"][i]))
        parts[f"down{i}"] = deep(a["ff_w_down"][i])
    w1 = a["rw_w1"][0]
    lora1 = [np.concatenate([w1[0], w1[1]], axis=1), np.concatenate([a["rw_a1"][0], z((D, 64), f32)], axis=1),
             a["rw_g1"][0]]
    parts.update({
        "rw_lora1": tall(np.concatenate(lora1, axis=1)),
        "rw_r": tall(a["rw_w_r"][0]), "rw_k": tall(a["rw_w_k"][0]), "rw_v": tall(a["rw_w_v"][0]),
        "rw_a2": np.concatenate([a["rw_a2"][0], z((64, D), f32)])[None],
        "rw_w2": a["rw_w2"][0].reshape(1, P, D), "rw_g2": a["rw_g2"], "rw_o": tall(a["rw_w_o"][0]),
    })
    w = a["w_in_2"][0]
    rot = z((D, P), f32)
    rot[:, NOPE:QKD] = w[:, 384:416]
    br = [a[n][0].reshape(2, P, D) for n in ("w_br_mla_2", "w_br_sg_2", "w_br_conv_2", "w_br_pool_2")]
    parts.update({
        "in2": tall(np.concatenate([w[:, :384], rot, w[:, 416:1952]], axis=1)), "gate2": tall(w[:, 1952:]),
        "br2_0": br[0], "br2_1": br[1], "br2_2": br[2], "br2_3": br[3], "out2": tall(a["w_out_2"][0]),
        **ffn_halves(2, tall(a["w_ff1_2"][0]), deep(a["w_ff2_2"][0])),
    })
    w = a["w_in_3"][0]
    q, k, v, iq, ik, iw, ca, cg = np.split(w, np.cumsum([512, 512, 512, 512, 64, 8, 512]), axis=1)
    iws = z((1, P, SLAB), f32)
    iws[0, :, :DT * AH] = iw.reshape(DT, P, AH).transpose(1, 0, 2).reshape(P, DT * AH)
    parts.update({
        "ada3": tall(a["w_ada_3"][0]), "in3": tall(np.concatenate([ca, cg, iq, ik, ik, q, k], axis=1)), "iw3": iws,
        "v3": v.reshape(4, 2, P, S).transpose(0, 2, 1, 3).reshape(4, P, SLAB), "out3": tall(a["w_out_3"][0]),
        **ffn_halves(3, tall(a["w_ff1_3"][0]), deep(a["w_ff2_3"][0])),
    })
    out = [parts[n] if n in parts else z((s, P, SLAB), f32) for n, _, _, s in STREAM]
    for (n, _, _, s), part in zip(STREAM, out):
        assert part.shape == (s, P, SLAB), (n, part.shape)
    return np.concatenate(out)


def parameters(a):
    order = lambda v: np.concatenate([v[..., D:2 * D], v[..., 2 * D:], v[..., :D]], axis=-1)
    p = {
        "norm_mix": vec(a["norm_mix_g"]), "norm_ffn": vec(a["norm_ffn_g"]), "final_norm": vec(a["final_norm_g"]),
        "hy_b_in": vec(order(a["hy_b_in"][0])), "hy_conv_w": vec(order(a["hy_conv_w"][0])),
        "hy_conv_b": vec(order(a["hy_conv_b"][0])), "hy_skip": vec(a["hy_skip"]), "hy_b_out": vec(a["hy_b_out"]),
        "hy_f_b": np.concatenate([col64(a["hy_f_b1"]), col64(a["hy_f_b2"]), col64(a["hy_f_b3"])], axis=1),
        "hy_f_freq": col64(a["hy_f_freq"]),
        "ff_conv_w": vec(pairs(a["ff_conv_w"])), "ff_conv_b": vec(pairs(a["ff_conv_b"])),
    }
    p.update({"rw_" + n: vec(a["rw_" + n]) for n in ("mu", "w0", "a0", "k_k", "k_a", "r_k", "ln_w", "ln_b")})
    p.update({
        "norm_mix_pre2": vec(a["norm_mix_pre_2"]), "gate_b2": vec(a["gate_b_2"]), "q_norm2": vec(a["q_norm_2"]),
        "kv_norm2": vec(a["kv_norm_2"]), "sg_ln_g2": vec(a["sg_ln_g_2"]), "sg_ln_b2": vec(a["sg_ln_b_2"]),
        "conv_w2": vec(a["conv_w_2"]), "pool_scale2": vec(a["pool_scale_2"]),
        "norm_mix_post2": vec(a["norm_mix_post_2"]), "norm_ffn_pre2": vec(a["norm_ffn_pre_2"]),
        "norm_ffn_post2": vec(a["norm_ffn_post_2"]),
    })
    two = lambda g: vec(np.concatenate([g[0], g[0]]))
    p.update({
        "c3": vec(a["c_3"]), "b_ada3": vec(a["b_ada_3"]), "g_norm13": vec(a["g_norm1_3"]), "g_q3": two(a["g_q_3"]),
        "g_k3": two(a["g_k_3"]), "w_dw3": a["w_dw_3"][0].reshape(CONVK, 4, P).transpose(2, 1, 0).reshape(P, -1),
        "b_dw3": vec(a["b_dw_3"]), "g_conv_ln3": vec(a["g_conv_ln_3"]), "b_conv_ln3": vec(a["b_conv_ln_3"]),
        "g_out_attn3": vec(a["g_out_attn_3"]), "g_out_conv3": vec(a["g_out_conv_3"]), "g_norm23": vec(a["g_norm2_3"]),
    })
    cols = [p[n] if n in p else np.zeros((P, w), np.float32) for n, w in PARAMS]
    for (n, w), c in zip(PARAMS, cols):
        assert c.shape == (P, w), (n, c.shape)
    return np.ascontiguousarray(np.concatenate(cols, axis=1))


def small_two(a):
    kv = a["w_ukv_2"][0].reshape(P, MLA_H, NOPE + VH)
    pw = a["pool_w_2"][0]
    return np.ascontiguousarray(np.concatenate([
        a["w_uq_2"][0].reshape(2, P, MLA_H * QKD).transpose(1, 0, 2).reshape(P, -1),
        kv[:, :, :NOPE].reshape(P, -1), kv[:, :, NOPE:].reshape(P, -1),
        a["sg_w_2"][0].transpose(2, 0, 1).reshape(P, -1),
        pw.reshape(2, 2, 64, 64).transpose(1, 2, 0, 3).reshape(P, -1),
        np.triu(np.ones((P, P), np.float32))], axis=1))


def window_counts():
    t = np.arange(S)
    c = np.stack([1.0 / np.minimum(t + 1, w) for w in POOL_WIN])
    return np.ascontiguousarray(np.repeat(c, 64, axis=0).reshape(2, P, S).transpose(1, 0, 2).astype(np.float32))


def rotation():
    inv = (500000.0 ** (-np.arange(0, 16, 2, dtype=np.float32) / 16)).astype(np.float32)
    ang = np.arange(S, dtype=np.float32)[None, :] * inv[:, None]
    c, s = np.ones((2, 64, S), np.float32), np.zeros((2, 64, S), np.float32)
    c[:, 0:8] = c[:, 8:16] = np.cos(ang)
    s[:, 0:8], s[:, 8:16] = -np.sin(ang), np.sin(ang)
    return c.reshape(P, S), s.reshape(P, S)


PHASES = 99


def host_arrays(a):
    z, delta = filter_constants()
    x = np.ascontiguousarray(a["x"][0].T.reshape(DT, P, S).transpose(1, 0, 2))
    return {
        "x": x, "par": parameters(a), "cst": constants(), "weights": weight_stream(a),
        "hy_z": z, "hy_delta": delta, "hy_f_w1": np.ascontiguousarray(a["hy_f_w1"][0]),
        "hy_f_w23": np.ascontiguousarray(np.concatenate([a["hy_f_w2"][0], a["hy_f_w3"][0]], axis=1)),
        "hy_f_w4": np.ascontiguousarray(a["hy_f_w4"][0]),
        "sm2": small_two(a), "sg_b": np.ascontiguousarray(a["sg_b_2"][0].reshape(1, 4 * SGC)),
        "rcnt": window_counts(), "pos": np.ascontiguousarray(a["positions_2"].reshape(S).astype(np.int32)),
        "rotc": rotation()[0], "rots": rotation()[1],
    }


def kernel(**inputs):
    import concourse.bacc as bacc
    from concourse.bass_utils import run_bass_kernel_spmd

    arrays = host_arrays({k: np.asarray(v) for k, v in inputs.items()})
    nc = bacc.Bacc("TRN2", target_bir_lowering=False, num_devices=1)
    d = {n: nc.dram_tensor(f"in_{n}", list(a.shape), mybir.dt.from_np(a.dtype), kind="ExternalInput").ap()
         for n, a in arrays.items()}
    out = nc.dram_tensor("out_x", [DT, P, S], F32, kind="ExternalOutput").ap()
    build(nc, d, out, PHASES)
    r = run_bass_kernel_spmd(nc, [{f"in_{n}": a for n, a in arrays.items()}], core_ids=[0])
    y = r.results[0]["out_x"]
    return np.ascontiguousarray(y.reshape(D, S).T).reshape(1, S, D)
```

```python
from contextlib import ExitStack, nullcontext

import numpy as np

import concourse.bass as bass
from concourse import mybir

F32 = mybir.dt.float32
F32R = mybir.dt.float32r
I32 = mybir.dt.int32
ACT = mybir.ActivationFunctionType
ALU = mybir.AluOpType
AX = mybir.AxisListType

P = 128
S = 512
D = 1024
DT = D // P
F1 = 2816
F1T = F1 // P
F2T = 4 * D // P
RING = 4
PARTS = 2
SLAB = 1024
BANKS = 4
NT = 66
EPS = 1e-6
NEG = -1e30

HD = 64
CH = 64
NCH = S // CH
KAPPA = float(np.exp(-0.5))
LEVELS = 6

HY_EMB, HY_W = 33, 64

MLA_H, NOPE, ROPE, VH = 4, 64, 32, 64
QKD = NOPE + ROPE
SGC = 128
POOL_WIN = (2, 4, 8, 16)

AH = 8
CONVK = 31
TOPK = 128
MODS = 6 * DT

PARAMS = [
    ("norm_mix", 16), ("norm_ffn", 16), ("final_norm", 8),
    ("hy_b_in", 24), ("hy_conv_w", 72), ("hy_conv_b", 24), ("hy_skip", 8), ("hy_b_out", 8),
    ("hy_f_b", 3), ("hy_f_freq", 1),
    ("rw_mu", 48), ("rw_w0", 16), ("rw_a0", 8), ("rw_k_k", 8), ("rw_k_a", 8), ("rw_r_k", 8),
    ("rw_ln_w", 8), ("rw_ln_b", 8),
    ("ff_conv_w", 2 * 3 * 2 * F1T), ("ff_conv_b", 2 * 2 * F1T),
    ("norm_mix_pre2", 8), ("gate_b2", 32), ("q_norm2", 2), ("kv_norm2", 1), ("sg_ln_g2", 2), ("sg_ln_b2", 2),
    ("conv_w2", 6), ("pool_scale2", 2), ("norm_mix_post2", 8), ("norm_ffn_pre2", 8), ("norm_ffn_post2", 8),
    ("mod_sums3", 8), ("b_ada3", 48), ("g_norm13", 8), ("g_q3", 1), ("g_k3", 1), ("w_dw3", 4 * CONVK), ("b_dw3", 4),
    ("g_conv_ln3", 4), ("b_conv_ln3", 4), ("g_out_attn3", 4), ("g_out_conv3", 4), ("g_norm23", 8),
]
POFF, NPAR = {}, 0
for _name, _w in PARAMS:
    POFF[_name] = NPAR
    NPAR += _w

CONSTS = [("ident", 128), ("ones", 128), ("bones", 128), ("eye64", 64), ("strict", 128), ("incl", 128),
          ("level", (LEVELS + 1) * 64), ("causal", 128), ("chunked", 64), ("perm_mla", 96), ("perm_dsa", 128),
          ("eps", 1), ("gn_eps", 1), ("invf", 1), ("rsign", 1), ("ntime", 4)]
COFF, NCST = {}, 0
for _name, _w in CONSTS:
    COFF[_name] = NCST
    NCST += _w

STREAM = [
    ("hy_in", 24, 1, 24), ("hy_dft", 0, 0, 4), ("hy_idft", 8, 0, 4), ("hy_out", 8, 1, 8),
    ("up0", 2 * F1T, 1, 2 * F1T), ("down0", 8, 3, 24),
    ("rw_lora1", 3, 1, 3), ("rw_r", 8, 1, 8), ("rw_k", 8, 1, 8), ("rw_v", 8, 1, 8), ("rw_a2", 8, 0, 1),
    ("rw_w2", 16, 0, 1), ("rw_g2", 8, 0, 1), ("rw_o", 8, 1, 8),
    ("up1", 2 * F1T, 1, 2 * F1T), ("down1", 8, 3, 24),
    ("in2", 16, 1, 16), ("gate2", 32, 1, 32), ("br2_0", 8, 0, 2), ("br2_1", 8, 0, 2), ("br2_2", 8, 0, 2),
    ("br2_3", 8, 0, 2), ("out2", 8, 1, 8),
    ("ff1a_2", F2T // 2, 1, F2T // 2), ("ff2a_2", 8, 2, 16), ("ff1b_2", F2T // 2, 1, F2T // 2), ("ff2b_2", 8, 2, 16),
    ("iw3", 4, 0, 1), ("in3a", 5, 1, 5), ("in3b", 16, 1, 16), ("v3", 4, 0, 4), ("out3", 8, 1, 8),
    ("ff1a_3", F2T // 2, 1, F2T // 2), ("ff2a_3", 8, 2, 16), ("ff1b_3", F2T // 2, 1, F2T // 2), ("ff2b_3", 8, 2, 16),
]
SPLIT = [("up0", "down0"), ("rw_r", "rw_k", "rw_v"), ("up1", "down1"), ("in2",), ("ff1a_2", "ff2a_2", "ff1b_2", "ff2b_2"), ("in3a", "in3b"),
         ("ff1a_3", "ff2a_3", "ff1b_3", "ff2b_3")]


class Stage:

    def __init__(self, name, tiles, per_tile, slabs, slab0, tile0, shared0):
        self.name, self.tiles, self.per_tile, self.slabs = name, tiles, per_tile, slabs
        self.slab0, self.tile0, self.shared0 = slab0, tile0, shared0
        self.split0 = self.run_end = None


STAGE = {}
NSLAB = _tile = _shared = 0
for _name, _n, _s, _all in STREAM:
    STAGE[_name] = Stage(_name, _n, _s, _all, NSLAB, _tile, _shared)
    NSLAB += _all
    _tile += _n
    _shared += 0 if _s or not _n else _n - 1
_split = 0
for _run in SPLIT:
    for _name in _run:
        STAGE[_name].split0, STAGE[_name].run_end = _split, STAGE[_run[-1]].slab0 + STAGE[_run[-1]].slabs
        _split += STAGE[_name].slabs


class Steps:

    def __init__(self, eng, sem):
        self.eng, self.sem, self.n = eng, sem, 0

    def go(self, ins):
        ins.then_inc(self.sem, 1)
        self.n += 1

    def carry(self):
        self.eng.sem_inc(self.sem, 1)
        self.n += 1

    def settle(self):
        if self.n:
            self.eng.wait_ge(self.sem, self.n)

    def __call__(self, ins):
        self.go(ins)
        self.settle()

    def tell(self, *sems):
        self.settle()
        for s in sems:
            self.eng.sem_inc(s, 1)

    def restart(self):
        self.settle()
        if self.n:
            self.eng.sem_clear(self.sem)
        self.n = 0


class Tile:

    def __init__(self, st, j, it, body):
        self.st, self.j, self.it, self.body = st, j, it, body
        self.idx = j if it is None else it * body + j
        self.bank = (st.tile0 + j) % BANKS

    def ready(self):
        v = self.st.slab0 + (self.j + 1) * self.st.per_tile
        return v if self.it is None else self.it * (self.body * self.st.per_tile) + v

    def bank_uses(self):
        v = (self.st.tile0 + self.j) // BANKS
        return v if self.it is None else self.it * (self.body // BANKS) + v


def loop_tiles(eng, st, steps=None, body=8):
    full = st.tiles // body if st.per_tile and st.tiles >= 2 * body else 0
    if full:
        if steps:
            steps.restart()
        with eng.Fori(0, full) as it:
            for j in range(body):
                yield Tile(st, j, it, body)
            if steps:
                steps.restart()
    for j in range(full * body, st.tiles):
        yield Tile(st, j, None, body)


def build(nc, d, out):
    ctx = ExitStack()
    with ctx:
        sems = {}

        def sem(name):
            if name not in sems:
                sems[name] = ctx.enter_context(nc.semaphore(name))
            return sems[name]

        def sb(name, shape, dt=F32):
            return ctx.enter_context(nc.sbuf_tensor(name, shape, dt))

        with nc.sbuf_tensor("w_high", [P, PARTS, SLAB], F32R) as w_high, \
                nc.sbuf_tensor("w_low", [P, PARTS, SLAB], F32R) as w_low:
            pass
        scratch = sb("scratch", [P, 2 * PARTS, SLAB])

        def in_arena(*tensors):
            with ExitStack() as place:
                return [place.enter_context(nc.sbuf_tensor(n, [P, tiles, S], F32R)) for n, tiles in tensors]

        ffG_high, ffG_low, _, ffH = in_arena(("ffn1_high", F1T), ("ffn1_low", F1T), ("gap1", 4), ("ffn1_h", 2 * DT))
        _, f_high, f_low, fH = in_arena(("gap2", 16), ("ffn2_high", F2T // 2), ("ffn2_low", F2T // 2),
                                        ("ffn2_h", 2 * DT))
        _, mixB_high, mixA_low, mixB_low, _, mixA_high = in_arena(
            ("gap5", 24), ("mix_b_high", DT), ("mix_a_low", DT), ("mix_b_low", DT), ("gap6", DT), ("mix_a_high", DT))
        _, bH = in_arena(("gap3", 16), ("in2_h", 2 * DT))
        _, H3_high, _, H3_low = in_arena(("gap4", 21), ("in3_high", DT), ("gap7", 24), ("in3_low", DT))
        arena = sb("arena", [P, NT, S])
        ring = sb("ring", [P, RING, SLAB])
        X = sb("X", [P, DT, S])
        H = sb("H", [P, DT, S])
        root = sb("root", [P, S])
        par = sb("par", [P, NPAR])
        cst = sb("cst", [P, NCST])
        gp = ctx.enter_context(nc.psum_tensor("gp", [P, BANKS, S], F32))
        aux = ctx.enter_context(nc.psum_tensor("aux", [P, BANKS, S], F32))

        def pcol(name, i=0):
            return par[:, bass.ds(POFF[name] + i, 1)]

        def const(name, lo=0, hi=None):
            w = dict(CONSTS)[name]
            return cst[:, COFF[name] + lo:COFF[name] + (w if hi is None else hi)]

        ident, ones, bones = const("ident"), const("ones"), const("bones")

        landed = [sem(f"landed{i}") for i in range(RING)]
        slab_done = sem("slab_done")
        shared_done = sem("shared_done")
        drained = [sem(f"drained{i}") for i in range(BANKS)]
        x_ready = sem("x_ready")
        h_ready = sem("h_ready")
        inputs_in = sem("inputs_in")
        sum_ready, stat_ready = sem("sum_ready"), sem("stat_ready")
        sq_ready = sem("sq_ready")
        out_stored = sem("out_stored")
        pe_s = sem("pe_steps")

        class Count:

            def __init__(self):
                self.x = self.h = self.sums = self.sq = 0

        def slab_wait(pe, slab, it=None, per_it=0):
            v = 16 * (slab // RING + 1)
            pe.wait_ge(landed[slab % RING], v if it is None else it * (16 * per_it // RING) + v)

        def bank_wait(pe, t):
            if t.it is not None or t.st.tile0 + t.j >= BANKS:
                pe.wait_ge(drained[t.bank], t.bank_uses())

        def stream_pe(pe, name, rhs, ksizes=None, width=P, before=None, body=8):
            st = STAGE[name]
            kt = ksizes or [DT] * st.per_tile
            for t in loop_tiles(pe, st, None, body):
                if before:
                    before(t)
                bank_wait(pe, t)
                k = 0
                for s, n in enumerate(kt):
                    slab = st.slab0 + t.j * st.per_tile + s
                    slab_wait(pe, slab, t.it, t.body * st.per_tile)
                    for i in range(n):
                        last = nc.tensor.matmul(gp[0:width, t.bank, :], ring[:, slab % RING, i * P:i * P + width],
                                                rhs(k, t), start=(k == 0), stop=(k == sum(kt) - 1))
                        k += 1
                    last.then_inc(slab_done, 1)

        high_ready, low_ready = sem("high_ready"), sem("low_ready")

        def split_act(act, slab, st, it=None, per_it=0):
            v = 16 * (slab // RING + 1)
            act.wait_ge(landed[slab % RING], v if it is None else it * (16 * per_it // RING) + v)
            nc.scalar.activation(w_high[:, slab % PARTS, :], ring[:, slab % RING, :], ACT.Copy).then_inc(high_ready, 1)

        def split_first_act(act, name):
            st = STAGE[name]
            for s in range(PARTS):
                split_act(act, st.slab0 + s, st)

        def split_ahead_act(act, t):
            st, per = t.st, t.st.per_tile
            for s in range(per):
                slab = st.slab0 + t.j * per + s
                if t.it is None and slab + PARTS >= st.run_end:
                    continue
                act.wait_ge(slab_done, slab + 1 if t.it is None else t.it * (t.body * per) + (slab + 1))
                split_act(act, slab + PARTS, st, t.it, t.body * per)

        def split_stage_act(act, a, name, body=8):
            for t in loop_tiles(act, STAGE[name], a, body):
                split_ahead_act(act, t)

        def split_pool(pool, g, run, lo=0, hi=None):
            st = STAGE[run[0]]
            n = (st.run_end - st.slab0 if hi is None else hi) - lo
            slab0, split0, body = st.slab0 + lo, st.split0 + lo, 8

            def low(slab, count):
                pool.wait_ge(high_ready, count)
                nc.gpsimd.tensor_tensor(w_low[:, slab % PARTS, :], ring[:, slab % RING, :], w_high[:, slab % PARTS, :],
                                        ALU.subtract).then_inc(low_ready, 1)

            if n >= body:
                with pool.Fori(0, n // body) as it:
                    for j in range(body):
                        low(slab0 + j, it * body + (split0 + j + 1))
            for j in range(n // body * body, n):
                low(slab0 + j, split0 + j + 1)

        def split_pe(pe, name, high, low, ksizes=None, before=None, body=8, beside=None):
            st = STAGE[name]
            kt = ksizes or [DT] * st.per_tile
            for t in loop_tiles(pe, st, None, body):
                if beside:
                    beside(t.j)
                bank_wait(pe, t)
                k = 0
                for s, n in enumerate(kt):
                    j = t.j * st.per_tile + s
                    slab = st.slab0 + j
                    pe.wait_ge(low_ready, st.split0 + j + 1 if t.it is None else
                               t.it * (t.body * st.per_tile) + (st.split0 + j + 1))
                    for i in range(n):
                        if before and t.j == 0:
                            before(k)
                        w = slice(i * P, (i + 1) * P)
                        for q, (wt, x) in enumerate(((w_high, high), (w_high, low), (w_low, high))):
                            last = nc.tensor.matmul(gp[:, t.bank, :], wt[:, slab % PARTS, w], x(k),
                                                    start=(k == 0 and q == 0), stop=(k == sum(kt) - 1 and q == 2))
                        k += 1
                    last.then_inc(slab_done, 1)

        def tiles_of(tensor, base=0):
            return lambda k: tensor[:, base + k, :]

        def split_h_dve(dve, v, high, low, make):
            made = []
            for k in range(DT + 2):
                if k < DT:
                    v.go(make(k))
                    made.append(v.n)
                if 1 <= k <= DT:
                    dve.wait_ge(v.sem, made[k - 1])
                    v.go(nc.vector.tensor_copy(high(k - 1), H[:, k - 1, :]))
                    made[k - 1] = v.n
                if k >= 2:
                    dve.wait_ge(v.sem, made[k - 2])
                    nc.vector.tensor_tensor(low(k - 2), H[:, k - 2, :], high(k - 2),
                                            ALU.subtract).then_inc(h_ready, 1)
            v.settle()
            n_dve.h += DT

        def split_norm_dve(dve, v, gain, parts, g0=0):
            n_dve.sums += 1
            dve.wait_ge(stat_ready, n_dve.sums)
            v(nc.vector.reciprocal(root[:], root[:]))
            split_h_dve(dve, v, tiles_of(parts), tiles_of(parts, DT), lambda k: nc.vector.scalar_tensor_tensor(
                out=H[:, k, :], in0=X[:, k, :], scalar=pcol(gain, g0 + k), in1=root[:], op0=ALU.mult, op1=ALU.mult))

        def h_parts_before(pe):
            n_pe.h += DT
            base = n_pe.h - DT
            return lambda k: pe.wait_ge(h_ready, base + k + 1)

        def split_tile_dve(dve, v, src, high, low, done):
            v(nc.vector.tensor_copy(high, src))
            v.go(nc.vector.tensor_tensor(low, src, high, ALU.subtract))
            v.tell(done)

        def consume_wait(eng, t):
            st = t.st
            if st.per_tile:
                eng.wait_ge(slab_done, t.ready())
            elif t.j < st.tiles - 1:
                eng.wait_ge(shared_done, st.shared0 + t.j + 1)
            else:
                eng.wait_ge(slab_done, st.slab0 + st.slabs)

        def shared_tile_done(t, last):
            if t.j < t.st.tiles - 1:
                last.then_inc(shared_done, 1)

        def at(base, t, per):
            return base + per * t.j if t.it is None else t.it * (per * t.body) + (base + per * t.j)

        def norm_act(act, a, n, src, sq, src_wait, scale, eps="eps", root_wait=None):
            for k in range(n):
                src_wait(k)
                nc.scalar.activation(sq(k), src(k), ACT.Square).then_inc(sq_ready, 1)
            n_act.sums += 1
            act.wait_ge(sum_ready, n_act.sums)
            if root_wait:
                root_wait()
            nc.scalar.activation(root[:], aux[:, 0, :], ACT.Sqrt, scale=scale, bias=const(eps)).then_inc(stat_ready, 1)

        def norm_pe(pe, n, sq):
            if n_pe.sums:
                pe.wait_ge(stat_ready, n_pe.sums)
            for k in range(n):
                n_pe.sq += 1
                pe.wait_ge(sq_ready, n_pe.sq)
                last = nc.tensor.matmul(aux[:, 0, :], ones, sq(k), start=(k == 0), stop=(k == n - 1))
            last.then_inc(sum_ready, 1)
            n_pe.sums += 1

        def norm_dve(dve, v, n, src, gain, dst, done):
            n_dve.sums += 1
            dve.wait_ge(stat_ready, n_dve.sums)
            v(nc.vector.reciprocal(root[:], root[:]))
            for k in range(n):
                nc.vector.scalar_tensor_tensor(out=dst(k), in0=src(k), scalar=gain(k), in1=root[:],
                                               op0=ALU.mult, op1=ALU.mult).then_inc(done, 1)

        n_pe, n_act, n_dve = Count(), Count(), Count()
        Xk, Hk = (lambda k: X[:, k, :]), (lambda k: H[:, k, :])

        def arena_tiles(base):
            return lambda k: arena[:, base + k, :]

        def x_wait(eng, count):
            base = count.x - DT

            def wait(k):
                if base >= 0:
                    eng.wait_ge(x_ready, base + k + 1)
                else:
                    eng.wait_ge(inputs_in, INPUTS)
            return wait

        INPUTS = 16 * 3

        def pre_norm_act(act, a):
            norm_act(act, a, DT, Xk, Hk, x_wait(act, n_act), 1.0 / D)
            n_act.x += DT

        def pre_norm_dve(dve, v, gain, g0=0):
            norm_dve(dve, v, DT, Xk, lambda k: pcol(gain, g0 + k), Hk, h_ready)
            n_dve.h += DT

        def h_before(pe):
            n_pe.h += DT
            need = n_pe.h

            def before(t):
                if t.j == 0:
                    pe.wait_ge(h_ready, need)
            return before

        def residual_dve(dve, v, name, bias=None, body=8):
            st = STAGE[name]
            for t in loop_tiles(dve, st, v, body):
                consume_wait(dve, t)
                if bias is None:
                    ins = nc.vector.tensor_tensor(X[:, t.idx, :], gp[:, t.bank, :], X[:, t.idx, :], ALU.add)
                else:
                    ins = nc.vector.scalar_tensor_tensor(out=X[:, t.idx, :], in0=gp[:, t.bank, :],
                                                         scalar=bias(t.idx), in1=X[:, t.idx, :],
                                                         op0=ALU.add, op1=ALU.add)
                v.go(ins)
                v.tell(drained[t.bank], x_ready)
            n_dve.x += DT

        def copy_act(act, a, name, dst, func=ACT.Copy, bias=None, rows=P, done=None, body=8):
            st = STAGE[name]
            for t in loop_tiles(act, st, a, body):
                if st.split0 is not None:
                    split_ahead_act(act, t)
                consume_wait(act, t)
                kw = {} if bias is None else {"bias": bias(t.idx)}
                a.go(nc.scalar.activation(dst(t.idx), gp[0:rows, t.bank, :], func, **kw))
                a.tell(*([drained[t.bank]] + ([done] if done else [])))

        hX1, hU, hX0, hKS, hKD, hDEC, hYR, hYI, hTMP = 0, 8, 16, 24, 32, 40, 48, 56, 64
        hUT = hDEC
        TAP0 = 5
        f_in = sem("hy_filter_in")
        f_w4 = arena[0:HY_W, hYR:hYR + 4, :].rearrange("p a b -> p (a b)")
        f_delta = arena[:, hYR + 4:hYR + 6, :].rearrange("p a b -> p (a b)")
        f_z = arena[0:HY_EMB, hYR + 6, :]
        f_w = arena[0:HY_W, hYR + 7, 0:3 * HY_W]
        f_h = [arena[0:HY_W, hYI + i, :] for i in range(3)]
        f_t = [arena[0:HY_W, hYI + 3 + i, :] for i in range(2)]
        f_pre, f_arg, f_sin = sem("f_pre"), sem("f_arg"), sem("f_sin")
        f_k, f_kread = sem("f_k"), sem("f_kread")
        f_dec, f_comb = sem("f_dec"), sem("f_comb")
        hz_ready, hz_used = sem("hz_ready"), sem("hz_used")
        u_ready, ut_psum, ut_ready = sem("u_ready"), sem("ut_psum"), sem("ut_ready")
        dft_set, kspec, yspec = sem("dft_set"), sem("kspec"), sem("yspec")
        hy_ready = sem("hy_ready")
        TWO_PI_HI = 6.28125
        TWO_PI_LO = float(2 * np.pi - 6.28125)
        MAGIC = 12582912.0

        def reduce_angle(v, eng, x, tmp, shift=0.0):
            v(eng.tensor_scalar(tmp, x, float(1 / (2 * np.pi)), MAGIC + shift, ALU.mult, ALU.add) if not shift else
              eng.tensor_scalar(tmp, x, float(1 / (2 * np.pi)), shift, ALU.mult, ALU.add))
            if shift:
                v(eng.tensor_scalar(tmp, tmp, MAGIC, None, ALU.add))
            v(eng.tensor_scalar(tmp, tmp, -MAGIC, None, ALU.add))
            v(eng.scalar_tensor_tensor(out=x, in0=tmp, scalar=-TWO_PI_HI, in1=x, op0=ALU.mult, op1=ALU.add))
            v(eng.scalar_tensor_tensor(out=x, in0=tmp, scalar=-TWO_PI_LO, in1=x, op0=ALU.mult, op1=ALU.add))

        def hyena_pe(pe):
            pe.wait_ge(inputs_in, INPUTS)
            norm_pe(pe, DT, Hk)
            h_wait = h_before(pe)

            def before(t):
                h_wait(t)
                if 1 <= t.j <= 3:
                    i = t.j - 1
                    if i:
                        pe.wait_ge(f_sin, i)
                    else:
                        pe.wait_ge(f_in, 16 * 5)
                    rows = HY_EMB if i == 0 else HY_W
                    nc.tensor.matmul(aux[0:HY_W, 1, :], f_w[0:rows, i * HY_W:(i + 1) * HY_W],
                                     f_z if i == 0 else f_h[i - 1], start=True, stop=True).then_inc(f_pre, 1)
                if TAP0 <= t.j < TAP0 + 8:
                    n = t.j - TAP0
                    tk, c = n // 2, n % 2
                    pe.wait_ge(f_sin, 3)
                    for b in range(2):
                        if n:
                            pe.wait_ge(f_kread, 2 * n + b - 1)
                        nc.tensor.matmul(aux[:, 2 + b, :], f_h[2][:, tk * P:(tk + 1) * P],
                                         f_w4[:, b * D + c * S:b * D + (c + 1) * S],
                                         start=True, stop=True).then_inc(f_k, 1)

            stream_pe(pe, "hy_in", lambda k, t: H[:, k, :], before=before, body=24)
            pe.wait_ge(f_kread, 16)
            for i in range(DT):
                pe.wait_ge(u_ready, i + 1)
                if i >= 2:
                    pe.wait_ge(ut_ready, i - 1)
                for tk in range(4):
                    last = nc.tensor.transpose(aux[:, 2 + i % 2, tk * P:(tk + 1) * P],
                                               arena[:, hU + i, tk * P:(tk + 1) * P], ident)
                last.then_inc(ut_psum, 1)
            pe.wait_ge(ut_ready, DT)
            pe.wait_ge(f_comb, 8)
            for b in range(BANKS):
                pe.wait_ge(drained[b], 24 // BANKS)
            st = STAGE["hy_dft"]
            for j in range(4):
                slot = (st.slab0 + j) % RING
                slab_wait(pe, st.slab0 + j)
                for c in range(2):
                    ps = gp if c == 0 else aux
                    if j:
                        pe.wait_ge(yspec, 2 * (j - 1) + c + 1)
                    for q, (lo, base) in enumerate(((0, hUT), (P, hUT), (0, hKS), (P, hKD))):
                        for tk in range(4):
                            last = nc.tensor.matmul(ps[:, q, :],
                                                    ring[:, slot, tk * 256 + lo:tk * 256 + lo + P],
                                                    arena[:, base + 2 * tk + c, :], start=(tk == 0), stop=(tk == 3))
                    if j == 0:
                        for tk in range(4):
                            last = nc.tensor.matmul(ps[0:1, 3, :], ring[:, slot, tk * 256 + P:tk * 256 + P + 1],
                                                    arena[:, hKS + 2 * tk + c, :], start=(tk == 0), stop=(tk == 3))
                    last.then_inc(dft_set if c == 0 else slab_done, 1)
            pe.wait_ge(yspec, 8)
            st = STAGE["hy_idft"]
            for t in loop_tiles(pe, st):
                bank_wait(pe, t)
                for s in range(4):
                    slot = (st.slab0 + s) % RING
                    if t.j == 0:
                        slab_wait(pe, st.slab0 + s)
                    for f in range(2):
                        fi = (s % 2) * 2 + f
                        y = arena[:, (hYR if s < 2 else hYI) + 2 * fi + t.j // 4, (t.j % 4) * P:(t.j % 4 + 1) * P]
                        last = nc.tensor.matmul(gp[:, t.bank, :], y, ring[:, slot, f * S:(f + 1) * S],
                                                start=(s == 0 and f == 0), stop=(s == 3 and f == 1))
                    if t.j == st.tiles - 1:
                        last.then_inc(slab_done, 1)
                shared_tile_done(t, last)
            pe.wait_ge(hy_ready, DT)
            stream_pe(pe, "hy_out", lambda k, t: arena[:, hU + k, :])

        def hyena_act(act, a):
            pre_norm_act(act, a)
            for t in loop_tiles(act, STAGE["hy_in"], a, body=24):
                if 1 <= t.j <= 3:
                    act.wait_ge(f_arg, t.j)
                    nc.scalar.activation(f_h[t.j - 1], f_t[0], ACT.Sin).then_inc(f_sin, 1)
                if t.j == TAP0:
                    act.wait_ge(f_in, 16 * 5)
                    for n in range(8):
                        nc.scalar.activation(arena[:, hDEC + n, :], f_delta[:, n % 2 * S:(n % 2 + 1) * S], ACT.Exp,
                                             scale=const("ntime", n // 2, n // 2 + 1)).then_inc(f_dec, 1)
                consume_wait(act, t)
                act.wait_ge(hz_used, at(1, t, 1))
                a.go(nc.scalar.activation(arena[:, hTMP + t.j % 2, :], gp[:, t.bank, :], ACT.Identity,
                                          bias=pcol("hy_b_in", t.idx)))
                a.tell(drained[t.bank])
                nc.scalar.activation(arena[:, hX1 + t.idx, :], arena[:, hTMP + t.j % 2, :], ACT.Identity,
                                     scale=pcol("hy_conv_w", 24 + t.idx),
                                     bias=pcol("hy_conv_b", t.idx)).then_inc(hz_ready, 1)
            for i in range(DT):
                act.wait_ge(ut_psum, i + 1)
                dst = arena[:, hUT:hUT + 8, :].rearrange("p (t c) s -> p t (c s)", c=2)[:, :, i * P:(i + 1) * P]
                if i == 0:
                    act.wait_ge(f_comb, 8)
                nc.scalar.activation(dst, aux[:, 2 + i % 2, :].rearrange("p (t c) -> p t c", t=4),
                                     ACT.Copy).then_inc(ut_ready, 1)
            st = STAGE["hy_dft"]
            for j in range(4):
                for c in range(2):
                    ps = gp if c == 0 else aux
                    if c == 0:
                        act.wait_ge(dft_set, j + 1)
                    else:
                        act.wait_ge(slab_done, st.slab0 + j + 1)
                    if j:
                        act.wait_ge(yspec, 2 * (j - 1) + c + 1)
                    a(nc.scalar.activation(arena[:, hX1 + 2 * c, :], ps[:, 2, :], ACT.Copy))
                    nc.scalar.activation(arena[:, hX1 + 2 * c + 1, :], ps[:, 3, :], ACT.Copy).then_inc(kspec, 1)

        def hyena_dve(dve, v):
            dve.sem_inc(hz_used, 2)
            dve.wait_ge(inputs_in, INPUTS)
            dve.wait_ge(f_in, 16 * 5)
            pre_norm_dve(dve, v, "norm_mix", 0)

            def filter_layer(i):
                dve.wait_ge(f_pre, i + 1)
                v(nc.vector.tensor_scalar(f_t[0], aux[0:HY_W, 1, :], pcol("hy_f_b", i)[0:HY_W],
                                          pcol("hy_f_freq")[0:HY_W], ALU.add, ALU.mult))
                reduce_angle(v, nc.vector, f_t[0], f_t[1])
                v.tell(f_arg)

            def filter_taps(n):
                dve.wait_ge(f_dec, n + 1)
                dec = arena[:, hDEC + n, :]
                kb = arena[:, hYI + 5 + n % 2, :]
                dve.wait_ge(f_k, 2 * n + 1)
                v(nc.vector.tensor_tensor(arena[:, hKD + n, :], aux[:, 2, :], dec, ALU.mult))
                v.tell(f_kread)
                dve.wait_ge(f_k, 2 * n + 2)
                v(nc.vector.tensor_tensor(kb, aux[:, 3, :], dec, ALU.mult))
                v.tell(f_kread)
                v(nc.vector.tensor_tensor(arena[:, hKS + n, :], arena[:, hKD + n, :], kb, ALU.add))
                v(nc.vector.tensor_tensor(arena[:, hKD + n, :], arena[:, hKD + n, :], kb, ALU.subtract))
                v.tell(f_comb)

            for t in loop_tiles(dve, STAGE["hy_in"], v, body=24):
                if 1 <= t.j <= 3:
                    filter_layer(t.j - 1)
                if TAP0 <= t.j < TAP0 + 8:
                    filter_taps(t.j - TAP0)
                z, y = arena[:, hTMP + t.j % 2, :], arena[:, hX1 + t.idx, :]
                dve.wait_ge(hz_ready, at(1, t, 1))
                v(nc.vector.scalar_tensor_tensor(out=y[:, 1:S], in0=z[:, 0:S - 1], scalar=pcol("hy_conv_w", t.idx),
                                                 in1=y[:, 1:S], op0=ALU.mult, op1=ALU.add))
                v.go(nc.vector.scalar_tensor_tensor(out=y[:, 0:S - 1], in0=z[:, 1:S],
                                                    scalar=pcol("hy_conv_w", 48 + t.idx), in1=y[:, 0:S - 1],
                                                    op0=ALU.mult, op1=ALU.add))
                v.tell(hz_used)
            for i in range(DT):
                v.go(nc.vector.tensor_tensor(arena[:, hU + i, :], arena[:, hU + i, :], arena[:, hX1 + i, :], ALU.mult))
                v.tell(u_ready)
            for j in range(4):
                for c in range(2):
                    ps = gp if c == 0 else aux
                    dve.wait_ge(kspec, 2 * j + c + 1)
                    kr, ki = arena[:, hX1 + 2 * c, :], arena[:, hX1 + 2 * c + 1, :]
                    t1, t2, t3, t4 = (arena[:, hX1 + 4 + i, :] for i in range(4))
                    yr, yi = arena[:, hYR + 2 * j + c, :], arena[:, hYI + 2 * j + c, :]
                    v.go(nc.vector.tensor_tensor(t1, ps[:, 0, :], kr, ALU.mult))
                    v.go(nc.vector.tensor_tensor(t2, ps[:, 1, :], ki, ALU.mult))
                    v.go(nc.vector.tensor_tensor(t3, ps[:, 0, :], ki, ALU.mult))
                    v(nc.vector.tensor_tensor(t4, ps[:, 1, :], kr, ALU.mult))
                    v.go(nc.vector.tensor_tensor(yr, t1, t2, ALU.subtract))
                    v(nc.vector.tensor_tensor(yi, t3, t4, ALU.add))
                    if j == 0:
                        v.go(nc.vector.tensor_copy(yr[0:1, :], t1[0:1, :]))
                        v(nc.vector.tensor_copy(yi[0:1, :], t2[0:1, :]))
                    v.tell(yspec)
            for t in loop_tiles(dve, STAGE["hy_idft"]):
                consume_wait(dve, t)
                u = arena[:, hU + t.j, :]
                v(nc.vector.scalar_tensor_tensor(out=u, in0=u, scalar=pcol("hy_skip", t.j), in1=gp[:, t.bank, :],
                                                 op0=ALU.mult, op1=ALU.add))
                v.go(nc.vector.tensor_tensor(u, u, arena[:, hX0 + t.j, :], ALU.mult))
                v.tell(drained[t.bank], hy_ready)
            residual_dve(dve, v, "hy_out", lambda i: pcol("hy_b_out", i))

        ffT = 2 * F1T
        aff_ready, gate_conv, gate_act, pair_done = sem("aff_ready"), sem("gate_conv"), sem("gate_act"), sem("pair_done")

        def ffn1_pe(pe, layer):
            norm_pe(pe, DT, Hk)
            split_pe(pe, f"up{layer}", tiles_of(ffH), tiles_of(ffH, DT), before=h_parts_before(pe))
            pe.wait_ge(pair_done, (layer + 1) * F1T + 2)
            split_pe(pe, f"down{layer}", tiles_of(ffG_high), tiles_of(ffG_low), ksizes=[8, 8, 6])

        ADA_C = H[:, 0:2, :].rearrange("p a b -> p (a b)")
        ADA_W = [H[:, 2 + 2 * i:4 + 2 * i, :].rearrange("p a b -> p (a b)") for i in range(2)]
        ada_c, mod_act, ada_used = sem("ada_c"), sem("mod_act"), sem("ada_used")
        ada_in = [sem(f"ada_in{i}") for i in range(2)]
        ADA0 = STAGE["up1"].slab0 + RING

        def ada_load(sp, i, it=None, per_it=0):
            if i >= 2:
                sp.wait_ge(ada_used, i - 1 if it is None else it * per_it + (i - 1))
            src = d["ada"][i] if it is None else d["ada"][per_it:][it * per_it + (i - per_it)]
            sp.dma_start(ADA_W[i % 2], src).then_inc(ada_in[i % 2], 16)

        def ada_dve(dve, v, j, it=None):
            n = 16 * (j // 2 + 1)
            dve.wait_ge(ada_in[j % 2], n if it is None else it * 64 + n)
            v.go(nc.vector.scalar_tensor_tensor(out=ADA_W[j % 2], in0=ADA_W[j % 2], scalar=1.0, in1=ADA_C, op0=ALU.mult,
                                                op1=ALU.mult, accum_out=pcol("mod_sums3", j % 8)))
            v.tell(ada_used)
            if j % 8 == 7:
                sums = par[:, POFF["mod_sums3"]:POFF["mod_sums3"] + 8]
                b = par[:, bass.ds(POFF["b_ada3"] + (j - 7 if it is None else it * 8 + (j - 7)), 8)]
                v(nc.vector.tensor_tensor(b, sums, b, ALU.add))

        def ffn1_pool(pool, g, layer):
            split_pool(pool, g, (f"up{layer}", f"down{layer}"))

        def ff_cols(layer, t, tap):
            return pcol("ff_conv_w", layer * 6 * F1T + tap * 2 * F1T + t.idx)

        def ffn1_act(act, a, layer):
            pre_norm_act(act, a)
            split_first_act(act, f"up{layer}")
            if layer:
                act.wait_ge(ada_c, 16)
                nc.scalar.activation(ADA_C, ADA_C, ACT.Silu).then_inc(mod_act, 1)
            base = layer * F1T
            for t in loop_tiles(act, STAGE[f"up{layer}"], a):
                tmp = arena[:, ffT + t.j % 4, :]
                split_ahead_act(act, t)
                consume_wait(act, t)
                p = t.j // 2 if t.it is None else t.it * 4 + t.j // 2
                act.wait_ge(pair_done, p + (base + 1))
                nc.scalar.activation(tmp, gp[:, t.bank, :], ACT.Identity, scale=ff_cols(layer, t, 1),
                                     bias=pcol("ff_conv_b", layer * 2 * F1T + t.idx)).then_inc(aff_ready, 1)
                if t.j % 2:
                    g = arena[:, ffT + (t.j - 1) % 4, :]
                    act.wait_ge(gate_conv, p + (base + 1))
                    nc.scalar.activation(g, g, ACT.Silu).then_inc(gate_act, 1)
            split_stage_act(act, a, f"down{layer}")

        def ffn1_dve(dve, v, layer):
            if layer == 0:
                dve.sem_inc(pair_done, 2)
            split_norm_dve(dve, v, "norm_ffn", ffH, layer * DT)
            base = layer * F1T
            if layer:
                dve.wait_ge(mod_act, 1)
            for t in loop_tiles(dve, STAGE[f"up{layer}"], v):
                y = arena[:, ffT + t.j % 4, :]
                z = gp[:, t.bank, :]
                p = t.j // 2 if t.it is None else t.it * 4 + t.j // 2
                dve.wait_ge(aff_ready, at(2 * base + 1, t, 1))
                v(nc.vector.scalar_tensor_tensor(out=y[:, 1:S], in0=z[:, 0:S - 1], scalar=ff_cols(layer, t, 0),
                                                 in1=y[:, 1:S], op0=ALU.mult, op1=ALU.add))
                v.go(nc.vector.scalar_tensor_tensor(out=y[:, 0:S - 1], in0=z[:, 1:S], scalar=ff_cols(layer, t, 2),
                                                    in1=y[:, 0:S - 1], op0=ALU.mult, op1=ALU.add))
                if t.j % 2 == 0:
                    v.tell(drained[t.bank], gate_conv)
                else:
                    v.tell(drained[t.bank])
                    dve.wait_ge(gate_act, p + (base + 1))
                    v(nc.vector.tensor_tensor(y, y, arena[:, ffT + (t.j - 1) % 4, :], ALU.mult))
                    split_tile_dve(dve, v, y, ffG_high[:, p, :], ffG_low[:, p, :], pair_done)
                if layer:
                    ada_dve(dve, v, t.j, t.it)
            if layer:
                for j in range(2 * F1T, MODS):
                    ada_dve(dve, v, j)
            residual_dve(dve, v, f"down{layer}")

        wR, wK, wV, wA, wS, wXX, wMA, wMB, wLA, wLB = 0, 8, 16, 24, 32, 48, 56, 24, 32, 40
        wTA, wTG = 64, 65
        HOLD = STAGE["rw_g2"].slab0
        rw_xx = sem("rw_mix")
        MIX = (1, 4, 5, 0, 2, 3)
        MIX_STAGE = ("rw_lora1", "rw_lora1", "rw_lora1", "rw_r", "rw_k", "rw_v")
        MIX_PARTS = (mixA_high, mixA_low), (mixB_high, mixB_low)
        lora_ready = sem("lora_ready")
        rkv_ready = sem("rkv_ready")

        def bd(t):
            return t.rearrange("p (c x) -> p c x", x=2 * CH)

        Hf = H[:, :, :].rearrange("p a b -> p (a b)")
        LO, HI = slice(0, 64), slice(64, 128)
        BETA, KT = ([bd(Hf[:, (2 * i + d_) * 1024:(2 * i + d_ + 1) * 1024]) for d_ in range(2)] for i in range(2))
        XTB, BTOK = ([bd(ring[:, 2 * i + d_, :]) for d_ in range(2)] for i in range(2))
        AR = [bd(scratch[:, d_, :]) for d_ in range(2)]
        MAK = bd(scratch[:, 2, :])
        MBD, KTOK, T1B = BETA, KT, KT
        ARB, ARK, W0, KVP, XT, T1 = ([arena[:, 48 + 2 * i + d_, :] for d_ in range(2)] for i in range(6))
        XS = T1
        T3 = [arena[:, 60, :], root[:]]
        VCOPY = arena[:, 60, :]
        KK, VT, VTN = (arena[:, 61 + i, :] for i in range(3))
        RESET = arena[:, wTA, :]
        small = lambda lo, n: [scratch[:, 3, lo + d_ * n:lo + (d_ + 1) * n] for d_ in range(2)]
        SB, SPC, WS, US = small(0, 128), small(256, 64), small(384, 64), small(512, 64)
        PC, PCN = small(640, NCH), small(640 + 2 * NCH, NCH)
        ZEROED = BETA + KT + XTB + [MAK]
        ch = lambda t: t.rearrange("p (c x) -> p c x", x=CH)
        two = lambda ps, b: ps[:, b:b + 2, :].rearrange("p b (c x) -> p (b c) x", x=2 * CH)
        over = lambda m: m.unsqueeze(1).broadcast_to((P, NCH, CH))
        (rw_kkr, rw_ksq, rw_ksum, rw_kroot, rw_vtok, rw_vnext, rw_vt, rw_cum, rw_exp, rw_prep, rw_beta, rw_M,
         rw_tok, rw_tokst, rw_mask, rw_w0, rw_kv, rw_w0st, rw_kvst, rw_XTst, rw_XT, rw_X1, rw_X1st, rw_X, rw_T1,
         rw_T1st, rw_T1bd, rw_dX, rw_dXT, rw_W, rw_Wst, rw_U, rw_Ust, rw_Sp, rw_S, rw_Y, rw_yst, rw_bon, rw_bsum,
         rw_mean, rw_yc, rw_sq2, rw_var, rw_root2, rw_gn, rw_zero) = (
            sem("rw_" + x) for x in
            ("kkr ksq ksum kroot vtok vnext vt cum exp prep beta M tok tokst mask w0 kv w0st kvst XTst XT X1 "
             "X1st X T1 T1st T1bd dX dXT W Wst U Ust Sp S Y yst bon bsum mean yc sq2 var root2 gn zero").split())
        DIRS = range(2)
        BONUS, YSQ, YROOT = (lambda p: H[:, p % 4, :]), (lambda p: H[:, 4 + p % 2, :]), (lambda p: H[:, 6 + p % 2, :])

        def n2(it, d):
            return it * 2 + (d + 1)

        def n_level(it, lv, d):
            return it * (2 * (LEVELS - 1)) + (2 * (lv - 1) + d + 1)

        def n_xt(it, lv, d):
            return it * (2 * LEVELS) + (2 * lv + d + 1)

        def n_x(it, lv, d):
            return it * (2 * (LEVELS - 2)) + (2 * (lv - 1) + d + 1)

        def n_chunk(it, j, d):
            return it * (2 * NCH) + (2 * j + d + 1)

        def n_link(it, j, d):
            return it * (2 * (NCH - 1)) + (2 * j + d + 1)

        def each_pair(eng, body, steps=None):
            if steps:
                steps.restart()
            with eng.Fori(0, DT - 1) as it:
                body(it, True)
                if steps:
                    steps.restart()
            body(DT - 1, False)

        yg_ready = sem("yg_ready")
        order = lambda d: range(NCH) if d == 0 else range(NCH - 1, -1, -1)

        def rwkv_pe(pe):
            norm_pe(pe, DT, Hk)
            n_pe.h += DT

            def mix_before(m):
                def before(t):
                    if t.j == 0 or m == 0:
                        pe.wait_ge(rw_xx, (m + (t.j if m == 0 else 0) + 1) * DT)
                return before

            buf = lambda m: wMA if m % 2 == 0 else wMB
            stream_pe(pe, "rw_lora1", lambda k, t: arena[:, buf(t.j) + k, :], before=mix_before(0))
            for m in (3, 4, 5):
                split_pe(pe, MIX_STAGE[m], *(tiles_of(x) for x in MIX_PARTS[m % 2]),
                         before=lambda k, m=m: pe.wait_ge(rw_xx, m * DT + k + 1))
            pe.wait_ge(lora_ready, 3)
            for name in ("rw_a2", "rw_w2"):
                st = STAGE[name]
                slab_wait(pe, st.slab0)
                slot = st.slab0 % RING
                for t in loop_tiles(pe, st):
                    bank_wait(pe, t)
                    half = LO if t.j < DT else HI
                    src = arena[LO, wTA, :] if name == "rw_a2" else root[half, :]
                    i = t.j % DT
                    last = nc.tensor.matmul(gp[:, t.bank, :], ring[half, slot, i * P:(i + 1) * P], src,
                                            start=True, stop=True)
                    if t.j == st.tiles - 1:
                        last.then_inc(slab_done, 1)
                    shared_tile_done(t, last)
            t0 = STAGE["rw_g2"].tile0
            for b in range(BANKS):
                pe.wait_ge(drained[b], (t0 - b + BANKS - 1) // BANKS)
            pe.wait_ge(rw_zero, 1)

            def keys_values(nxt):
                pe.wait_ge(rw_ksq, nxt + 1)
                nc.tensor.matmul(gp[:, 0, :], bones, root[:], start=True, stop=True).then_inc(rw_ksum, 1)
                for c in range(NCH):
                    for h in (LO, HI):
                        last = nc.tensor.matmul(gp[h, 1, c * CH:(c + 1) * CH], VCOPY[h, c * CH:(c + 1) * CH],
                                                cst[h, COFF["eye64"]:COFF["eye64"] + 64], start=True, stop=True)
                last.then_inc(rw_vtok, 1)

            def inner_values(d, c, start):
                cs = slice(c * CH, (c + 1) * CH)
                for h in (LO, HI):
                    nc.tensor.matmul(aux[h, 2 + d, cs], VT[h, cs], ARK[d][h, cs], start=start, stop=False,
                                     skip_group_check=True)

            def pair(it, more):
                for d in DIRS:
                    pe.wait_ge(rw_beta, n2(it, d))
                    if d:
                        pe.wait_ge(rw_tokst, n2(it, 0))
                    for q, src in enumerate((BETA[d], KT[d])):
                        for c in range(NCH):
                            last = nc.tensor.matmul(two(gp, 2 * q)[:, c, :], src[:, c, :], ident,
                                                    start=True, stop=True)
                    last.then_inc(rw_tok, 1)
                    pe.wait_ge(rw_prep, n2(it, d))
                    if d:
                        pe.wait_ge(rw_mask, n2(it, 0))
                    else:
                        pe.wait_ge(rw_yst, it)
                    for q, src in enumerate((BETA[d], KT[d])):
                        for c in range(NCH):
                            last = nc.tensor.matmul(two(aux, 2 * q)[:, c, :], src[:, c, :], AR[d][:, c, :],
                                                    start=True, stop=True)
                    last.then_inc(rw_M, 1)
                pe.wait_ge(rw_tokst, n2(it, 1))
                pe.wait_ge(rw_vt, it + 1)
                for d in DIRS:
                    pe.wait_ge(rw_mask, n2(it, d))
                    bank = (gp, aux)[d]
                    for c in range(NCH):
                        cs = slice(c * CH, (c + 1) * CH)
                        last = nc.tensor.matmul(bank[:, 2 * d, cs], MAK[:, c, :], VT[:, cs], start=True, stop=True)
                    last.then_inc(rw_w0, 1)
                    for c in range(NCH):
                        cs = slice(c * CH, (c + 1) * CH)
                        last = nc.tensor.matmul(bank[:, 2 * d + 1, cs], KTOK[d][:, c, :], VT[:, cs],
                                                start=True, stop=True)
                    last.then_inc(rw_kv, 1)
                    pe.wait_ge(rw_XT, n_xt(it, 0, d))
                    for c in range(NCH):
                        last = nc.tensor.matmul(gp[:, 2 + d, c * CH:(c + 1) * CH], XTB[d][:, c, :],
                                                const("eye64"), start=True, stop=True)
                    last.then_inc(rw_X1, 1)
                for lv in range(1, LEVELS):
                    for d in DIRS:
                        if lv == 1:
                            pe.wait_ge(rw_X1st, n2(it, d))
                        else:
                            pe.wait_ge(rw_X, n_x(it, lv - 1, d))
                        for c in range(NCH):
                            last = nc.tensor.matmul(aux[:, d, c * CH:(c + 1) * CH], MBD[d][:, c, :],
                                                    XS[d][:, c * CH:(c + 1) * CH], start=True, stop=True)
                        last.then_inc(rw_T1, 1)
                    if lv < LEVELS - 1:
                        for d in DIRS:
                            if lv == 1:
                                pe.wait_ge(rw_w0st, n2(it, 1))
                                pe.wait_ge(rw_kvst, n2(it, 1))
                            pe.wait_ge(rw_T1st, n_level(it, lv, d))
                            pe.wait_ge(rw_XT, n_xt(it, lv - 1, d))
                            for c in range(NCH):
                                last = nc.tensor.matmul(aux[:, 2 + d, c * CH:(c + 1) * CH], XTB[d][:, c, :],
                                                        arena[:, wS + DT * d + it, c * CH:(c + 1) * CH],
                                                        start=True, stop=True)
                            last.then_inc(rw_dX, 1)
                    for d in DIRS:
                        pe.wait_ge(rw_XT, n_xt(it, lv - 1, d))
                        pe.wait_ge(rw_T1bd, n_level(it, lv, d))
                        for c in range(NCH):
                            last = nc.tensor.matmul(gp[:, 2 + d, c * CH:(c + 1) * CH], T1B[d][:, c, :],
                                                    XT[d][:, c * CH:(c + 1) * CH], start=True, stop=True)
                        last.then_inc(rw_dXT, 1)
                    if lv == 2 and more:
                        keys_values(it + 1)
                if more:
                    pe.wait_ge(rw_kroot, it + 2)
                    pe.wait_ge(rw_vnext, it + 2)
                for j in range(NCH):
                    for d in DIRS:
                        c = order(d)[j]
                        cs = slice(c * CH, (c + 1) * CH)
                        if j:
                            pe.wait_ge(rw_S, n_link(it, j - 1, d))
                            pe.sem_inc(pe_s, 1)
                            for h in (LO, HI):
                                last = nc.tensor.matmul(gp[h, d, 0:64], AR[d][h, c, 0:64], SB[d][h, h],
                                                        start=True, stop=True)
                            last.then_inc(rw_W, 1)
                            nc.tensor.matmul(aux[:, 2 + d, cs], SB[d], AR[d][:, c, 64:128], start=True, stop=False,
                                             skip_group_check=True)
                            inner_values(d, c, False)
                    for d in DIRS:
                        c = order(d)[j]
                        if j:
                            pe.wait_ge(rw_Wst, n_link(it, j - 1, d))
                        else:
                            pe.wait_ge(rw_XT, n_xt(it, LEVELS - 1, d))
                        nc.tensor.matmul(gp[:, 2 + d, 0:64], XTB[d][:, c, :],
                                         WS[d] if j else W0[d][:, c * CH:(c + 1) * CH],
                                         start=True, stop=True).then_inc(rw_U, 1)
                        if not j:
                            inner_values(d, c, True)
                    for d in DIRS:
                        c = order(d)[j]
                        cs = slice(c * CH, (c + 1) * CH)
                        pe.wait_ge(rw_Ust, n_chunk(it, j, d))
                        last = nc.tensor.matmul(aux[:, d, 0:64], BTOK[d][:, c, :], US[d], start=True, stop=True)
                        if j < NCH - 1:
                            last.then_inc(rw_Sp, 1)
                        for h in (LO, HI):
                            last = nc.tensor.matmul(aux[h, 2 + d, cs], US[d][h, :], ARB[d][h, cs], start=False,
                                                    stop=True, skip_group_check=True)
                        if j == NCH - 1 and d:
                            last.then_inc(rw_Y, 1)

            keys_values(0)
            pe.wait_ge(rw_kroot, 1)
            pe.wait_ge(rw_vnext, 1)
            each_pair(pe, pair)
            pe.wait_ge(rw_yst, DT)
            for p in range(DT + 1):
                if p < DT:
                    if p >= BANKS:
                        pe.wait_ge(rw_root2, p - BANKS + 1)
                    nc.tensor.matmul(aux[:, p % BANKS, :], bones, arena[:, wS + p, :], start=True,
                                     stop=True).then_inc(rw_mean, 1)
                    pe.wait_ge(rw_bon, p + 1)
                    if p >= BANKS:
                        pe.wait_ge(rw_gn, p - BANKS + 1)
                    nc.tensor.matmul(gp[:, p % BANKS, :], bones, BONUS(p), start=True, stop=True).then_inc(rw_bsum, 1)
                if p:
                    pe.wait_ge(rw_sq2, p)
                    nc.tensor.matmul(aux[:, (p - 1) % BANKS, :], bones, YSQ(p - 1), start=True,
                                     stop=True).then_inc(rw_var, 1)
            pe.wait_ge(rw_gn, DT)
            st = STAGE["rw_g2"]
            slab_wait(pe, st.slab0)
            for t in loop_tiles(pe, st):
                bank_wait(pe, t)
                last = nc.tensor.matmul(gp[:, t.bank, :], ring[:, st.slab0 % RING, t.j * P:(t.j + 1) * P],
                                        arena[:, wTG, :], start=True, stop=True)
                if t.j == st.tiles - 1:
                    last.then_inc(slab_done, 1)
                shared_tile_done(t, last)
            pe.wait_ge(yg_ready, DT)
            stream_pe(pe, "rw_o", lambda k, t: arena[:, wS + k, :])

        def rwkv_act(act, a):
            pre_norm_act(act, a)
            for t, (dst, func) in zip(loop_tiles(act, STAGE["rw_lora1"]),
                                      ((root[:], ACT.Tanh), (arena[:, wTA, :], ACT.Copy),
                                       (arena[:, wTG, :], ACT.Sigmoid))):
                consume_wait(act, t)
                a.go(nc.scalar.activation(dst, gp[:, t.bank, :], func))
                a.tell(drained[t.bank], lora_ready)
            split_first_act(act, "rw_r")
            for name, base in (("rw_r", wR), ("rw_k", wK), ("rw_v", wV)):
                copy_act(act, a, name, arena_tiles(base), done=rkv_ready)
            copy_act(act, a, "rw_a2", arena_tiles(wA), ACT.Sigmoid, lambda i: pcol("rw_a0", i), done=rkv_ready)
            copy_act(act, a, "rw_w2", arena_tiles(wS), ACT.Sigmoid, lambda i: pcol("rw_w0", i), done=rkv_ready)
            act.wait_ge(rw_zero, 1)

            def keys_values(nxt):
                act.wait_ge(rw_kkr, nxt + 1)
                a.go(nc.scalar.activation(root[:], KK, ACT.Square))
                nc.scalar.activation(VCOPY, arena[:, wV + nxt, :], ACT.Copy).then_inc(rw_ksq, 1)

            def keys_root(nxt):
                act.wait_ge(rw_ksum, nxt + 1)
                nc.scalar.activation(root[:], gp[:, 0, :], ACT.Sqrt).then_inc(rw_kroot, 1)

            def decays(nxt, d, part):
                before = arena[:, wS + DT * d + nxt, :]
                if part == 0:
                    act.wait_ge(rw_cum, n2(nxt, d))
                    a.go(nc.scalar.activation(T3[d], T1[d], ACT.Exp, scale=KAPPA))
                    a.go(nc.scalar.activation(before, before, ACT.Exp, scale=-KAPPA))
                else:
                    a.go(nc.scalar.activation(PCN[d], PCN[d], ACT.Exp, scale=-KAPPA))
                    a.settle()
                    nc.scalar.activation(T1[d], T1[d], ACT.Exp, scale=-KAPPA).then_inc(rw_exp, 1)

            def pair(it, more):
                act.wait_ge(rw_prep, n2(it, 0))
                act.wait_ge(rw_vnext, it + 1)
                nc.scalar.activation(VT, VTN, ACT.Copy).then_inc(rw_vt, 1)
                for d in DIRS:
                    act.wait_ge(rw_tok, n2(it, d))
                    a.go(nc.scalar.activation(BTOK[d], two(gp, 0), ACT.Copy))
                    act.wait_ge(rw_M, n2(it, d))
                    nc.scalar.activation(KTOK[d], two(gp, 2), ACT.Copy).then_inc(rw_tokst, 1)
                    act.wait_ge(rw_XTst, n_xt(it, 0, d))
                    a.go(nc.scalar.activation(XTB[d][LO, :, 0:64], ch(XT[d])[LO], ACT.Copy))
                    nc.scalar.activation(XTB[d][HI, :, 64:128], ch(XT[d])[HI], ACT.Copy).then_inc(rw_XT, 1)
                for d in DIRS:
                    act.wait_ge(rw_w0, n2(it, d))
                    nc.scalar.activation(W0[d], (gp, aux)[d][:, 2 * d, :], ACT.Copy).then_inc(rw_w0st, 1)
                    act.wait_ge(rw_X1, n2(it, d))
                    nc.scalar.activation(XS[d], gp[:, 2 + d, :], ACT.Copy).then_inc(rw_X1st, 1)
                for lv in range(1, LEVELS):
                    for d in DIRS:
                        if lv == 1:
                            act.wait_ge(rw_kv, n2(it, d))
                        act.wait_ge(rw_T1st, n_level(it, lv, d))
                        a.carry()
                        t = ch(arena[:, wS + DT * d + it, :])
                        a.go(nc.scalar.activation(T1B[d][LO, :, 0:64], t[LO], ACT.Copy))
                        nc.scalar.activation(T1B[d][HI, :, 64:128], t[HI], ACT.Copy).then_inc(rw_T1bd, 1)
                    if more and lv == LEVELS - 1:
                        decays(it + 1, 0, 0)
                        decays(it + 1, 0, 1)
                    for d in DIRS:
                        act.wait_ge(rw_XTst, n_xt(it, lv, d))
                        a.go(nc.scalar.activation(XTB[d][LO, :, 0:64], ch(XT[d])[LO], ACT.Copy))
                        nc.scalar.activation(XTB[d][HI, :, 64:128], ch(XT[d])[HI], ACT.Copy).then_inc(rw_XT, 1)
                    if more and lv == 1:
                        keys_values(it + 1)
                    if more and lv == 2:
                        keys_root(it + 1)
                for j in range(NCH):
                    for d in DIRS:
                        act.wait_ge(rw_U, n_chunk(it, j, d))
                        nc.scalar.activation(US[d], gp[:, 2 + d, 0:64], ACT.Copy).then_inc(rw_Ust, 1)
                    if more and j in (5, 6):
                        decays(it + 1, 1, j - 5)

            keys_values(0)
            keys_root(0)
            for d in DIRS:
                decays(0, d, 0)
                decays(0, d, 1)
            each_pair(act, pair, a)
            for p in range(DT + 1):
                if p < DT:
                    act.wait_ge(rw_yc, p + 1)
                    nc.scalar.activation(YSQ(p), arena[:, wS + p, :], ACT.Square).then_inc(rw_sq2, 1)
                if p:
                    act.wait_ge(rw_var, p)
                    if p > 2:
                        act.wait_ge(rw_gn, p - 2)
                    nc.scalar.activation(YROOT(p - 1), aux[:, (p - 1) % BANKS, :], ACT.Sqrt, scale=1.0 / HD,
                                         bias=const("gn_eps")).then_inc(rw_root2, 1)

        def rwkv_pool(pool, g):
            split_pool(pool, g, SPLIT[1])
            pool.wait_ge(slab_done, HOLD)
            for buf in XTB + [MAK]:
                g.go(nc.gpsimd.memset(buf, 0.0))
            for d in DIRS:
                g.go(nc.gpsimd.memset(SB[d], 0.0))
            g(nc.gpsimd.memset(RESET, 1.0))
            g(nc.gpsimd.memset(ch(RESET)[:, :, 0:1], 0.0))
            g.tell(rw_zero)

            def betas(nxt, before):
                for d in DIRS:
                    if before is not None:
                        pool.wait_ge(rw_dXT, n_level(before, LEVELS - 1, d))
                    pool.wait_ge(rw_exp, n2(nxt, d))
                    g.carry()
                    for dst, base in ((BETA, wA), (KT, wK)):
                        for h, cols in ((LO, slice(0, 64)), (HI, slice(64, 128))):
                            last = nc.gpsimd.tensor_tensor(dst[d][h, :, cols], ch(arena[:, base + nxt, :])[h],
                                                           ch(T3[d])[h], ALU.mult)
                            if dst is BETA or h is LO:
                                g.go(last)
                    last.then_inc(rw_beta, 1)

            def pair(it, more):
                if more:
                    betas(it + 1, it)

            betas(0, None)
            each_pair(pool, pair, g)

        def rwkv_dve(dve, v):
            pre_norm_dve(dve, v, "norm_mix", DT)
            v.settle()
            dve.wait_ge(h_ready, n_dve.h)
            for i in range(DT):
                xx, h = arena[:, wXX + i, :], H[:, i, :]
                v.go(nc.vector.tensor_tensor(xx[:, 1:S - 1], h[:, 0:S - 2], h[:, 2:S], ALU.add))
                v.go(nc.vector.tensor_copy(xx[:, 0:1], h[:, 1:2]))
                v(nc.vector.tensor_copy(xx[:, S - 1:S], h[:, S - 2:S - 1]))
                v(nc.vector.scalar_tensor_tensor(out=xx, in0=xx, scalar=0.5, in1=h, op0=ALU.mult, op1=ALU.subtract))
            for m, j in enumerate(MIX):
                if m >= 2:
                    st = STAGE[MIX_STAGE[m - 2]]
                    dve.wait_ge(slab_done, st.slab0 + (m - 1 if m - 2 < 3 else st.slabs))
                for i in range(DT):
                    dst = arena[:, (wMA, wMB)[m % 2] + i if m < 3 else (wLA, wLB)[m % 2] + i, :]
                    mixed = nc.vector.scalar_tensor_tensor(out=dst, in0=arena[:, wXX + i, :],
                                                           scalar=pcol("rw_mu", j * DT + i), in1=H[:, i, :],
                                                           op0=ALU.mult, op1=ALU.add)
                    if m < 3:
                        mixed.then_inc(rw_xx, 1)
                    else:
                        v(mixed)
                        split_tile_dve(dve, v, dst, *(x[:, i, :] for x in MIX_PARTS[m % 2]), rw_xx)
            v.go(nc.vector.memset(Hf[:, 0:4 * 1024], 0.0))
            dve.wait_ge(rkv_ready, 6 * DT)
            dve.wait_ge(rw_zero, 1)
            dve.wait_ge(slab_done, STAGE["rw_w2"].slab0 + 1)

            def keys(nxt):
                k, aa = arena[:, wK + nxt, :], arena[:, wA + nxt, :]
                v.go(nc.vector.tensor_scalar(KK, k, pcol("rw_k_k", nxt), None, ALU.mult))
                v(nc.vector.tensor_scalar(root[:], aa, 1.0, pcol("rw_k_a", nxt), ALU.subtract, ALU.mult))
                v(nc.vector.scalar_tensor_tensor(out=k, in0=root[:], scalar=1.0, in1=k, op0=ALU.add, op1=ALU.mult))
                v.tell(rw_kkr)

            def keys_normed(nxt, parts_=range(3)):
                aa = arena[:, wA + nxt, :]
                if 0 in parts_:
                    dve.wait_ge(rw_kroot, nxt + 1)
                    v(nc.vector.tensor_scalar(root[:], root[:], 1e-12, None, ALU.max))
                for half_ in range(2):
                    if half_ in parts_:
                        cols = slice(half_ * S // 2, (half_ + 1) * S // 2)
                        v.go(nc.vector.reciprocal(root[:, cols], root[:, cols]))
                if 2 in parts_:
                    v.settle()
                    v(nc.vector.tensor_tensor(KK, KK, root[:], ALU.mult))
                    v(nc.vector.tensor_tensor(aa, KK, aa, ALU.mult))

            def values(nxt, more):
                dve.wait_ge(rw_vtok, nxt + 1)
                if more:
                    dve.wait_ge(rw_vt, nxt)
                nc.vector.tensor_copy(VTN, gp[:, 1, :]).then_inc(rw_vnext, 1)

            def decays(nxt, d, parts_):
                s = arena[:, wS + DT * d + nxt, :]
                c0 = (T1[0], root[:])[d]
                ends = ch(c0)[:, :, CH - 1:CH]
                if 0 in parts_:
                    v(nc.vector.tensor_tensor_scan(c0, RESET, s, 0.0, ALU.mult, ALU.add))
                    v.go(nc.vector.tensor_copy(PCN[d].unsqueeze(2), ends))
                if 1 in parts_:
                    v(nc.vector.tensor_tensor(s, c0, s, ALU.subtract))
                if d and 2 in parts_:
                    v(nc.vector.tensor_tensor(ch(T1[d]), ends.broadcast_to((P, NCH, CH)), ch(s), ALU.subtract))
                if d and 3 in parts_:
                    v(nc.vector.tensor_tensor(ch(s), ends.broadcast_to((P, NCH, CH)), ch(c0), ALU.subtract))
                if 3 in parts_:
                    v.tell(rw_cum)

            def alphas(nxt, d):
                dve.wait_ge(rw_exp, n2(nxt, d))
                v.go(nc.vector.tensor_copy(PC[d], PCN[d]))
                v.go(nc.vector.scalar_tensor_tensor(out=AR[d][:, :, 0:64], in0=ch(KK), scalar=-1.0,
                                                    in1=ch(arena[:, wS + DT * d + nxt, :]), op0=ALU.mult, op1=ALU.mult))
                nc.vector.tensor_tensor(AR[d][:, :, 64:128], ch(arena[:, wR + nxt, :]), ch(T1[d]),
                                        ALU.mult).then_inc(rw_prep, 1)

            def pair(it, more):
                yt = arena[:, wS + it, :]
                for d in DIRS:
                    strict, incl = over(const("strict", 64 * d, 64 * d + 64)), over(const("incl", 64 * d, 64 * d + 64))
                    first = over(const("level", (0, LEVELS * 64)[d], (0, LEVELS * 64)[d] + 64))
                    pb, pk = two(aux, 0), two(aux, 2)
                    dve.wait_ge(rw_M, n2(it, d))
                    v(nc.vector.tensor_tensor(ch(XT[d]), pb[:, :, 0:64], first, ALU.mult))
                    nc.vector.tensor_tensor(ch(XT[d]), ch(XT[d]), over(const("eye64")), ALU.add).then_inc(rw_XTst, 1)
                    v.go(nc.vector.tensor_tensor(ch(ARB[d]), pb[:, :, 64:128], incl, ALU.mult))
                    v.go(nc.vector.tensor_tensor(ch(ARK[d]), pk[:, :, 64:128], incl, ALU.mult))
                    dve.wait_ge(rw_tok, n2(it, d))
                    for h, cols in ((LO, slice(0, 64)), (HI, slice(64, 128))):
                        v.go(nc.vector.tensor_tensor(MBD[d][h, :, cols], pb[h, :, 0:64], strict[h], ALU.mult))
                    if d:
                        dve.wait_ge(rw_w0, n2(it, 0))
                    v.go(nc.vector.tensor_tensor(MAK[LO, :, 0:64], pk[LO, :, 0:64], strict[LO], ALU.mult))
                    nc.vector.tensor_tensor(MAK[HI, :, 64:128], pk[HI, :, 0:64], strict[HI],
                                            ALU.mult).then_inc(rw_mask, 1)
                for d in DIRS:
                    dve.wait_ge(rw_kv, n2(it, d))
                    nc.vector.tensor_tensor(ch(KVP[d]), ch((gp, aux)[d][:, 2 * d + 1, :]),
                                            PC[d].unsqueeze(2).broadcast_to((P, NCH, CH)), ALU.mult).then_inc(rw_kvst, 1)
                for lv in range(1, LEVELS):
                    m = over(const("level", lv * 64, lv * 64 + 64))
                    for d in DIRS:
                        dve.wait_ge(rw_T1, n_level(it, lv, d))
                        nc.vector.tensor_tensor(ch(arena[:, wS + DT * d + it, :]), ch(aux[:, d, :]), m,
                                                ALU.mult).then_inc(rw_T1st, 1)
                    if lv < LEVELS - 1:
                        for d in DIRS:
                            dve.wait_ge(rw_dX, n_x(it, lv, d))
                            if lv == 1:
                                dve.wait_ge(rw_X1st, n2(it, d))
                            else:
                                dve.wait_ge(rw_X, n_x(it, lv - 1, d))
                            nc.vector.tensor_tensor(XS[d], aux[:, 2 + d, :], XS[d], ALU.add).then_inc(rw_X, 1)
                    if more and lv == LEVELS - 1:
                        keys_normed(it + 1, (2,))
                        decays(it + 1, 0, (0, 1, 3))
                    for d in DIRS:
                        dve.wait_ge(rw_dXT, n_level(it, lv, d))
                        dve.wait_ge(rw_XT, n_xt(it, lv - 1, d))
                        nc.vector.tensor_tensor(XT[d], gp[:, 2 + d, :], XT[d], ALU.add).then_inc(rw_XTst, 1)
                    if more and lv == 1:
                        keys(it + 1)
                    if more and lv in (3, 4):
                        keys_normed(it + 1, (lv - 3,))
                    if more and lv == 3:
                        values(it + 1, True)
                dve.wait_ge(rw_kvst, n2(it, 1))
                dve.wait_ge(rw_w0st, n2(it, 1))
                v.settle()
                halves = ((LO, slice(0, 64)), (HI, slice(64, 128)))
                for j in range(NCH):
                    for d in DIRS:
                        c = order(d)[j]
                        if j:
                            dve.wait_ge(rw_W, n_link(it, j - 1, d))
                            nc.vector.tensor_tensor(WS[d], gp[:, d, 0:64], W0[d][:, c * CH:(c + 1) * CH],
                                                    ALU.add).then_inc(rw_Wst, 1)
                    for d in DIRS:
                        c = order(d)[j]
                        pc, kv = PC[d][:, c:c + 1], KVP[d][:, c * CH:(c + 1) * CH]
                        if 0 < j < NCH - 1:
                            dve.wait_ge(rw_S, n_link(it, j - 1, d))
                            for h, cols in halves:
                                v.go(nc.vector.scalar_tensor_tensor(out=SPC[d][h, :], in0=SB[d][h, cols], scalar=pc[h],
                                                                    in1=kv[h], op0=ALU.mult, op1=ALU.add))
                    if more and 0 < j < 5:
                        decays(it + 1, 1, (j - 1,))
                    if j < NCH - 1:
                        v.settle()
                        for d in DIRS:
                            c = order(d)[j]
                            pc = PC[d][:, c:c + 1]
                            dve.wait_ge(rw_Sp, n_link(it, j, d))
                            for h, cols in halves:
                                last = nc.vector.scalar_tensor_tensor(
                                    out=SB[d][h, cols], in0=aux[h, d, 0:64], scalar=pc[h],
                                    in1=SPC[d][h, :] if j else KVP[d][h, c * CH:(c + 1) * CH], op0=ALU.mult, op1=ALU.add)
                            last.then_inc(rw_S, 1)
                dve.wait_ge(rw_Y, it + 1)
                if more:
                    alphas(it + 1, 0)
                v(nc.vector.tensor_scalar(yt, aux[:, 2, :], 1.0, None, ALU.mult))
                nc.vector.tensor_tensor(yt, aux[:, 3, :], yt, ALU.add).then_inc(rw_yst, 1)
                if more:
                    alphas(it + 1, 1)

            keys(0)
            keys_normed(0)
            values(0, False)
            for d in DIRS:
                decays(0, d, range(4))
            for d in DIRS:
                alphas(0, d)
            each_pair(dve, pair, v)
            dve.wait_ge(rw_yst, DT)
            for p in range(DT + 1):
                if p < DT:
                    y = arena[:, wS + p, :]
                    nc.vector.scalar_tensor_tensor(out=BONUS(p), in0=arena[:, wR + p, :], scalar=pcol("rw_r_k", p),
                                                   in1=arena[:, wK + p, :], op0=ALU.mult, op1=ALU.mult).then_inc(rw_bon, 1)
                    dve.wait_ge(rw_mean, p + 1)
                    nc.vector.scalar_tensor_tensor(out=y, in0=aux[:, p % BANKS, :], scalar=-1.0 / HD, in1=y,
                                                   op0=ALU.mult, op1=ALU.add).then_inc(rw_yc, 1)
                if p:
                    q = p - 1
                    y = arena[:, wS + q, :]
                    dve.wait_ge(rw_bsum, p)
                    v.go(nc.vector.tensor_tensor(BONUS(q), gp[:, q % BANKS, :], arena[:, wV + q, :], ALU.mult))
                    dve.wait_ge(rw_root2, p)
                    v(nc.vector.reciprocal(YROOT(q), YROOT(q)))
                    v(nc.vector.scalar_tensor_tensor(out=y, in0=y, scalar=pcol("rw_ln_w", q), in1=YROOT(q),
                                                     op0=ALU.mult, op1=ALU.mult))
                    nc.vector.scalar_tensor_tensor(out=y, in0=y, scalar=pcol("rw_ln_b", q), in1=BONUS(q),
                                                   op0=ALU.add, op1=ALU.add).then_inc(rw_gn, 1)
            dve.wait_ge(rw_gn, DT)
            for t in loop_tiles(dve, STAGE["rw_g2"]):
                consume_wait(dve, t)
                y = arena[:, wS + t.j, :]
                v.go(nc.vector.tensor_tensor(y, gp[:, t.bank, :], y, ALU.mult))
                v.tell(drained[t.bank], yg_ready)
            residual_dve(dve, v, "rw_o")

        def final1_pe(pe):
            norm_pe(pe, DT, Hk)

        def final1_act(act, a):
            pre_norm_act(act, a)

        def final1_dve(dve, v):
            norm_dve(dve, v, DT, Xk, lambda k: pcol("final_norm", k), Xk, x_ready)
            n_dve.x += DT

        lat_ready, ln_c, ln_ready = sem("lat_ready"), sem("ln_c"), sem("ln_ready")

        def sum_pe(pe, n, src):
            pe.wait_ge(stat_ready, n_pe.sums)
            for k in range(n):
                last = nc.tensor.matmul(aux[:, 0, :], ones, src(k), start=(k == 0), stop=(k == n - 1))
            last.then_inc(sum_ready, 1)
            n_pe.sums += 1

        def mean_act(act, width):
            n_act.sums += 1
            act.wait_ge(sum_ready, n_act.sums)
            nc.scalar.activation(root[:], aux[:, 0, :], ACT.Copy, scale=1.0 / width).then_inc(stat_ready, 1)

        def centre_dve(dve, v, n, src):
            n_dve.sums += 1
            dve.wait_ge(stat_ready, n_dve.sums)
            for k in range(n):
                v.go(nc.vector.tensor_tensor(src(k), src(k), root[:], ALU.subtract))
            v.tell(ln_c)

        def scale_shift_dve(dve, v, n, src, gain, bias, dst, done):
            n_dve.sums += 1
            dve.wait_ge(stat_ready, n_dve.sums)
            v(nc.vector.reciprocal(root[:], root[:]))
            for k in range(n):
                v(nc.vector.scalar_tensor_tensor(out=dst(k), in0=src(k), scalar=gain(k), in1=root[:],
                                                 op0=ALU.mult, op1=ALU.mult))
                nc.vector.tensor_scalar(dst(k), dst(k), bias(k), None, ALU.add).then_inc(done, 1)

        at_score, at_max, at_exp, at_norm, at_tr, at_pt, at_pv = (
            sem("at_" + x) for x in "score max exp norm tr pt pv".split())

        class Unit:
            def __init__(self, q, k, mask, nk, v, out):
                self.q, self.k, self.mask, self.nk, self.v, self.out = q, k, mask, nk, v, out

        class Attention:

            def __init__(self, units, p, pt, scale, u0):
                self.units, self.p, self.pt, self.scale, self.u0 = units, p, pt, scale, u0

        def attention_pe(pe, A):
            def score(i):
                u, n = A.units[i], A.u0 + i
                if n >= 3:
                    pe.wait_ge(at_exp, n - 2)
                nc.tensor.matmul(gp[:, n % 3, 0:u.nk], u.q, u.k, start=True, stop=False, skip_group_check=True)
                lo, m = u.mask
                nc.tensor.matmul(gp[:, n % 3, lo:u.nk], ident, m, start=False, stop=True,
                                 skip_group_check=True).then_inc(at_score, 1)

            def values(i):
                u, n = A.units[i], A.u0 + i
                pe.wait_ge(at_pt, n + 1)
                for b in range(u.nk // P):
                    last = nc.tensor.matmul(u.out, u.v(b), A.pt(n)[:, b * P:(b + 1) * P],
                                            start=(b == 0), stop=(b == u.nk // P - 1))
                last.then_inc(at_pv, 1)

            score(0)
            score(1)
            for i, u in enumerate(A.units):
                n = A.u0 + i
                if i + 2 < len(A.units):
                    score(i + 2)
                pe.wait_ge(at_norm, n + 1)
                if n:
                    pe.wait_ge(at_pt, n)
                for b in range(u.nk // P):
                    last = nc.tensor.transpose(gp[:, 3, b * P:(b + 1) * P], A.p(n)[:, b * P:(b + 1) * P], ident)
                last.then_inc(at_tr, 1)
                if i:
                    values(i - 1)
            values(len(A.units) - 1)

        def stat(n, i):
            return root[:, 4 * (n % 2) + i:4 * (n % 2) + i + 1]

        def attention_act(act, A):
            def copy(i):
                u, n = A.units[i], A.u0 + i
                act.wait_ge(at_tr, n + 1)
                if n >= 2:
                    act.wait_ge(at_pv, n - 1)
                nc.scalar.activation(A.pt(n)[:, 0:u.nk], gp[:, 3, 0:u.nk], ACT.Copy).then_inc(at_pt, 1)

            def exp(i):
                u, n = A.units[i], A.u0 + i
                act.wait_ge(at_max, n + 1)
                if n >= 2:
                    act.wait_ge(at_tr, n - 1)
                nc.scalar.activation(A.p(n)[:, 0:u.nk], gp[:, n % 3, 0:u.nk], ACT.Exp, bias=stat(n, 1), scale=A.scale,
                                     accum_out=stat(n, 2)).then_inc(at_exp, 1)

            exp(0)
            for i in range(len(A.units)):
                if i + 1 < len(A.units):
                    exp(i + 1)
                copy(i)

        def attention_dve(dve, v, A, beside=None):
            def maximum(i):
                u, n = A.units[i], A.u0 + i
                dve.wait_ge(at_score, n + 1)
                v(nc.vector.tensor_reduce(stat(n, 0), gp[:, n % 3, 0:u.nk], AX.X, ALU.max))
                nc.vector.tensor_scalar(stat(n, 1), stat(n, 0), -A.scale, None, ALU.mult).then_inc(at_max, 1)

            maximum(0)
            maximum(1)
            for i, u in enumerate(A.units):
                n = A.u0 + i
                dve.wait_ge(at_exp, n + 1)
                v(nc.vector.reciprocal(stat(n, 3), stat(n, 2)))
                p = A.p(n)[:, 0:u.nk]
                nc.vector.tensor_scalar(p, p, stat(n, 3), None, ALU.mult).then_inc(at_norm, 1)
                if i + 2 < len(A.units):
                    maximum(i + 2)
                if beside:
                    beside(i)

        relu_ready, f_ready, o_sum = sem("relu_ready"), sem("f_ready"), sem("o_sum")
        fT = 64
        F2H = F2T // 2

        def ffn2_pe(pe, b):
            before = h_parts_before(pe)
            for i, half_ in enumerate("ab"):
                split_pe(pe, f"ff1{half_}_{b}", tiles_of(fH), tiles_of(fH, DT), before=None if i else before)
                pe.wait_ge(f_ready, F2T * (b - 2) + F2H * (i + 1) + 2)
                split_pe(pe, f"ff2{half_}_{b}", tiles_of(f_high), tiles_of(f_low), ksizes=[DT] * 2)

        def ffn2_pool(pool, g, b):
            split_pool(pool, g, SPLIT[4 if b == 2 else 6])

        def ffn2_relu_act(act, a, b, i):
            base = F2T * (b - 2) + F2H * i
            for t in loop_tiles(act, STAGE[f"ff1{'ab'[i]}_{b}"], a):
                split_ahead_act(act, t)
                consume_wait(act, t)
                act.wait_ge(f_ready, at(base + 1, t, 1))
                a.go(nc.scalar.activation(arena[:, fT + t.j % 2, :], gp[:, t.bank, :], ACT.Relu))
                a.tell(drained[t.bank], relu_ready)

        def ffn2_square_dve(dve, v, b, i):
            base = F2T * (b - 2) + F2H * i
            if base == 0:
                dve.sem_inc(f_ready, 2)
            for t in loop_tiles(dve, STAGE[f"ff1{'ab'[i]}_{b}"], v):
                f = arena[:, fT + t.j % 2, :]
                dve.wait_ge(relu_ready, at(base + 1, t, 1))
                v(nc.vector.tensor_tensor(f, f, f, ALU.mult))
                split_tile_dve(dve, v, f, f_high[:, t.idx, :], f_low[:, t.idx, :], f_ready)

        bCQ, bCKV, bKR, bU, bV, bCX, bCB, bCC, bP, bG, bOUT = 0, 2, 3, 4, 6, 8, 10, 12, 14, 16, 48
        sm = arena[:, 56:61, :].rearrange("p a b -> p (a b)")
        UQ = sm[:, 0:768].rearrange("p (k n) -> p k n", k=2)
        WK, WV = sm[:, 768:1024], sm[:, 1024:1280]
        SGW = sm[:, 1280:1792]
        POOLW = sm[:, 1792:1920].rearrange("p (t n) -> p t n", t=2)
        UPPER = sm[:, 1920:2048]
        SGB = sm[0:1, 2048:2560]
        POS = arena[:, 61, :]
        RCNT = arena[:, 62:64, :]
        VM = arena[:, 64:66, :].rearrange("p a b -> p (a b)").rearrange("p (t n) -> p t n", t=4)
        COS, SIN, ANG, TMP = (arena[:, 8 + i, :] for i in range(4))
        RP = slice(NOPE, QKD)
        sm_in = sem("sm_in")
        in2_ready = sem("in2_ready")
        sgw_ready, sgt_psum, sgt_ready, sg_psum, sg_out = (sem(x) for x in "sgw_ready sgt_psum sgt_ready sg_psum sg_out".split())
        pooled, pool_psum, pool_out, conv_out = (sem(x) for x in "pooled pool_psum pool_out conv_out".split())
        mq_psum, mq_ready, mrot, mroped, mk_psum, mk_ready, mv_psum, mv_ready, trig, mla_out = (
            sem(x) for x in "mq_psum mq_ready mrot mroped mk_psum mk_ready mv_psum mv_ready trig mla_out".split())
        merged = sem("merged")
        mla_units = [Unit(H[0:QKD, h, qb * P:(qb + 1) * P], H[0:QKD, 4 + h, 0:(qb + 1) * P],
                          (qb * P, const("causal")), (qb + 1) * P,
                          lambda b, h=h: VM[:, b, h * VH:(h + 1) * VH],
                          aux[(h % 2) * 64:(h % 2) * 64 + 64, 1 + h // 2, qb * P:(qb + 1) * P])
                     for h in range(MLA_H) for qb in range(4)]
        MLA = Attention(mla_units, lambda n: arena[:, 10 + n % 2, :], lambda n: arena[:, 12 + n % 2, :],
                        float(QKD) ** -0.5, 0)
        bsq = arena_tiles(bOUT)

        def two_pool(pool, g):
            split_pool(pool, g, SPLIT[3], 0, PARTS)
            pool.wait_ge(h_ready, 5 * DT)
            for dst, name in ((sm[:, 0:2048], "sm2"), (SGB, "sg_b"), (RCNT, "rcnt")):
                pool.dma_start(dst, d[name]).then_inc(sm_in, 16)
            pool.dma_start(POS.bitcast(I32), d["pos"].partition_broadcast(P)).then_inc(sm_in, 16)
            split_pool(pool, g, SPLIT[3], PARTS)
            ffn2_pool(pool, g, 2)

        def two_pe(pe):
            norm_pe(pe, DT, Hk)
            split_pe(pe, "in2", tiles_of(bH), tiles_of(bH, DT), before=h_parts_before(pe))
            norm_pe(pe, 2, bsq)
            norm_pe(pe, 1, arena_tiles(bOUT + 2))
            pe.wait_ge(in2_ready, 8)
            sum_pe(pe, 2, arena_tiles(bV))
            norm_pe(pe, 2, arena_tiles(bOUT + 3))
            stream_pe(pe, "gate2", lambda k, t: H[:, k, :])
            for b in range(BANKS):
                pe.wait_ge(drained[b], (STAGE["br2_0"].tile0 - b + BANKS - 1) // BANKS)
            pe.wait_ge(sm_in, 16 * 4)
            pe.wait_ge(ln_ready, 2)
            for i in range(2):
                for n in range(4):
                    last = nc.tensor.transpose(gp[:, i, n * P:(n + 1) * P], arena[:, bV + i, n * P:(n + 1) * P], ident)
                last.then_inc(sgt_psum, 1)
            pe.wait_ge(sgw_ready, 1)
            pe.wait_ge(sgt_ready, 2)
            for g in range(4):
                rows = slice((g % 2) * 64, (g % 2) * 64 + 64)
                for n in range(4):
                    o = gp[rows, 2 + g // 2, n * P:(n + 1) * P]
                    nc.tensor.matmul(o, arena[:, bOUT + g // 2, n * P + (g % 2) * 64:n * P + (g % 2) * 64 + 64],
                                     SGW[:, g * P:(g + 1) * P], start=True, stop=False)
                    last = nc.tensor.matmul(o, ones[0:1, 0:64], SGB[:, g * P:(g + 1) * P], start=False, stop=True)
                if g % 2:
                    last.then_inc(sg_psum, 1)
            pe.wait_ge(pooled, 2)
            for i in range(2):
                for h in (LO, HI):
                    last = nc.tensor.matmul(aux[h, 2 + i, :], POOLW[h, i, :], arena[h, bP + i, :], start=True, stop=True)
                last.then_inc(pool_psum, 1)
            pe.wait_ge(lat_ready, 3)
            pe.wait_ge(sgt_ready, 2)
            pe.wait_ge(sg_out, 2)
            for h in range(MLA_H):
                for k in range(2):
                    last = nc.tensor.matmul(gp[0:QKD, h, :], UQ[:, k, h * QKD:(h + 1) * QKD], arena[:, bCQ + k, :],
                                            start=(k == 0), stop=(k == 1))
                last.then_inc(mq_psum, 1)
            pe.wait_ge(stat_ready, n_pe.sums)
            nc.tensor.matmul(aux[0:QKD, 0, :], const("perm_mla")[0:QKD], arena[0:QKD, bKR, :], start=True,
                             stop=True).then_inc(mrot, 1)
            for h in range(MLA_H):
                pe.wait_ge(mq_ready, h + 1)
                pe.wait_ge(mroped, h + 1)
                nc.tensor.matmul(aux[0:QKD, 0, :], const("perm_mla")[0:QKD], H[0:QKD, h, :], start=True,
                                 stop=True).then_inc(mrot, 1)
                nc.tensor.matmul(gp[0:NOPE, h, :], WK[:, h * NOPE:(h + 1) * NOPE], arena[:, bCKV, :], start=True,
                                 stop=True).then_inc(mk_psum, 1)
            pe.wait_ge(pool_out, 2)
            for tk in range(4):
                last = nc.tensor.matmul(aux[:, 2 + tk // 2, (tk % 2) * 256:(tk % 2) * 256 + 256],
                                        arena[:, bCKV, tk * P:(tk + 1) * P], WV, start=True, stop=True)
            last.then_inc(mv_psum, 1)
            pe.wait_ge(mk_ready, MLA_H)
            pe.wait_ge(mv_ready, 1)
            pe.wait_ge(mroped, MLA_H + 1)
            attention_pe(pe, MLA)
            for b in range(4):
                pe.wait_ge((mla_out, sg_out, conv_out, pool_out)[b], 2)
                st = STAGE[f"br2_{b}"]
                for t in loop_tiles(pe, st):
                    bank_wait(pe, t)
                    for k in range(2):
                        slab = st.slab0 + k
                        if t.j == 0:
                            slab_wait(pe, slab)
                        last = nc.tensor.matmul(gp[:, t.bank, :], ring[:, slab % RING, t.j * P:(t.j + 1) * P],
                                                arena[:, bOUT + 2 * b + k, :], start=(k == 0), stop=(k == 1))
                        if t.j == st.tiles - 1:
                            last.then_inc(slab_done, 1)
                    shared_tile_done(t, last)
            pe.wait_ge(merged, DT)
            stream_pe(pe, "out2", lambda k, t: H[:, k, :])
            norm_pe(pe, DT, arena_tiles(8))
            norm_pe(pe, DT, Hk)
            ffn2_pe(pe, 2)
            norm_pe(pe, DT, arena_tiles(8))

        def post_norm_act(act, a, name, ready, base):
            copy_act(act, a, name, arena_tiles(0), done=ready)
            norm_act(act, a, DT, arena_tiles(0), arena_tiles(8), lambda k: act.wait_ge(ready, base + k + 1), 1.0 / D)

        def post_norm_dve(dve, v, gain):
            n_dve.sums += 1
            dve.wait_ge(stat_ready, n_dve.sums)
            v(nc.vector.reciprocal(root[:], root[:]))
            for k in range(DT):
                o = arena[:, k, :]
                v(nc.vector.scalar_tensor_tensor(out=o, in0=o, scalar=pcol(gain, k), in1=root[:],
                                                 op0=ALU.mult, op1=ALU.mult))
                nc.vector.tensor_tensor(X[:, k, :], X[:, k, :], o, ALU.add).then_inc(x_ready, 1)
            n_dve.x += DT

        o_ready = sem("o_ready")

        def two_act(act, a):
            pre_norm_act(act, a)
            split_first_act(act, "in2")
            for t in loop_tiles(act, STAGE["in2"], a, body=16):
                split_ahead_act(act, t)
                consume_wait(act, t)
                a.go(nc.scalar.activation(arena[:, t.j, :], gp[:, t.bank, :],
                                          ACT.Gelu_apprx_tanh if bU <= t.j < bCX else ACT.Copy))
                a.tell(drained[t.bank], in2_ready)
            norm_act(act, a, 2, arena_tiles(bCQ), bsq, lambda k: None, 1.0 / 256)
            norm_act(act, a, 1, arena_tiles(bCKV), arena_tiles(bOUT + 2), lambda k: None, 1.0 / 128,
                     root_wait=lambda: act.wait_ge(lat_ready, 2))
            act.wait_ge(lat_ready, 3)
            mean_act(act, 256)
            norm_act(act, a, 2, arena_tiles(bV), arena_tiles(bOUT + 3), lambda k: act.wait_ge(ln_c, 1), 1.0 / 256)
            copy_act(act, a, "gate2", lambda i: arena[:, bG + i, :], ACT.Sigmoid, lambda i: pcol("gate_b2", i))
            act.wait_ge(trig, 1)
            for x in (SIN, COS):
                nc.scalar.activation(x[RP], x[RP], ACT.Sin).then_inc(trig_done, 1)
            for i in range(2):
                act.wait_ge(sgt_psum, i + 1)
                nc.scalar.activation(arena[:, bOUT + i, :], gp[:, i, :], ACT.Copy).then_inc(sgt_ready, 1)
            for i in range(2):
                act.wait_ge(pool_psum, i + 1)
                nc.scalar.activation(arena[:, bOUT + 6 + i, :], aux[:, 2 + i, :], ACT.Copy,
                                     scale=pcol("pool_scale2", i)).then_inc(pool_out, 1)
            for h in range(MLA_H):
                act.wait_ge(mq_psum, h + 1)
                nc.scalar.activation(H[0:QKD, h, :], gp[0:QKD, h, :], ACT.Copy).then_inc(mq_ready, 1)
            act.wait_ge(mroped, 1)
            for h in range(MLA_H):
                a.go(nc.scalar.activation(H[RP, 4 + h, :], arena[RP, bKR, :], ACT.Copy))
                act.wait_ge(mk_psum, h + 1)
                nc.scalar.activation(H[0:NOPE, 4 + h, :], gp[0:NOPE, h, :], ACT.Copy).then_inc(mk_ready, 1)
            act.wait_ge(mv_psum, 1)
            nc.scalar.activation(VM, aux[:, 2:4, :].rearrange("p a (c n) -> p (a c) n", c=2),
                                 ACT.Copy).then_inc(mv_ready, 1)
            attention_act(act, MLA)
            act.wait_ge(at_pv, len(mla_units))
            act.wait_ge(sg_psum, 2)
            for i in range(2):
                nc.scalar.activation(arena[:, bOUT + i, :], aux[:, 1 + i, :], ACT.Copy).then_inc(mla_out, 1)
            post_norm_act(act, a, "out2", o_ready, 0)
            pre_norm_act(act, a)
            split_first_act(act, "ff1a_2")
            ffn2_relu_act(act, a, 2, 0)
            copy_act(act, a, "ff2a_2", arena_tiles(0), done=o_ready)
            ffn2_relu_act(act, a, 2, 1)
            split_stage_act(act, a, "ff2b_2")
            norm_act(act, a, DT, arena_tiles(0), arena_tiles(8), lambda k: act.wait_ge(o_sum, k + 1), 1.0 / D)

        def trig_dve(v):
            ang, s, c, t = ANG[RP], SIN[RP], COS[RP], TMP[RP]
            v(nc.vector.tensor_copy(ang, POS[RP].bitcast(I32)))
            v(nc.vector.tensor_scalar(ang, ang, const("invf")[RP], None, ALU.mult))
            v(nc.vector.tensor_copy(s, ang))
            reduce_angle(v, nc.vector, s, t)
            v(nc.vector.tensor_copy(c, ang))
            reduce_angle(v, nc.vector, c, t, 0.25)
            v(nc.vector.tensor_scalar(c, c, float(np.pi / 2), None, ALU.add))
            for x in (s, c):
                v(nc.vector.tensor_scalar(x, x, float(np.float32(3.1415925)), float(np.float32(-3.1415925)), ALU.min, ALU.max))

        def two_dve(dve, v):
            split_norm_dve(dve, v, "norm_mix_pre2", bH)
            for n, base, gain in ((2, bCQ, "q_norm2"), (1, bCKV, "kv_norm2")):
                norm_dve(dve, v, n, arena_tiles(base), lambda k, gain=gain: pcol(gain, k), arena_tiles(base), lat_ready)
            centre_dve(dve, v, 2, arena_tiles(bV))
            scale_shift_dve(dve, v, 2, arena_tiles(bV), lambda k: pcol("sg_ln_g2", k), lambda k: pcol("sg_ln_b2", k),
                            arena_tiles(bV), ln_ready)
            dve.wait_ge(sm_in, 16 * 4)
            for g in range(4):
                v.go(nc.vector.tensor_tensor(SGW[:, g * P:(g + 1) * P], SGW[:, g * P:(g + 1) * P], UPPER,
                                             ALU.mult))
            v.tell(sgw_ready)
            dve.wait_ge(in2_ready, 16)
            for i in range(2):
                z, y = arena[:, bCC + i, :], arena[:, bOUT + 4 + i, :]
                v(nc.vector.tensor_tensor(z, z, arena[:, bCX + i, :], ALU.mult))
                v(nc.vector.tensor_scalar(y, z, pcol("conv_w2", 4 + i), None, ALU.mult))
                for k in (1, 0):
                    lag = 2 - k
                    v(nc.vector.scalar_tensor_tensor(out=y[:, lag:S], in0=z[:, 0:S - lag],
                                                     scalar=pcol("conv_w2", 2 * k + i), in1=y[:, lag:S],
                                                     op0=ALU.mult, op1=ALU.add))
                v.go(nc.vector.tensor_tensor(y, y, arena[:, bCB + i, :], ALU.mult))
                v.tell(conv_out)
            for i in range(2):
                x = arena[:, bP + i, :]
                src, lag = x, 1
                for lv in range(2 * i + 2):
                    dst = arena[:, bOUT + 2 + lv % 2, :]
                    v.go(nc.vector.tensor_copy(dst[:, 0:lag], src[:, 0:lag]))
                    v(nc.vector.tensor_tensor(dst[:, lag:S], src[:, lag:S], src[:, 0:S - lag], ALU.add))
                    if lv >= 2 * i:
                        h = (LO, HI)[lv - 2 * i]
                        v(nc.vector.tensor_tensor(RCNT[h, i, :], dst[h], RCNT[h, i, :], ALU.mult))
                    src, lag = dst, lag * 2
                v.go(nc.vector.tensor_tensor(x, RCNT[:, i, :], x, ALU.subtract))
                v.tell(pooled)
            trig_dve(v)
            v.tell(trig)
            dve.wait_ge(trig_done, 2)
            v(nc.vector.tensor_scalar(SIN[RP], SIN[RP], const("rsign")[RP], None, ALU.mult))
            for i in range(2):
                dve.wait_ge(sg_psum, i + 1)
                v.go(nc.vector.tensor_tensor(arena[:, bOUT + 2 + i, :], gp[:, 2 + i, :], arena[:, bU + i, :], ALU.mult))
                v.tell(sg_out)
            for h in range(MLA_H + 1):
                x = arena[RP, bKR, :] if h == 0 else H[RP, h - 1, :]
                dve.wait_ge(mrot, h + 1)
                v.go(nc.vector.tensor_tensor(TMP[RP], aux[RP, 0, :], SIN[RP], ALU.mult))
                v(nc.vector.tensor_tensor(x, x, COS[RP], ALU.mult))
                v.go(nc.vector.tensor_tensor(x, x, TMP[RP], ALU.add))
                v.tell(mroped)
            attention_dve(dve, v, MLA)
            for b in range(4):
                for t in loop_tiles(dve, STAGE[f"br2_{b}"]):
                    g, m = arena[:, bG + b * DT + t.j, :], H[:, t.j, :]
                    consume_wait(dve, t)
                    if b == 0:
                        v.go(nc.vector.tensor_tensor(m, gp[:, t.bank, :], g, ALU.mult))
                        v.tell(drained[t.bank])
                    else:
                        v(nc.vector.tensor_tensor(g, gp[:, t.bank, :], g, ALU.mult))
                        dve.sem_inc(drained[t.bank], 1)
                        v(nc.vector.tensor_tensor(m, m, g, ALU.add))
                        if b == 3:
                            dve.sem_inc(merged, 1)
            post_norm_dve(dve, v, "norm_mix_post2")
            split_norm_dve(dve, v, "norm_ffn_pre2", fH)
            ffn2_square_dve(dve, v, 2, 0)
            ffn2_square_dve(dve, v, 2, 1)
            for t in loop_tiles(dve, STAGE["ff2b_2"], v):
                o = arena[:, t.idx, :]
                dve.wait_ge(o_ready, DT + t.j + 1)
                consume_wait(dve, t)
                v.go(nc.vector.tensor_tensor(o, gp[:, t.bank, :], o, ALU.add))
                v.tell(drained[t.bank], o_sum)
            post_norm_dve(dve, v, "norm_ffn_post2")

        trig_done = sem("trig_done")

        dCA, dCG, dIQ, dIK, dQ, dK, dV, dAT, dCV = 0, 4, 8, 12, 13, 17, 21, 25, 29
        ROTC, ROTS = arena[:, 33, :], arena[:, 34, :]
        SELM = lambda qb: arena[:, 34 + qb, 0:(qb + 1) * P]
        SCORE, WORK = arena[:, 38, :], arena[:, 40, :]
        REL = lambda n: arena[:, 39 + 2 * (n % 2), :]
        IW = arena[:, 45, 0:4 * AH]
        TOP8 = arena[:, 45, 64:72]
        CNT = arena[:, 45, 72:73]
        padded = lambda lo: arena[:, lo:lo + 2, :].rearrange("p a b -> p (a b)")[:, 0:CONVK - 1 + S]
        PAD, POOL_PAD = padded(51), padded(62)
        POOL_TOKENS = S // 2
        tap = lambda i, k: pcol("w_dw3", i * CONVK + k)
        TAPPED = arena[:, 61, :]
        hsq = arena_tiles(53)
        NHT = 2 * AH
        HROOT = arena[0:NHT, 49, :]
        HSUM = lambda i: arena[:, 50, NHT - 2 - 2 * i:2 * NHT - 2 - 2 * i]
        HBACK = lambda i: arena[0:NHT, 64 + i // 4, i % 4 * P:(i % 4 + 1) * P]
        hback = lambda i: (gp if i < 4 else aux)[:, i % 4, :]
        MOD = lambda j, k: pcol("b_ada3", j * DT + k)
        rot_in = sem("rot_in")
        in3_ready, iw_ready = sem("in3_ready"), sem("iw_ready")
        hd_sum, hd_root, hd_normed = sem("hd_sum"), sem("hd_root"), sem("hd_normed")
        ro_psum, ro_ready = sem("ro_psum"), sem("ro_ready")
        ix_psum, ix_relu, ix_used, sel_ready = sem("ix_psum"), sem("ix_relu"), sem("ix_used"), sem("sel_ready")
        dsa_out, an_ready, cv_ready, cl_ready, cn_ready = (
            sem(x) for x in "dsa_out an_ready cv_ready cl_ready cn_ready".split())
        half = lambda h: slice((h % 2) * 64, (h % 2) * 64 + 64)
        dsa_units = [Unit(arena[half(h), dQ + h // 2, qb * P:(qb + 1) * P], arena[half(h), dK + h // 2, 0:(qb + 1) * P],
                          (64, const("chunked")) if qb == 0 else (0, SELM(qb)), (qb + 1) * P,
                          lambda b, h=h: arena[:, dV + b, h * HD:(h + 1) * HD],
                          aux[half(h), h // 2, qb * P:(qb + 1) * P])
                     for qb in range(4) for h in range(AH)]
        DSA = Attention(dsa_units, lambda n: arena[:, 42 + n % 2, :], lambda n: arena[:, 46 + n % 2, :],
                        HD ** -0.5, len(mla_units))
        ro_bank = lambda n: aux[:, 1 + n % 3, :] if n < 5 else gp[:, n % 4, :]
        ix_bank = lambda n: aux[:, 1 + n % 3, :]
        INDEX_AT = {3: 0, 4: 4, 7: 8, 8: 12, 12: 16, 13: 20}
        index_heads = lambda j: range(INDEX_AT[j], INDEX_AT[j] + 4) if j in INDEX_AT else ()
        ROTATED = list(range(dIQ, dIK + 1)) + list(range(dQ, dV))

        def three_pool(pool, g):
            pool.wait_ge(x_ready, 7 * DT)
            pool.dma_start(ROTC, d["rotc"]).then_inc(rot_in, 16)
            pool.dma_start(ROTS, d["rots"]).then_inc(rot_in, 16)
            pool.dma_start(arena[:, 50, 0:2 * NHT - 2], d["hsum"]).then_inc(rot_in, 16)
            pool.dma_start(arena[0:NHT, 64:66, :], d["hback"]).then_inc(rot_in, 16)
            split_pool(pool, g, SPLIT[5])
            g(nc.gpsimd.memset(POOL_PAD[:, 0:CONVK - 1], 0.0))
            for i, n in ((0, S), (3, POOL_TOKENS)):
                y = arena[:, dCV + i, 0:n]
                pool.wait_ge(in3_ready, 5 + 8 + dCG + i + 1)
                g(nc.gpsimd.tensor_tensor(POOL_PAD[:, CONVK - 1:CONVK - 1 + n], arena[:, dCA + i, 0:n],
                                          arena[:, dCG + i, 0:n], ALU.mult))
                g(nc.gpsimd.tensor_scalar(y, POOL_PAD[:, CONVK - 1:CONVK - 1 + n], tap(i, CONVK - 1), pcol("b_dw3", i),
                                          ALU.mult, ALU.add))
                for k in range(CONVK - 1):
                    g(nc.gpsimd.tensor_scalar(TAPPED[:, 0:n], POOL_PAD[:, k:k + n], tap(i, k), None, ALU.mult))
                    g(nc.gpsimd.tensor_tensor(y, y, TAPPED[:, 0:n], ALU.add))
                g.tell(cv_ready)
            ffn2_pool(pool, g, 3)

        def three_pe(pe):
            norm_pe(pe, DT, Hk)
            before = h_parts_before(pe)
            st = STAGE["iw3"]
            slab_wait(pe, st.slab0)
            token_tiles = list(loop_tiles(pe, st))
            for t in token_tiles:
                bank_wait(pe, t)
            for k in range(DT):
                before(k)
                for t in token_tiles:
                    last = nc.tensor.matmul(gp[:, t.bank, 0:AH], H[:, k, t.j * P:(t.j + 1) * P],
                                            ring[:, st.slab0 % RING, k * AH:(k + 1) * AH],
                                            start=(k == 0), stop=(k == DT - 1))
                    if k == DT - 1:
                        if t.j == st.tiles - 1:
                            last.then_inc(slab_done, 1)
                        shared_tile_done(t, last)
            split_pe(pe, "in3a", tiles_of(H3_high), tiles_of(H3_low))
            pe.wait_ge(stat_ready, n_pe.sums)

            def beside(j):
                if j == 1:
                    for n in range(5):
                        pe.wait_ge(in3_ready, n + 1)
                        if n >= 3:
                            pe.wait_ge(ro_ready, n - 2)
                        nc.tensor.matmul(ro_bank(n), const("perm_dsa"), arena[:, ROTATED[n], :], start=True,
                                         stop=True).then_inc(ro_psum, 1)
                for n in index_heads(j):
                    qb, h = n // AH + 1, n % AH
                    pe.wait_ge(ro_ready, 5)
                    if n >= 3:
                        pe.wait_ge(ix_relu, n - 2)
                    nc.tensor.matmul(ix_bank(n)[:, 0:(qb + 1) * P], arena[half(h), dIQ + h // 2, qb * P:(qb + 1) * P],
                                     arena[half(h), dIK, 0:(qb + 1) * P], start=True, stop=True).then_inc(ix_psum, 1)

            split_pe(pe, "in3b", tiles_of(H3_high), tiles_of(H3_low), body=16, beside=beside)
            st = STAGE["v3"]
            for t in loop_tiles(pe, st):
                bank_wait(pe, t)
                for k in range(DT):
                    slab = st.slab0 + k // 2
                    if t.j == 0 and k % 2 == 0:
                        slab_wait(pe, slab)
                    last = nc.tensor.matmul(gp[:, t.bank, :], H[:, k, t.j * P:(t.j + 1) * P],
                                            ring[:, slab % RING, (k % 2) * S:(k % 2 + 1) * S],
                                            start=(k == 0), stop=(k == DT - 1))
                    if t.j == st.tiles - 1 and k % 2:
                        last.then_inc(slab_done, 1)
                shared_tile_done(t, last)
            for b in range(BANKS):
                pe.wait_ge(drained[b], (STAGE["out3"].tile0 - b + BANKS - 1) // BANKS)
            pe.wait_ge(ix_relu, 3 * AH)
            pe.wait_ge(rot_in, 64)
            for i in range(8):
                n_pe.sq += 1
                pe.wait_ge(sq_ready, n_pe.sq)
                last = nc.tensor.matmul(gp[0:NHT, 0, :], HSUM(i), hsq(i), start=(i == 0), stop=(i == 7))
            last.then_inc(hd_sum, 1)
            pe.wait_ge(hd_root, 2)
            for i in range(8):
                nc.tensor.matmul(hback(i), HBACK(i), HROOT, start=True, stop=True).then_inc(hd_sum, 1)
            for n in range(5, 13):
                pe.wait_ge(hd_normed, max(n - 4, n % 4 + 1))
                if n >= 9:
                    pe.wait_ge(ro_ready, n - 3)
                nc.tensor.matmul(ro_bank(n), const("perm_dsa"), arena[:, ROTATED[n], :], start=True,
                                 stop=True).then_inc(ro_psum, 1)
            pe.wait_ge(ro_ready, len(ROTATED))
            pe.wait_ge(sel_ready, 3)
            attention_pe(pe, DSA)
            norm_pe_at(pe)
            stream_pe(pe, "out3", lambda k, t: arena[:, dAT + k, :])
            norm_pe(pe, DT, Hk)
            ffn2_pe(pe, 3)

        def norm_pe_at(pe):
            pe.wait_ge(dsa_out, 4)
            pe.wait_ge(cv_ready, 5)
            sum_pe(pe, 4, arena_tiles(dCV))
            norm_pe(pe, 4, arena_tiles(46))
            norm_pe(pe, 4, arena_tiles(46))
            norm_pe(pe, 4, arena_tiles(46))
            pe.wait_ge(an_ready, 4)
            pe.wait_ge(cn_ready, 4)

        def three_act(act, a):
            act.wait_ge(x_ready, 7 * DT)
            pre_norm_act(act, a)
            split_first_act(act, "in3a")
            for t in loop_tiles(act, STAGE["iw3"]):
                consume_wait(act, t)
                a.go(nc.scalar.activation(IW[:, t.j * AH:(t.j + 1) * AH], gp[:, t.bank, 0:AH], ACT.Copy,
                                          scale=float(AH ** -0.5 * HD ** -0.5)))
                a.tell(drained[t.bank], iw_ready)
            copy_act(act, a, "in3a", arena_tiles(dIQ), done=in3_ready)
            for t in loop_tiles(act, STAGE["in3b"], a, body=32):
                for n in index_heads(t.j):
                    w = (n // AH + 2) * P
                    act.wait_ge(ix_psum, n + 1)
                    if n >= 2:
                        act.wait_ge(ix_used, n - 1)
                    nc.scalar.activation(REL(n)[:, 0:w], ix_bank(n)[:, 0:w], ACT.Relu).then_inc(ix_relu, 1)
                split_ahead_act(act, t)
                consume_wait(act, t)
                a.go(nc.scalar.activation(arena[:, dQ + t.j if t.j < 8 else t.j - 8, :], gp[:, t.bank, :],
                                          ACT.Sigmoid if t.j >= 8 + dCG else ACT.Copy))
                a.tell(drained[t.bank], in3_ready)
            copy_act(act, a, "v3", arena_tiles(dV))
            for i in range(8):
                nc.scalar.activation(hsq(i), arena[:, dQ + i, :], ACT.Square).then_inc(sq_ready, 1)
            act.wait_ge(hd_sum, 1)
            nc.scalar.activation(HROOT, gp[0:NHT, 0, :], ACT.Sqrt, scale=1.0 / HD,
                                 bias=const("eps")[0:NHT]).then_inc(hd_root, 1)
            attention_act(act, DSA)
            act.wait_ge(at_pv, DSA.u0 + len(dsa_units))
            for i in range(4):
                nc.scalar.activation(arena[:, dAT + i, :], aux[:, i, :], ACT.Copy).then_inc(dsa_out, 1)
            mean_act(act, 512)
            act.wait_ge(ln_c, 2)
            norm_act(act, a, 4, arena_tiles(dCV), arena_tiles(46), lambda k: None, 1.0 / 512)
            for k in range(4):
                act.wait_ge(cl_ready, k + 1)
                a(nc.scalar.activation(arena[:, dCV + k, :], arena[:, dCV + k, :], ACT.Silu))
            norm_act(act, a, 4, arena_tiles(dCV), arena_tiles(46), lambda k: None, 1.0 / 512)
            act.wait_ge(cn_ready, 4)
            norm_act(act, a, 4, arena_tiles(dAT), arena_tiles(46), lambda k: act.wait_ge(dsa_out, k + 1), 1.0 / 512)
            pre_norm_act(act, a)
            split_first_act(act, "ff1a_3")
            for i in range(2):
                ffn2_relu_act(act, a, 3, i)
                split_stage_act(act, a, f"ff2{'ab'[i]}_3")

        def modulated_norm_dve(dve, v, gain, shift, high, low):
            n_dve.sums += 1
            dve.wait_ge(stat_ready, n_dve.sums)
            v(nc.vector.reciprocal(root[:], root[:]))

            def make(k):
                v(nc.vector.scalar_tensor_tensor(out=H[:, k, :], in0=X[:, k, :], scalar=pcol(gain, k), in1=root[:],
                                                 op0=ALU.mult, op1=ALU.mult))
                return nc.vector.tensor_scalar(H[:, k, :], H[:, k, :], MOD(shift, k), None, ALU.add)

            split_h_dve(dve, v, high, low, make)

        def gated_residual_dve(dve, v, name, gate, body=8):
            for t in loop_tiles(dve, STAGE[name], v, body):
                consume_wait(dve, t)
                x = X[:, t.idx, :]
                v.go(nc.vector.scalar_tensor_tensor(out=x, in0=gp[:, t.bank, :], scalar=MOD(gate, t.idx), in1=x,
                                                    op0=ALU.mult, op1=ALU.add))
                v.tell(drained[t.bank], x_ready)
            n_dve.x += DT

        def three_dve(dve, v):
            mod = par[:, POFF["b_ada3"]:POFF["b_ada3"] + MODS]
            for gain, j in (("g_norm13", 1), ("g_norm23", 4)):
                g = par[:, POFF[gain]:POFF[gain] + DT]
                v(nc.vector.scalar_tensor_tensor(out=g, in0=mod[:, j * DT:(j + 1) * DT], scalar=1.0, in1=g,
                                                 op0=ALU.add, op1=ALU.mult))
            modulated_norm_dve(dve, v, "g_norm13", 0, tiles_of(H3_high), tiles_of(H3_low))
            def rotate(n):
                x, tmp = arena[:, ROTATED[n], :], arena[:, 48, :]
                dve.wait_ge(ro_psum, n + 1)
                v.go(nc.vector.tensor_tensor(tmp, ro_bank(n), ROTS, ALU.mult))
                v(nc.vector.tensor_tensor(x, x, ROTC, ALU.mult))
                v.go(nc.vector.tensor_tensor(x, x, tmp, ALU.add))
                v.tell(ro_ready)

            dve.wait_ge(rot_in, 64)
            for n in range(5):
                rotate(n)
            dve.wait_ge(iw_ready, 4)
            n = 0
            for qb in range(1, 4):
                w = (qb + 1) * P
                sc, wk = SCORE[:, 0:w], WORK[:, 0:w]
                for h in range(AH):
                    iw = IW[:, qb * AH + h:qb * AH + h + 1]
                    dve.wait_ge(ix_relu, n + 1)
                    if h == 0:
                        v(nc.vector.tensor_scalar(sc, REL(n)[:, 0:w], iw, None, ALU.mult))
                    else:
                        v(nc.vector.scalar_tensor_tensor(out=sc, in0=REL(n)[:, 0:w], scalar=iw, in1=sc,
                                                         op0=ALU.mult, op1=ALU.add))
                    dve.sem_inc(ix_used, 1)
                    n += 1
                last = SCORE[:, w - 64:w]
                v(nc.vector.tensor_tensor(last, last, const("chunked"), ALU.add))
                v(nc.vector.max(out=TOP8, in_=sc))
                for k in range(TOPK // 8 - 1):
                    v(nc.vector.match_replace(out=wk, in_to_replace=TOP8, in_values=sc if k == 0 else wk,
                                              imm_value=-3e38))
                    v(nc.vector.max(out=TOP8, in_=wk))
                thr = TOP8[:, 7:8]
                sel = SELM(qb)
                v(nc.vector.tensor_scalar(sel, sc, thr, None, ALU.is_gt))
                v(nc.vector.tensor_reduce(CNT, sel, AX.X, ALU.add))
                v(nc.vector.tensor_scalar(CNT, CNT, -1.0, float(TOPK), ALU.mult, ALU.add))
                v(nc.vector.tensor_scalar(sc, sc, thr, None, ALU.is_equal))
                v(nc.vector.tensor_tensor_scan(wk, sc, sc, 0.0, ALU.add, ALU.max))
                v(nc.vector.tensor_scalar(wk, wk, CNT, None, ALU.is_le))
                v(nc.vector.tensor_tensor(wk, wk, sc, ALU.mult))
                v(nc.vector.tensor_tensor(sel, sel, wk, ALU.add))
                v(nc.vector.tensor_scalar(sel, sel, -NEG, NEG, ALU.mult, ALU.add))
                v.tell(sel_ready)
            v(nc.vector.memset(PAD[:, 0:CONVK - 1], 0.0))

            def convolve(i, steps, t0=0):
                y = arena[:, dCV + i, t0:]
                dve.wait_ge(in3_ready, 5 + 8 + dCG + i + 1)
                for step in steps:
                    if step == 0:
                        v(nc.vector.tensor_tensor(PAD[:, CONVK - 1:], arena[:, dCA + i, :], arena[:, dCG + i, :], ALU.mult))
                    elif step == 1:
                        v(nc.vector.tensor_scalar(y, PAD[:, CONVK - 1 + t0:], tap(i, CONVK - 1), pcol("b_dw3", i), ALU.mult,
                                                  ALU.add))
                    else:
                        v(nc.vector.scalar_tensor_tensor(out=y, in0=PAD[:, step - 2 + t0:step - 2 + S], scalar=tap(i, step - 2),
                                                         in1=y, op0=ALU.mult, op1=ALU.add))
                if steps.stop == CONVK + 1:
                    v.tell(cv_ready)

            convolve(1, range(CONVK + 1))
            dve.wait_ge(hd_root, 1)
            v.go(nc.vector.reciprocal(HROOT, HROOT))
            v.tell(hd_root)
            for i in range(8):
                dve.wait_ge(hd_sum, i + 2)
                x = arena[:, dQ + i, :]
                nc.vector.scalar_tensor_tensor(out=x, in0=x, scalar=pcol("g_q3" if i < 4 else "g_k3"), in1=hback(i),
                                               op0=ALU.mult, op1=ALU.mult).then_inc(hd_normed, 1)
            dve.wait_ge(hd_normed, 8)
            for n in range(5, 13):
                rotate(n)
            attention_dve(dve, v, DSA, lambda u: convolve(2 + u // 16, range(u % 16 * 2, u % 16 * 2 + 2),
                                                                u // 16 * POOL_TOKENS))
            dve.wait_ge(cv_ready, 5)
            centre_dve(dve, v, 4, arena_tiles(dCV))
            scale_shift_dve(dve, v, 4, arena_tiles(dCV), lambda k: pcol("g_conv_ln3", k), lambda k: pcol("b_conv_ln3", k),
                            arena_tiles(dCV), cl_ready)
            norm_dve(dve, v, 4, arena_tiles(dCV), lambda k: pcol("g_out_conv3", k), arena_tiles(dCV), cn_ready)
            norm_dve(dve, v, 4, arena_tiles(dAT), lambda k: pcol("g_out_attn3", k), arena_tiles(dAT), an_ready)
            gated_residual_dve(dve, v, "out3", 2)
            modulated_norm_dve(dve, v, "g_norm23", 3, tiles_of(fH), tiles_of(fH, DT))
            for i in range(2):
                ffn2_square_dve(dve, v, 3, i)
                gated_residual_dve(dve, v, f"ff2{'ab'[i]}_3", 5)

        def store(sp):
            for k in range(DT):
                sp.wait_ge(x_ready, DT * (X_UPDATES - 1) + k + 1)
                sp.dma_start(out[k], X[:, k, :]).then_inc(out_stored, 16)
            sp.wait_ge(out_stored, 16 * DT)

        def load_slabs(sp, lo, hi, beside=None):
            w = d["weights"]

            def straight(g):
                sp.wait_ge(slab_done, g - RING + 1)
                sp.dma_start(ring[:, g % RING, :], w[g]).then_inc(landed[g % RING], 16)
                if beside:
                    beside(sp, g - lo)

            for g in range(lo, lo + RING if beside else lo):
                straight(g)
            first = lo + RING if beside else lo
            full = (hi - first) // RING
            groups = w[first:first + full * RING].rearrange("(n s) p c -> n s p c", s=RING)
            with sp.Fori(0, full) as it:
                for j in range(RING):
                    slot = (first + j) % RING
                    sp.wait_ge(slab_done, it * RING + (first + j - RING + 1))
                    sp.dma_start(ring[:, slot, :], groups[it, j]).then_inc(landed[slot], 16)
                    if beside:
                        beside(sp, RING + j, it, RING)
            for g in range(first + full * RING, hi):
                straight(g)

        PH = [
            (hyena_pe, hyena_act, hyena_dve, None, ()),
            (ffn1_pe, ffn1_act, ffn1_dve, ffn1_pool, (0,)),
            (rwkv_pe, rwkv_act, rwkv_dve, rwkv_pool, ()),
            (ffn1_pe, ffn1_act, ffn1_dve, ffn1_pool, (1,)),
            (final1_pe, final1_act, final1_dve, None, ()),
            (two_pe, two_act, two_dve, two_pool, ()),
            (three_pe, three_act, three_dve, three_pool, ()),
        ]
        X_UPDATES = 1 + 1 + 1 + 1 + 1 + 2 + 3
        block = ctx.enter_context(nc.Block())

        @block.sync
        def _(sp):
            sp.dma_start(par[:], d["par"]).then_inc(inputs_in, 16)
            sp.dma_start(cst[:], d["cst"]).then_inc(inputs_in, 16)
            sp.dma_start(X[:], d["x"]).then_inc(inputs_in, 16)
            w = d["weights"]
            for s in range(RING):
                sp.dma_start(ring[:, s, :], w[s]).then_inc(landed[s], 16)
            load_slabs(sp, RING, HOLD)
            sp.wait_ge(rw_yst, DT)
            load_slabs(sp, HOLD, ADA0)
            sp.wait_ge(h_ready, 4 * DT)
            sp.dma_start(ADA_C, d["c"].partition_broadcast(P)).then_inc(ada_c, 16)
            load_slabs(sp, ADA0, ADA0 + MODS, ada_load)
            load_slabs(sp, ADA0 + MODS, NSLAB)

        @block.gpsimd
        def _(pool):
            pool.dma_start(f_z, d["hy_z"]).then_inc(f_in, 16)
            pool.dma_start(f_w[0:HY_EMB, 0:HY_W], d["hy_f_w1"]).then_inc(f_in, 16)
            pool.dma_start(f_w[:, HY_W:3 * HY_W], d["hy_f_w23"]).then_inc(f_in, 16)
            pool.dma_start(f_w4, d["hy_f_w4"]).then_inc(f_in, 16)
            pool.dma_start(f_delta, d["hy_delta"]).then_inc(f_in, 16)
            g = Steps(pool, sem("pool_steps"))
            for _, _, _, f, args in PH:
                if f:
                    f(pool, g, *args)

        @block.tensor
        def _(pe):
            for f, _, _, _, args in PH:
                f(pe, *args)

        @block.scalar
        def _(act):
            a = Steps(act, sem("act_steps"))
            act.wait_ge(inputs_in, INPUTS)
            for _, f, _, _, args in PH:
                f(act, a, *args)

        @block.vector
        def _(dve):
            v = Steps(dve, sem("dve_steps"))
            for _, _, f, _, args in PH:
                f(dve, v, *args)

        @block.sync
        def _(sp):
            store(sp)


def vec(a):
    return np.asarray(a).reshape(-1, P).T


def col64(a):
    a = np.asarray(a).reshape(-1, 64)
    return np.concatenate([a, np.zeros_like(a)], axis=1).T


def tall(w):
    k, n = w.shape
    pad = (-n) % P
    if pad:
        w = np.concatenate([w, np.zeros((k, pad), w.dtype)], axis=1)
    return w.reshape(DT, P, -1, P).transpose(2, 1, 0, 3).reshape(-1, P, SLAB)


def deep(w):
    k = w.shape[0] // P
    groups = -(-k // DT)
    w = np.concatenate([w, np.zeros(((groups * DT - k) * P, w.shape[1]), w.dtype)])
    return w.reshape(groups, DT, P, -1, P).transpose(3, 0, 2, 1, 4).reshape(-1, P, SLAB)


def pairs(a):
    return np.stack([a[..., :F1].reshape(a.shape[:-1] + (F1T, P)), a[..., F1:].reshape(a.shape[:-1] + (F1T, P))],
                    axis=-2).reshape(a.shape)


def dft_tables():
    n = 2 * S
    tok = np.arange(S)
    f = np.arange(S)
    ang = 2 * np.pi * ((f[:, None] * tok[None, :]) % n) / n
    re, im = np.cos(ang), -np.sin(ang)
    im[0] = np.cos(np.pi * tok)
    fw = np.stack([re.reshape(4, P, 4, P), im.reshape(4, P, 4, P)], axis=2)
    fw = fw.transpose(0, 4, 3, 2, 1).reshape(4, P, SLAB)
    cr = 2 * re / n
    cr[0] = 1 / n
    ci = 2 * im / n
    ci[0] = im[0] / n
    inv = np.stack([cr.reshape(2, 2, P, S), ci.reshape(2, 2, P, S)])
    inv = inv.transpose(0, 1, 3, 2, 4).reshape(4, P, SLAB)
    return fw.astype(np.float32), inv.astype(np.float32)


def constants():
    c = np.zeros((P, NCST), np.float32)

    def put(name, a):
        a = np.asarray(a, np.float32)
        c[:a.shape[0], COFF[name]:COFF[name] + a.shape[1]] = a

    p = np.arange(P)
    put("ident", np.eye(P))
    put("ones", np.ones((P, P)))
    put("bones", (p[:, None] // HD == p[None, :] // HD))
    s, t = p[:, None] % CH, np.arange(CH)[None, :]
    put("eye64", s == t)
    put("strict", np.concatenate([s < t, s > t], axis=1))
    put("incl", np.concatenate([s <= t, s >= t], axis=1))
    merge = [(s >> (i + 1) == t >> (i + 1)) & (s >> i != t >> i) for i in range(LEVELS)]
    put("level", np.concatenate([merge[0] & (s < t)] + merge[1:] + [merge[0] & (s > t)], axis=1))
    put("causal", np.where(p[None, :] <= p[:, None], 0.0, NEG))
    put("chunked", np.tile(np.where(p[:, None] < 64, NEG, 0.0), (1, 64)))
    half = ROPE // 2
    m = np.zeros((P, QKD))
    for i in range(half):
        m[NOPE + half + i, NOPE + i] = 1
        m[NOPE + i, NOPE + half + i] = 1
    put("perm_mla", m)
    m = np.zeros((P, P))
    for h in range(2):
        for i in range(8):
            m[h * 64 + 8 + i, h * 64 + i] = 1
            m[h * 64 + i, h * 64 + 8 + i] = 1
    put("perm_dsa", m)
    put("eps", np.full((P, 1), EPS))
    put("gn_eps", np.full((P, 1), HD * 1e-5))
    inv = 10000.0 ** (-np.arange(0, ROPE, 2, dtype=np.float32) / ROPE)
    col = np.zeros((P, 1))
    col[NOPE:NOPE + ROPE, 0] = np.concatenate([inv, inv])
    put("invf", col)
    sg = np.zeros((P, 1))
    sg[NOPE:NOPE + half], sg[NOPE + half:NOPE + ROPE] = -1, 1
    put("rsign", sg)
    put("ntime", -(np.arange(S).reshape(4, P).T / (S - 1)))
    return c


def filter_constants():
    bands = (HY_EMB - 1) // 2
    n = np.arange(S, dtype=np.float32)
    fr = np.linspace(1e-4, bands - 1, bands, dtype=np.float32)
    ang = np.float32(2 * np.pi / S) * n[:, None] * fr[None, :]
    z = np.concatenate([(n / np.float32(S - 1))[:, None], np.cos(ang), -np.sin(ang)], axis=-1)
    deltas = np.abs(np.linspace(np.log(1e-2) / 1.5, np.log(1e-2) / 0.3, D, dtype=np.float32))
    return np.ascontiguousarray(z.T.astype(np.float32)), np.ascontiguousarray(np.tile(deltas, (P, 1)))


def ffn_halves(b, up, down):
    down = down.reshape(DT, 4, P, SLAB)
    return {f"ff1a_{b}": up[:F2T // 2], f"ff1b_{b}": up[F2T // 2:],
            f"ff2a_{b}": down[:, :2].reshape(16, P, SLAB), f"ff2b_{b}": down[:, 2:].reshape(16, P, SLAB)}


def weight_stream(a):
    fw, inv = dft_tables()
    z = np.zeros
    f32 = np.float32
    w_in = a["hy_w_in"][0]
    parts = {
        "hy_in": tall(np.concatenate([w_in[:, D:2 * D], w_in[:, 2 * D:], w_in[:, :D]], axis=1)),
        "hy_dft": fw, "hy_idft": inv, "hy_out": tall(a["hy_w_out"][0]),
    }
    for i in range(2):
        parts[f"up{i}"] = tall(pairs(a["ff_w_up"][i]))
        parts[f"down{i}"] = deep(a["ff_w_down"][i])
    w1 = a["rw_w1"][0]
    lora1 = [np.concatenate([w1[0], w1[1]], axis=1), np.concatenate([a["rw_a1"][0], z((D, 64), f32)], axis=1),
             a["rw_g1"][0]]
    parts.update({
        "rw_lora1": tall(np.concatenate(lora1, axis=1)),
        "rw_r": tall(a["rw_w_r"][0]), "rw_k": tall(a["rw_w_k"][0]), "rw_v": tall(a["rw_w_v"][0]),
        "rw_a2": np.concatenate([a["rw_a2"][0], z((64, D), f32)])[None],
        "rw_w2": a["rw_w2"][0].reshape(1, P, D), "rw_g2": a["rw_g2"], "rw_o": tall(a["rw_w_o"][0]),
    })
    w = a["w_in_2"][0]
    rot = z((D, P), f32)
    rot[:, NOPE:QKD] = w[:, 384:416]
    br = [a[n][0].reshape(2, P, D) for n in ("w_br_mla_2", "w_br_sg_2", "w_br_conv_2", "w_br_pool_2")]
    parts.update({
        "in2": tall(np.concatenate([w[:, :384], rot, w[:, 416:1952]], axis=1)), "gate2": tall(w[:, 1952:]),
        "br2_0": br[0], "br2_1": br[1], "br2_2": br[2], "br2_3": br[3], "out2": tall(a["w_out_2"][0]),
        **ffn_halves(2, tall(a["w_ff1_2"][0]), deep(a["w_ff2_2"][0])),
    })
    w = a["w_in_3"][0]
    q, k, v, iq, ik, iw, ca, cg = np.split(w, np.cumsum([512, 512, 512, 512, 64, 8, 512]), axis=1)
    iws = z((1, P, SLAB), f32)
    iws[0, :, :DT * AH] = iw.reshape(DT, P, AH).transpose(1, 0, 2).reshape(P, DT * AH)
    parts.update({
        "iw3": iws,
        "in3a": tall(np.concatenate([iq, ik, ik], axis=1)), "in3b": tall(np.concatenate([q, k, ca, cg], axis=1)),
        "v3": v.reshape(4, 2, P, S).transpose(0, 2, 1, 3).reshape(4, P, SLAB), "out3": tall(a["w_out_3"][0]),
        **ffn_halves(3, tall(a["w_ff1_3"][0]), deep(a["w_ff2_3"][0])),
    })
    out = [parts[n] if n in parts else z((s, P, SLAB), f32) for n, _, _, s in STREAM]
    for (n, _, _, s), part in zip(STREAM, out):
        assert part.shape == (s, P, SLAB), (n, part.shape)
    return np.concatenate(out)


def parameters(a):
    order = lambda v: np.concatenate([v[..., D:2 * D], v[..., 2 * D:], v[..., :D]], axis=-1)
    p = {
        "norm_mix": vec(a["norm_mix_g"]), "norm_ffn": vec(a["norm_ffn_g"]), "final_norm": vec(a["final_norm_g"]),
        "hy_b_in": vec(order(a["hy_b_in"][0])), "hy_conv_w": vec(order(a["hy_conv_w"][0])),
        "hy_conv_b": vec(order(a["hy_conv_b"][0])), "hy_skip": vec(a["hy_skip"]), "hy_b_out": vec(a["hy_b_out"]),
        "hy_f_b": np.concatenate([col64(a["hy_f_b1"]), col64(a["hy_f_b2"]), col64(a["hy_f_b3"])], axis=1),
        "hy_f_freq": col64(a["hy_f_freq"]),
        "ff_conv_w": vec(pairs(a["ff_conv_w"])), "ff_conv_b": vec(pairs(a["ff_conv_b"])),
    }
    p.update({"rw_" + n: vec(a["rw_" + n]) for n in ("mu", "w0", "a0", "k_k", "k_a", "r_k", "ln_w", "ln_b")})
    p.update({
        "norm_mix_pre2": vec(a["norm_mix_pre_2"]), "gate_b2": vec(a["gate_b_2"]), "q_norm2": vec(a["q_norm_2"]),
        "kv_norm2": vec(a["kv_norm_2"]), "sg_ln_g2": vec(a["sg_ln_g_2"]), "sg_ln_b2": vec(a["sg_ln_b_2"]),
        "conv_w2": vec(a["conv_w_2"]), "pool_scale2": vec(a["pool_scale_2"]),
        "norm_mix_post2": vec(a["norm_mix_post_2"]), "norm_ffn_pre2": vec(a["norm_ffn_pre_2"]),
        "norm_ffn_post2": vec(a["norm_ffn_post_2"]),
    })
    two = lambda g: vec(np.concatenate([g[0], g[0]]))
    p.update({
        "b_ada3": vec(a["b_ada_3"]), "g_norm13": vec(a["g_norm1_3"]), "g_q3": two(a["g_q_3"]),
        "g_k3": two(a["g_k_3"]), "w_dw3": a["w_dw_3"][0].reshape(CONVK, 4, P).transpose(2, 1, 0).reshape(P, -1),
        "b_dw3": vec(a["b_dw_3"]), "g_conv_ln3": vec(a["g_conv_ln_3"]), "b_conv_ln3": vec(a["b_conv_ln_3"]),
        "g_out_attn3": vec(a["g_out_attn_3"]), "g_out_conv3": vec(a["g_out_conv_3"]), "g_norm23": vec(a["g_norm2_3"]),
    })
    cols = [p[n] if n in p else np.zeros((P, w), np.float32) for n, w in PARAMS]
    for (n, w), c in zip(PARAMS, cols):
        assert c.shape == (P, w), (n, c.shape)
    return np.ascontiguousarray(np.concatenate(cols, axis=1))


def small_two(a):
    kv = a["w_ukv_2"][0].reshape(P, MLA_H, NOPE + VH)
    pw = a["pool_w_2"][0]
    return np.ascontiguousarray(np.concatenate([
        a["w_uq_2"][0].reshape(2, P, MLA_H * QKD).transpose(1, 0, 2).reshape(P, -1),
        kv[:, :, :NOPE].reshape(P, -1), kv[:, :, NOPE:].reshape(P, -1),
        a["sg_w_2"][0].transpose(2, 0, 1).reshape(P, -1),
        pw.reshape(2, 2, 64, 64).transpose(1, 2, 0, 3).reshape(P, -1),
        np.triu(np.ones((P, P), np.float32))], axis=1))


def window_counts():
    t = np.arange(S)
    c = np.stack([1.0 / np.minimum(t + 1, w) for w in POOL_WIN])
    return np.ascontiguousarray(np.repeat(c, 64, axis=0).reshape(2, P, S).transpose(1, 0, 2).astype(np.float32))


def rotation():
    inv = (500000.0 ** (-np.arange(0, 16, 2, dtype=np.float32) / 16)).astype(np.float32)
    ang = np.arange(S, dtype=np.float32)[None, :] * inv[:, None]
    c, s = np.ones((2, 64, S), np.float32), np.zeros((2, 64, S), np.float32)
    c[:, 0:8] = c[:, 8:16] = np.cos(ang)
    s[:, 0:8], s[:, 8:16] = -np.sin(ang), np.sin(ang)
    return c.reshape(P, S), s.reshape(P, S)


def head_sums():
    first, n = np.arange(P) < HD, 2 * AH
    cols = np.zeros((P, 2 * n - 2), np.float32)
    cols[:, n - 2], cols[:, n - 1] = first, ~first
    back = np.zeros((n, n // 2, P), np.float32)
    for i in range(n // 2):
        back[2 * i, i], back[2 * i + 1, i] = first, ~first
    return cols, back.reshape(n, 2, S)


def host_arrays(a):
    z, delta = filter_constants()
    x = np.ascontiguousarray(a["x"][0].T.reshape(DT, P, S).transpose(1, 0, 2))
    return {
        "x": x, "par": parameters(a), "cst": constants(), "weights": weight_stream(a),
        "hy_z": z, "hy_delta": delta, "hy_f_w1": np.ascontiguousarray(a["hy_f_w1"][0]),
        "hy_f_w23": np.ascontiguousarray(np.concatenate([a["hy_f_w2"][0], a["hy_f_w3"][0]], axis=1)),
        "hy_f_w4": np.ascontiguousarray(a["hy_f_w4"][0]),
        "sm2": small_two(a), "sg_b": np.ascontiguousarray(a["sg_b_2"][0].reshape(1, 4 * SGC)),
        "rcnt": window_counts(), "pos": np.ascontiguousarray(a["positions_2"].reshape(S).astype(np.int32)),
        "ada": np.ascontiguousarray(a["w_ada_3"][0].T.reshape(MODS, P, D)),
        "c": np.ascontiguousarray(a["c_3"].reshape(D)),
        "rotc": rotation()[0], "rots": rotation()[1],
        "hsum": head_sums()[0], "hback": head_sums()[1],
    }


def kernel(**inputs):
    import concourse.bacc as bacc
    from concourse.bass_utils import run_bass_kernel_spmd

    arrays = host_arrays({k: np.asarray(v) for k, v in inputs.items()})
    nc = bacc.Bacc("TRN2", target_bir_lowering=False, num_devices=1)
    d = {n: nc.dram_tensor(f"in_{n}", list(a.shape), mybir.dt.from_np(a.dtype), kind="ExternalInput").ap()
         for n, a in arrays.items()}
    out = nc.dram_tensor("out_x", [DT, P, S], F32, kind="ExternalOutput").ap()
    build(nc, d, out)
    r = run_bass_kernel_spmd(nc, [{f"in_{n}": a for n, a in arrays.items()}], core_ids=[0])
    y = r.results[0]["out_x"]
    return np.ascontiguousarray(y.reshape(D, S).T).reshape(1, S, D)
```
